# Optimizing a Trainium2 kernel written in Bass

```python
import jax, jax.numpy as jnp
from jax import lax
import numpy as np

D_MODEL = 1024
BATCH = 1
SEQ = 1024
DEPTH = 1

D_MIX = D_MODEL
GROUP_W = D_MIX // 4
GRID_W = 64
NA_HEADS = 8
NA_HEAD_DIM = GROUP_W // NA_HEADS
NA_ROWS = 8
NA_COLS = 16
CONV_WIDTH = 31
POOL_WINDOWS = (2, 4, 8, 16)
POOL_GROUPS = len(POOL_WINDOWS)
POOL_GROUP_W = GROUP_W // POOL_GROUPS
SGU_HEADS = 4
SGU_HEAD_DIM = GROUP_W // SGU_HEADS
SGU_CHUNK = 128
D_IN = 8 * GROUP_W + D_MIX
RMS_EPS = 1e-6
LN_EPS = 1e-5


def rmsnorm(x, g):
    xf = x.astype(jnp.float32)
    y = xf * lax.rsqrt(jnp.mean(xf * xf, axis=-1, keepdims=True) + RMS_EPS)
    return (y * g.astype(jnp.float32)).astype(x.dtype)

def layernorm(x, g, b):
    xf = x.astype(jnp.float32)
    mu = jnp.mean(xf, axis=-1, keepdims=True)
    var = jnp.mean(jnp.square(xf - mu), axis=-1, keepdims=True)
    y = (xf - mu) * lax.rsqrt(var + LN_EPS)
    return (y * g.astype(jnp.float32) + b.astype(jnp.float32)).astype(x.dtype)

def neighborhood_attention(q, k, v, rpb):
    B, S, _ = q.shape
    rows = S // GRID_W
    kh = min(NA_ROWS, rows)
    kw = NA_COLS
    H, dh = NA_HEADS, NA_HEAD_DIM
    r = jnp.arange(rows)
    row_start = jnp.clip(r - kh // 2, 0, rows - kh)
    row_idx = row_start[:, None] + jnp.arange(kh)[None, :]
    c = jnp.arange(GRID_W)
    col_start = jnp.clip(c - kw // 2, 0, GRID_W - kw)
    col_ok = (c[None, :] >= col_start[:, None]) & (c[None, :] < col_start[:, None] + kw)
    qg = q.reshape(B, rows, GRID_W, H, dh)
    kband = jnp.take(k.reshape(B, rows, GRID_W, H, dh), row_idx, axis=1)
    vband = jnp.take(v.reshape(B, rows, GRID_W, H, dh), row_idx, axis=1)
    s = jnp.einsum('brqhd,brjkhd->bhrqjk', qg, kband).astype(jnp.float32) * (dh ** -0.5)
    dr = row_idx - r[:, None]
    dc = jnp.clip(c[None, :] - c[:, None], -(kw - 1), kw - 1)
    idx_r = (dr + NA_ROWS - 1)[:, None, :, None]
    idx_c = (dc + NA_COLS - 1)[None, :, None, :]
    bias = rpb[:, idx_r, idx_c].astype(jnp.float32)
    s = jnp.where(col_ok[None, None, None, :, None, :], s + bias[None], -jnp.inf)
    p = jax.nn.softmax(s.reshape(B, H, rows, GRID_W, kh * GRID_W), axis=-1)
    p = p.reshape(B, H, rows, GRID_W, kh, GRID_W).astype(v.dtype)
    out = jnp.einsum('bhrqjk,brjkhd->brqhd', p, vband)
    return out.reshape(B, S, H * dh)

def conformer_conv(a, b, dw_w, dw_b, ln_g, ln_b, pw):
    h = a * jax.nn.sigmoid(b)
    h = lax.conv_general_dilated(h, dw_w[:, None, :], window_strides=(1,),
                                 padding=[(CONV_WIDTH // 2, CONV_WIDTH // 2)],
                                 dimension_numbers=('NWC', 'WIO', 'NWC'),
                                 feature_group_count=h.shape[-1]) + dw_b
    h = jax.nn.silu(layernorm(h, ln_g, ln_b))
    return h @ pw

def multiscale_pool(xc, pool_w, pool_scale):
    B, S, _ = xc.shape
    xg = xc.reshape(B, S, POOL_GROUPS, POOL_GROUP_W).astype(jnp.float32)
    csum = jnp.concatenate([jnp.zeros((B, 1, POOL_GROUPS, POOL_GROUP_W), jnp.float32),
                            jnp.cumsum(xg, axis=1)], axis=1)
    t = jnp.arange(S)[:, None]
    w = jnp.array(POOL_WINDOWS, dtype=jnp.int32)[None, :]
    lo = jnp.clip(t - w // 2, 0, S)
    hi = jnp.clip(t - w // 2 + w, 0, S)
    g_idx = jnp.arange(POOL_GROUPS)[None, :]
    win_sum = csum[:, hi, g_idx] - csum[:, lo, g_idx]
    count = (hi - lo).astype(jnp.float32)[None, :, :, None]
    pooled = (win_sum / count - xg).astype(xc.dtype)
    y = jnp.einsum('bsgc,gcd->bsgd', pooled, pool_w).reshape(B, S, GROUP_W)
    return y * pool_scale

def spatial_gating(u, v, ln_g, ln_b, ws, bs):
    B, S, _ = u.shape
    v = layernorm(v, ln_g, ln_b)
    vc = v.reshape(B, S // SGU_CHUNK, SGU_CHUNK, SGU_HEADS, SGU_HEAD_DIM)
    mixed = jnp.einsum('hpq,bnqhd->bnphd', ws, vc) + bs.T[None, None, :, :, None]
    return u * mixed.reshape(B, S, GROUP_W)

def first_inputs(seed: int = 0) -> dict:
    key = jax.random.key(seed)
    ks = jax.random.split(key, 20)
    f32 = jnp.float32
    nrm = lambda k, shape, s: jax.random.normal(k, shape, f32) * s
    return {
        "x": nrm(ks[0], (BATCH, SEQ, D_MODEL), 1.0),
        "norm_g": 1.0 + nrm(ks[1], (DEPTH, D_MODEL), 0.02),
        "w_in": nrm(ks[2], (DEPTH, D_MODEL, D_IN), D_MODEL ** -0.5),
        "na_rpb": nrm(ks[3], (DEPTH, NA_HEADS, 2 * NA_ROWS - 1, 2 * NA_COLS - 1), 0.1),
        "conv_dw_w": nrm(ks[4], (DEPTH, CONV_WIDTH, GROUP_W), CONV_WIDTH ** -0.5),
        "conv_dw_b": nrm(ks[5], (DEPTH, GROUP_W), 0.02),
        "conv_ln_g": 1.0 + nrm(ks[6], (DEPTH, GROUP_W), 0.02),
        "conv_ln_b": nrm(ks[7], (DEPTH, GROUP_W), 0.02),
        "conv_pw": nrm(ks[8], (DEPTH, GROUP_W, GROUP_W), GROUP_W ** -0.5),
        "pool_w": nrm(ks[9], (DEPTH, POOL_GROUPS, POOL_GROUP_W, POOL_GROUP_W), POOL_GROUP_W ** -0.5),
        "pool_scale": 1.0 + nrm(ks[10], (DEPTH, GROUP_W), 0.02),
        "sgu_ln_g": 1.0 + nrm(ks[11], (DEPTH, GROUP_W), 0.02),
        "sgu_ln_b": nrm(ks[12], (DEPTH, GROUP_W), 0.02),
        "sgu_w": nrm(ks[13], (DEPTH, SGU_HEADS, SGU_CHUNK, SGU_CHUNK), SGU_CHUNK ** -0.5),
        "sgu_b": 1.0 + nrm(ks[14], (DEPTH, SGU_HEADS, SGU_CHUNK), 0.02),
        "w_out": nrm(ks[15], (DEPTH, D_MIX, D_MODEL), D_MIX ** -0.5),
        "final_g": 1.0 + nrm(ks[16], (D_MODEL,), 0.02),
    }

def first_block(x, norm_g, w_in, na_rpb, conv_dw_w, conv_dw_b, conv_ln_g, conv_ln_b, conv_pw,
              pool_w, pool_scale, sgu_ln_g, sgu_ln_b, sgu_w, sgu_b, w_out, final_g):
    split_at = [GROUP_W * i for i in range(1, 9)]
    for l in range(DEPTH):
        h = rmsnorm(x, norm_g[l])
        z = h @ w_in[l]
        qa, ka, va, glu_a, glu_b, pool_in, sgu_u, sgu_v, gates = jnp.split(z, split_at, axis=-1)
        y_a = neighborhood_attention(qa, ka, va, na_rpb[l])
        y_b = conformer_conv(glu_a, glu_b, conv_dw_w[l], conv_dw_b[l], conv_ln_g[l], conv_ln_b[l], conv_pw[l])
        y_c = multiscale_pool(pool_in, pool_w[l], pool_scale[l])
        y_d = spatial_gating(jax.nn.gelu(sgu_u), jax.nn.gelu(sgu_v), sgu_ln_g[l], sgu_ln_b[l], sgu_w[l], sgu_b[l])
        y = jnp.concatenate([y_a, y_b, y_c, y_d], axis=-1) * jax.nn.silu(gates)
        x = x + y @ w_out[l]
    return rmsnorm(x, final_g)


_first_inputs = first_inputs


def first_inputs(seed=0):
    import zlib

    import numpy as np

    out = dict(_first_inputs(seed))
    spreads = {}
    factors = {'norm_g': 4.372,
     'na_rpb': 30.6,
     'conv_dw_b': 57.344,
     'conv_ln_g': 64.0,
     'conv_ln_b': 64.0,
     'pool_scale': 33.088,
     'sgu_ln_g': 45.603,
     'sgu_ln_b': 45.772,
     'sgu_b': 48.425,
     'final_g': 8.184}
    for name, (base, spread) in spreads.items():
        noise = np.random.default_rng([zlib.crc32(name.encode()), seed]).standard_normal(out[name].shape)
        drawn = base * np.exp(spread * noise) if base else spread * noise
        out[name] = __import__('jax').numpy.asarray(drawn.astype(out[name].dtype))
    for name, factor in factors.items():
        out[name] = (out[name] * factor).astype(out[name].dtype)
    return out


_narrow_inputs = first_inputs


def first_inputs(seed=0):

    out = dict(_narrow_inputs(seed))
    wider = {'na_rpb': 7.72,
     'conv_ln_g': 12.0,
     'conv_ln_b': 12.0,
     'pool_scale': 5.72,
     'sgu_ln_g': 5.89,
     'sgu_ln_b': 5.87,
     'sgu_b': 5.92,
     'final_g': 3.22}
    for name, times in wider.items():
        mean = out[name].mean()
        out[name] = (mean + times * (out[name] - mean)).astype(out[name].dtype)
    return out


N_META = 16
EPS = 1e-6
ATT_HEADS = 8
ATT_KV_HEADS = 2
ATT_GROUP = ATT_HEADS // ATT_KV_HEADS
HEAD_DIM = 64
WINDOW = 128
ATT_BLOCK = 128
ROPE_THETA = 10000.0
GLA_HEADS = 4
GLA_DK = 256
GLA_DV = 512
GLA_DK_HEAD = GLA_DK // GLA_HEADS
GLA_DV_HEAD = GLA_DV // GLA_HEADS
GLA_RANK = 16
GLA_TAU = 16.0
GLA_CHUNK = 16
D_FF = 2816
CONV_WIDTH_2 = 3

ATT_Q = ATT_HEADS * HEAD_DIM
ATT_KV = ATT_KV_HEADS * HEAD_DIM
SPLIT_SIZES = (ATT_Q, ATT_KV, ATT_KV, GLA_DK, GLA_DK, GLA_DV, GLA_DV, GLA_RANK, D_MODEL, D_MODEL)
SPLIT_POINTS = tuple(int(s) for s in np.cumsum(SPLIT_SIZES)[:-1])
D_IN_2 = int(sum(SPLIT_SIZES))


def rmsnorm_2(x, g):
    xf = x.astype(jnp.float32)
    y = xf * lax.rsqrt(jnp.mean(xf * xf, axis=-1, keepdims=True) + EPS) * g.astype(jnp.float32)
    return y.astype(x.dtype)

def rope(x, pos):
    half = x.shape[-1] // 2
    inv_freq = ROPE_THETA ** (-jnp.arange(half, dtype=jnp.float32) / half)
    ang = pos.astype(jnp.float32)[:, None] * inv_freq[None, :]
    cos = jnp.concatenate([jnp.cos(ang), jnp.cos(ang)], -1)[None, :, None, :]
    sin = jnp.concatenate([jnp.sin(ang), jnp.sin(ang)], -1)[None, :, None, :]
    xf = x.astype(jnp.float32)
    rot = jnp.concatenate([-xf[..., half:], xf[..., :half]], -1)
    return (xf * cos + rot * sin).astype(x.dtype)

def swa_attention(q, k, v, sinks):
    B, L = q.shape[:2]
    pad = (-L) % ATT_BLOCK
    T = L + pad
    NB = T // ATT_BLOCK
    padf = lambda t: jnp.pad(t, ((0, 0), (pad, 0), (0, 0), (0, 0)))
    qb = padf(q).reshape(B, NB, ATT_BLOCK, ATT_KV_HEADS, ATT_GROUP, HEAD_DIM)
    kb = padf(k).reshape(B, NB, ATT_BLOCK, ATT_KV_HEADS, HEAD_DIM)
    vb = padf(v).reshape(B, NB, ATT_BLOCK, ATT_KV_HEADS, HEAD_DIM)
    prev = lambda t: jnp.concatenate([jnp.zeros_like(t[:, :1]), t[:, :-1]], axis=1)
    kk = jnp.concatenate([prev(kb), kb], axis=2)
    vv = jnp.concatenate([prev(vb), vb], axis=2)
    s = jnp.einsum('bnqkgd,bnskd->bnkgqs', qb, kk,
                   preferred_element_type=jnp.float32) * (HEAD_DIM ** -0.5)
    pos = jnp.arange(T) - pad
    qpos = pos.reshape(NB, ATT_BLOCK)
    kpos = jnp.concatenate([qpos - ATT_BLOCK, qpos], axis=1)
    rel = qpos[:, :, None] - kpos[:, None, :]
    valid = (rel >= 0) & (rel < WINDOW) & (kpos[:, None, :] >= 0)
    s = jnp.where(valid[None, :, None, None], s, -jnp.inf)
    sink = sinks.astype(jnp.float32).reshape(ATT_KV_HEADS, ATT_GROUP)[None, None, :, :, None, None]
    sink = jnp.broadcast_to(sink, s.shape[:-1] + (1,))
    p = jax.nn.softmax(jnp.concatenate([s, sink], axis=-1), axis=-1)[..., :-1]
    o = jnp.einsum('bnkgqs,bnskd->bnqkgd', p.astype(v.dtype), vv)
    return o.reshape(B, T, ATT_Q)[:, pad:]

def gla(q, k, v, log_a):
    B, L, H, Dk = q.shape
    Dv = v.shape[-1]
    C = GLA_CHUNK
    N = L // C
    to_chunks = lambda t: t.astype(jnp.float32).reshape(B, N, C, H, t.shape[-1]).transpose(1, 0, 3, 2, 4)
    qc, kc, vc, gc = (to_chunks(t) for t in (q * (Dk ** -0.5), k, v, log_a))
    causal = jnp.tril(jnp.ones((C, C), dtype=bool))[:, :, None]

    def step(S, inp):
        qi, ki, vi, gi = inp
        b = jnp.cumsum(gi, axis=2)
        o_inter = jnp.einsum('bhcd,bhde->bhce', qi * jnp.exp(b), S)
        diff = b[:, :, :, None, :] - b[:, :, None, :, :]
        decay = jnp.exp(jnp.where(causal, diff, -jnp.inf))
        a = jnp.einsum('bhid,bhjd,bhijd->bhij', qi, ki, decay)
        o = o_inter + jnp.einsum('bhij,bhje->bhie', a, vi)
        b_last = b[:, :, -1:, :]
        S = jnp.exp(b_last[:, :, 0, :])[..., None] * S + \
            jnp.einsum('bhcd,bhce->bhde', ki * jnp.exp(b_last - b), vi)
        return S, o

    S0 = jnp.zeros((B, H, Dk, Dv), jnp.float32)
    _, o = lax.scan(step, S0, (qc, kc, vc, gc))
    return o.transpose(1, 0, 3, 2, 4).reshape(B, L, H, Dv).astype(v.dtype)

def causal_dwconv(a, w, b):
    y = lax.conv_general_dilated(a, w[:, None, :].astype(a.dtype), window_strides=(1,),
                                 padding=[(CONV_WIDTH_2 - 1, 0)],
                                 dimension_numbers=('NWC', 'WIO', 'NWC'),
                                 feature_group_count=a.shape[-1])
    return y + b.astype(a.dtype)

def second_inputs(seed: int = 0) -> dict:
    key = jax.random.key(seed)
    ks = jax.random.split(key, 20)
    nrm = lambda k, shape, scale: jax.random.normal(k, shape, jnp.float32) * scale
    gain = lambda k, shape: 1.0 + 0.01 * jax.random.normal(k, shape, jnp.float32)
    return {
        "x": nrm(ks[0], (BATCH, SEQ, D_MODEL), 1.0),
        "meta_tokens": nrm(ks[1], (N_META, D_MODEL), 1.0),
        "mix_norm": gain(ks[2], (DEPTH, D_MODEL)),
        "w_in": nrm(ks[3], (DEPTH, D_MODEL, D_IN_2), D_MODEL ** -0.5),
        "b_in": nrm(ks[4], (DEPTH, D_IN_2), 0.01),
        "w_alpha": nrm(ks[5], (DEPTH, GLA_RANK, GLA_DK), GLA_RANK ** -0.5),
        "b_alpha": nrm(ks[6], (DEPTH, GLA_DK), 0.1),
        "attn_sinks": nrm(ks[7], (DEPTH, ATT_HEADS), 0.5),
        "gla_head_norm": gain(ks[8], (DEPTH, GLA_DV_HEAD)),
        "w_proj_attn": nrm(ks[9], (DEPTH, ATT_Q, D_MODEL), ATT_Q ** -0.5),
        "w_proj_gla": nrm(ks[10], (DEPTH, GLA_DV, D_MODEL), GLA_DV ** -0.5),
        "w_out": nrm(ks[11], (DEPTH, D_MODEL, D_MODEL), D_MODEL ** -0.5),
        "ffn_norm": gain(ks[12], (DEPTH, D_MODEL)),
        "w_up": nrm(ks[13], (DEPTH, D_MODEL, 2 * D_FF), D_MODEL ** -0.5),
        "conv_w": nrm(ks[14], (DEPTH, CONV_WIDTH_2, D_FF), CONV_WIDTH_2 ** -0.5),
        "conv_b": nrm(ks[15], (DEPTH, D_FF), 0.01),
        "w_down": nrm(ks[16], (DEPTH, D_FF, D_MODEL), D_FF ** -0.5),
        "final_norm": gain(ks[17], (D_MODEL,)),
    }

def second_block(x, meta_tokens, mix_norm, w_in, b_in, w_alpha, b_alpha, attn_sinks, gla_head_norm,
              w_proj_attn, w_proj_gla, w_out, ffn_norm, w_up, conv_w, conv_b, w_down, final_norm):
    B = x.shape[0]
    meta = jnp.broadcast_to(meta_tokens.astype(x.dtype)[None], (B, N_META, D_MODEL))
    h = jnp.concatenate([meta, x], axis=1)
    L = h.shape[1]
    pos = jnp.arange(L)
    for l in range(DEPTH):
        u = rmsnorm_2(h, mix_norm[l])
        proj = u @ w_in[l] + b_in[l]
        aq, ak, av, gq, gk, gv, gr, g_low, gate_a, gate_b = jnp.split(proj, SPLIT_POINTS, axis=-1)
        aq = rope(aq.reshape(B, L, ATT_HEADS, HEAD_DIM), pos)
        ak = rope(ak.reshape(B, L, ATT_KV_HEADS, HEAD_DIM), pos)
        av = av.reshape(B, L, ATT_KV_HEADS, HEAD_DIM)
        y_att = swa_attention(aq, ak, av, attn_sinks[l])
        z = (g_low @ w_alpha[l] + b_alpha[l]).astype(jnp.float32)
        log_a = (jax.nn.log_sigmoid(z) / GLA_TAU).reshape(B, L, GLA_HEADS, GLA_DK_HEAD)
        y_gla = gla(gq.reshape(B, L, GLA_HEADS, GLA_DK_HEAD), gk.reshape(B, L, GLA_HEADS, GLA_DK_HEAD),
                    gv.reshape(B, L, GLA_HEADS, GLA_DV_HEAD), log_a)
        y_gla = rmsnorm_2(y_gla, gla_head_norm[l]).reshape(B, L, GLA_DV) * jax.nn.silu(gr)
        mixed = jax.nn.sigmoid(gate_a) * (y_att @ w_proj_attn[l]) + \
            jax.nn.sigmoid(gate_b) * (y_gla @ w_proj_gla[l])
        h = h + mixed @ w_out[l]
        u = rmsnorm_2(h, ffn_norm[l])
        a, v = jnp.split(u @ w_up[l], 2, axis=-1)
        h = h + (jax.nn.gelu(causal_dwconv(a, conv_w[l], conv_b[l])) * v) @ w_down[l]
    return rmsnorm_2(h, final_norm)[:, N_META:]


_first_inputs_2 = second_inputs


def second_inputs(seed=0):
    import zlib

    import numpy as np

    out = dict(_first_inputs_2(seed))
    spreads = {}
    factors = {'mix_norm': 7.371,
     'b_in': 5.522,
     'b_alpha': 3.46,
     'attn_sinks': 8.0,
     'gla_head_norm': 8.0,
     'ffn_norm': 7.575,
     'conv_b': 8.0,
     'final_norm': 5.747}
    for name, (base, spread) in spreads.items():
        noise = np.random.default_rng([zlib.crc32(name.encode()), seed]).standard_normal(out[name].shape)
        drawn = base * np.exp(spread * noise) if base else spread * noise
        out[name] = __import__('jax').numpy.asarray(drawn.astype(out[name].dtype))
    for name, factor in factors.items():
        out[name] = (out[name] * factor).astype(out[name].dtype)
    return out


_narrow_inputs_2 = second_inputs


def second_inputs(seed=0):

    out = dict(_narrow_inputs_2(seed))
    wider = {'gla_head_norm': 4.82, 'ffn_norm': 5.58, 'conv_b': 7.09, 'final_norm': 6.45}
    for name, times in wider.items():
        mean = out[name].mean()
        out[name] = (mean + times * (out[name] - mean)).astype(out[name].dtype)
    return out


D_PLE = 256
RET_HEAD_DIM = 128
RET_WIDTH = D_MODEL // 2
RET_HEADS = RET_WIDTH // RET_HEAD_DIM
RET_CHUNK = 128
RWKV_HEAD_DIM = 64
RWKV_WIDTH = D_MODEL - RET_WIDTH
RWKV_HEADS = RWKV_WIDTH // RWKV_HEAD_DIM
DECAY_LORA = 64
AAA_LORA = 64
GATE_LORA = 128
D_FF_3 = ((8 * D_MODEL + 3 * 256 - 1) // (3 * 256)) * 256
RET_COLS = 4 * RET_WIDTH
RWKV_COLS = 3 * RWKV_WIDTH + DECAY_LORA + AAA_LORA + GATE_LORA
IN_COLS = RET_COLS + RWKV_COLS
NORM_EPS = 1e-6
RET_GN_EPS = 1e-5
RWKV_GN_EPS = 64e-5


def rms_norm(x, w):
    x32 = x.astype(jnp.float32)
    y = x32 * lax.rsqrt(jnp.mean(x32 * x32, axis=-1, keepdims=True) + NORM_EPS)
    return (y * w.astype(jnp.float32)).astype(x.dtype)

def head_norm(y, eps):
    mu = jnp.mean(y, axis=-1, keepdims=True)
    var = jnp.mean(jnp.square(y - mu), axis=-1, keepdims=True)
    return (y - mu) * lax.rsqrt(var + eps)

def rotate_every_two(t):
    t1 = t[..., 0::2]
    t2 = t[..., 1::2]
    return jnp.stack((-t2, t1), axis=-1).reshape(t.shape)

def retention(q, k, v):
    B, S, H, d = q.shape
    C = RET_CHUNK
    N = S // C
    pos = jnp.arange(S, dtype=jnp.float32)
    angle = 1.0 / (10000.0 ** jnp.linspace(0.0, 1.0, d // 2, dtype=jnp.float32))
    angle = jnp.repeat(angle, 2)
    phase = pos[:, None] * angle[None, :]
    sin = jnp.sin(phase)[:, None, :]
    cos = jnp.cos(phase)[:, None, :]
    q = q * cos + rotate_every_two(q) * sin
    k = (k * cos + rotate_every_two(k) * sin) * (d ** -0.5)
    log_g = jnp.log(1.0 - 2.0 ** (-5.0 - jnp.arange(H, dtype=jnp.float32)))

    def chunks(t):
        return t.reshape(B, N, C, H, t.shape[-1]).transpose(0, 3, 1, 2, 4)

    qc, kc, vc = chunks(q), chunks(k), chunks(v)
    idx = jnp.arange(C, dtype=jnp.float32)
    rel = idx[:, None] - idx[None, :]
    inner_decay = jnp.where(rel[None] >= 0,
                            jnp.exp(log_g[:, None, None] * jnp.maximum(rel, 0.0)[None]),
                            0.0)
    scores = jnp.einsum('bhncd,bhnmd->bhncm', qc, kc) * inner_decay[None, :, None]
    inner = jnp.einsum('bhncm,bhnme->bhnce', scores, vc)
    k_to_end = jnp.exp(log_g[:, None] * (C - 1 - idx)[None])
    chunk_state = jnp.einsum('bhnmd,bhnme->bhnde',
                             kc * k_to_end[None, :, None, :, None], vc)
    chunk_decay = jnp.exp(log_g * C)[None, :, None, None]

    def step(R, U):
        return R * chunk_decay + U, R

    _, R_prev = lax.scan(step, jnp.zeros((B, H, d, vc.shape[-1]), jnp.float32),
                         chunk_state.transpose(2, 0, 1, 3, 4))
    R_prev = R_prev.transpose(1, 2, 0, 3, 4)
    q_from_start = jnp.exp(log_g[:, None] * (idx + 1.0)[None])
    cross = jnp.einsum('bhncd,bhnde->bhnce', qc, R_prev) * q_from_start[None, :, None, :, None]
    return (inner + cross).transpose(0, 2, 3, 1, 4).reshape(B, S, H, vc.shape[-1])

def rwkv7_mix(h, mu, w0, w2, a0, a2, g2, k_k, k_a, r_k, ln_w, ln_b):
    B, S, _ = h.shape
    H, N, W = RWKV_HEADS, RWKV_HEAD_DIM, RWKV_WIDTH
    prev = jnp.pad(h, ((0, 0), (1, 0), (0, 0)))[:, :S]
    h = h + (prev - h) * mu
    r = h[..., :W]
    k = h[..., W:2 * W]
    v = h[..., 2 * W:3 * W]
    o = 3 * W
    wd = h[..., o:o + DECAY_LORA]
    o += DECAY_LORA
    ad = h[..., o:o + AAA_LORA]
    o += AAA_LORA
    gd = h[..., o:o + GATE_LORA]
    w_log = -jax.nn.softplus(-(w0 + jnp.tanh(wd) @ w2)) - 0.5
    decay = jnp.exp(-jnp.exp(w_log))
    a = jax.nn.sigmoid(a0 + ad @ a2)
    g = jax.nn.sigmoid(gd) @ g2

    def heads(t):
        return t.reshape(B, S, H, N)

    r, k, v, decay, a = heads(r), heads(k), heads(v), heads(decay), heads(a)
    kk = k * k_k.reshape(H, N)
    kk = kk * lax.rsqrt(jnp.maximum(jnp.sum(kk * kk, axis=-1, keepdims=True), 1e-24))
    k = k * (1.0 + (a - 1.0) * k_a.reshape(H, N))

    def step(state, inp):
        r_t, w_t, k_t, v_t, kk_t, b_t = inp
        sa = jnp.einsum('bhvk,bhk->bhv', state, -kk_t)
        state = (state * w_t[:, :, None, :] + sa[..., None] * b_t[:, :, None, :]
                 + v_t[..., None] * k_t[:, :, None, :])
        return state, jnp.einsum('bhvk,bhk->bhv', state, r_t)

    def tm(t):
        return jnp.swapaxes(t, 0, 1)

    _, y = lax.scan(step, jnp.zeros((B, H, N, N), jnp.float32),
                    (tm(r), tm(decay), tm(k), tm(v), tm(kk), tm(kk * a)))
    y = tm(y)
    y = head_norm(y, RWKV_GN_EPS).reshape(B, S, W) * ln_w + ln_b
    bonus = jnp.sum(r * k * r_k, axis=-1, keepdims=True) * v
    return (y + bonus.reshape(B, S, W)) * g

def third_inputs(seed: int = 0) -> dict:
    key = jax.random.key(seed)
    ks = jax.random.split(key, 32)
    f32 = jnp.float32

    def nrm(k, shape, scale):
        return jax.random.normal(k, shape, f32) * scale

    def gain(k, shape):
        return 1.0 + 0.02 * jax.random.normal(k, shape, f32)

    L = DEPTH
    return {
        "x": nrm(ks[0], (BATCH, SEQ, D_MODEL), 1.0),
        "p": nrm(ks[1], (DEPTH, BATCH, SEQ, D_PLE), 1.0),
        "norm_mix_w": gain(ks[2], (L, D_MODEL)),
        "w_in": nrm(ks[3], (L, D_MODEL, IN_COLS), D_MODEL ** -0.5),
        "ret_norm_w": gain(ks[4], (L, RET_WIDTH)),
        "rw_mu": jax.random.uniform(ks[5], (L, RWKV_COLS), f32, 0.0, 1.0),
        "rw_w0": jax.random.uniform(ks[6], (L, RWKV_WIDTH), f32, -6.0, 0.0),
        "rw_w2": nrm(ks[7], (L, DECAY_LORA, RWKV_WIDTH), 0.1 * DECAY_LORA ** -0.5),
        "rw_a0": nrm(ks[8], (L, RWKV_WIDTH), 0.1),
        "rw_a2": nrm(ks[9], (L, AAA_LORA, RWKV_WIDTH), 0.1 * AAA_LORA ** -0.5),
        "rw_g2": nrm(ks[10], (L, GATE_LORA, RWKV_WIDTH), GATE_LORA ** -0.5),
        "rw_k_k": 0.85 + 0.02 * jax.random.normal(ks[11], (L, RWKV_WIDTH), f32),
        "rw_k_a": gain(ks[12], (L, RWKV_WIDTH)),
        "rw_r_k": nrm(ks[13], (L, RWKV_HEADS, RWKV_HEAD_DIM), 0.1),
        "rw_ln_w": gain(ks[14], (L, RWKV_WIDTH)),
        "rw_ln_b": nrm(ks[15], (L, RWKV_WIDTH), 0.01),
        "w_o": nrm(ks[16], (L, D_MODEL, D_MODEL), D_MODEL ** -0.5),
        "norm_ffn_w": gain(ks[17], (L, D_MODEL)),
        "w_gate": nrm(ks[18], (L, D_MODEL, D_FF_3), D_MODEL ** -0.5),
        "w_up": nrm(ks[19], (L, D_MODEL, D_FF_3), D_MODEL ** -0.5),
        "w_down": nrm(ks[20], (L, D_FF_3, D_MODEL), D_FF_3 ** -0.5),
        "norm_ple_w": gain(ks[21], (L, D_MODEL)),
        "w_ple_gate": nrm(ks[22], (L, D_MODEL, D_MODEL), D_MODEL ** -0.5),
        "w_ple_up": nrm(ks[23], (L, D_PLE, D_MODEL), D_PLE ** -0.5),
        "final_norm_w": gain(ks[24], (D_MODEL,)),
    }

def third_block(x, p, norm_mix_w, w_in, ret_norm_w, rw_mu, rw_w0, rw_w2, rw_a0, rw_a2,
              rw_g2, rw_k_k, rw_k_a, rw_r_k, rw_ln_w, rw_ln_b, w_o, norm_ffn_w,
              w_gate, w_up, w_down, norm_ple_w, w_ple_gate, w_ple_up, final_norm_w):
    B, S, _ = x.shape
    for i in range(DEPTH):
        hn = rms_norm(x, norm_mix_w[i])
        proj = (hn @ w_in[i]).astype(jnp.float32)
        q = proj[..., 0:RET_WIDTH].reshape(B, S, RET_HEADS, RET_HEAD_DIM)
        k = proj[..., RET_WIDTH:2 * RET_WIDTH].reshape(B, S, RET_HEADS, RET_HEAD_DIM)
        v = proj[..., 2 * RET_WIDTH:3 * RET_WIDTH].reshape(B, S, RET_HEADS, RET_HEAD_DIM)
        ret_gate = proj[..., 3 * RET_WIDTH:RET_COLS]
        y_ret = head_norm(retention(q, k, v), RET_GN_EPS).reshape(B, S, RET_WIDTH)
        y_ret = y_ret * ret_norm_w[i] * jax.nn.silu(ret_gate)
        y_rw = rwkv7_mix(proj[..., RET_COLS:], rw_mu[i], rw_w0[i], rw_w2[i], rw_a0[i],
                         rw_a2[i], rw_g2[i], rw_k_k[i], rw_k_a[i], rw_r_k[i],
                         rw_ln_w[i], rw_ln_b[i])
        mixed = jnp.concatenate([y_ret, y_rw], axis=-1).astype(x.dtype)
        x = x + mixed @ w_o[i]
        hf = rms_norm(x, norm_ffn_w[i])
        x = x + (jax.nn.silu(hf @ w_gate[i]) * (hf @ w_up[i])) @ w_down[i]
        hp = rms_norm(x, norm_ple_w[i])
        x = x + (p[i] @ w_ple_up[i]) * jax.nn.sigmoid(hp @ w_ple_gate[i])
    return rms_norm(x, final_norm_w)


_first_inputs_3 = third_inputs


def third_inputs(seed=0):
    import zlib

    import numpy as np

    out = dict(_first_inputs_3(seed))
    spreads = {}
    factors = {'ret_norm_w': 7.627,
     'rw_w2': 8.0,
     'rw_a0': 4.119,
     'rw_a2': 4.142,
     'rw_k_k': 8.0,
     'rw_k_a': 8.0,
     'rw_ln_w': 8.0,
     'rw_ln_b': 8.0,
     'norm_ffn_w': 4.627,
     'norm_ple_w': 8.0,
     'final_norm_w': 2.85}
    for name, (base, spread) in spreads.items():
        noise = np.random.default_rng([zlib.crc32(name.encode()), seed]).standard_normal(out[name].shape)
        drawn = base * np.exp(spread * noise) if base else spread * noise
        out[name] = __import__('jax').numpy.asarray(drawn.astype(out[name].dtype))
    for name, factor in factors.items():
        out[name] = (out[name] * factor).astype(out[name].dtype)
    return out


_narrow_inputs_3 = third_inputs


def third_inputs(seed=0):

    out = dict(_narrow_inputs_3(seed))
    wider = {'ret_norm_w': 3.27,
     'rw_k_k': 3.65,
     'rw_ln_w': 3.39,
     'rw_ln_b': 6.77,
     'norm_ple_w': 12.0,
     'final_norm_w': 3.21}
    for name, times in wider.items():
        mean = out[name].mean()
        out[name] = (mean + times * (out[name] - mean)).astype(out[name].dtype)
    return out


def setup_inputs(seed=0):
    out = dict(first_inputs(seed))
    for name, value in second_inputs(seed + 1).items():
        if name != "x":
            out[name + "_2"] = value
    for name, value in third_inputs(seed + 2).items():
        if name != "x":
            out[name + "_3"] = value
    return out


def reference(
    x, norm_g, w_in, na_rpb, conv_dw_w, conv_dw_b, conv_ln_g, conv_ln_b, conv_pw, pool_w,
    pool_scale, sgu_ln_g, sgu_ln_b, sgu_w, sgu_b, w_out, final_g, meta_tokens_2, mix_norm_2,
    w_in_2, b_in_2, w_alpha_2, b_alpha_2, attn_sinks_2, gla_head_norm_2, w_proj_attn_2,
    w_proj_gla_2, w_out_2, ffn_norm_2, w_up_2, conv_w_2, conv_b_2, w_down_2, final_norm_2, p_3,
    norm_mix_w_3, w_in_3, ret_norm_w_3, rw_mu_3, rw_w0_3, rw_w2_3, rw_a0_3, rw_a2_3, rw_g2_3,
    rw_k_k_3, rw_k_a_3, rw_r_k_3, rw_ln_w_3, rw_ln_b_3, w_o_3, norm_ffn_w_3, w_gate_3, w_up_3,
    w_down_3, norm_ple_w_3, w_ple_gate_3, w_ple_up_3, final_norm_w_3,
):
    x = first_block(
        x, norm_g, w_in, na_rpb, conv_dw_w, conv_dw_b, conv_ln_g, conv_ln_b, conv_pw, pool_w,
        pool_scale, sgu_ln_g, sgu_ln_b, sgu_w, sgu_b, w_out, final_g,
    )
    x = second_block(
        x, meta_tokens_2, mix_norm_2, w_in_2, b_in_2, w_alpha_2, b_alpha_2, attn_sinks_2,
        gla_head_norm_2, w_proj_attn_2, w_proj_gla_2, w_out_2, ffn_norm_2, w_up_2, conv_w_2,
        conv_b_2, w_down_2, final_norm_2,
    )
    return third_block(
        x, p_3, norm_mix_w_3, w_in_3, ret_norm_w_3, rw_mu_3, rw_w0_3, rw_w2_3, rw_a0_3, rw_a2_3,
        rw_g2_3, rw_k_k_3, rw_k_a_3, rw_r_k_3, rw_ln_w_3, rw_ln_b_3, w_o_3, norm_ffn_w_3,
        w_gate_3, w_up_3, w_down_3, norm_ple_w_3, w_ple_gate_3, w_ple_up_3, final_norm_w_3,
    )


_drawn_inputs = setup_inputs


def setup_inputs(seed=0):
    import zlib

    import numpy as np

    out = dict(_drawn_inputs(seed))
    spreads = {}
    factors = {'rw_k_a_3': 14.259, 'norm_ple_w_3': 26.88, 'rw_w2_3': 2.668}
    for name, (base, spread) in spreads.items():
        noise = np.random.default_rng([zlib.crc32(name.encode()), seed]).standard_normal(out[name].shape)
        drawn = base * np.exp(spread * noise) if base else spread * noise
        out[name] = __import__('jax').numpy.asarray(drawn.astype(out[name].dtype))
    for name, factor in factors.items():
        out[name] = (out[name] * factor).astype(out[name].dtype)
    return out
```

```python
from contextlib import ExitStack, contextmanager

import numpy as np

import concourse.bass as bass
from concourse import mybir

F32 = mybir.dt.float32
ALU = mybir.AluOpType
ACT = mybir.ActivationFunctionType
AX = mybir.AxisListType

P = 128
D = 1024
SEQ = 1024
META = 16
KT = D // P
LTOK = META + SEQ
COLS = LTOK + 1
NEG = -1.0e30


class Core:

    def __init__(self, nc):
        self.nc, self.now, self.before, self.eps = nc, [], [], {}

    def sem(self, name):
        self.now.append(self.nc.alloc_semaphore(name=name))
        return self.now[-1]

    @contextmanager
    def block(self):
        if self.before:
            self.nc.clear_and_free_semaphores(self.before)
        with self.nc.Block() as block:
            yield block
        self.before, self.now = self.now, []


def pieces(total):
    n = -(-total // 512)
    assert total % n == 0
    return n, total // n


def rms_stage(core, name, x_t, h_t, gain, eps, c0, total):
    nc = core.nc
    n, w = pieces(total)
    squared, summed, root, normed = (core.sem(f"{name}_{s}") for s in ("squared", "summed", "root", "normed"))
    with ExitStack() as mem:
        sq = mem.enter_context(nc.sbuf_tensor(f"{name}_sq", [P, 2, total], F32))
        rstd = mem.enter_context(nc.sbuf_tensor(f"{name}_rstd", [P, total], F32))
        ones = mem.enter_context(nc.sbuf_tensor(f"{name}_ones", [P, P], F32))
        ss = mem.enter_context(nc.psum_tensor(f"{name}_ss", [P, n, 512], F32))
        ready = core.sem(f"{name}_ones_ready")
        block = mem.enter_context(core.block())
        rows = rstd[:, :].rearrange("p (c w) -> p c w", c=n)

        @block.scalar
        def _(act):
            for k in range(KT):
                if k >= 2:
                    act.wait_ge(summed, k - 1)
                nc.scalar.activation(sq[:, k % 2, :], x_t[:, k, c0:c0 + total], ACT.Square).then_inc(squared, 1)
            act.wait_ge(summed, KT)
            nc.scalar.activation(rows, ss[:, :, 0:w], ACT.Sqrt, scale=1.0 / D, bias=core.eps[eps]).then_inc(root, 1)

        @block.tensor
        def _(pe):
            pe.wait_ge(ready, 1)
            for k in range(KT):
                pe.wait_ge(squared, k + 1)
                for c in range(n):
                    last = nc.tensor.matmul(ss[:, c, 0:w], ones[:, :], sq[:, k % 2, c * w:(c + 1) * w],
                                            start=(k == 0), stop=(k == KT - 1))
                last.then_inc(summed, 1)

        @block.vector
        def _(dve):
            nc.vector.memset(ones[:, :], 1.0).then_inc(ready, 1)
            dve.wait_ge(root, 1)
            nc.vector.reciprocal(rstd[:, :], rstd[:, :])
            dve.drain()
            for k in range(KT):
                nc.vector.scalar_tensor_tensor(out=h_t[:, k, c0:c0 + total], in0=x_t[:, k, c0:c0 + total],
                                               scalar=gain[:, k:k + 1], in1=rstd[:, :],
                                               op0=ALU.mult, op1=ALU.mult).then_inc(normed, 1)


def gemm_stage(core, name, units, steps, total, act_part, dve_part, out=None, extras=(), temps=(), chained=False):
    nc = core.nc
    n, w = pieces(total)
    kts = [wt.shape[2] // P for wt, _, _ in units]
    mm_done, act_done, unit_done = (core.sem(f"{name}_{s}") for s in ("mm_done", "act_done", "unit_done"))
    w_here, x_here, stored = ([core.sem(f"{name}_{s}{u}") for u in range(2)] for s in ("w_here", "x_here", "stored"))
    AHEAD = 2
    with ExitStack() as mem:
        wb = [mem.enter_context(nc.sbuf_tensor(f"{name}_w{u}", [P, kts[u], P], F32)) for u in range(2)]
        ps = mem.enter_context(nc.psum_tensor(f"{name}_ps", [P, 2, n, 512], F32))
        t = {k: mem.enter_context(nc.sbuf_tensor(f"{name}_{k}", [P, size], F32)) for k, size in temps}
        for u, _, k in extras:
            t[k] = mem.enter_context(nc.sbuf_tensor(f"{name}_{k}", [P, total], F32))
        if out:
            t["out"] = mem.enter_context(nc.sbuf_tensor(f"{name}_out", [P, 2, total], F32))
        view = lambda a: a.rearrange("p (c w) -> p c w", c=n)
        t["view"] = view
        nx = [sum(1 for e in extras if e[0] == u) for u in range(2)]
        has_out = [bool(out and out[u]) for u in range(2)]
        block = mem.enter_context(core.block())

        @block.sync
        def _(sp):
            def load(j, u):
                wt, _, at = units[u]
                sp.dma_start(wb[u][:, :, :], wt[bass.ds(at(j), 1)].rearrange("o p (k c) -> p (o k) c", c=P)
                             ).then_inc(w_here[u], 16)

            def load_extras(j, u):
                for ux, rows, k in extras:
                    if ux == u:
                        sp.dma_start(t[k][:, :], rows(j)).then_inc(x_here[u], 16)

            def step(j, more):
                for u in range(2):
                    if more:
                        sp.wait_ge(mm_done, 2 * j + u + 1)
                        load(j + 1, u)
                    if has_out[u] or (nx[u] and more):
                        sp.wait_ge(unit_done, 2 * j + u + 1 + AHEAD)
                    if has_out[u]:
                        sp.dma_start(out[u](j), t["out"][:, u, :]).then_inc(stored[u], 16)
                    if more:
                        load_extras(j + 1, u)

            for u in range(2):
                load(0, u)
                load_extras(0, u)
            if steps > 1:
                with sp.Fori(0, steps - 1) as j:
                    step(j, True)
            step(steps - 1, False)
            for u in range(2):
                if has_out[u]:
                    sp.wait_ge(stored[u], 16 * (steps + 1))

        @block.tensor
        def _(pe):
            with pe.Fori(0, steps) as j:
                for u in range(2):
                    pe.wait_ge(w_here[u], 16 * (j + 1))
                    pe.wait_ge(unit_done, 2 * j + u + 1)
                    for c in range(n):
                        for k in range(kts[u]):
                            last = nc.tensor.matmul(ps[:, u, c, 0:w], wb[u][:, k, :], units[u][1](k, c * w, w),
                                                    start=(k == 0), stop=(k == kts[u] - 1))
                    last.then_inc(mm_done, 1)

        @block.scalar
        def _(act):
            if act_part is None:
                return
            with act.Fori(0, steps) as j:
                for u in range(2):
                    act.wait_ge(mm_done, 2 * j + u + 1)
                    act.wait_ge(unit_done, 2 * j + u + 1 + (1 if chained and u else 0))
                    if nx[u]:
                        act.wait_ge(x_here[u], 16 * nx[u] * (j + 1))
                    act_part(act, u, j, ps[:, u, :, 0:w], t)
                    act.drain().then_inc(act_done, 1)

        @block.vector
        def _(dve):
            dve.sem_inc(unit_done, AHEAD)
            for u in range(2):
                if has_out[u]:
                    dve.sem_inc(stored[u], 16)
            with dve.Fori(0, steps) as j:
                for u in range(2):
                    dve.wait_ge(act_done if act_part else mm_done, 2 * j + u + 1)
                    if nx[u]:
                        dve.wait_ge(x_here[u], 16 * nx[u] * (j + 1))
                    if has_out[u]:
                        dve.wait_ge(stored[u], 16 * (j + 1))
                    dve_part(dve, u, j, ps[:, u, :, 0:w], t)
                    dve.drain().then_inc(unit_done, 1)


def turn_stage(core, name, load, store, blocks, steps, ident):
    nc = core.nc
    loaded, stored = ([core.sem(f"{name}_{s}{b}") for b in range(2)] for s in ("loaded", "stored"))
    turned, copied = core.sem(f"{name}_turned"), core.sem(f"{name}_copied")
    AHEAD = 2
    assert steps % 2 == 0 and blocks <= 8
    with ExitStack() as mem:
        src = mem.enter_context(nc.sbuf_tensor(f"{name}_src", [P, 2, blocks, P], F32))
        dst = mem.enter_context(nc.sbuf_tensor(f"{name}_dst", [P, 2, blocks * P], F32))
        ps = mem.enter_context(nc.psum_tensor(f"{name}_ps", [P, 2, -(-blocks // 4) * 4 * P], F32))
        block = mem.enter_context(core.block())

        @block.sync
        def _(sp):
            with sp.Fori(0, steps // 2) as jj:
                for b in range(2):
                    j = 2 * jj + b
                    sp.wait_ge(copied, j + 1)
                    sp.dma_start(src[:, b, :, :], load(j)).then_inc(loaded[b], 16)

        @block.tensor
        def _(pe):
            with pe.Fori(0, steps // 2) as jj:
                for b in range(2):
                    j = 2 * jj + b
                    pe.wait_ge(loaded[b], 16 * (jj + 1))
                    pe.wait_ge(copied, j + 1)
                    for c in range(blocks):
                        last = nc.tensor.transpose(ps[:, b, c * P:(c + 1) * P], src[:, b, c, :], ident[:, :])
                    last.then_inc(turned, 1)

        @block.vector
        def _(dve):
            dve.sem_inc(copied, AHEAD)
            for b in range(2):
                dve.sem_inc(stored[b], 16)
            with dve.Fori(0, steps // 2) as jj:
                for b in range(2):
                    j = 2 * jj + b
                    dve.wait_ge(turned, j + 1)
                    dve.wait_ge(stored[b], 16 * (jj + 1))
                    nc.vector.tensor_copy(dst[:, b, :], ps[:, b, 0:blocks * P]).then_inc(copied, 1)

        @block.scalar
        def _(act):
            with act.Fori(0, steps // 2) as jj:
                for b in range(2):
                    j = 2 * jj + b
                    act.wait_ge(copied, j + 1 + AHEAD)
                    act.dma_start(store(j), dst[:, b, :]).then_inc(stored[b], 16)
            for b in range(2):
                act.wait_ge(stored[b], 16 * (steps // 2 + 1))


NA_HEADS, GRID_W, NA_ROWS, NA_COLS = 8, 64, 8, 16
GRID_H = SEQ // GRID_W
NA_DH = 32
BAND = NA_ROWS * GRID_W


def na_stage(core, z, v_tok, bias, ya_tok, ident):
    nc = core.nc
    DR = 2 * NA_ROWS - 1
    PAIRS = NA_HEADS // 2
    s_done, p_done, t_done, c_done, o_done, y_done, m_done, used, bias_here = (
        core.sem(f"na_{s}") for s in ("scores", "probs", "turned", "copied", "outs", "ys", "softmaxed", "used", "bias"))
    row_here, y_stored, y_free = ([core.sem(f"na_{s}{b}") for b in range(2)] for s in ("row", "stored", "free"))
    zr = z.rearrange("t c (r w) -> c t r w", w=GRID_W)
    ranges = [(0, 2, lambda r: 0, lambda r: r * -GRID_W + 7 * GRID_W), (2, 6, lambda r: r - 4, lambda r: 3 * GRID_W), (6, 8, lambda r: 8, lambda r: r * -GRID_W + 15 * GRID_W)]
    with ExitStack() as mem:
        sb = lambda n, s: mem.enter_context(nc.sbuf_tensor(f"na_{n}", s, F32))
        q = sb("q", [P, 2, 2, GRID_W])
        kb = sb("k", [P, 2, 2, BAND])
        vb = sb("v", [P, 2, 4, 2 * P])
        bt = sb("bias_t", [P, PAIRS, DR * GRID_W])
        sc = sb("sc", [P, 2, BAND])
        pr = sb("pr", [P, 2, BAND])
        pt = sb("pt", [P, 2, 4, P])
        st = sb("st", [P, 3, 2, PAIRS])
        y = sb("y", [P, 2, PAIRS, NA_DH])
        ps_s = mem.enter_context(nc.psum_tensor("na_ps_s", [P, 2, BAND], F32))
        ps_t = mem.enter_context(nc.psum_tensor("na_ps_t", [P, 2, 4, P], F32))
        ps_o = mem.enter_context(nc.psum_tensor("na_ps_o", [P, 2, 512], F32))
        block = mem.enter_context(core.block())

        def rows(eng, body):
            for lo, hi, start, first in ranges:
                with eng.Fori(lo, hi) as rr:
                    for b in range(2):
                        body(2 * rr + b, rr, b, start(2 * rr + b), first(2 * rr + b))

        @block.sync
        def _(sp):
            sp.dma_start(bt[:, :, :], bias).then_inc(bias_here, 16)

            def body(r, rr, b, start, at):
                sp.wait_ge(used, r + 1)
                sp.dma_start(q[:, b, :, :], zr[:, 0:2, bass.ds(r, 1), :].rearrange("c t o w -> c t (o w)")
                             ).then_inc(row_here[b], 16)
                sp.dma_start(kb[:, b, :, :].rearrange("c t (r w) -> c t r w", w=GRID_W),
                             zr[:, 2:4, bass.ds(start, NA_ROWS), :]).then_inc(row_here[b], 16)
                sp.dma_start(vb[:, b, :, :], v_tok.rearrange("(r w) c -> r w c", w=GRID_W)[bass.ds(start, NA_ROWS)]
                             .rearrange("(t a) w c -> (a w) t c", a=2)).then_inc(row_here[b], 16)

            rows(sp, body)

        @block.tensor
        def _(pe):
            def scores(r, b, p):
                u = 4 * r + p
                pe.wait_ge(m_done, u + 1)
                for a in range(2):
                    h = 2 * p + a
                    at = NA_DH * (h % 4)
                    last = nc.tensor.matmul(ps_s[64 * a:64 * a + 64, p % 2, :], q[at:at + NA_DH, b, h // 4, :],
                                            kb[at:at + NA_DH, b, h // 4, :], start=True, stop=True)
                last.then_inc(s_done, 1)

            def outs(r, b, p):
                u = 4 * r + p
                pe.wait_ge(p_done, u + 1)
                pe.wait_ge(c_done, u + 1)
                for c in range(4):
                    last = nc.tensor.transpose(ps_t[:, p % 2, c, :], pr[:, p % 2, c * P:(c + 1) * P], ident[:, :])
                last.then_inc(t_done, 1)
                pe.wait_ge(c_done, u + 3)
                pe.wait_ge(y_done, u + 1)
                for c in range(4):
                    last = nc.tensor.matmul(ps_o[:, p % 2, 0:64], pt[:, p % 2, c, :],
                                            vb[:, b, c, 64 * p:64 * p + 64], start=(c == 0), stop=(c == 3))
                last.then_inc(o_done, 1)

            def body(r, rr, b, start, at):
                pe.wait_ge(row_here[b], 48 * (rr + 1))
                scores(r, b, 0)
                for p in range(1, PAIRS):
                    scores(r, b, p)
                    outs(r, b, p - 1)
                outs(r, b, PAIRS - 1)

            rows(pe, body)

        @block.scalar
        def _(act):
            act.sem_inc(c_done, 2)

            def probs(r, b, p):
                u = 4 * r + p
                act.wait_ge(m_done, u + 3)
                nc.scalar.activation(pr[:, p % 2, :], sc[:, p % 2, :], ACT.Exp, bias=st[:, 0, b, p:p + 1],
                                     accum_out=st[:, 1, b, p:p + 1]).then_inc(p_done, 1)

            def copy(r, b, p):
                u = 4 * r + p
                act.wait_ge(t_done, u + 1)
                nc.scalar.activation(pt[:, p % 2, :, :], ps_t[:, p % 2, :, :], ACT.Copy).then_inc(c_done, 1)

            def body(r, rr, b, start, at):
                probs(r, b, 0)
                for p in range(1, PAIRS):
                    probs(r, b, p)
                    copy(r, b, p - 1)
                copy(r, b, PAIRS - 1)

            rows(act, body)

        @block.vector
        def _(dve):
            dve.sem_inc(m_done, 2)
            dve.sem_inc(y_done, 2)
            dve.sem_inc(used, 2)
            for b in range(2):
                dve.sem_inc(y_free[b], 1)
            dve.wait_ge(bias_here, 16)

            def softmax(r, b, p, at):
                u = 4 * r + p
                dve.wait_ge(s_done, u + 1)
                nc.vector.scalar_tensor_tensor(out=sc[:, p % 2, :], in0=ps_s[:, p % 2, :], scalar=NA_DH ** -0.5,
                                               in1=bt[:, p, bass.ds(at, BAND)], op0=ALU.mult, op1=ALU.add)
                dve.drain()
                nc.vector.tensor_reduce(st[:, 0, b, p:p + 1], sc[:, p % 2, :], AX.X, ALU.max, negate=True)
                dve.drain().then_inc(m_done, 1)

            def norm(r, rr, b, p):
                u = 4 * r + p
                dve.wait_ge(o_done, u + 1)
                if p == 0:
                    dve.wait_ge(y_free[b], rr + 1)
                nc.vector.reciprocal(st[:, 2, b, p:p + 1], st[:, 1, b, p:p + 1])
                dve.drain()
                for a in range(2):
                    rows_a = slice(64 * a, 64 * a + 64)
                    nc.vector.tensor_scalar(y[rows_a, b, p, :], ps_o[rows_a, p % 2, NA_DH * a:NA_DH * (a + 1)],
                                            st[rows_a, 2, b, p:p + 1], None, ALU.mult)
                dve.drain().then_inc(y_done, 1)

            def body(r, rr, b, start, at):
                softmax(r, b, 0, at)
                for p in range(1, PAIRS):
                    softmax(r, b, p, at)
                    norm(r, rr, b, p - 1)
                norm(r, rr, b, PAIRS - 1)
                dve.sem_inc(used, 1)

            rows(dve, body)

        @block.gpsimd
        def _(pool):
            yr = ya_tok.rearrange("(r w) (p a d) -> a r w p d", w=GRID_W, a=2, d=NA_DH)

            def body(r, rr, b, start, at):
                pool.wait_ge(y_done, 4 * (r + 1) + 2)
                for a in range(2):
                    pool.dma_start(yr[a, bass.ds(r, 1)].rearrange("o w p d -> (o w) p d"),
                                   y[64 * a:64 * a + 64, b, :, :]).then_inc(y_stored[b], 16)
                pool.wait_ge(y_stored[b], 32 * (rr + 1))
                pool.sem_inc(y_free[b], 1)

            rows(pool, body)


def norm_stage(core, name, v, groups, stat, eps, mean, scale, bias, func):
    nc = core.nc
    total = v.shape[2]
    n, w = pieces(total)
    m_done, sub, squared, v_done, root, normed, ended = (
        core.sem(f"{name}_{s}") for s in ("mean", "centred", "squared", "var", "root", "normed", "ended"))
    with ExitStack() as mem:
        sq = mem.enter_context(nc.sbuf_tensor(f"{name}_sq", [P, len(groups[0]), total], F32))
        rstd = mem.enter_context(nc.sbuf_tensor(f"{name}_rstd", [P, total], F32))
        ps = mem.enter_context(nc.psum_tensor(f"{name}_ps", [P, 2, n, 512], F32))
        cut = lambda a: a.rearrange("p (c w) -> p c w", c=n)
        block = mem.enter_context(core.block())

        @block.tensor
        def _(pe):
            for g, tiles in enumerate(groups):
                if mean:
                    if g:
                        pe.wait_ge(sub, g)
                    for c in range(n):
                        for i, k in enumerate(tiles):
                            last = nc.tensor.matmul(ps[:, 0, c, 0:w], stat, v[:, k, c * w:(c + 1) * w],
                                                    start=(i == 0), stop=(i == len(tiles) - 1))
                    last.then_inc(m_done, 1)
                pe.wait_ge(squared, g + 1)
                for c in range(n):
                    for i, k in enumerate(tiles):
                        last = nc.tensor.matmul(ps[:, 1, c, 0:w], stat, sq[:, i, c * w:(c + 1) * w],
                                                start=(i == 0), stop=(i == len(tiles) - 1))
                last.then_inc(v_done, 1)

        @block.vector
        def _(dve):
            for g, tiles in enumerate(groups):
                if mean:
                    dve.wait_ge(m_done, g + 1)
                    for k in tiles:
                        nc.vector.tensor_tensor(cut(v[:, k, :]), cut(v[:, k, :]), ps[:, 0, :, 0:w], ALU.subtract)
                    dve.drain().then_inc(sub, 1)
                dve.wait_ge(root, g + 1)
                nc.vector.reciprocal(rstd[:, :], rstd[:, :])
                dve.drain()
                for k in tiles:
                    nc.vector.tensor_tensor(v[:, k, :], v[:, k, :], rstd[:, :], ALU.mult)
                dve.drain().then_inc(normed, 1)

        @block.scalar
        def _(act):
            for g, tiles in enumerate(groups):
                if mean:
                    act.wait_ge(sub, g + 1)
                for i, k in enumerate(tiles):
                    nc.scalar.activation(sq[:, i, :], v[:, k, :], ACT.Square)
                act.drain().then_inc(squared, 1)
                act.wait_ge(v_done, g + 1)
                nc.scalar.activation(cut(rstd[:, :]), ps[:, 1, :, 0:w], ACT.Sqrt, bias=core.eps[eps]).then_inc(root, 1)
                act.wait_ge(normed, g + 1)
                for k in tiles:
                    nc.scalar.activation(v[:, k, :], v[:, k, :], func, scale=scale[:, k:k + 1],
                                         bias=bias[:, k:k + 1] if bias is not None else 0.0)
                act.drain().then_inc(ended, 1)


CONV_W = 31


def conv_stage(core, z, v, taps, dw_b):
    nc = core.nc
    half = CONV_W // 2
    here, sig = core.sem("conv_here"), core.sem("conv_sigmoid")
    with ExitStack() as mem:
        a = mem.enter_context(nc.sbuf_tensor("conv_a", [P, 2, SEQ + 2 * half], F32))
        b = mem.enter_context(nc.sbuf_tensor("conv_b", [P, 2, SEQ], F32))
        zero = core.sem("conv_zero")
        block = mem.enter_context(core.block())

        @block.sync
        def _(sp):
            sp.dma_start(a[:, :, half:half + SEQ], z[6:8].rearrange("t c s -> c t s")).then_inc(here, 16)
            sp.dma_start(b[:, :, :], z[8:10].rearrange("t c s -> c t s")).then_inc(here, 16)

        @block.scalar
        def _(act):
            act.wait_ge(here, 32)
            nc.scalar.activation(b[:, :, :], b[:, :, :], ACT.Sigmoid).then_inc(sig, 1)

        @block.vector
        def _(dve):
            nc.vector.memset(a[:, :, 0:half], 0.0)
            nc.vector.memset(a[:, :, half + SEQ:], 0.0)
            dve.wait_ge(sig, 1)
            nc.vector.tensor_tensor(a[:, :, half:half + SEQ], a[:, :, half:half + SEQ], b[:, :, :], ALU.mult)
            dve.drain()
            for k in range(2):
                nc.vector.tensor_scalar(v[:, k, :], a[:, k, 0:SEQ], taps[:, k, 0:1], dw_b[:, k:k + 1],
                                        ALU.mult, ALU.add)
            dve.drain()
            with dve.Fori(1, CONV_W) as i:
                for k in range(2):
                    nc.vector.scalar_tensor_tensor(out=v[:, k, :], in0=a[:, k, bass.ds(i, SEQ)],
                                                   scalar=taps[:, k, bass.ds(i, 1)], in1=v[:, k, :],
                                                   op0=ALU.mult, op1=ALU.add)
                    dve.drain()


def product_stage(core, name, out, mats, v, scale=None):
    nc = core.nc
    n, w = pieces(v.shape[2])
    done = core.sem(f"{name}_done")
    with ExitStack() as mem:
        ps = mem.enter_context(nc.psum_tensor(f"{name}_ps", [P, len(mats), n, 512], F32))
        block = mem.enter_context(core.block())

        @block.tensor
        def _(pe):
            for m, parts in enumerate(mats):
                for c in range(n):
                    for lhs, rows, orows, k, first, end in parts:
                        last = nc.tensor.matmul(ps[orows, m, c, 0:w], lhs, v[rows, k, c * w:(c + 1) * w],
                                                start=first, stop=end)
                last.then_inc(done, 1)

        @block.vector
        def _(dve):
            for m in range(len(mats)):
                dve.wait_ge(done, m + 1)
                o = out[:, m, :].rearrange("p (c w) -> p c w", c=n)
                if scale is None:
                    nc.vector.tensor_copy(o, ps[:, m, :, 0:w])
                else:
                    nc.vector.tensor_scalar(o, ps[:, m, :, 0:w], scale[:, m:m + 1], None, ALU.mult)


def pool_stage(core, z, v, inv_count):
    nc = core.nc
    E = 8
    here = core.sem("pool_here")
    with ExitStack() as mem:
        x = mem.enter_context(nc.sbuf_tensor("pool_x", [P, 2, SEQ + 2 * E], F32))
        s = [mem.enter_context(nc.sbuf_tensor(f"pool_s{i}", [P, 2, SEQ + 2 * E], F32)) for i in range(3)]
        inv = mem.enter_context(nc.sbuf_tensor("pool_inv", [P, 2, SEQ], F32))
        block = mem.enter_context(core.block())

        @block.sync
        def _(sp):
            sp.dma_start(x[:, :, E:E + SEQ], z[10:12].rearrange("t c s -> c t s")).then_inc(here, 16)
            sp.dma_start(inv[:, :, :], inv_count).then_inc(here, 16)

        @block.vector
        def _(dve):
            nc.vector.memset(x[:, :, 0:E], 0.0)
            nc.vector.memset(x[:, :, E + SEQ:], 0.0)
            dve.drain()
            dve.wait_ge(here, 32)
            end = SEQ + 2 * E
            top, low = slice(64, 128), slice(0, 64)
            add = lambda out, a, b: nc.vector.tensor_tensor(out, a, b, ALU.add)
            s2, s4, s8 = s
            add(s2[:, :, 1:end], x[:, :, 0:end - 1], x[:, :, 1:end])
            dve.drain()
            add(s4[:, :, 2:end - 1], s2[:, :, 1:end - 2], s2[:, :, 3:end])
            dve.drain()
            add(s8[:, 1, 4:end - 3], s4[:, 1, 2:end - 5], s4[:, 1, 6:end - 1])
            dve.drain()
            tok = slice(E, E + SEQ)
            mul = lambda out, a, b: nc.vector.tensor_tensor(out, a, b, ALU.mult)
            mul(v[low, 0, :], s2[low, 0, tok], inv[low, 0, :])
            mul(v[top, 0, :], s4[top, 0, tok], inv[top, 0, :])
            mul(v[low, 1, :], s8[low, 1, tok], inv[low, 1, :])
            add(v[top, 1, :], s8[top, 1, E - 4:E - 4 + SEQ], s8[top, 1, E + 4:E + 4 + SEQ])
            dve.drain()
            mul(v[top, 1, :], v[top, 1, :], inv[top, 1, :])
            dve.drain()
            nc.vector.tensor_tensor(v[:, :, :], v[:, :, :], x[:, :, tok], ALU.subtract)


def load_stage(core, name, loads, func=None):
    nc = core.nc
    here = [core.sem(f"{name}_here{i}") for i in range(len(loads))]
    with ExitStack() as mem:
        block = mem.enter_context(core.block())

        @block.sync
        def _(sp):
            for (dst, src), h in zip(loads, here):
                sp.dma_start(dst, src).then_inc(h, 16)
            if func is None:
                for h in here:
                    sp.wait_ge(h, 16)

        @block.scalar
        def _(act):
            if func is not None:
                for (dst, _), h in zip(loads, here):
                    act.wait_ge(h, 16)
                    nc.scalar.activation(dst, dst, func)


SGU_HEADS, SGU_CHUNK = 4, 128


def mix_stage(core, v, u, y, ws, bs, ident):
    nc = core.nc
    chunks = SEQ // SGU_CHUNK
    turned, copied, mixed, added = (core.sem(f"mix_{s}") for s in ("turned", "copied", "mixed", "added"))
    with ExitStack() as mem:
        vt = mem.enter_context(nc.sbuf_tensor("mix_vt", [P, 2, 2 * P], F32))
        m = mem.enter_context(nc.sbuf_tensor("mix_m", [P, 2, P], F32))
        ps_t = mem.enter_context(nc.psum_tensor("mix_ps_t", [P, 2, 512], F32))
        ps_m = mem.enter_context(nc.psum_tensor("mix_ps_m", [P, 2, 512], F32))
        block = mem.enter_context(core.block())

        @block.tensor
        def _(pe):
            for i in range(chunks):
                b, tok = i % 2, slice(i * P, (i + 1) * P)
                if i >= 2:
                    pe.wait_ge(copied, i - 1)
                for k in range(2):
                    last = nc.tensor.transpose(ps_t[:, b, k * P:(k + 1) * P], v[:, k, tok], ident[:, :])
                last.then_inc(turned, 1)
                pe.wait_ge(copied, i + 1)
                if i >= 2:
                    pe.wait_ge(added, i - 1)
                for h in range(SGU_HEADS):
                    a, k = 64 * (h % 2), h // 2
                    last = nc.tensor.matmul(ps_m[a:a + 64, b, k * P:(k + 1) * P], vt[:, b, 64 * h:64 * h + 64],
                                            ws[:, h, :], start=True, stop=True)
                last.then_inc(mixed, 1)

        @block.scalar
        def _(act):
            for i in range(chunks):
                act.wait_ge(turned, i + 1)
                nc.scalar.activation(vt[:, i % 2, :], ps_t[:, i % 2, 0:2 * P], ACT.Copy).then_inc(copied, 1)

        @block.vector
        def _(dve):
            for i in range(chunks):
                tok = slice(i * P, (i + 1) * P)
                dve.wait_ge(mixed, i + 1)
                nc.vector.tensor_tensor(m[:, :, :], ps_m[:, i % 2, 0:2 * P].rearrange("p (k s) -> p k s", k=2),
                                        bs[:, :, :], ALU.add)
                dve.drain().then_inc(added, 1)
                nc.vector.tensor_tensor(y[:, :, tok], u[:, :, tok], m[:, :, :], ALU.mult)
                dve.drain()


def gate_stage(core, name, z, y, tiles, func):
    nc = core.nc
    here = [core.sem(f"{name}_here{b}") for b in range(2)]
    opened, used = core.sem(f"{name}_opened"), core.sem(f"{name}_used")
    total = y.shape[2]
    with ExitStack() as mem:
        g = mem.enter_context(nc.sbuf_tensor(f"{name}_g", [P, 2, total], F32))
        block = mem.enter_context(core.block())

        @block.sync
        def _(sp):
            for i in range(tiles):
                if i >= 2:
                    sp.wait_ge(used, i - 1)
                sp.dma_start(g[:, i % 2, :], z(i)).then_inc(here[i % 2], 16)

        @block.scalar
        def _(act):
            for i in range(tiles):
                act.wait_ge(here[i % 2], 16 * (i // 2 + 1))
                nc.scalar.activation(g[:, i % 2, :], g[:, i % 2, :], func).then_inc(opened, 1)

        @block.vector
        def _(dve):
            for i in range(tiles):
                dve.wait_ge(opened, i + 1)
                nc.vector.tensor_tensor(y[:, i, :], y[:, i, :], g[:, i % 2, :], ALU.mult).then_inc(used, 1)


LEAD = 240
WIDE = LEAD + COLS
AHEADS, HEAD, KV = 8, 64, 2
BLOCKS = 9


def zero_stage(core, x_t, h_t, meta, z2, width):
    nc = core.nc
    here, zeroed = core.sem("zero_here"), core.sem("zeroed")
    with core.block() as block:
        @block.sync
        def _(sp):
            with nc.allow_non_contiguous_dma(reason="16 columns of each row"):
                sp.dma_start(x_t[:, :, 0:META], meta).then_inc(here, 16)
            sp.wait_ge(zeroed, 1)
            sp.dma_start(z2[0:width, :, 0:LEAD].rearrange("t c s -> c t s"), h_t[:, 0:1, 0:LEAD].broadcast_to([P, width, LEAD])
                         ).then_inc(here, 16)
            sp.wait_ge(here, 32)

        @block.vector
        def _(dve):
            nc.vector.memset(x_t[:, :, COLS - 1:COLS], 0.0)
            nc.vector.memset(h_t[:, 0, 0:LEAD], 0.0).then_inc(zeroed, 1)


def rope_stage(core, name, z, qk, tables, perm, count, lead, total):
    nc = core.nc
    n, w = pieces(total)
    here = [core.sem(f"{name}_here{b}") for b in range(2)]
    tab, rotated, ended, stored = (core.sem(f"{name}_{s}") for s in ("tables", "rotated", "ended", "stored"))
    with ExitStack() as mem:
        cs = mem.enter_context(nc.sbuf_tensor(f"{name}_cs", [P, 2, total], F32))
        x = mem.enter_context(nc.sbuf_tensor(f"{name}_x", [P, 2, total], F32))
        o = mem.enter_context(nc.sbuf_tensor(f"{name}_o", [P, count, lead + total], F32))
        r = mem.enter_context(nc.sbuf_tensor(f"{name}_r", [P, total], F32))
        ps = mem.enter_context(nc.psum_tensor(f"{name}_ps", [P, 2, n, 512], F32))
        block = mem.enter_context(core.block())

        @block.sync
        def _(sp):
            sp.dma_start(cs[:, :, :], tables).then_inc(tab, 16)
            for i in range(count):
                if i >= 2:
                    sp.wait_ge(ended, i - 1)
                sp.dma_start(x[:, i % 2, :], z[i]).then_inc(here[i % 2], 16)
            sp.wait_ge(ended, count)
            sp.dma_start(qk.rearrange("t c s -> c t s"), o[:, :, :]).then_inc(stored, 16)
            sp.wait_ge(stored, 16)

        @block.tensor
        def _(pe):
            for i in range(count):
                pe.wait_ge(here[i % 2], 16 * (i // 2 + 1))
                if i >= 2:
                    pe.wait_ge(ended, i - 1)
                for c in range(n):
                    last = nc.tensor.matmul(ps[:, i % 2, c, 0:w], perm, x[:, i % 2, c * w:(c + 1) * w], start=True, stop=True)
                last.then_inc(rotated, 1)

        @block.vector
        def _(dve):
            if lead:
                nc.vector.memset(o[:, :, 0:lead], 0.0)
            dve.wait_ge(tab, 16)
            cut = lambda a: a.rearrange("p (c w) -> p c w", c=n)
            for i in range(count):
                dve.wait_ge(rotated, i + 1)
                nc.vector.tensor_tensor(cut(r[:, :]), ps[:, i % 2, :, 0:w], cut(cs[:, 1, :]), ALU.mult)
                nc.vector.tensor_tensor(o[:, i, lead:], x[:, i % 2, :], cs[:, 0, :], ALU.mult)
                dve.drain()
                nc.vector.tensor_tensor(o[:, i, lead:], o[:, i, lead:], r[:, :], ALU.add)
                dve.drain().then_inc(ended, 1)


def swa_stage(core, qk, v_tok, masks, sinks, yatt, ident):
    nc = core.nc
    G = AHEADS // KV
    s_done, m_done, p_done, n_done, t_done, c_done, o_done, y_done, used, zero, sinks_here = (
        core.sem(f"swa_{s}") for s in ("scores", "maxed", "probs", "normed", "turned", "copied", "outs", "ys", "used", "zero", "sinks"))
    row_here, y_stored, y_free = ([core.sem(f"swa_{s}{b}") for b in range(2)] for s in ("row", "stored", "free"))
    with ExitStack() as mem:
        sb = lambda n, s: mem.enter_context(nc.sbuf_tensor(f"swa_{n}", s, F32))
        q = sb("q", [P, 2, 4, P])
        kk = sb("kk", [P, 2, KV, 2, 2 * P])
        vb = sb("v", [P, 2, 2, P])
        mk = sb("mask", [P, 2, 2 * P])
        sk = sb("sinks", [P, AHEADS])
        sc = sb("sc", [P, 2, G, 2 * P])
        st = sb("st", [P, 2, 6, G])
        pt = sb("pt", [P, 2, 2, G, P])
        y = sb("y", [64, 2, KV, G, P])
        ps_s = mem.enter_context(nc.psum_tensor("swa_ps_s", [P, 2, G, 2 * P], F32))
        ps_t = mem.enter_context(nc.psum_tensor("swa_ps_t", [P, 2, G, P], F32))
        ps_o = mem.enter_context(nc.psum_tensor("swa_ps_o", [64, G, P], F32))
        block = mem.enter_context(core.block())

        def blocks(eng, body):
            with eng.Fori(0, BLOCKS // 2) as ii:
                for b in range(2):
                    body(2 * ii + b, ii, b)
            body(BLOCKS - 1, BLOCKS // 2, 0)

        @block.sync
        def _(sp):
            sp.dma_start(sk[:, :], sinks.partition_broadcast(P)).then_inc(sinks_here, 16)
            sp.wait_ge(zero, 1)

            def body(i, ii, b):
                sp.wait_ge(used, i + 1)
                at = i * P
                sp.dma_start(q[:, b, :, :], qk[0:4, :, bass.ds(at + P, P)].rearrange("t c s -> c t s")).then_inc(row_here[b], 16)
                for a in range(2):
                    sp.dma_start(kk[64 * a:64 * a + 64, b, :, a, :],
                                 qk[4].rearrange("(g c) s -> c g s", g=KV)[:, :, bass.ds(at, 2 * P)]).then_inc(row_here[b], 16)
                sp.dma_start(vb[:, b, :, :], v_tok[bass.ds(at, 2 * P), 0:P].rearrange("(t s) c -> s t c", t=2)).then_inc(row_here[b], 16)
                sp.dma_start(mk[:, b, :], masks[bass.ds(i, 1)].rearrange("o q k -> (o q) k")).then_inc(row_here[b], 16)

            blocks(sp, body)

        @block.gpsimd
        def _(pool):
            nc.gpsimd.memset(kk[:, :, :, :, :], 0.0).then_inc(zero, 1)
            yv = yatt.rearrange("(g h d) s -> d g h s", g=KV, h=G)

            def body(i, ii, b):
                pool.wait_ge(y_done, 2 * (i + 1) + 1)
                for g in range(KV):
                    pool.dma_start(yv[:, g, :, bass.ds(i * P, P)], y[:, b, g, :, :]).then_inc(y_stored[b], 16)
                pool.wait_ge(y_stored[b], 32 * (ii + 1))
                pool.sem_inc(y_free[b], 1)

            blocks(pool, body)

        @block.tensor
        def _(pe):
            def body(i, ii, b):
                pe.wait_ge(row_here[b], 80 * (ii + 1))
                for g in range(KV):
                    u = 2 * i + g
                    pe.wait_ge(m_done, u + 1)
                    for t in range(2):
                        last = nc.tensor.matmul(ps_s[:, g, 2 * t:2 * t + 2, :], q[:, b, 2 * g + t, :], kk[:, b, g, :, :],
                                                start=True, stop=True)
                    last.then_inc(s_done, 1)
                for g in range(KV):
                    u = 2 * i + g
                    pe.wait_ge(n_done, u + 1)
                    pe.wait_ge(c_done, u + 1)
                    for k in range(2):
                        for h in range(G):
                            last = nc.tensor.transpose(ps_t[:, k, h, :], sc[:, g, h, k * P:(k + 1) * P], ident[:, :])
                    last.then_inc(t_done, 1)
                    pe.wait_ge(c_done, u + 2)
                    pe.wait_ge(y_done, u + 1)
                    for k in range(2):
                        last = nc.tensor.matmul(ps_o[:, :, :], vb[:, b, k, 64 * g:64 * g + 64], pt[:, g, k, :, :],
                                                start=(k == 0), stop=(k == 1))
                    last.then_inc(o_done, 1)

            blocks(pe, body)

        @block.scalar
        def _(act):
            act.sem_inc(c_done, 1)

            def body(i, ii, b):
                for g in range(KV):
                    u = 2 * i + g
                    act.wait_ge(m_done, u + 3)
                    for h in range(G):
                        nc.scalar.activation(sc[:, g, h, :], sc[:, g, h, :], ACT.Exp, bias=st[:, g, 1, h:h + 1],
                                             accum_out=st[:, g, 2, h:h + 1])
                    nc.scalar.activation(st[:, g, 4, :], st[:, g, 3, :], ACT.Exp)
                    act.drain().then_inc(p_done, 1)
                for g in range(KV):
                    u = 2 * i + g
                    act.wait_ge(t_done, u + 1)
                    nc.scalar.activation(pt[:, g, :, :, :], ps_t[:, :, :, :], ACT.Copy).then_inc(c_done, 1)

            blocks(act, body)

        @block.vector
        def _(dve):
            dve.sem_inc(m_done, 2)
            dve.sem_inc(y_done, 1)
            dve.sem_inc(used, 2)
            dve.wait_ge(sinks_here, 16)

            def body(i, ii, b):
                for g in range(KV):
                    u = 2 * i + g
                    dve.wait_ge(s_done, u + 1)
                    if g == 0:
                        dve.wait_ge(row_here[b], 80 * (ii + 1))
                    nc.vector.scalar_tensor_tensor(out=sc[:, g, :, :], in0=ps_s[:, g, :, :], scalar=HEAD ** -0.5,
                                                   in1=mk[:, b:b + 1, :].broadcast_to([P, G, 2 * P]), op0=ALU.mult, op1=ALU.add)
                    dve.drain()
                    nc.vector.tensor_reduce(st[:, g, 0, :], sc[:, g, :, :], AX.X, ALU.max)
                    dve.drain()
                    nc.vector.tensor_tensor(st[:, g, 0, :], st[:, g, 0, :], sk[:, G * g:G * g + G], ALU.max)
                    dve.drain()
                    nc.vector.tensor_scalar(st[:, g, 1, :], st[:, g, 0, :], -1.0, None, ALU.mult)
                    nc.vector.tensor_tensor(st[:, g, 3, :], sk[:, G * g:G * g + G], st[:, g, 0, :], ALU.subtract)
                    dve.drain().then_inc(m_done, 1)
                for g in range(KV):
                    u = 2 * i + g
                    dve.wait_ge(p_done, u + 1)
                    nc.vector.tensor_tensor(st[:, g, 5, :], st[:, g, 2, :], st[:, g, 4, :], ALU.add)
                    dve.drain()
                    nc.vector.reciprocal(st[:, g, 5, :], st[:, g, 5, :])
                    dve.drain()
                    for h in range(G):
                        nc.vector.tensor_scalar(sc[:, g, h, :], sc[:, g, h, :], st[:, g, 5, h:h + 1], None, ALU.mult)
                    dve.drain().then_inc(n_done, 1)
                dve.wait_ge(y_free[b], ii + 1)
                for g in range(KV):
                    u = 2 * i + g
                    dve.wait_ge(o_done, u + 1)
                    nc.vector.tensor_copy(y[:, b, g, :, :], ps_o[:, :, :]).then_inc(y_done, 1)
                dve.sem_inc(used, 1)

            for b in range(2):
                dve.sem_inc(y_free[b], 1)
            blocks(dve, body)


LEVELS = (64, 32, 16, 8, 4, 2, 1)
NL = len(LEVELS)
GLA_H, GLA_DV = 4, 128


def decay_stage(core, h_t, w_low, w_alpha, b_low, b_alpha, la):
    nc = core.nc
    n, w = pieces(COLS)
    low_done, low_here, z_done, z_here, soft = (core.sem(f"decay_{s}") for s in ("low_mm", "low", "z_mm", "z", "soft"))
    with ExitStack() as mem:
        low = mem.enter_context(nc.sbuf_tensor("decay_low", [16, COLS], F32))
        z = mem.enter_context(nc.sbuf_tensor("decay_z", [P, 2, COLS], F32))
        e = mem.enter_context(nc.sbuf_tensor("decay_e", [P, 2, COLS], F32))
        ps = mem.enter_context(nc.psum_tensor("decay_ps", [P, 2, n, 512], F32))
        cut = lambda a: a.rearrange("p (c w) -> p c w", c=n)
        block = mem.enter_context(core.block())

        @block.tensor
        def _(pe):
            for c in range(n):
                for k in range(KT):
                    last = nc.tensor.matmul(ps[0:16, 0, c, 0:w], w_low[:, k, :], h_t[:, k, c * w:(c + 1) * w],
                                            start=(k == 0), stop=(k == KT - 1))
            last.then_inc(low_done, 1)
            pe.wait_ge(low_here, 1)
            for m in range(2):
                for c in range(n):
                    last = nc.tensor.matmul(ps[:, m, c, 0:w], w_alpha[:, m * P:(m + 1) * P], low[:, c * w:(c + 1) * w],
                                            start=True, stop=True)
                last.then_inc(z_done, 1)

        @block.vector
        def _(dve):
            nc.vector.memset(la[:, :, 0:LEAD - P], 0.0)
            dve.wait_ge(low_done, 1)
            nc.vector.tensor_scalar(cut(low[:, :]), ps[0:16, 0, :, 0:w], b_low, None, ALU.add).then_inc(low_here, 1)
            for m in range(2):
                dve.wait_ge(z_done, m + 1)
                nc.vector.tensor_scalar(cut(z[:, m, :]), ps[:, m, :, 0:w], b_alpha[:, m:m + 1], None, ALU.add)
            dve.drain().then_inc(z_here, 1)
            dve.wait_ge(soft, 1)
            nc.vector.tensor_scalar(z[:, :, :], z[:, :, :], 0.0, None, ALU.min)
            dve.drain()
            nc.vector.tensor_tensor(z[:, :, :], z[:, :, :], e[:, :, :], ALU.subtract)
            dve.drain()
            nc.vector.tensor_scalar(la[:, :, LEAD - P:], z[:, :, 0:LTOK], 1.0 / 16, None, ALU.mult)

        @block.scalar
        def _(act):
            act.wait_ge(z_here, 1)
            nc.scalar.activation(e[:, :, :], z[:, :, :], ACT.Abs)
            act.drain()
            nc.scalar.activation(e[:, :, :], e[:, :, :], ACT.Exp, scale=-1.0)
            act.drain()
            nc.scalar.activation(e[:, :, :], e[:, :, :], ACT.Ln, bias=1.0).then_inc(soft, 1)


def gla_stage(core, z2, v_tok, la, y, level_masks, ident):
    nc = core.nc
    d_done, e_done, k_done, a_done, m_done, t_done, c_done, o_done, y_done, u_done, s_done, q_here, seen = (
        core.sem(f"gla_{s}") for s in ("diffs", "exps", "scaled", "scores", "masked", "turned", "copied", "outs", "ys",
                                       "update", "state", "here", "seen"))
    v_here = [core.sem(f"gla_v{b}") for b in range(2)]
    with ExitStack() as mem:
        sb = lambda n, s: mem.enter_context(nc.sbuf_tensor(f"gla_{n}", s, F32))
        q, k = sb("q", [P, 2, BLOCKS * P]), sb("k", [P, 2, BLOCKS * P])
        one = sb("one", [P, P])
        e = sb("e", [P, NL + 2, 2, P])
        qz = sb("qz", [P, NL + 2, 2, 2, P])
        ke = sb("ke", [P, NL + 1, 2, P])
        kd = sb("kd", [P, 2, P])
        kt = sb("kt", [P, 2, P])
        bs = sb("bs", [P, 2, P])
        v = sb("v", [P, 2, GLA_H * GLA_DV])
        a_t = sb("a_t", [P, GLA_H, P])
        mk = sb("mk", [P, NL + 1, P])
        s = sb("s", [P, GLA_H, GLA_DV])
        ps_a = mem.enter_context(nc.psum_tensor("gla_ps_a", [P, 2, GLA_H, P], F32))
        ps_t = mem.enter_context(nc.psum_tensor("gla_ps_t", [P, 512], F32))
        ps_o = mem.enter_context(nc.psum_tensor("gla_ps_o", [P, GLA_H, P], F32))
        ps_u = mem.enter_context(nc.psum_tensor("gla_ps_u", [P, 2, 2 * P], F32))
        block = mem.enter_context(core.block())

        def chunks(eng, body):
            body(0, 0, 1)
            with eng.Fori(0, BLOCKS // 2) as ii:
                body(2 * ii + 1, 1, ii + 1)
                body(2 * ii + 2, 0, ii + 2)

        @block.sync
        def _(sp):
            cols = slice(P, P + BLOCKS * P)
            sp.dma_start(q[:, :, :], z2[5:7, :, cols].rearrange("t c s -> c t s")).then_inc(q_here, 16)
            sp.dma_start(k[:, :, :], z2[7:9, :, cols].rearrange("t c s -> c t s")).then_inc(q_here, 16)
            sp.dma_start(mk[:, :, :], level_masks).then_inc(q_here, 16)

            def load(c, b):
                sp.dma_start(v[:, b, :], v_tok[bass.ds(c * P + P, P), P:]).then_inc(v_here[b], 16)

            load(0, 0)
            load(1, 1)
            with sp.Fori(0, (BLOCKS - 3) // 2) as ii:
                for b in range(2):
                    sp.wait_ge(s_done, 2 * ii + b + 1)
                    load(2 * ii + b + 2, b)
            sp.wait_ge(s_done, BLOCKS - 2)
            load(BLOCKS - 1, 0)

        @block.tensor
        def _(pe):
            def body(c, b, turn):
                pe.wait_ge(k_done, c + 1)
                for t in range(2):
                    last = nc.tensor.transpose(ps_t[:, t * P:(t + 1) * P], kd[:, t, :], ident[:, :])
                last.then_inc(t_done, 1)
                for l in range(NL + 1):
                    if l >= 2:
                        pe.wait_ge(m_done, c * (NL + 1) + l - 1)
                    for t in range(2):
                        last = nc.tensor.matmul(ps_a[:, l % 2, 2 * t:2 * t + 2, :], ke[:, l, t, :],
                                                qz[:, l if l < NL else NL + 1, t, :, :], start=True, stop=True)
                    last.then_inc(a_done, 1)
                pe.wait_ge(v_here[b], 16 * turn)
                pe.wait_ge(m_done, (c + 1) * (NL + 1))
                if not isinstance(c, int):
                    pe.wait_ge(s_done, c)
                    pe.wait_ge(y_done, c)
                for h in range(GLA_H):
                    nc.tensor.matmul(ps_o[:, h, :], v[:, b, h * GLA_DV:(h + 1) * GLA_DV], a_t[:, h, :], start=True, stop=False)
                    last = nc.tensor.matmul(ps_o[:, h, :], s[:, h, :], qz[:, NL, h // 2, h % 2, :], start=False, stop=True)
                last.then_inc(o_done, 1)
                pe.wait_ge(c_done, c + 1)
                for t in range(2):
                    last = nc.tensor.matmul(ps_u[:, t, :], kt[:, t, :], v[:, b, 2 * t * P:2 * (t + 1) * P], start=True, stop=True)
                last.then_inc(u_done, 1)

            chunks(pe, body)

        @block.scalar
        def _(act):
            def body(c, b, turn):
                act.wait_ge(d_done, c + 1)
                nc.scalar.activation(e[:, :, :, :], e[:, :, :, :], ACT.Exp).then_inc(e_done, 1)
                act.wait_ge(t_done, c + 1)
                nc.scalar.activation(kt[:, :, :], ps_t[:, 0:2 * P].rearrange("p (t s) -> p t s", t=2), ACT.Copy).then_inc(c_done, 1)
                act.wait_ge(o_done, c + 1)
                if isinstance(c, int):
                    nc.scalar.activation(y[:, :, 0:META], ps_o[:, :, P - META:P], ACT.Copy, scale=0.125).then_inc(y_done, 1)
                else:
                    nc.scalar.activation(y[:, :, bass.ds(c * P + (META - P), P)], ps_o[:, :, :], ACT.Copy,
                                         scale=0.125).then_inc(y_done, 1)

            chunks(act, body)

        @block.vector
        def _(dve):
            for tile, value in ((one[:, :], 1.0), (qz[:, :, :, :, :], 0.0), (a_t[:, :, :], 0.0), (s[:, :, :], 0.0)):
                nc.vector.memset(tile, value)
            dve.drain()
            dve.wait_ge(q_here, 48)
            halves = [slice(0, 64), slice(64, 128)]
            TT = nc.vector.tensor_tensor

            def body(c, b, turn):
                cols = bass.ds(c * P, P)
                for t in range(2):
                    nc.vector.tensor_tensor_scan(bs[:, t, :], one[:, :], la[:, t, cols], 0.0, ALU.mult, ALU.add)
                dve.drain()
                for l, half in enumerate(LEVELS):
                    cut = lambda a: a.rearrange("p t (n r) -> p t n r", r=2 * half)
                    mid = cut(bs[:, :, :])[:, :, :, half - 1:half].broadcast_to([P, 2, P // (2 * half), half])
                    src, dst = cut(bs[:, :, :]), cut(e[:, l, :, :])
                    TT(dst[:, :, :, 0:half], mid, src[:, :, :, 0:half], ALU.subtract)
                    TT(dst[:, :, :, half:], src[:, :, :, half:], mid, ALU.subtract)
                nc.vector.tensor_copy(e[:, NL, :, :], bs[:, :, :])
                TT(e[:, NL + 1, :, :], bs[:, :, P - 1:P].broadcast_to([P, 2, P]), bs[:, :, :], ALU.subtract)
                dve.drain().then_inc(d_done, 1)
                dve.wait_ge(e_done, c + 1)
                TT(kd[:, :, :], k[:, :, cols], e[:, NL + 1, :, :], ALU.mult)
                TT(ke[:, 0:NL, :, :], k[:, :, cols].unsqueeze(1).broadcast_to([P, NL, 2, P]), e[:, 0:NL, :, :], ALU.mult)
                nc.vector.tensor_copy(ke[:, NL, :, :], k[:, :, cols])
                for a, r in enumerate(halves):
                    TT(qz[r, 0:NL + 1, :, a, :], q[r, :, cols].unsqueeze(1).broadcast_to([64, NL + 1, 2, P]),
                       e[r, 0:NL + 1, :, :], ALU.mult)
                    nc.vector.tensor_copy(qz[r, NL + 1, :, a, :], q[r, :, cols])
                dve.drain().then_inc(k_done, 1)
                for l in range(NL + 1):
                    dve.wait_ge(a_done, c * (NL + 1) + l + 1)
                    dve.sem_inc(seen, 1)
                    nc.vector.copy_predicated(a_t[:, :, :], mk[:, l:l + 1, :].bitcast(mybir.dt.int32).broadcast_to([P, GLA_H, P]),
                                              ps_a[:, l % 2, :, :])
                    dve.drain().then_inc(m_done, 1)
                dve.wait_ge(u_done, c + 1)
                for h in range(GLA_H):
                    t, a = h // 2, h % 2
                    r = halves[a]
                    nc.vector.scalar_tensor_tensor(out=s[r, h, :], in0=s[r, h, :], scalar=e[r, NL, t, P - 1:P],
                                                   in1=ps_u[r, t, a * P:(a + 1) * P], op0=ALU.mult, op1=ALU.add)
                dve.drain().then_inc(s_done, 1)

            chunks(dve, body)


FF = 2816
FT = FF // P


def block_two(core, A, x_t, h_t, mats, vec, dram, stop):
    nc = core.nc
    ident = mats["ident"]
    z2, v_tok, qk, yatt = dram("z2", (34, P, WIDE)), dram("v_tok2", (LEAD + LTOK, 640)), dram("qk", (5, P, WIDE)), dram("yatt", (512, BLOCKS * P))
    acts = lambda src: (lambda k, at, w: src[:, k, at:at + w])
    zero_stage(core, x_t, h_t, A["meta"], z2, 14)
    rms_stage(core, "rms2", x_t, h_t, vec["mix_norm"], 1e-6, 0, COLS)
    zrow = lambda u: (lambda j: z2[bass.ds(2 * j + u, 1), :, LEAD:].rearrange("o p s -> p (o s)"))
    gemm_stage(core, "in2", [(A["w_in2"], acts(h_t), lambda j: 2 * j), (A["w_in2"], acts(h_t), lambda j: 2 * j + 1)],
               17, COLS, None, plain_out(nc, vec["b_in"]), out=[zrow(0), zrow(1)])
    if stop == "z2": return z2[:, :, LEAD:]
    with ExitStack() as mem:
        la = mem.enter_context(nc.sbuf_tensor("b2_la", [P, 2, BLOCKS * P], F32))
        with ExitStack() as inner:
            wl = inner.enter_context(nc.sbuf_tensor("b2_wl", [P, KT, 16], F32))
            wa = inner.enter_context(nc.sbuf_tensor("b2_wa", [16, 2 * P], F32))
            bl = inner.enter_context(nc.sbuf_tensor("b2_bl", [16, 1], F32))
            with nc.allow_non_contiguous_dma(reason="16 biases"):
                load_stage(core, "w2", [(wl[:, :, :], A["w_low"]), (wa[:, :], A["w_alpha"]), (bl[:, :], A["b_low"])])
            decay_stage(core, h_t, wl, wa, bl[:, 0:1], vec["b_alpha"], la)
        turn_stage(core, "turn2", lambda j: z2[9:14, :, bass.ds(P * j, P)].rearrange("t c s -> c t s"),
                   lambda j: v_tok[bass.ds(P * j, P), :], 5, (LEAD + LTOK) // P, ident)
        gla_stage(core, z2, v_tok, la, h_t[:, 4:8, :], A["level_masks"], ident)
    norm_stage(core, "gla_norm", h_t[:, 4:8, :], [[k] for k in range(4)], mats["mean128"], 1e-6, False,
               vec["gla_norm"], None, ACT.Identity)
    if stop == "gla": return h_t[:, 4:8, 0:LTOK]
    gate_stage(core, "gate2", lambda i: z2[14 + i, :, LEAD:], h_t[:, 4:8, :], 4, ACT.Silu)
    rope_stage(core, "rope2", z2[:, :, LEAD:], qk, A["rope_tables"], mats["rope"], 5, LEAD, COLS)
    swa_stage(core, qk, v_tok, A["swa_masks"], A["sinks"], yatt, ident)
    load_stage(core, "yatt", [(h_t[:, 0:4, 0:LTOK], yatt[:, P - META:].rearrange("(t c) s -> c t s", c=P))])
    if stop == "yatt": return h_t[:, 0:4, 0:LTOK]
    with ExitStack() as mem:
        mix = mem.enter_context(nc.sbuf_tensor("b2_mix", [P, KT, COLS], F32))

        def open_gates(act, u, j, ps, t):
            nc.scalar.activation(t[f"gate{u}"][:, :], t[f"gate{u}"][:, :], ACT.Sigmoid)

        def join(dve, u, j, ps, t):
            g = t["view"](t[f"gate{u}"][:, :])
            row = t["view"](mix[:, bass.ds(j, 1), :].rearrange("p o s -> p (o s)"))
            if u == 0:
                nc.vector.tensor_tensor(row, ps, g, ALU.mult)
            else:
                nc.vector.tensor_tensor(g, ps, g, ALU.mult)
                dve.drain()
                nc.vector.tensor_tensor(row, row, g, ALU.add)

        grow = lambda first: (lambda j: z2[bass.ds(j + first, 1), :, LEAD:].rearrange("o p s -> p (o s)"))
        gemm_stage(core, "proj", [(A["w_att"], acts(h_t), lambda j: j), (A["w_gla"], acts(h_t[:, 4:8, :]), lambda j: j)],
                   8, COLS, open_gates, join, extras=[(0, grow(18), "gate0"), (1, grow(26), "gate1")])
        gemm_stage(core, "out2", [(A["w_out2"], acts(mix), lambda j: 2 * j), (A["w_out2"], acts(mix), lambda j: 2 * j + 1)],
                   4, COLS, None, add_part(nc, x_t, 0, COLS))
    if stop == "h2": return x_t[:, :, 0:LTOK]
    rms_stage(core, "rms2b", x_t, h_t, vec["ffn_norm"], 1e-6, 0, COLS)
    with ExitStack() as mem:
        g = mem.enter_context(nc.sbuf_tensor("b2_ff", [P, FT, COLS], F32))

        def act_ff(act, u, j, ps, t):
            if u == 0:
                nc.scalar.activation(t["view"](t["a"][:, 2:2 + COLS]), ps, ACT.Copy)
            else:
                nc.scalar.activation(t["conv"][:, :], t["conv"][:, :], ACT.Gelu_apprx_tanh)

        def dve_ff(dve, u, j, ps, t):
            cw, cb = vec["ff_conv"], vec["ff_conv_b"]
            if u == 0:
                nc.vector.memset(t["a"][:, 0:2], 0.0)
                nc.vector.tensor_scalar(t["conv"][:, :], t["a"][:, 2:2 + COLS], cw[:, bass.ds(j + 2 * FT, 1)], cb[:, bass.ds(j, 1)],
                                        ALU.mult, ALU.add)
                for i in (1, 0):
                    dve.drain()
                    nc.vector.scalar_tensor_tensor(out=t["conv"][:, :], in0=t["a"][:, i:i + COLS], scalar=cw[:, bass.ds(j + i * FT, 1)],
                                                   in1=t["conv"][:, :], op0=ALU.mult, op1=ALU.add)
            else:
                row = t["view"](g[:, bass.ds(j, 1), :].rearrange("p o s -> p (o s)"))
                nc.vector.tensor_tensor(row, ps, t["view"](t["conv"][:, :]), ALU.mult)

        gemm_stage(core, "up2", [(A["w_up2"], acts(h_t), lambda j: j), (A["w_up2"], acts(h_t), lambda j: j + FT)],
                   FT, COLS, act_ff, dve_ff, temps=[("a", COLS + 2), ("conv", COLS)], chained=True)
        gemm_stage(core, "down2", [(A["w_down2"], acts(g), lambda j: 2 * j), (A["w_down2"], acts(g), lambda j: 2 * j + 1)],
                   4, COLS, None, add_part(nc, x_t, 0, COLS))
    rms_stage(core, "rms2f", x_t, x_t, vec["final_norm2"], 1e-6, META, SEQ)


RET_H, RET_D, RET_C = 4, 128, 128


def retention_stage(core, qk, v_tok, y, decay, from_start, to_end, chunk_decay, ident):
    nc = core.nc
    s_done, a_done, t_done, c_done, q_done, o_done, y_done, u_done, r_done, tabs = (
        core.sem(f"ret_{s}") for s in ("scores", "decayed", "turned", "copied", "scaled", "outs", "ys", "update", "state", "tables"))
    here = [core.sem(f"ret_here{b}") for b in range(2)]
    with ExitStack() as mem:
        sb = lambda n, s: mem.enter_context(nc.sbuf_tensor(f"ret_{n}", s, F32))
        x = sb("qk", [P, 2, 2 * RET_H, P])
        v = sb("v", [P, 2, RET_H * P])
        dk = sb("decay", [P, RET_H, P])
        fs = sb("from_start", [P, RET_H, P])
        te = sb("to_end", [P, RET_H])
        a_t = sb("a_t", [P, RET_H, P])
        qs = sb("qs", [P, RET_H, P])
        kt = sb("kt", [P, RET_H, P])
        r = sb("r", [P, RET_H, P])
        ps = [mem.enter_context(nc.psum_tensor(f"ret_ps{i}", [P, RET_H, P], F32)) for i in range(4)]
        ps_s, ps_t, ps_o, ps_u = ps
        block = mem.enter_context(core.block())
        chunks = SEQ // RET_C

        def loop(eng, body):
            with eng.Fori(0, chunks // 2) as ii:
                for b in range(2):
                    body(2 * ii + b, ii, b)

        @block.sync
        def _(sp):
            for dst, src in ((dk[:, :, :], decay), (fs[:, :, :], from_start), (te[:, :], to_end)):
                sp.dma_start(dst, src).then_inc(tabs, 16)

            def body(c, ii, b):
                sp.wait_ge(r_done, c + 1)
                sp.dma_start(x[:, b, :, :], qk[:, :, bass.ds(c * P, P)].rearrange("t c s -> c t s")).then_inc(here[b], 16)
                sp.dma_start(v[:, b, :], v_tok[bass.ds(c * P, P), :]).then_inc(here[b], 16)

            loop(sp, body)

        @block.tensor
        def _(pe):
            def body(c, ii, b):
                pe.wait_ge(here[b], 32 * (ii + 1))
                for h in range(RET_H):
                    last = nc.tensor.matmul(ps_s[:, h, :], x[:, b, RET_H + h, :], x[:, b, h, :], start=True, stop=True)
                last.then_inc(s_done, 1)
                for h in range(RET_H):
                    last = nc.tensor.transpose(ps_t[:, h, :], x[:, b, RET_H + h, :], ident[:, :])
                last.then_inc(t_done, 1)
                pe.wait_ge(a_done, c + 1)
                pe.wait_ge(q_done, c + 1)
                pe.wait_ge(r_done, c + 2)
                pe.wait_ge(y_done, c + 1)
                for h in range(RET_H):
                    nc.tensor.matmul(ps_o[:, h, :], v[:, b, h * P:(h + 1) * P], a_t[:, h, :], start=True, stop=False)
                    last = nc.tensor.matmul(ps_o[:, h, :], r[:, h, :], qs[:, h, :], start=False, stop=True)
                last.then_inc(o_done, 1)
                pe.wait_ge(c_done, c + 1)
                for h in range(RET_H):
                    last = nc.tensor.matmul(ps_u[:, h, :], kt[:, h, :], v[:, b, h * P:(h + 1) * P], start=True, stop=True)
                last.then_inc(u_done, 1)

            loop(pe, body)

        @block.scalar
        def _(act):
            act.sem_inc(y_done, 1)
            act.wait_ge(tabs, 48)

            def body(c, ii, b):
                act.wait_ge(t_done, c + 1)
                for h in range(RET_H):
                    nc.scalar.activation(kt[:, h, :], ps_t[:, h, :], ACT.Copy, scale=te[:, h:h + 1])
                act.drain().then_inc(c_done, 1)
                act.wait_ge(o_done, c + 1)
                nc.scalar.activation(y[:, :, bass.ds(c * P, P)], ps_o[:, :, :], ACT.Copy).then_inc(y_done, 1)

            loop(act, body)

        @block.vector
        def _(dve):
            nc.vector.memset(r[:, :, :], 0.0)
            dve.drain().then_inc(r_done, 2)
            dve.wait_ge(tabs, 48)

            def body(c, ii, b):
                dve.wait_ge(s_done, c + 1)
                nc.vector.tensor_tensor(a_t[:, :, :], ps_s[:, :, :], dk[:, :, :], ALU.mult).then_inc(a_done, 1)
                nc.vector.tensor_tensor(qs[:, :, :], x[:, b, 0:RET_H, :], fs[:, :, :], ALU.mult).then_inc(q_done, 1)
                dve.wait_ge(u_done, c + 1)
                for h in range(RET_H):
                    nc.vector.scalar_tensor_tensor(out=r[:, h, :], in0=r[:, h, :], scalar=chunk_decay[h], in1=ps_u[:, h, :],
                                                   op0=ALU.mult, op1=ALU.add)
                dve.drain().then_inc(r_done, 1)

            loop(dve, body)


RW_C = 64
RW_CH = SEQ // RW_C
PAIRS = 4
KINDS = 5
RW_LEVELS = (2, 4, 8, 16, 32)


def rwkv_prep_stage(core, z, mats, vec, w2a2, g2, rw, late):
    nc = core.nc
    rw_x, rw_e = rw
    here, lora, mm, u_here, lw_done, e_done, kk_done, sq_done, n_mm, n_here, root, bt, b_mm, out_done, x_free, g_copied, zeroed = (
        core.sem(f"prep_{s}") for s in ("here", "lora", "lora_mm", "sigmoids", "sums", "exps", "kk", "squares", "norm_mm", "norm",
                                        "root", "bonus", "bonus_mm", "out", "x_free", "g_copied", "zeroed"))
    stored = core.sem("prep_stored")
    with ExitStack() as mem:
        sb = lambda n, s: mem.enter_context(nc.sbuf_tensor(f"prep_{n}", s, F32))
        raw = sb("raw", [P, 3, SEQ + 1])
        lo = sb("lora", [P, 2, SEQ + 1])
        ls = sb("lora_s", [P, 2, SEQ])
        w = sb("w", [P, 512])
        g = sb("g2", [P, 512])
        reset = sb("reset", [P, SEQ])
        t = {k: sb(k, [P, SEQ]) for k in ("r", "k", "v", "tmp", "lw", "a", "g", "w_in", "w_ex", "kk", "sq", "rn", "bv")}
        out = sb("out", [P, KINDS, SEQ])
        ew = sb("ew", [P, RW_CH, PAIRS])
        ps = mem.enter_context(nc.psum_tensor("prep_ps", [P, 4, 2, 512], F32))
        cut = lambda x: x.rearrange("p (c w) -> p c w", c=2)
        block = mem.enter_context(core.block())
        TT, TS, STT = nc.vector.tensor_tensor, nc.vector.tensor_scalar, nc.vector.scalar_tensor_tensor

        @block.sync
        def _(sp):
            sp.dma_start(w[:, :], w2a2).then_inc(here, 16)
            sp.dma_start(g[:, :], g2).then_inc(here, 16)
            sp.dma_start(lo[:, :, 1:], z[28:30].rearrange("t c s -> c t s")).then_inc(here, 16)
            for m in range(4):
                if m:
                    sp.wait_ge(x_free, m)
                for i in range(3):
                    sp.dma_start(raw[:, i, 1:], z[16 + 4 * i + m]).then_inc(here, 16)
                sp.wait_ge(out_done, m + 1)
                for k in range(KINDS):
                    sp.dma_start(rw_x[:, :, k, m, :].rearrange("n c s -> c n s"),
                                 out[:, k, :].rearrange("c (n s) -> c n s", s=RW_C)).then_inc(stored, 16)
                sp.dma_start(late[m], t["g"][:, :]).then_inc(stored, 16)
                sp.dma_start(late[4 + m], t["bv"][:, :]).then_inc(stored, 16)
            sp.dma_start(rw_e, ew[:, :, :]).then_inc(stored, 16)
            sp.wait_ge(stored, 16 * (4 * (KINDS + 2) + 1))

        @block.tensor
        def _(pe):
            for m in range(4):
                cols = slice(m * P, (m + 1) * P)
                if m == 0:
                    pe.wait_ge(lora, 2)
                else:
                    pe.wait_ge(u_here, m)
                for c in range(2):
                    tok = slice(c * 512, (c + 1) * 512)
                    nc.tensor.matmul(ps[:, 0, c, :], w[0:64, cols], ls[0:64, 0, tok], start=True, stop=True)
                    nc.tensor.matmul(ps[:, 1, c, :], w[64:128, cols], ls[64:128, 0, tok], start=True, stop=True)
                    last = nc.tensor.matmul(ps[:, 2, c, :], g[:, cols], ls[:, 1, tok], start=True, stop=True)
                last.then_inc(mm, 1)
                pe.wait_ge(sq_done, m + 1)
                for c in range(2):
                    last = nc.tensor.matmul(ps[:, 3, c, :], mats["mean64"], t["sq"][:, c * 512:(c + 1) * 512], start=True, stop=True)
                last.then_inc(n_mm, 1)
                pe.wait_ge(bt, m + 1)
                for c in range(2):
                    last = nc.tensor.matmul(ps[:, 3, c, :], mats["mean64"], t["tmp"][:, c * 512:(c + 1) * 512], start=True, stop=True)
                last.then_inc(b_mm, 1)

        @block.scalar
        def _(act):
            act.wait_ge(lora, 1)
            nc.scalar.activation(ls[0:64, 0, :], ls[0:64, 0, :], ACT.Tanh)
            nc.scalar.activation(ls[:, 1, :], ls[:, 1, :], ACT.Sigmoid)
            act.drain().then_inc(lora, 1)
            for m in range(4):
                act.wait_ge(mm, m + 1)
                if m:
                    act.wait_ge(g_copied, m)
                nc.scalar.activation(cut(t["lw"][:, :]), ps[:, 0, :, :], ACT.Sigmoid, bias=vec["rw_w0"][:, m:m + 1])
                nc.scalar.activation(cut(t["a"][:, :]), ps[:, 1, :, :], ACT.Sigmoid, bias=vec["rw_a0"][:, m:m + 1])
                nc.scalar.activation(cut(t["g"][:, :]), ps[:, 2, :, :], ACT.Copy)
                act.drain().then_inc(u_here, 1)
                act.wait_ge(lw_done, m + 1)
                nc.scalar.activation(t["rn"][:, :], t["w_in"][:, :], ACT.Exp, scale=-1.0)
                nc.scalar.activation(t["w_ex"][:, :], t["w_ex"][:, :], ACT.Exp)
                act.drain()
                nc.scalar.activation(t["w_in"][:, :], t["w_in"][:, :], ACT.Exp)
                act.drain().then_inc(e_done, 1)
                act.wait_ge(kk_done, m + 1)
                nc.scalar.activation(t["sq"][:, :], t["kk"][:, :], ACT.Square).then_inc(sq_done, 1)
                act.wait_ge(n_here, m + 1)
                nc.scalar.activation(t["sq"][:, :], t["sq"][:, :], ACT.Sqrt).then_inc(root, 1)

        @block.vector
        def _(dve):
            nc.vector.memset(raw[:, :, 0:1], 0.0)
            nc.vector.memset(lo[:, :, 0:1], 0.0)
            nc.vector.memset(reset[:, :], 1.0)
            dve.drain()
            nc.vector.memset(reset[:, :].rearrange("p (n s) -> p n s", s=RW_C)[:, :, 0:1], 0.0)
            dve.wait_ge(here, 96)

            def shift(dst, src, mu, tmp):
                TT(tmp, src[:, 0:SEQ], src[:, 1:], ALU.subtract)
                dve.drain()
                STT(out=dst, in0=tmp, scalar=mu, in1=src[:, 1:], op0=ALU.mult, op1=ALU.add)
                dve.drain()

            for i in range(2):
                shift(ls[:, i, :], lo[:, i, :], vec["rw_mu"][:, 12 + i:13 + i], t["tmp"][:, :])
            dve.drain().then_inc(lora, 1)
            for m in range(4):
                col = slice(m, m + 1)
                dve.wait_ge(here, 48 * (m + 2))
                if m:
                    dve.wait_ge(stored, 16 * (KINDS + 2) * m)
                    dve.sem_inc(g_copied, 1)
                for i, name in enumerate("rkv"):
                    shift(t[name][:, :], raw[:, i, :], vec["rw_mu"][:, 4 * i + m:4 * i + m + 1], t["tmp"][:, :])
                dve.sem_inc(x_free, 1)
                TS(t["kk"][:, :], t["k"][:, :], vec["rw_kk"][:, col], None, ALU.mult)
                dve.drain().then_inc(kk_done, 1)
                dve.wait_ge(u_here, m + 1)
                TS(t["lw"][:, :], t["lw"][:, :], -float(np.exp(-0.5)), None, ALU.mult)
                dve.drain()
                nc.vector.tensor_tensor_scan(t["w_in"][:, :], reset[:, :], t["lw"][:, :], 0.0, ALU.mult, ALU.add)
                dve.drain()
                TT(t["w_ex"][:, :], t["w_in"][:, :], t["lw"][:, :], ALU.subtract)
                dve.drain().then_inc(lw_done, 1)
                dve.wait_ge(n_mm, m + 1)
                TS(cut(t["sq"][:, :]), ps[:, 3, :, :], 64.0, 1e-24, ALU.mult, ALU.max)
                TS(t["tmp"][:, :], t["a"][:, :], -1.0, vec["rw_ka"][:, col], ALU.add, ALU.mult)
                dve.drain().then_inc(n_here, 1)
                STT(out=t["k"][:, :], in0=t["tmp"][:, :], scalar=1.0, in1=t["k"][:, :], op0=ALU.add, op1=ALU.mult)
                dve.drain()
                STT(out=t["tmp"][:, :], in0=t["r"][:, :], scalar=vec["rw_rk"][:, col], in1=t["k"][:, :], op0=ALU.mult, op1=ALU.mult)
                dve.drain().then_inc(bt, 1)
                dve.wait_ge(e_done, m + 1)
                dve.wait_ge(root, m + 1)
                nc.vector.reciprocal(t["sq"][:, :], t["sq"][:, :])
                TT(out[:, 1, :], t["r"][:, :], t["w_in"][:, :], ALU.mult)
                TT(out[:, 3, :], t["k"][:, :], t["rn"][:, :], ALU.mult)
                nc.vector.tensor_copy(out[:, 4, :], t["v"][:, :])
                nc.vector.tensor_copy(ew[:, :, m], t["w_in"][:, :].rearrange("p (n s) -> p n s", s=RW_C)[:, :, RW_C - 1])
                dve.drain()
                TT(t["kk"][:, :], t["kk"][:, :], t["sq"][:, :], ALU.mult)
                dve.drain()
                TT(out[:, 0, :], t["kk"][:, :], t["w_ex"][:, :], ALU.mult)
                TT(out[:, 2, :], t["kk"][:, :], t["a"][:, :], ALU.mult)
                dve.drain()
                TT(out[:, 2, :], out[:, 2, :], t["rn"][:, :], ALU.mult)
                dve.wait_ge(b_mm, m + 1)
                STT(out=cut(t["bv"][:, :]), in0=ps[:, 3, :, :], scalar=64.0, in1=cut(t["v"][:, :]), op0=ALU.mult, op1=ALU.mult)
                dve.drain().then_inc(out_done, 1)


def rwkv_stage(core, rw, y, mask4, neg1, level_masks, ident):
    nc = core.nc
    rw_x, rw_e = rw
    NV = len(RW_LEVELS)
    sc_done, tr_done, lt_done, tok_done, off_done, off_used, x_mm, x_copied, t_mm, t_done = (
        core.sem(f"rw_{s}") for s in ("scores", "turned", "masked", "copied", "offs", "offs_used", "lt_mm", "lt_copied", "tlt_mm", "inverse"))
    cx, cxn, cu, cuc, cy, y_out, s_done, tabs, zero = (
        core.sem(f"rw_{s}") for s in ("chain_x", "chain_x_sb", "chain_u", "chain_u_sb", "chain_y", "y_out", "state", "tables", "zero"))
    here = [core.sem(f"rw_here{g}") for g in range(2)]
    with ExitStack() as mem:
        sb = lambda n, s: mem.enter_context(nc.sbuf_tensor(f"rw_{n}", s, F32))
        z = sb("z", [P, 2, KINDS, PAIRS, 2, RW_C])
        tok = sb("tok", [P, 2, PAIRS, 3, P])
        lt = sb("lt", [P, 2, PAIRS, 4, P])
        ti = sb("t", [P, 2, PAIRS, P])
        tt = sb("tt", [P, 2, PAIRS, P])
        off = sb("off", [P, 2, 2, PAIRS, P])
        xl = sb("xl", [P, 2, PAIRS, P])
        xn, us, s = sb("xn", [P, PAIRS, P]), sb("us", [P, PAIRS, P]), sb("s", [P, PAIRS, P])
        ew = sb("ew", [P, RW_CH, PAIRS])
        m4, n1, lm = sb("m4", [P, 4, P]), sb("n1", [P, 2, P]), sb("lm", [P, NV, P])
        bank = mem.enter_context(nc.psum_tensor("rw_ps", [P, 8, PAIRS, P], F32))
        block = mem.enter_context(core.block())
        pad = lambda g, kind, p: z[:, g, kind, p, :, :].rearrange("c a s -> c (a s)")

        def steps(eng, body):
            with eng.Fori(0, RW_CH // 2) as i:
                body(i)

        @block.sync
        def _(sp):
            for dst, src in ((ew[:, :, :], rw_e), (m4[:, :, :], mask4), (n1[:, :, :], neg1), (lm[:, :, :], level_masks[:, 1:6, :])):
                sp.dma_start(dst, src).then_inc(tabs, 16)
            sp.wait_ge(zero, 1)

            def body(i):
                for g in range(2):
                    sp.wait_ge(s_done, 2 * i + g + 1)
                    for a in range(2):
                        r = slice(64 * a, 64 * a + 64)
                        sp.dma_start(z[r, g, :, :, a, :].rearrange("c k p s -> c (k p) s"),
                                     rw_x[bass.ds(2 * i + g, 1), r].rearrange("o c k p s -> (o c) (k p) s")).then_inc(here[g], 16)

            steps(sp, body)

        @block.gpsimd
        def _(pool):
            nc.gpsimd.memset(z[:, :, :, :, :, :], 0.0).then_inc(zero, 1)
            pool.wait_ge(tabs, 64)

            def body(i):
                for l in range(NV):
                    for g in range(2):
                        if l == 0:
                            pool.wait_ge(lt_done, 2 * i + g + 1)
                        pool.wait_ge(off_used, 2 * NV * i + 2 * l + g + 1)
                        nc.gpsimd.tensor_tensor(off[:, g, l % 2, :, :], lt[:, g, :, 0, :],
                                                lm[:, NV - 1 - l:NV - l, :].broadcast_to([P, PAIRS, P]), ALU.mult).then_inc(off_done, 1)

            steps(pool, body)

        @block.tensor
        def _(pe):
            pe.sem_inc(off_used, 4)
            mm = nc.tensor.matmul

            def chain(i, g):
                c = 2 * i + g
                pe.wait_ge(s_done, c + 2)
                for p in range(PAIRS):
                    mm(bank[:, 6, p, :], lt[:, g, p, 2, :], tok[:, g, p, 2, :], start=True, stop=False)
                    last = mm(bank[:, 6, p, :], pad(g, 0, p), s[:, p, :], start=False, stop=True)
                last.then_inc(cx, 1)
                pe.wait_ge(cxn, c + 1)
                for p in range(PAIRS):
                    last = mm(bank[:, 7, p, :], tt[:, g, p, :], xn[:, p, :], start=True, stop=True)
                last.then_inc(cu, 1)
                pe.wait_ge(cuc, c + 1)
                for p in range(PAIRS):
                    mm(bank[:, 2 + g, p, :], tok[:, g, p, 0, :], us[:, p, :], start=True, stop=False)
                    mm(bank[:, 2 + g, p, :], tok[:, g, p, 1, :], tok[:, g, p, 2, :], start=False, stop=True)
                for p in range(PAIRS):
                    mm(bank[:, g, p, :], s[:, p, :], pad(g, 1, p), start=True, stop=False)
                    mm(bank[:, g, p, :], us[:, p, :], lt[:, g, p, 1, :], start=False, stop=False)
                    last = mm(bank[:, g, p, :], tok[:, g, p, 2, :], lt[:, g, p, 3, :], start=False, stop=True)
                last.then_inc(cy, 1)

            def body(i):
                pe.wait_ge(y_out, 2 * i + 1)
                pe.wait_ge(s_done, 2 * i + 2)
                for g in range(2):
                    pe.wait_ge(here[g], 32 * (i + 1))
                    if g:
                        pe.wait_ge(lt_done, 2 * i + 1)
                    for p in range(PAIRS):
                        for n, kind in enumerate((2, 3)):
                            mm(bank[:, p, 2 * n:2 * n + 2, :], pad(g, kind, p),
                               z[:, g, 0:2, p, :, :].rearrange("c k a s -> c k (a s)"), start=True, stop=True)
                        last = mm(bank[:, 4, p, :], pad(g, 0, p), pad(g, 2, p), start=True, stop=True)
                    last.then_inc(sc_done, 1)
                    if g:
                        pe.wait_ge(tok_done, 2 * i + 1)
                    for p in range(PAIRS):
                        for n in range(3):
                            last = nc.tensor.transpose(bank[:, 5 + n, p, :], pad(g, 2 + n, p), ident[:, :])
                    last.then_inc(tr_done, 1)
                pe.wait_ge(lt_done, 2 * i + 2)
                pe.wait_ge(tok_done, 2 * i + 2)
                for l in range(NV):
                    k = 2 * NV * i + 2 * l
                    for g in range(2):
                        pe.wait_ge(off_done, k + g + 1)
                        if l:
                            pe.wait_ge(t_done, k + g - 1)
                        for p in range(PAIRS):
                            last = mm(bank[:, g, p, :], off[:, g, l % 2, p, :], ti[:, g, p, :], start=True, stop=True)
                        last.then_inc(x_mm, 1)
                    for g in range(2):
                        pe.wait_ge(x_copied, k + g + 1)
                        for p in range(PAIRS):
                            mm(bank[:, 2 + g, p, :], tt[:, g, p, :], xl[:, g, p, :], start=True, stop=True)
                            last = mm(bank[:, 4 + g, p, :], xl[:, g, p, :], tt[:, g, p, :], start=True, stop=True)
                        last.then_inc(t_mm, 1)
                for g in range(2):
                    pe.wait_ge(t_done, 2 * NV * (i + 1) - 1 + g)
                    chain(i, g)

            steps(pe, body)

        @block.scalar
        def _(act):
            act.sem_inc(y_out, 1)

            def body(i):
                for g in range(2):
                    act.wait_ge(tr_done, 2 * i + g + 1)
                    nc.scalar.activation(tok[:, g, :, :, :], bank[:, 5:8, :, :].rearrange("c n p s -> c p n s"),
                                         ACT.Copy).then_inc(tok_done, 1)
                for l in range(NV):
                    for g in range(2):
                        act.wait_ge(x_mm, 2 * NV * i + 2 * l + g + 1)
                        nc.scalar.activation(xl[:, g, :, :], bank[:, g, :, :], ACT.Copy)
                        act.drain().then_inc(x_copied, 1)
                for g in range(2):
                    c = 2 * i + g
                    act.wait_ge(cx, c + 1)
                    nc.scalar.activation(xn[:, :, :], bank[:, 6, :, :], ACT.Copy, scale=-1.0).then_inc(cxn, 1)
                    act.wait_ge(cu, c + 1)
                    nc.scalar.activation(us[:, :, :], bank[:, 7, :, :], ACT.Copy).then_inc(cuc, 1)
                    act.wait_ge(cy, c + 1)
                    for a in range(2):
                        r = slice(64 * a, 64 * a + 64)
                        nc.scalar.activation(y[r, :, bass.ds(c * RW_C, RW_C)], bank[r, g, :, RW_C * a:RW_C * (a + 1)], ACT.Copy)
                act.drain().then_inc(y_out, 2)

            steps(act, body)

        @block.vector
        def _(dve):
            nc.vector.memset(s[:, :, :], 0.0)
            dve.drain().then_inc(s_done, 2)
            dve.wait_ge(tabs, 64)
            TT = nc.vector.tensor_tensor
            all_p = lambda x: x.unsqueeze(1).broadcast_to([P, PAIRS, P])

            def body(i):
                for g in range(2):
                    dve.wait_ge(sc_done, 2 * i + g + 1)
                    TT(lt[:, g, :, :, :], bank[:, 0:4, :, :], m4[:, :, :].unsqueeze(1).broadcast_to([P, PAIRS, 4, P]), ALU.mult)
                    TT(ti[:, g, :, :], bank[:, 4, :, :], all_p(n1[:, 0, :]), ALU.mult)
                    dve.drain()
                    TT(tt[:, g, :, :], lt[:, g, :, 0, :], all_p(n1[:, 1, :]), ALU.mult)
                    TT(ti[:, g, :, :], ti[:, g, :, :], all_p(ident[:, :]), ALU.add)
                    dve.drain()
                    TT(tt[:, g, :, :], tt[:, g, :, :], all_p(ident[:, :]), ALU.add)
                    dve.drain().then_inc(lt_done, 1)
                for l in range(NV):
                    for g in range(2):
                        dve.wait_ge(t_mm, 2 * NV * i + 2 * l + g + 1)
                        dve.sem_inc(off_used, 1)
                        TT(ti[:, g, :, :], ti[:, g, :, :], bank[:, 2 + g, :, :], ALU.subtract)
                        TT(tt[:, g, :, :], tt[:, g, :, :], bank[:, 4 + g, :, :], ALU.subtract)
                        dve.drain().then_inc(t_done, 1)
                for g in range(2):
                    c = 2 * i + g
                    dve.wait_ge(cy, c + 1)
                    TT(s[:, :, :], s[:, :, :], bank[:, 2 + g, :, :], ALU.add)
                    dve.drain()
                    for p in range(PAIRS):
                        nc.vector.tensor_scalar(s[:, p, :], s[:, p, :], ew[:, bass.ds(c, 1), p], None, ALU.mult)
                    dve.drain().then_inc(s_done, 1)

            steps(dve, body)


def finish_stage(core, late, y):
    nc = core.nc
    here, used = [core.sem(f"fin_here{b}") for b in range(2)], core.sem("fin_used")
    with ExitStack() as mem:
        x = mem.enter_context(nc.sbuf_tensor("fin_x", [P, 2, 2, SEQ], F32))
        block = mem.enter_context(core.block())

        @block.sync
        def _(sp):
            for m in range(4):
                if m >= 2:
                    sp.wait_ge(used, m - 1)
                for i in range(2):
                    sp.dma_start(x[:, m % 2, i, :], late[4 * i + m]).then_inc(here[m % 2], 16)

        @block.vector
        def _(dve):
            for m in range(4):
                dve.wait_ge(here[m % 2], 32 * (m // 2 + 1))
                nc.vector.tensor_tensor(y[:, m, :], y[:, m, :], x[:, m % 2, 1, :], ALU.add)
                dve.drain()
                nc.vector.tensor_tensor(y[:, m, :], y[:, m, :], x[:, m % 2, 0, :], ALU.mult)
                dve.drain().then_inc(used, 1)


def block_three(core, A, x_t, h_t, mats, vec, dram, stop):
    nc = core.nc
    ident = mats["ident"]
    z3, v_tok, qk = dram("z3", (30, P, SEQ)), dram("v_tok3", (SEQ, 512)), dram("qk3", (8, P, SEQ))
    rw = dram("rw_x", (RW_CH, P, KINDS, PAIRS, RW_C)), dram("rw_e", (P, RW_CH, PAIRS))
    late = dram("rw_late", (8, P, SEQ))
    T = slice(META, META + SEQ)
    acts = lambda src, off=META: (lambda k, at, w: src[:, k, off + at:off + at + w])
    row = lambda d, u: (lambda j: d[bass.ds(2 * j + u, 1)].rearrange("o p s -> p (o s)"))
    rms_stage(core, "rms3", x_t, h_t, vec["norm_mix"], 1e-6, META, SEQ)
    gemm_stage(core, "in3", [(A["w_in3"], acts(h_t), lambda j: 2 * j), (A["w_in3"], acts(h_t), lambda j: 2 * j + 1)],
               15, SEQ, None, plain_out(nc), out=[row(z3, 0), row(z3, 1)])
    rope_stage(core, "rope3", z3, qk, A["ret_tables"], mats["rot2"], 8, 0, SEQ)
    turn_stage(core, "turn3", lambda j: z3[8:12, :, bass.ds(P * j, P)].rearrange("t c s -> c t s"),
               lambda j: v_tok[bass.ds(P * j, P), :], 4, SEQ // P, ident)
    retention_stage(core, qk, v_tok, h_t[:, 0:4, T], A["ret_decay"], A["ret_start"], A["ret_end"], chunk_decays(), ident)
    norm_stage(core, "ret_norm", h_t[:, 0:4, T], [[k] for k in range(4)], mats["mean128"], 1e-5, True, vec["ret_norm"], None, ACT.Identity)
    gate_stage(core, "gate3", lambda i: z3[12 + i], h_t[:, 0:4, T], 4, ACT.Silu)
    if stop == "yret": return h_t[:, 0:4, T]
    rwkv_prep_stage(core, z3, mats, vec, A["rw_w2a2"], A["rw_g2"], rw, late)
    rwkv_stage(core, rw, h_t[:, 4:8, T], A["rw_mask4"], A["rw_neg1"], A["level_masks"], ident)
    norm_stage(core, "rw_norm", h_t[:, 4:8, T], [[k] for k in range(4)], mats["mean64"], 64e-5, True, vec["rw_ln_w"], vec["rw_ln_b"], ACT.Identity)
    finish_stage(core, late, h_t[:, 4:8, T])
    if stop == "yrw": return h_t[:, 4:8, T]
    gemm_stage(core, "out3", [(A["w_o3"], acts(h_t), lambda j: 2 * j), (A["w_o3"], acts(h_t), lambda j: 2 * j + 1)],
               4, SEQ, None, add_part(nc, x_t, META, SEQ))
    if stop == "x3a": return x_t[:, :, T]
    rms_stage(core, "rms3b", x_t, h_t, vec["norm_ffn"], 1e-6, META, SEQ)
    with ExitStack() as mem:
        g = mem.enter_context(nc.sbuf_tensor("b3_ff", [P, FT, SEQ], F32))

        def act_ff(act, u, j, ps, t):
            if u == 0:
                nc.scalar.activation(t["view"](t["s"][:, :]), ps, ACT.Silu)
            else:
                nc.scalar.activation(t["view"](t["up"][:, :]), ps, ACT.Copy)

        def dve_ff(dve, u, j, ps, t):
            r = g[:, bass.ds(j, 1), :].rearrange("p o s -> p (o s)")
            if u == 0:
                nc.vector.tensor_copy(r, t["s"][:, :])
            else:
                nc.vector.tensor_tensor(r, r, t["up"][:, :], ALU.mult)

        gemm_stage(core, "up3", [(A["w_gate3"], acts(h_t), lambda j: j), (A["w_up3"], acts(h_t), lambda j: j)],
                   FT, SEQ, act_ff, dve_ff, temps=[("s", SEQ), ("up", SEQ)])
        gemm_stage(core, "down3", [(A["w_down3"], acts(g, 0), lambda j: 2 * j), (A["w_down3"], acts(g, 0), lambda j: 2 * j + 1)],
                   4, SEQ, None, add_part(nc, x_t, META, SEQ))
    rms_stage(core, "rms3c", x_t, h_t, vec["norm_ple"], 1e-6, META, SEQ)
    with ExitStack() as mem:
        p_t = mem.enter_context(nc.sbuf_tensor("b3_p", [P, 2, SEQ], F32))
        load_stage(core, "p", [(p_t[:, :, :], A["p3"].rearrange("(k p) s -> p k s", p=P))])

        def act_ple(act, u, j, ps, t):
            if u == 0:
                nc.scalar.activation(t["view"](t["gate"][:, :]), ps, ACT.Sigmoid)
            else:
                nc.scalar.activation(t["view"](t["up"][:, :]), ps, ACT.Copy)

        def dve_ple(dve, u, j, ps, t):
            if u == 0:
                nc.vector.tensor_copy(t["gate_sb"][:, :], t["gate"][:, :])
            else:
                x_row = x_t[:, bass.ds(j, 1), T].rearrange("p o s -> p (o s)")
                nc.vector.tensor_tensor(t["gate_sb"][:, :], t["gate_sb"][:, :], t["up"][:, :], ALU.mult)
                dve.drain()
                nc.vector.tensor_tensor(x_row, x_row, t["gate_sb"][:, :], ALU.add)

        gemm_stage(core, "ple", [(A["w_ple_gate"], acts(h_t), lambda j: j), (A["w_ple_up"], acts(p_t, 0), lambda j: j)],
                   8, SEQ, act_ple, dve_ple, temps=[("gate", SEQ), ("up", SEQ), ("gate_sb", SEQ)])
    rms_stage(core, "rms3f", x_t, x_t, vec["final_norm3"], 1e-6, META, SEQ)


def log_gammas():
    return np.log(np.float32(1.0) - np.float32(2.0) ** (-5.0 - np.arange(RET_H, dtype=np.float32))).astype(np.float64)


def chunk_decays():
    return [float(np.exp(g * RET_C)) for g in log_gammas()]


def retention_tables():
    ang = (np.float32(1.0) / (np.float32(10000.0) ** np.linspace(0.0, 1.0, RET_D // 2, dtype=np.float32))).astype(np.float32)
    phase = np.arange(SEQ, dtype=np.float32)[None] * np.repeat(ang, 2)[:, None]
    tables = np.stack([np.cos(phase), np.sin(phase)], axis=1).astype(np.float32)
    g = log_gammas()
    j, i = np.arange(P)[:, None, None], np.arange(P)[None, None]
    scale = RET_D ** -0.5
    decay = np.where(i >= j, np.exp(g[None, :, None] * np.maximum(i - j, 0)), 0.0) * scale
    start = np.broadcast_to(np.exp(g[None, :, None] * (i + 1.0)), (P, RET_H, P))
    end = np.exp(g[None] * (P - 1 - np.arange(P)[:, None])) * scale
    return tables, decay.astype(np.float32), np.ascontiguousarray(start.astype(np.float32)), end.astype(np.float32)


def rwkv_masks():
    s, t = np.arange(P)[:, None], np.arange(P)[None]
    strict, incl = (s < t).astype(np.float32), (s <= t).astype(np.float32)
    one = ((s // 2 == t // 2) & (s < t)).astype(np.float32)
    return np.ascontiguousarray(np.stack([strict, incl, strict, incl], axis=1)), np.ascontiguousarray(np.stack([-one.T, -one], axis=1))


def start_stage(core, loads):
    nc = core.nc
    here = core.sem("start_here")
    with core.block() as block:
        @block.sync
        def _(sp):
            for dst, src in loads:
                sp.dma_start(dst, src).then_inc(here, 16)
            sp.wait_ge(here, 16 * len(loads))

        @block.vector
        def _(dve):
            for value, tile in core.eps.items():
                nc.vector.memset(tile, value)


def copy_part(nc):
    def part(act, u, j, ps, t):
        nc.scalar.activation(t["view"](t[f"raw{u}"][:, :]), ps, ACT.Copy)
    return part


def plain_out(nc, bias=None):
    def part(dve, u, j, ps, t):
        if bias is None:
            nc.vector.tensor_copy(t["view"](t["out"][:, u, :]), ps)
        else:
            nc.vector.tensor_scalar(t["view"](t["out"][:, u, :]), ps, bias[:, bass.ds(2 * j + u, 1)], None, ALU.add)
    return part


def add_part(nc, x_t, c0, total):
    def part(dve, u, j, ps, t):
        row = t["view"](x_t[:, bass.ds(2 * j + u, 1), c0:c0 + total].rearrange("p o s -> p (o s)"))
        nc.vector.tensor_tensor(row, ps, row, ALU.add)
    return part


def block_one(core, A, x_t, h_t, mats, vec, dram, stop):
    nc = core.nc
    T = slice(META, META + SEQ)
    hcols = h_t[:, :, T]
    x_main, y = x_t[:, :, T], h_t[:, :, T]
    z1, v_tok, ya_tok, ya = dram("z1", (24, P, SEQ)), dram("v_tok", (SEQ, 256)), dram("ya_tok", (SEQ, 256)), dram("ya", (2, P, SEQ))
    ident = mats["ident"]
    load_stage(core, "x", [(x_main, A["x"].rearrange("(k p) s -> p k s", p=P))])
    rms_stage(core, "rms1", x_t, h_t, vec["norm_g"], 1e-6, META, SEQ)
    acts = lambda src: (lambda k, at, w: src[:, k, META + at:META + at + w])
    gemm_stage(core, "in1", [(A["w_in"], acts(h_t), lambda j: 2 * j), (A["w_in"], acts(h_t), lambda j: 2 * j + 1)],
               12, SEQ, None, plain_out(nc),
               out=[lambda j: z1[bass.ds(2 * j, 1)].rearrange("o p s -> p (o s)"),
                    lambda j: z1[bass.ds(2 * j + 1, 1)].rearrange("o p s -> p (o s)")])
    if stop == "z1": return z1
    turn_stage(core, "turn_v", lambda j: z1[4:6, :, bass.ds(P * j, P)].rearrange("t c s -> c t s"),
               lambda j: v_tok[bass.ds(P * j, P), :], 2, SEQ // P, ident)
    na_stage(core, z1, v_tok, A["na_bias"], ya_tok, ident)
    turn_stage(core, "turn_y", lambda j: ya_tok[bass.ds(P * j, P), :].rearrange("s (t c) -> s t c", t=2),
               lambda j: ya[:, :, bass.ds(P * j, P)].rearrange("t c s -> c t s"), 2, SEQ // P, ident)
    if stop == "ya": return ya
    with ExitStack() as mem:
        sb = lambda n, s: mem.enter_context(nc.sbuf_tensor(f"b1_{n}", s, F32))
        v, u = sb("v", [P, 2, SEQ]), sb("u", [P, 2, SEQ])
        taps, pw, pool_w, ws, bs = sb("taps", [P, 2, CONV_W]), sb("pw", [P, 2, 2 * P]), sb("pool_w", [P, 2, 64]), sb("ws", [P, 4, P]), sb("bs", [P, 2, P])
        load_stage(core, "w1", [(taps[:, :, :], A["conv_w"]), (pw[:, :, :], A["conv_pw"]), (pool_w[:, :, :], A["pool_w"]),
                                (ws[:, :, :], A["sgu_w"]), (bs[:, :, :], A["sgu_b"]),
                                (h_t[:, 0:2, T], ya.rearrange("t c s -> c t s"))])
        conv_stage(core, z1, v, taps, vec["dw_b"])
        norm_stage(core, "ln_b", v, [[0, 1]], mats["mean256"], 1e-5, True, vec["conv_g"], vec["conv_b"], ACT.Silu)
        full = slice(0, P)
        product_stage(core, "pw", h_t[:, 2:4, T],
                      [[(pw[:, k, m * P:(m + 1) * P], full, full, k, k == 0, k == 1) for k in range(2)] for m in range(2)], v)
        pool_stage(core, z1, v, A["inv_count"])
        halves = [slice(0, 64), slice(64, 128)]
        product_stage(core, "pool_w", h_t[:, 4:6, T],
                      [[(pool_w[r, k, :], r, r, k, True, True) for r in halves] for k in range(2)], v, vec["pool_scale"])
        load_stage(core, "sgu", [(u[:, :, :], z1[12:14].rearrange("t c s -> c t s")),
                                 (v[:, :, :], z1[14:16].rearrange("t c s -> c t s"))], ACT.Gelu_apprx_tanh)
        norm_stage(core, "ln_d", v, [[0, 1]], mats["mean256"], 1e-5, True, vec["sgu_g"], vec["sgu_bb"], ACT.Identity)
        mix_stage(core, v, u, h_t[:, 6:8, T], ws, bs, ident)
    gate_stage(core, "gate1", lambda i: z1[16 + i], y, 8, ACT.Silu)
    gemm_stage(core, "out1", [(A["w_out"], acts(h_t), lambda j: 2 * j), (A["w_out"], acts(h_t), lambda j: 2 * j + 1)],
               4, SEQ, None, add_part(nc, x_t, META, SEQ))
    rms_stage(core, "rms1f", x_t, x_t, vec["final_g"], 1e-6, META, SEQ)


VECS = {}


def program(nc, A, out, stop=None):
    with ExitStack() as ctx:
        core = Core(nc)
        sb = lambda n, s: ctx.enter_context(nc.sbuf_tensor(n, s, F32))
        dram = lambda n, s: nc.dram_tensor(f"scratch_{n}", s, F32, kind="Internal").ap()
        x_t, h_t = sb("x_t", [P, KT, COLS]), sb("h_t", [P, KT, COLS])
        mat = sb("mats", [P, len(MATS), P])
        vecs = sb("vecs", [P, A["vecs"].shape[1]])
        core.eps = {e: sb(f"eps{i}", [P, 1])[:, :] for i, e in enumerate(EPSILONS)}
        mats = {name: mat[:, i, :] for i, name in enumerate(MATS)}
        vec, at = {}, 0
        for name, _, count in VEC_LIST:
            vec[name] = vecs[:, at:at + count]
            at += count
        start_stage(core, [(mat[:, :, :], A["mats"]), (vecs[:, :], A["vecs"])])
        res = block_one(core, A, x_t, h_t, mats, vec, dram, stop)
        if res is None and stop != "b1":
            res = block_two(core, A, x_t, h_t, mats, vec, dram, stop)
        if res is None and stop not in ("b1", "b2"):
            res = block_three(core, A, x_t, h_t, mats, vec, dram, stop)
        done = core.sem("out_done")
        with core.block() as block:
            @block.sync
            def _(sp):
                if res is not None:
                    sp.dma_start(out, res).then_inc(done, 16)
                else:
                    sp.dma_start(out.rearrange("(k p) s -> p k s", p=P), x_t[:, :, META:META + SEQ]).then_inc(done, 16)
                sp.wait_ge(done, 16)


EPSILONS = (1e-6, 1e-5, 64e-5)
MATS = ("ident", "mean256", "mean128", "mean64", "rope", "rot2", "causal")
VEC_LIST = [("norm_g", "norm_g", 8), ("dw_b", "conv_dw_b", 2), ("conv_g", "conv_ln_g", 2), ("conv_b", "conv_ln_b", 2),
            ("pool_scale", "pool_scale", 2), ("sgu_g", "sgu_ln_g", 2), ("sgu_bb", "sgu_ln_b", 2), ("final_g", "final_g", 8),
            ("mix_norm", "mix_norm_2", 8), ("b_in", "b_in_2", 34), ("b_alpha", "b_alpha_2", 2), ("gla_norm", "gla_head_norm_2", 4),
            ("ffn_norm", "ffn_norm_2", 8), ("ff_conv", "conv_w_2", 66), ("ff_conv_b", "conv_b_2", 22), ("final_norm2", "final_norm_2", 8),
            ("norm_mix", "norm_mix_w_3", 8), ("ret_norm", "ret_norm_w_3", 4), ("rw_mu", "rw_mu_3", 14), ("rw_w0", "rw_w0_3", 4),
            ("rw_a0", "rw_a0_3", 4), ("rw_kk", "rw_k_k_3", 4), ("rw_ka", "rw_k_a_3", 4), ("rw_rk", "rw_r_k_3", 4),
            ("rw_ln_w", "rw_ln_w_3", 4), ("rw_ln_b", "rw_ln_b_3", 4), ("norm_ffn", "norm_ffn_w_3", 8), ("norm_ple", "norm_ple_w_3", 8),
            ("final_norm3", "final_norm_w_3", 8)]


def tiles(w):
    k, n = w.shape
    return np.ascontiguousarray(w.reshape(k // P, P, n // P, P).transpose(2, 1, 0, 3).reshape(n // P, P, k))


def columns(v):
    return v.reshape(-1, P).T


def constants():
    i = np.arange(P)
    eye = np.eye(P, dtype=np.float32)
    rope = np.zeros((P, P), np.float32)
    for d in range(P):
        o = d % 64
        if o < 32:
            rope[d + 32, d] = -1
        else:
            rope[d - 32, d] = 1
    rot2 = np.zeros((P, P), np.float32)
    rot2[i[1::2], i[0::2]] = -1
    rot2[i[0::2], i[1::2]] = 1
    m = {"ident": eye, "mean256": np.full((P, P), 1 / 256, np.float32), "mean128": np.full((P, P), 1 / 128, np.float32),
         "mean64": ((i[:, None] // 64 == i[None] // 64) / 64).astype(np.float32), "rope": rope, "rot2": rot2,
         "causal": (i[:, None] <= i[None]).astype(np.float32)}
    return np.ascontiguousarray(np.stack([m[k] for k in MATS], axis=1))


def window_counts():
    t = np.arange(SEQ)
    out = np.zeros((P, 2, SEQ), np.float32)
    for g, w in enumerate((2, 4, 8, 16)):
        n = np.clip(t - w // 2 + w, 0, SEQ) - np.clip(t - w // 2, 0, SEQ)
        out[64 * (g % 2):64 * (g % 2) + 64, g // 2] = 1.0 / n.astype(np.float32)
    return out


def layout(i):
    c = np.ascontiguousarray
    A = {"x": c(i["x"][0].T), "w_in": tiles(i["w_in"][0]), "w_out": tiles(i["w_out"][0])}
    q, k = np.arange(GRID_W)[:, None], np.arange(GRID_W)[None]
    start = np.clip(q - NA_COLS // 2, 0, GRID_W - NA_COLS)
    ok = (k >= start) & (k < start + NA_COLS)
    rel = np.clip(k - q, 1 - NA_COLS, NA_COLS - 1) + NA_COLS - 1
    bias = i["na_rpb"][0][:, :, rel]
    bias = np.where(ok[None, None], bias, np.float32(NEG)).transpose(0, 2, 1, 3)
    A["na_bias"] = c(bias.reshape(4, 2, GRID_W, 15 * GRID_W).transpose(1, 2, 0, 3).reshape(P, 4, 15 * GRID_W))
    A["conv_w"] = c(i["conv_dw_w"][0].reshape(CONV_W, 2, P).transpose(2, 1, 0))
    A["conv_pw"] = c(i["conv_pw"][0].reshape(2, P, 256).transpose(1, 0, 2))
    A["pool_w"] = c(i["pool_w"][0].reshape(2, 2, 64, 64).transpose(1, 2, 0, 3).reshape(P, 2, 64))
    A["inv_count"] = window_counts()
    A["sgu_w"] = c(i["sgu_w"][0].transpose(2, 0, 1))
    A["sgu_b"] = c(np.repeat(i["sgu_b"][0].reshape(2, 2, P).transpose(1, 0, 2), 64, axis=0))
    A["mats"] = constants()
    i = dict(i)
    cols = order_two()
    A["meta"] = c(i["meta_tokens_2"].T.reshape(KT, P, META).transpose(1, 0, 2))
    A["w_in2"] = tiles(c(i["w_in_2"][0][:, cols]))
    low = slice(2304, 2320)
    A["w_low"] = c(i["w_in_2"][0][:, low].reshape(KT, P, 16).transpose(1, 0, 2))
    A["b_low"] = c(i["b_in_2"][0][low].reshape(16, 1))
    A["w_alpha"] = c(i["w_alpha_2"][0])
    i["b_in_2"] = i["b_in_2"][0][cols]
    i["gla_head_norm_2"] = np.tile(i["gla_head_norm_2"].reshape(-1), 4)
    A["level_masks"], A["swa_masks"], A["rope_tables"] = level_masks(), swa_masks(), rope_tables()
    A["sinks"] = c(i["attn_sinks_2"][0])
    A["w_att"], A["w_gla"], A["w_out2"] = (tiles(i[n][0]) for n in ("w_proj_attn_2", "w_proj_gla_2", "w_out_2"))
    A["w_up2"], A["w_down2"] = tiles(i["w_up_2"][0]), tiles(i["w_down_2"][0])
    A["ret_tables"], A["ret_decay"], A["ret_start"], A["ret_end"] = retention_tables()
    A["rw_mask4"], A["rw_neg1"] = rwkv_masks()
    A["p3"] = c(i["p_3"][0, 0].T)
    A["rw_w2a2"] = c(np.concatenate([i["rw_w2_3"][0], i["rw_a2_3"][0]], axis=0))
    A["rw_g2"] = c(i["rw_g2_3"][0])
    for name, src in (("w_in3", "w_in_3"), ("w_o3", "w_o_3"), ("w_gate3", "w_gate_3"), ("w_up3", "w_up_3"), ("w_down3", "w_down_3"),
                      ("w_ple_gate", "w_ple_gate_3"), ("w_ple_up", "w_ple_up_3")):
        A[name] = tiles(i[src][0])
    A["vecs"] = c(np.concatenate([columns(np.asarray(i[src]).reshape(-1)) for _, src, _ in VEC_LIST], axis=1))
    return A


def order_two():
    r = lambda a, n: list(range(a, a + n))
    return r(0, 512) + r(512, 128) + r(768, 256) + r(1024, 256) + r(640, 128) + r(1280, 512) + r(1792, 512) + r(2320, 2048)


def level_masks():
    i, j = np.arange(P)[None], np.arange(P)[:, None]
    m = [(i // (2 * s) == j // (2 * s)) & (j % (2 * s) < s) & (i % (2 * s) >= s) for s in LEVELS] + [i == j]
    return np.ascontiguousarray(np.stack(m, axis=1).astype(np.float32))


def swa_masks():
    q, k = np.arange(P)[:, None], np.arange(2 * P)[None]
    rel = q + P - k
    out = []
    for i in range(BLOCKS):
        pos = i * P + k - LEAD
        out.append(np.where((rel >= 0) & (rel < P) & (pos >= 0), 0.0, NEG))
    return np.stack(out).astype(np.float32)


def rope_tables():
    half = HEAD // 2
    inv = (np.float32(10000.0) ** (-np.arange(half, dtype=np.float32) / np.float32(half))).astype(np.float32)
    ang = np.arange(COLS, dtype=np.float32)[None] * inv[np.arange(P) % half][:, None]
    return np.ascontiguousarray(np.stack([np.cos(ang), np.sin(ang)], axis=1).astype(np.float32))


def kernel(**inputs):
    import concourse.bacc as bacc
    from concourse.bass_utils import run_bass_kernel_spmd

    arrays = layout({k: np.asarray(v) for k, v in inputs.items()})
    nc = bacc.Bacc("TRN2", target_bir_lowering=False, num_devices=1)
    A = {n: nc.dram_tensor(f"in_{n}", a.shape, F32, kind="ExternalInput").ap() for n, a in arrays.items()}
    out = nc.dram_tensor("out", (D, SEQ), F32, kind="ExternalOutput").ap()
    program(nc, A, out)
    r = run_bass_kernel_spmd(nc, [{f"in_{n}": a for n, a in arrays.items()}], core_ids=[0])
    return np.ascontiguousarray(r.results[0]["out"].T).reshape(1, SEQ, D)
```

```python
from contextlib import ExitStack, contextmanager

import numpy as np

import concourse.bass as bass
from concourse import mybir

F32 = mybir.dt.float32
F32R = mybir.dt.float32r
ALU = mybir.AluOpType
ACT = mybir.ActivationFunctionType
AX = mybir.AxisListType

P = 128
D = 1024
SEQ = 1024
META = 16
KT = D // P
LTOK = META + SEQ
COLS = LTOK + 4
NEG = -1.0e30


class Core:

    def __init__(self, nc):
        self.nc, self.now, self.before, self.eps = nc, [], [], {}

    def sem(self, name):
        self.now.append(self.nc.alloc_semaphore(name=name))
        return self.now[-1]

    @contextmanager
    def block(self):
        if self.before:
            self.nc.clear_and_free_semaphores(self.before)
        with self.nc.Block() as block:
            yield block
        self.before, self.now = self.now, []


def pieces(total):
    n = -(-total // 512)
    assert total % n == 0
    return n, total // n


def rms_stage(core, name, x_t, gain, eps, c0, total):
    nc = core.nc
    n, w = pieces(total)
    ready, squared, summed, root, summing = (core.sem(f"{name}_{s}") for s in ("ones", "squared", "summed", "root", "summing"))
    with ExitStack() as mem:
        sq = mem.enter_context(nc.sbuf_tensor(f"{name}_sq", [P, 2, total], F32))
        total_sq = mem.enter_context(nc.sbuf_tensor(f"{name}_total", [P, total], F32))
        rstd = mem.enter_context(nc.sbuf_tensor(f"{name}_rstd", [P, total], F32))
        ones = mem.enter_context(nc.sbuf_tensor(f"{name}_ones", [P, P], F32))
        ss = mem.enter_context(nc.psum_tensor(f"{name}_ss", [P, n, 512], F32))
        block = mem.enter_context(core.block())
        cols = slice(c0, c0 + total)

        @block.scalar
        def _(act):
            for k in range(KT):
                if k >= 2:
                    act.wait_ge(summing, k - 1)
                nc.scalar.activation(sq[:, k % 2, :], x_t[:, k, cols], ACT.Square).then_inc(squared, 1)
            act.wait_ge(summed, 1)
            nc.scalar.activation(rstd[:, :].rearrange("p (c w) -> p c w", c=n), ss[:, :, 0:w], ACT.Sqrt,
                                 scale=1.0 / D, bias=core.eps[eps]).then_inc(root, 1)

        @block.tensor
        def _(pe):
            pe.wait_ge(ready, 1)
            pe.wait_ge(summing, KT)
            for c in range(n):
                last = nc.tensor.matmul(ss[:, c, 0:w], ones[:, :], total_sq[:, c * w:(c + 1) * w], start=True, stop=True)
            last.then_inc(summed, 1)

        @block.vector
        def _(dve):
            nc.vector.memset(ones[:, :], 1.0).then_inc(ready, 1)
            add_squares(dve, nc, total_sq, sq, squared, summing)
            dve.wait_ge(root, 1)
            nc.vector.reciprocal(rstd[:, :], rstd[:, :])
            dve.drain()
            for k in range(KT):
                nc.vector.scalar_tensor_tensor(out=x_t[:, k, cols], in0=x_t[:, k, cols], scalar=gain[:, k:k + 1], in1=rstd[:, :],
                                               op0=ALU.mult, op1=ALU.mult)


def add_squares(dve, nc, total_sq, sq, squared, summing, between=lambda k: None):
    for k in range(KT):
        dve.wait_ge(squared, k + 1)
        if k == 0:
            nc.vector.tensor_copy(total_sq[:, :], sq[:, 0, :])
        else:
            nc.vector.tensor_tensor(total_sq[:, :], total_sq[:, :], sq[:, k % 2, :], ALU.add)
        dve.drain().then_inc(summing, 1)
        between(k)


def rms_split_stage(core, name, x_t, out, rms, gain, eps, c0, total):
    nc = core.nc
    n, w = pieces(total)
    ready, squared, summed, rounded, summing = (core.sem(f"{name}_{s}") for s in ("ones", "squared", "summed", "rounded", "summing"))
    with ExitStack() as mem:
        sq = mem.enter_context(nc.sbuf_tensor(f"{name}_sq", [P, 2, total], F32))
        total_sq = mem.enter_context(nc.sbuf_tensor(f"{name}_total", [P, total], F32))
        ones = mem.enter_context(nc.sbuf_tensor(f"{name}_ones", [P, P], F32))
        ss = mem.enter_context(nc.psum_tensor(f"{name}_ss", [P, n, 512], F32))
        block = mem.enter_context(core.block())
        cols = slice(c0, c0 + total)

        @block.scalar
        def _(act):
            for k in range(KT):
                if k >= 2:
                    act.wait_ge(summing, k - 1)
                nc.scalar.activation(sq[:, k % 2, :], x_t[:, k, cols], ACT.Square).then_inc(squared, 1)
                nc.scalar.activation(out[0][:, k, cols], x_t[:, k, cols], ACT.Copy, scale=gain[:, k:k + 1]).then_inc(rounded, 1)
            act.wait_ge(summed, 1)
            nc.scalar.activation(rms[:, :].rearrange("p (c w) -> p c w", c=n), ss[:, :, 0:w], ACT.Sqrt,
                                 scale=1.0 / D, bias=core.eps[eps])

        @block.tensor
        def _(pe):
            pe.wait_ge(ready, 1)
            pe.wait_ge(summing, KT)
            for c in range(n):
                last = nc.tensor.matmul(ss[:, c, 0:w], ones[:, :], total_sq[:, c * w:(c + 1) * w], start=True, stop=True)
            last.then_inc(summed, 1)

        @block.vector
        def _(dve):
            nc.vector.memset(ones[:, :], 1.0).then_inc(ready, 1)

            def low(k):
                dve.wait_ge(rounded, k + 1)
                nc.vector.scalar_tensor_tensor(out=out[1][:, k, cols], in0=x_t[:, k, cols], scalar=gain[:, k:k + 1],
                                               in1=out[0][:, k, cols].bitcast(F32), op0=ALU.mult, op1=ALU.subtract)

            add_squares(dve, nc, total_sq, sq, squared, summing, low)


def split_stage(core, name, src, out):
    nc = core.nc
    high, low = core.sem(f"{name}_high"), core.sem(f"{name}_low")
    with core.block() as block:
        @block.scalar
        def _(act):
            for k in range(src.shape[1]):
                nc.scalar.activation(out[0][:, k, :], src[:, k, :], ACT.Copy).then_inc(high, 1)

        @block.vector
        def _(dve):
            for k in range(src.shape[1]):
                dve.wait_ge(high, k + 1)
                nc.vector.tensor_tensor(out[1][:, k, :], src[:, k, :], out[0][:, k, :].bitcast(F32), ALU.subtract).then_inc(low, 1)


def gemm_stage(core, name, units, steps, total, act_part, dve_part, out=None, extras=(), temps=(), chained=False, rms=None):
    nc = core.nc
    n, w = pieces(total)
    kts = [wt.shape[2] // P for wt, _, _ in units]
    mm_done, act_done, unit_done, w_high, w_split = (
        core.sem(f"{name}_{s}") for s in ("mm_done", "act_done", "unit_done", "w_high", "w_split"))
    w_here, x_here, stored = ([core.sem(f"{name}_{s}{u}") for u in range(2)] for s in ("w_here", "x_here", "stored"))
    AHEAD = 2
    with ExitStack() as mem:
        wb = [mem.enter_context(nc.sbuf_tensor(f"{name}_w{u}", [P, kts[u], P], F32)) for u in range(2)]
        wh = [mem.enter_context(nc.sbuf_tensor(f"{name}_wh{u}", [P, kts[u], P], F32R)) for u in range(2)]
        wl = [mem.enter_context(nc.sbuf_tensor(f"{name}_wl{u}", [P, kts[u], P], F32R)) for u in range(2)]
        ps = mem.enter_context(nc.psum_tensor(f"{name}_ps", [P, 2, n, 512], F32))
        t = {k: mem.enter_context(nc.sbuf_tensor(f"{name}_{k}", [P, size], F32)) for k, size in temps}
        for u, _, k in extras:
            t[k] = mem.enter_context(nc.sbuf_tensor(f"{name}_{k}", [P, total], F32))
        if out:
            t["out"] = mem.enter_context(nc.sbuf_tensor(f"{name}_out", [P, 2, total], F32))
        view = lambda a: a.rearrange("p (c w) -> p c w", c=n)
        t["view"] = view
        nx = [sum(1 for e in extras if e[0] == u) for u in range(2)]
        has_out = [bool(out and out[u]) for u in range(2)]
        block = mem.enter_context(core.block())

        @block.sync
        def _(sp):
            def load(j, u):
                wt, _, at = units[u]
                sp.dma_start(wb[u][:, :, :], wt[bass.ds(at(j), 1)].rearrange("o p (k c) -> p (o k) c", c=P)
                             ).then_inc(w_here[u], 16)

            def load_extras(j, u):
                for ux, rows, k in extras:
                    if ux == u:
                        sp.dma_start(t[k][:, :], rows(j)).then_inc(x_here[u], 16)

            def step(j, more):
                for u in range(2):
                    if more:
                        sp.wait_ge(w_split, 2 * j + u + 1)
                        load(j + 1, u)
                    if has_out[u] or (nx[u] and more):
                        sp.wait_ge(unit_done, 2 * j + u + 1 + AHEAD)
                    if has_out[u]:
                        sp.dma_start(out[u](j), t["out"][:, u, :]).then_inc(stored[u], 16)
                    if more:
                        load_extras(j + 1, u)

            for u in range(2):
                load(0, u)
                load_extras(0, u)
            if steps > 1:
                with sp.Fori(0, steps - 1) as j:
                    step(j, True)
            step(steps - 1, False)
            for u in range(2):
                if has_out[u]:
                    sp.wait_ge(stored[u], 16 * (steps + 1))

        @block.tensor
        def _(pe):
            pe.sem_inc(mm_done, AHEAD)
            with pe.Fori(0, steps) as j:
                for u in range(2):
                    pe.wait_ge(w_split, 2 * j + u + 1)
                    pe.wait_ge(unit_done, 2 * j + u + 1)
                    for c in range(n):
                        for k in range(kts[u]):
                            x_high, x_low = units[u][1](k, c * w, w)
                            for i, (a, x) in enumerate(((wh, x_high), (wh, x_low), (wl, x_high))):
                                last = nc.tensor.matmul(ps[:, u, c, 0:w], a[u][:, k, :], x, start=(k == 0 and i == 0),
                                                        stop=(k == kts[u] - 1 and i == 2))
                    last.then_inc(mm_done, 1)

        def lagged(eng, split, part, before=None):
            split(0, 0)
            if before:
                before()

            def step(j, more):
                split(j, 1)
                part(j, 0)
                if more:
                    split(j + 1, 0)
                part(j, 1)

            if steps > 1:
                with eng.Fori(0, steps - 1) as j:
                    step(j, True)
            step(steps - 1, False)

        @block.scalar
        def _(act):
            def split(j, u):
                act.wait_ge(w_here[u], 16 * (j + 1))
                act.wait_ge(mm_done, 2 * j + u + 1)
                nc.scalar.activation(wh[u][:, :, :], wb[u][:, :, :], ACT.Copy).then_inc(w_high, 1)

            def part(j, u):
                if act_part is None or (chained and u == 0):
                    return
                act.wait_ge(mm_done, 2 * j + u + 1 + AHEAD)
                act.wait_ge(unit_done, 2 * j + u + 1 + (1 if chained else 0))
                if nx[u]:
                    act.wait_ge(x_here[u], 16 * nx[u] * (j + 1))
                act_part(act, u, j, ps[:, u, :, 0:w], t)
                act.drain().then_inc(act_done, 1)

            lagged(act, split, part)

        @block.vector
        def _(dve):
            dve.sem_inc(unit_done, AHEAD)
            for u in range(2):
                if has_out[u]:
                    dve.sem_inc(stored[u], 16)

            def split(j, u):
                dve.wait_ge(w_high, 2 * j + u + 1)
                nc.vector.tensor_tensor(wl[u][:, :, :], wb[u][:, :, :], wh[u][:, :, :].bitcast(F32), ALU.subtract).then_inc(w_split, 1)

            def part(j, u):
                if chained and u:
                    dve.wait_ge(act_done, j + 1)
                elif act_part and not chained:
                    dve.wait_ge(act_done, 2 * j + u + 1)
                else:
                    dve.wait_ge(mm_done, 2 * j + u + 1 + AHEAD)
                if nx[u]:
                    dve.wait_ge(x_here[u], 16 * nx[u] * (j + 1))
                if has_out[u]:
                    dve.wait_ge(stored[u], 16 * (j + 1))
                dve_part(dve, u, j, ps[:, u, :, 0:w], t)
                dve.drain().then_inc(unit_done, 1)

            def invert():
                nc.vector.reciprocal(rms[:, :], rms[:, :])
                dve.drain()

            lagged(dve, split, part, invert if rms is not None else None)


def turn_stage(core, name, load, store, blocks, steps, ident):
    nc = core.nc
    loaded, stored = ([core.sem(f"{name}_{s}{b}") for b in range(2)] for s in ("loaded", "stored"))
    turned, copied = core.sem(f"{name}_turned"), core.sem(f"{name}_copied")
    AHEAD = 2
    assert steps % 2 == 0 and blocks <= 8
    with ExitStack() as mem:
        src = mem.enter_context(nc.sbuf_tensor(f"{name}_src", [P, 2, blocks, P], F32))
        dst = mem.enter_context(nc.sbuf_tensor(f"{name}_dst", [P, 2, blocks * P], F32))
        ps = mem.enter_context(nc.psum_tensor(f"{name}_ps", [P, 2, -(-blocks // 4) * 4 * P], F32))
        block = mem.enter_context(core.block())

        @block.sync
        def _(sp):
            with sp.Fori(0, steps // 2) as jj:
                for b in range(2):
                    j = 2 * jj + b
                    sp.wait_ge(copied, j + 1)
                    sp.dma_start(src[:, b, :, :], load(j)).then_inc(loaded[b], 16)

        @block.tensor
        def _(pe):
            with pe.Fori(0, steps // 2) as jj:
                for b in range(2):
                    j = 2 * jj + b
                    pe.wait_ge(loaded[b], 16 * (jj + 1))
                    pe.wait_ge(copied, j + 1)
                    for c in range(blocks):
                        last = nc.tensor.transpose(ps[:, b, c * P:(c + 1) * P], src[:, b, c, :], ident[:, :])
                    last.then_inc(turned, 1)

        @block.vector
        def _(dve):
            dve.sem_inc(copied, AHEAD)
            for b in range(2):
                dve.sem_inc(stored[b], 16)
            with dve.Fori(0, steps // 2) as jj:
                for b in range(2):
                    j = 2 * jj + b
                    dve.wait_ge(turned, j + 1)
                    dve.wait_ge(stored[b], 16 * (jj + 1))
                    nc.vector.tensor_copy(dst[:, b, :], ps[:, b, 0:blocks * P]).then_inc(copied, 1)

        @block.scalar
        def _(act):
            with act.Fori(0, steps // 2) as jj:
                for b in range(2):
                    j = 2 * jj + b
                    act.wait_ge(copied, j + 1 + AHEAD)
                    act.dma_start(store(j), dst[:, b, :]).then_inc(stored[b], 16)
            for b in range(2):
                act.wait_ge(stored[b], 16 * (steps // 2 + 1))


NA_HEADS, GRID_W, NA_ROWS, NA_COLS = 8, 64, 8, 16
GRID_H = SEQ // GRID_W
NA_DH = 32
BAND = NA_ROWS * GRID_W


def na_stage(core, z, v_tok, bias, ya_tok, ident):
    nc = core.nc
    DR = 2 * NA_ROWS - 1
    PAIRS = NA_HEADS // 2
    ROWS = 4
    UNITS = ROWS * PAIRS
    TURN_LAG, OUT_LAG = 2, 3
    s_done, p_done, t_done, c_done, o_done, y_done, m_done, row_scored, q_done, qk_here, v_here, bias_here = (
        core.sem(f"na_{s}") for s in ("scores", "probs", "turned", "copied", "outs", "ys", "softmaxed", "row_scored",
                                      "queries", "qk_here", "v_here", "bias"))
    y_stored = [core.sem(f"na_stored{b}") for b in range(2)]
    ranges = [(0, 1, lambda r: 0, lambda r: (NA_ROWS - 1 - r) * GRID_W),
              (1, 3, lambda r: r - NA_ROWS // 2, lambda r: (NA_ROWS // 2 - 1) * GRID_W),
              (3, 4, lambda r: GRID_H - NA_ROWS, lambda r: (GRID_H - 1 - r) * GRID_W)]
    with ExitStack() as mem:
        sb = lambda n, s: mem.enter_context(nc.sbuf_tensor(f"na_{n}", s, F32))
        q = sb("q", [P, 2, SEQ])
        kb = sb("k", [P, 2, SEQ])
        v = [sb(f"v{a}", [P, SEQ // P - a, 2 * P]) for a in range(2)]
        qz = sb("qz", [P, 2, PAIRS, P])
        bt = sb("bias_t", [P, PAIRS, DR * GRID_W])
        sc = sb("sc", [P, PAIRS, BAND])
        pr = sb("pr", [P, PAIRS, BAND])
        pt = sb("pt", [P, PAIRS, 4, P])
        st = sb("st", [P, 3, 2, PAIRS])
        y = sb("y", [P, 2, PAIRS, NA_DH])
        ps_s = mem.enter_context(nc.psum_tensor("na_ps_s", [P, PAIRS, BAND], F32))
        ps_t = mem.enter_context(nc.psum_tensor("na_ps_t", [P, 2, 4, P], F32))
        ps_o = mem.enter_context(nc.psum_tensor("na_ps_o", [P, 2, 512], F32))
        block = mem.enter_context(core.block())

        def bodies(eng, body):
            for lo, hi, start, first in ranges:
                if hi - lo == 1:
                    body(lo, start, first)
                else:
                    with eng.Fori(lo, hi) as g:
                        body(g, start, first)

        def pipeline(stages):
            for s in range(UNITS + OUT_LAG):
                for lag, stage in stages:
                    if 0 <= s - lag < UNITS:
                        stage((s - lag) // PAIRS, (s - lag) % PAIRS)

        @block.sync
        def _(sp):
            sp.dma_start(q[:, :, :], z[0:2].rearrange("t c s -> c t s")).then_inc(qk_here, 16)
            sp.dma_start(kb[:, :, :], z[2:4].rearrange("t c s -> c t s")).then_inc(qk_here, 16)
            for a in range(2):
                sp.dma_start(v[a][:, :, :], v_tok[GRID_W * a:SEQ - GRID_W * a].rearrange("(t p) c -> p t c", p=P)
                             ).then_inc(v_here, 16)
            yr = ya_tok.rearrange("(r w) (p a d) -> a r w p d", w=GRID_W, a=2, d=NA_DH)

            def body(g, start, first):
                for i in range(ROWS):
                    r = ROWS * g + i
                    sp.wait_ge(y_done, PAIRS * ROWS * g + PAIRS * (i + 1) + 2)
                    for a in range(2):
                        sp.dma_start(yr[a, bass.ds(r, 1)].rearrange("o w p d -> (o w) p d"),
                                     y[64 * a:64 * a + 64, i % 2, :, :]).then_inc(y_stored[i % 2], 16)

            bodies(sp, body)
            for b in range(2):
                sp.wait_ge(y_stored[b], 32 * (GRID_H // 2 + 1))

        @block.tensor
        def _(pe):
            pe.wait_ge(qk_here, 32)

            def body(g, start, first):
                def scores(i, p):
                    if p == 0:
                        pe.wait_ge(q_done, ROWS * g + i + 1)
                    pe.wait_ge(m_done, UNITS * g + PAIRS * i + p + 1)
                    nc.tensor.matmul(ps_s[:, p, :], qz[:, i % 2, p, :],
                                     kb[:, p // 2, bass.ds(start(ROWS * g + i) * GRID_W, BAND)], start=True, stop=True).then_inc(s_done, 1)

                def turn(i, p):
                    u = UNITS * g + PAIRS * i + p
                    pe.wait_ge(p_done, u + 1)
                    pe.wait_ge(c_done, u + 1)
                    for c in range(4):
                        last = nc.tensor.transpose(ps_t[:, p % 2, c, :], pr[:, p, c * P:(c + 1) * P], ident[:, :])
                    last.then_inc(t_done, 1)

                def outs(i, p):
                    u = UNITS * g + PAIRS * i + p
                    if lo_start(g, i) is None:
                        odd, tile = i % 2, lambda c: bass.ds(2 * g + (i // 2 + c - 2), 1)
                    else:
                        odd, tile = 0, lambda c: slice(lo_start(g, i) + c, lo_start(g, i) + c + 1)
                    pe.wait_ge(c_done, u + 3)
                    pe.wait_ge(y_done, u + 1)
                    for c in range(4):
                        last = nc.tensor.matmul(ps_o[:, p % 2, 0:64], pt[:, p, c, :],
                                                v[odd][:, tile(c), 64 * p:64 * p + 64].rearrange("k o d -> k (o d)"),
                                                start=(c == 0), stop=(c == 3))
                    last.then_inc(o_done, 1)

                def lo_start(g, i):
                    return start(0) // 2 if isinstance(g, int) else None

                if isinstance(g, int) and g == 0:
                    pe.wait_ge(v_here, 32)
                pipeline(((0, scores), (TURN_LAG, turn), (OUT_LAG, outs)))

            bodies(pe, body)

        @block.scalar
        def _(act):
            act.dma_start(bt[:, :, :], bias).then_inc(bias_here, 16)
            act.sem_inc(c_done, 2)

            def body(g, start, first):
                def probs(i, p):
                    act.wait_ge(m_done, UNITS * g + PAIRS * i + p + PAIRS + 1)
                    nc.scalar.activation(pr[:, p, :], sc[:, p, :], ACT.Exp, bias=st[:, 0, i % 2, p:p + 1],
                                         accum_out=st[:, 1, i % 2, p:p + 1]).then_inc(p_done, 1)

                def copy(i, p):
                    act.wait_ge(t_done, UNITS * g + PAIRS * i + p + 1)
                    nc.scalar.activation(pt[:, p, :, :], ps_t[:, p % 2, :, :], ACT.Copy).then_inc(c_done, 1)

                pipeline(((0, probs), (TURN_LAG, copy)))

            bodies(act, body)

        @block.vector
        def _(dve):
            dve.sem_inc(m_done, PAIRS)
            dve.sem_inc(y_done, 2)
            dve.sem_inc(row_scored, 2)
            for b in range(2):
                dve.sem_inc(y_stored[b], 32)
            dve.wait_ge(bias_here, 16)

            def body(g, start, first):
                def softmax(i, p):
                    dve.wait_ge(s_done, UNITS * g + PAIRS * i + p + 1)
                    at = first(ROWS * g + i)
                    nc.vector.scalar_tensor_tensor(out=sc[:, p, :], in0=ps_s[:, p, :], scalar=NA_DH ** -0.5,
                                                   in1=bt[:, p, at:at + BAND], op0=ALU.mult, op1=ALU.add)
                    dve.drain()
                    nc.vector.tensor_reduce(st[:, 0, i % 2, p:p + 1], sc[:, p, :], AX.X, ALU.max, negate=True)
                    dve.drain().then_inc(m_done, 1)
                    if p == PAIRS - 1:
                        dve.sem_inc(row_scored, 1)

                def norm(i, p):
                    dve.wait_ge(o_done, UNITS * g + PAIRS * i + p + 1)
                    if p == 0:
                        dve.wait_ge(y_stored[i % 2], ROWS * 16 * g + 32 * (i // 2 + 1))
                    nc.vector.reciprocal(st[:, 2, i % 2, p:p + 1], st[:, 1, i % 2, p:p + 1])
                    dve.drain()
                    for a in range(2):
                        rows_a = slice(64 * a, 64 * a + 64)
                        nc.vector.tensor_scalar(y[rows_a, i % 2, p, :], ps_o[rows_a, p % 2, NA_DH * a:NA_DH * (a + 1)],
                                                st[rows_a, 2, i % 2, p:p + 1], None, ALU.mult)
                    dve.drain().then_inc(y_done, 1)

                pipeline(((0, softmax), (OUT_LAG, norm)))

            bodies(dve, body)

        @block.gpsimd
        def _(pool):
            nc.gpsimd.memset(qz[:, :, :, :], 0.0)
            pool.drain()
            pool.wait_ge(qk_here, 32)

            def body(g, start, first):
                for i in range(ROWS):
                    r = ROWS * g + i
                    pool.wait_ge(row_scored, r + 1)
                    for h in range(PAIRS):
                        at = NA_DH * h
                        nc.gpsimd.tensor_copy(qz[at:at + NA_DH, i % 2, h // 2::2, 64 * (h % 2):64 * (h % 2) + 64],
                                              q[at:at + NA_DH, :, bass.ds(r * GRID_W, GRID_W)])
                    pool.drain().then_inc(q_done, 1)

            bodies(pool, body)




def norm_stage(core, name, v, groups, stat, eps, mean, scale, bias, func):
    nc = core.nc
    total = v.shape[2]
    n, w = pieces(total)
    m_done, sub, squared, v_done, root, normed, ended = (
        core.sem(f"{name}_{s}") for s in ("mean", "centred", "squared", "var", "root", "normed", "ended"))
    with ExitStack() as mem:
        sq = mem.enter_context(nc.sbuf_tensor(f"{name}_sq", [P, len(groups[0]), total], F32))
        rstd = mem.enter_context(nc.sbuf_tensor(f"{name}_rstd", [P, total], F32))
        ps = mem.enter_context(nc.psum_tensor(f"{name}_ps", [P, 2, n, 512], F32))
        cut = lambda a: a.rearrange("p (c w) -> p c w", c=n)
        block = mem.enter_context(core.block())

        @block.tensor
        def _(pe):
            for g, tiles in enumerate(groups):
                if mean:
                    if g:
                        pe.wait_ge(sub, g)
                    for c in range(n):
                        for i, k in enumerate(tiles):
                            last = nc.tensor.matmul(ps[:, 0, c, 0:w], stat, v[:, k, c * w:(c + 1) * w],
                                                    start=(i == 0), stop=(i == len(tiles) - 1))
                    last.then_inc(m_done, 1)
                pe.wait_ge(squared, g + 1)
                for c in range(n):
                    for i, k in enumerate(tiles):
                        last = nc.tensor.matmul(ps[:, 1, c, 0:w], stat, sq[:, i, c * w:(c + 1) * w],
                                                start=(i == 0), stop=(i == len(tiles) - 1))
                last.then_inc(v_done, 1)

        @block.vector
        def _(dve):
            for g, tiles in enumerate(groups):
                if mean:
                    dve.wait_ge(m_done, g + 1)
                    for k in tiles:
                        nc.vector.tensor_tensor(cut(v[:, k, :]), cut(v[:, k, :]), ps[:, 0, :, 0:w], ALU.subtract)
                    dve.drain().then_inc(sub, 1)
                dve.wait_ge(root, g + 1)
                nc.vector.reciprocal(rstd[:, :], rstd[:, :])
                dve.drain()
                for k in tiles:
                    nc.vector.tensor_tensor(v[:, k, :], v[:, k, :], rstd[:, :], ALU.mult)
                dve.drain().then_inc(normed, 1)

        @block.scalar
        def _(act):
            for g, tiles in enumerate(groups):
                if mean:
                    act.wait_ge(sub, g + 1)
                for i, k in enumerate(tiles):
                    nc.scalar.activation(sq[:, i, :], v[:, k, :], ACT.Square)
                act.drain().then_inc(squared, 1)
                act.wait_ge(v_done, g + 1)
                nc.scalar.activation(cut(rstd[:, :]), ps[:, 1, :, 0:w], ACT.Sqrt, bias=core.eps[eps]).then_inc(root, 1)
                act.wait_ge(normed, g + 1)
                for k in tiles:
                    nc.scalar.activation(v[:, k, :], v[:, k, :], func, scale=scale[:, k:k + 1],
                                         bias=bias[:, k:k + 1] if bias is not None else 0.0)
                act.drain().then_inc(ended, 1)


CONV_W = 31


def conv_stage(core, z, v, taps, dw_b):
    nc = core.nc
    half = CONV_W // 2
    here, sig = core.sem("conv_here"), core.sem("conv_sigmoid")
    with ExitStack() as mem:
        a = mem.enter_context(nc.sbuf_tensor("conv_a", [P, 2, SEQ + 2 * half], F32))
        b = mem.enter_context(nc.sbuf_tensor("conv_b", [P, 2, SEQ], F32))
        zero = core.sem("conv_zero")
        block = mem.enter_context(core.block())

        @block.sync
        def _(sp):
            sp.dma_start(a[:, :, half:half + SEQ], z[6:8].rearrange("t c s -> c t s")).then_inc(here, 16)
            sp.dma_start(b[:, :, :], z[8:10].rearrange("t c s -> c t s")).then_inc(here, 16)

        @block.scalar
        def _(act):
            act.wait_ge(here, 32)
            nc.scalar.activation(b[:, :, :], b[:, :, :], ACT.Sigmoid).then_inc(sig, 1)

        @block.vector
        def _(dve):
            nc.vector.memset(a[:, :, 0:half], 0.0)
            nc.vector.memset(a[:, :, half + SEQ:], 0.0)
            dve.wait_ge(sig, 1)
            nc.vector.tensor_tensor(a[:, :, half:half + SEQ], a[:, :, half:half + SEQ], b[:, :, :], ALU.mult)
            dve.drain()
            for k in range(2):
                nc.vector.tensor_scalar(v[:, k, :], a[:, k, 0:SEQ], taps[:, k, 0:1], dw_b[:, k:k + 1],
                                        ALU.mult, ALU.add)
            dve.drain()
            with dve.Fori(1, CONV_W) as i:
                for k in range(2):
                    nc.vector.scalar_tensor_tensor(out=v[:, k, :], in0=a[:, k, bass.ds(i, SEQ)],
                                                   scalar=taps[:, k, bass.ds(i, 1)], in1=v[:, k, :],
                                                   op0=ALU.mult, op1=ALU.add)
                    dve.drain()


def product_stage(core, name, out, mats, v, scale=None):
    nc = core.nc
    n, w = pieces(v.shape[2])
    done = core.sem(f"{name}_done")
    with ExitStack() as mem:
        ps = mem.enter_context(nc.psum_tensor(f"{name}_ps", [P, len(mats), n, 512], F32))
        block = mem.enter_context(core.block())

        @block.tensor
        def _(pe):
            for m, parts in enumerate(mats):
                for c in range(n):
                    for lhs, rows, orows, k, first, end in parts:
                        last = nc.tensor.matmul(ps[orows, m, c, 0:w], lhs, v[rows, k, c * w:(c + 1) * w],
                                                start=first, stop=end)
                last.then_inc(done, 1)

        @block.vector
        def _(dve):
            for m in range(len(mats)):
                dve.wait_ge(done, m + 1)
                o = out[:, m, :].rearrange("p (c w) -> p c w", c=n)
                if scale is None:
                    nc.vector.tensor_copy(o, ps[:, m, :, 0:w])
                else:
                    nc.vector.tensor_scalar(o, ps[:, m, :, 0:w], scale[:, m:m + 1], None, ALU.mult)


def pool_stage(core, z, v, inv_count):
    nc = core.nc
    E = 8
    here = core.sem("pool_here")
    with ExitStack() as mem:
        x = mem.enter_context(nc.sbuf_tensor("pool_x", [P, 2, SEQ + 2 * E], F32))
        s = [mem.enter_context(nc.sbuf_tensor(f"pool_s{i}", [P, 2, SEQ + 2 * E], F32)) for i in range(3)]
        inv = mem.enter_context(nc.sbuf_tensor("pool_inv", [P, 2, SEQ], F32))
        block = mem.enter_context(core.block())

        @block.sync
        def _(sp):
            sp.dma_start(x[:, :, E:E + SEQ], z[10:12].rearrange("t c s -> c t s")).then_inc(here, 16)
            sp.dma_start(inv[:, :, :], inv_count).then_inc(here, 16)

        @block.vector
        def _(dve):
            nc.vector.memset(x[:, :, 0:E], 0.0)
            nc.vector.memset(x[:, :, E + SEQ:], 0.0)
            dve.drain()
            dve.wait_ge(here, 32)
            end = SEQ + 2 * E
            top, low = slice(64, 128), slice(0, 64)
            add = lambda out, a, b: nc.vector.tensor_tensor(out, a, b, ALU.add)
            s2, s4, s8 = s
            add(s2[:, :, 1:end], x[:, :, 0:end - 1], x[:, :, 1:end])
            dve.drain()
            add(s4[:, :, 2:end - 1], s2[:, :, 1:end - 2], s2[:, :, 3:end])
            dve.drain()
            add(s8[:, 1, 4:end - 3], s4[:, 1, 2:end - 5], s4[:, 1, 6:end - 1])
            dve.drain()
            tok = slice(E, E + SEQ)
            mul = lambda out, a, b: nc.vector.tensor_tensor(out, a, b, ALU.mult)
            mul(v[low, 0, :], s2[low, 0, tok], inv[low, 0, :])
            mul(v[top, 0, :], s4[top, 0, tok], inv[top, 0, :])
            mul(v[low, 1, :], s8[low, 1, tok], inv[low, 1, :])
            add(v[top, 1, :], s8[top, 1, E - 4:E - 4 + SEQ], s8[top, 1, E + 4:E + 4 + SEQ])
            dve.drain()
            mul(v[top, 1, :], v[top, 1, :], inv[top, 1, :])
            dve.drain()
            nc.vector.tensor_tensor(v[:, :, :], v[:, :, :], x[:, :, tok], ALU.subtract)


def load_stage(core, name, loads, func=None):
    nc = core.nc
    here = [core.sem(f"{name}_here{i}") for i in range(len(loads))]
    with ExitStack() as mem:
        block = mem.enter_context(core.block())

        @block.sync
        def _(sp):
            for (dst, src), h in zip(loads, here):
                sp.dma_start(dst, src).then_inc(h, 16)
            if func is None:
                for h in here:
                    sp.wait_ge(h, 16)

        @block.scalar
        def _(act):
            if func is not None:
                for (dst, _), h in zip(loads, here):
                    act.wait_ge(h, 16)
                    nc.scalar.activation(dst, dst, func)


SGU_HEADS, SGU_CHUNK = 4, 128


def mix_stage(core, v, u, y, ws, bs, ident):
    nc = core.nc
    chunks = SEQ // SGU_CHUNK
    turned, copied, mixed, added = (core.sem(f"mix_{s}") for s in ("turned", "copied", "mixed", "added"))
    with ExitStack() as mem:
        vt = mem.enter_context(nc.sbuf_tensor("mix_vt", [P, 2, 2 * P], F32))
        m = mem.enter_context(nc.sbuf_tensor("mix_m", [P, 2, P], F32))
        ps_t = mem.enter_context(nc.psum_tensor("mix_ps_t", [P, 2, 512], F32))
        ps_m = mem.enter_context(nc.psum_tensor("mix_ps_m", [P, 2, 512], F32))
        block = mem.enter_context(core.block())

        @block.tensor
        def _(pe):
            for i in range(chunks):
                b, tok = i % 2, slice(i * P, (i + 1) * P)
                if i >= 2:
                    pe.wait_ge(copied, i - 1)
                for k in range(2):
                    last = nc.tensor.transpose(ps_t[:, b, k * P:(k + 1) * P], v[:, k, tok], ident[:, :])
                last.then_inc(turned, 1)
                pe.wait_ge(copied, i + 1)
                if i >= 2:
                    pe.wait_ge(added, i - 1)
                for h in range(SGU_HEADS):
                    a, k = 64 * (h % 2), h // 2
                    last = nc.tensor.matmul(ps_m[a:a + 64, b, k * P:(k + 1) * P], vt[:, b, 64 * h:64 * h + 64],
                                            ws[:, h, :], start=True, stop=True)
                last.then_inc(mixed, 1)

        @block.scalar
        def _(act):
            for i in range(chunks):
                act.wait_ge(turned, i + 1)
                nc.scalar.activation(vt[:, i % 2, :], ps_t[:, i % 2, 0:2 * P], ACT.Copy).then_inc(copied, 1)

        @block.vector
        def _(dve):
            for i in range(chunks):
                tok = slice(i * P, (i + 1) * P)
                dve.wait_ge(mixed, i + 1)
                nc.vector.tensor_tensor(m[:, :, :], ps_m[:, i % 2, 0:2 * P].rearrange("p (k s) -> p k s", k=2),
                                        bs[:, :, :], ALU.add)
                dve.drain().then_inc(added, 1)
                nc.vector.tensor_tensor(y[:, :, tok], u[:, :, tok], m[:, :, :], ALU.mult)
                dve.drain()


def gate_stage(core, name, z, y, tiles, func):
    nc = core.nc
    here = [core.sem(f"{name}_here{b}") for b in range(2)]
    opened, used = core.sem(f"{name}_opened"), core.sem(f"{name}_used")
    total = y.shape[2]
    with ExitStack() as mem:
        g = mem.enter_context(nc.sbuf_tensor(f"{name}_g", [P, 2, total], F32))
        block = mem.enter_context(core.block())

        @block.sync
        def _(sp):
            for i in range(tiles):
                if i >= 2:
                    sp.wait_ge(used, i - 1)
                sp.dma_start(g[:, i % 2, :], z(i)).then_inc(here[i % 2], 16)

        @block.scalar
        def _(act):
            for i in range(tiles):
                act.wait_ge(here[i % 2], 16 * (i // 2 + 1))
                nc.scalar.activation(g[:, i % 2, :], g[:, i % 2, :], func).then_inc(opened, 1)

        @block.vector
        def _(dve):
            for i in range(tiles):
                dve.wait_ge(opened, i + 1)
                nc.vector.tensor_tensor(y[:, i, :], y[:, i, :], g[:, i % 2, :], ALU.mult).then_inc(used, 1)


LEAD = 240
WIDE = LEAD + COLS
AHEADS, HEAD, KV = 8, 64, 2
BLOCKS = 9


def zero_stage(core, x_t, meta, z2, width):
    nc = core.nc
    here, zeroed = core.sem("zero_here"), core.sem("zeroed")
    with nc.sbuf_tensor("zero_row", [P, 1, LEAD], F32) as zero, core.block() as block:
        @block.sync
        def _(sp):
            with nc.allow_non_contiguous_dma(reason="16 columns of each row"):
                sp.dma_start(x_t[:, :, 0:META], meta).then_inc(here, 16)
            sp.wait_ge(zeroed, 1)
            sp.dma_start(z2[0:width, :, 0:LEAD].rearrange("t c s -> c t s"), zero[:, :, :].broadcast_to([P, width, LEAD])
                         ).then_inc(here, 16)
            sp.wait_ge(here, 32)

        @block.vector
        def _(dve):
            nc.vector.memset(x_t[:, :, LTOK:COLS], 0.0)
            nc.vector.memset(zero[:, :, :], 0.0).then_inc(zeroed, 1)


def rope_stage(core, name, z, qk, tables, perm, count, lead, total):
    nc = core.nc
    n, w = pieces(total)
    here = [core.sem(f"{name}_here{b}") for b in range(2)]
    tab, rotated, ended, stored = (core.sem(f"{name}_{s}") for s in ("tables", "rotated", "ended", "stored"))
    with ExitStack() as mem:
        cs = mem.enter_context(nc.sbuf_tensor(f"{name}_cs", [P, 2, total], F32))
        x = mem.enter_context(nc.sbuf_tensor(f"{name}_x", [P, 2, total], F32))
        o = mem.enter_context(nc.sbuf_tensor(f"{name}_o", [P, count, lead + total], F32))
        r = mem.enter_context(nc.sbuf_tensor(f"{name}_r", [P, total], F32))
        ps = mem.enter_context(nc.psum_tensor(f"{name}_ps", [P, 2, n, 512], F32))
        block = mem.enter_context(core.block())

        @block.sync
        def _(sp):
            sp.dma_start(cs[:, :, :], tables).then_inc(tab, 16)
            for i in range(count):
                if i >= 2:
                    sp.wait_ge(ended, i - 1)
                sp.dma_start(x[:, i % 2, :], z[i]).then_inc(here[i % 2], 16)
            sp.wait_ge(ended, count)
            sp.dma_start(qk.rearrange("t c s -> c t s"), o[:, :, :]).then_inc(stored, 16)
            sp.wait_ge(stored, 16)

        @block.tensor
        def _(pe):
            for i in range(count):
                pe.wait_ge(here[i % 2], 16 * (i // 2 + 1))
                if i >= 2:
                    pe.wait_ge(ended, i - 1)
                for c in range(n):
                    last = nc.tensor.matmul(ps[:, i % 2, c, 0:w], perm, x[:, i % 2, c * w:(c + 1) * w], start=True, stop=True)
                last.then_inc(rotated, 1)

        @block.vector
        def _(dve):
            if lead:
                nc.vector.memset(o[:, :, 0:lead], 0.0)
            dve.wait_ge(tab, 16)
            cut = lambda a: a.rearrange("p (c w) -> p c w", c=n)
            for i in range(count):
                dve.wait_ge(rotated, i + 1)
                nc.vector.tensor_tensor(cut(r[:, :]), ps[:, i % 2, :, 0:w], cut(cs[:, 1, :]), ALU.mult)
                nc.vector.tensor_tensor(o[:, i, lead:], x[:, i % 2, :], cs[:, 0, :], ALU.mult)
                dve.drain()
                nc.vector.tensor_tensor(o[:, i, lead:], o[:, i, lead:], r[:, :], ALU.add)
                dve.drain().then_inc(ended, 1)


def swa_stage(core, qk, v_tok, masks, sinks, yatt, ident):
    nc = core.nc
    G = AHEADS // KV
    s_done, m_done, p_done, n_done, t_done, c_done, o_done, y_done, used, zero, sinks_here = (
        core.sem(f"swa_{s}") for s in ("scores", "maxed", "probs", "normed", "turned", "copied", "outs", "ys", "used", "zero", "sinks"))
    row_here, y_stored, y_free = ([core.sem(f"swa_{s}{b}") for b in range(2)] for s in ("row", "stored", "free"))
    with ExitStack() as mem:
        sb = lambda n, s: mem.enter_context(nc.sbuf_tensor(f"swa_{n}", s, F32))
        q = sb("q", [P, 2, 4, P])
        kk = sb("kk", [P, 2, KV, 2, 2 * P])
        vb = sb("v", [P, 2, 2, P])
        mk = sb("mask", [P, 2, 2 * P])
        sk = sb("sinks", [P, AHEADS])
        sc = sb("sc", [P, 2, G, 2 * P])
        st = sb("st", [P, 2, 6, G])
        pt = sb("pt", [P, 2, 2, G, P])
        y = sb("y", [64, 2, KV, G, P])
        ps_s = mem.enter_context(nc.psum_tensor("swa_ps_s", [P, 2, G, 2 * P], F32))
        ps_t = mem.enter_context(nc.psum_tensor("swa_ps_t", [P, 2, G, P], F32))
        ps_o = mem.enter_context(nc.psum_tensor("swa_ps_o", [64, G, P], F32))
        block = mem.enter_context(core.block())

        def blocks(eng, body):
            with eng.Fori(0, BLOCKS // 2) as ii:
                for b in range(2):
                    body(2 * ii + b, ii, b)
            body(BLOCKS - 1, BLOCKS // 2, 0)

        @block.sync
        def _(sp):
            sp.dma_start(sk[:, :], sinks.partition_broadcast(P)).then_inc(sinks_here, 16)
            sp.wait_ge(zero, 1)

            def body(i, ii, b):
                sp.wait_ge(used, i + 1)
                at = i * P
                sp.dma_start(q[:, b, :, :], qk[0:4, :, bass.ds(at + P, P)].rearrange("t c s -> c t s")).then_inc(row_here[b], 16)
                for a in range(2):
                    sp.dma_start(kk[64 * a:64 * a + 64, b, :, a, :],
                                 qk[4].rearrange("(g c) s -> c g s", g=KV)[:, :, bass.ds(at, 2 * P)]).then_inc(row_here[b], 16)
                sp.dma_start(vb[:, b, :, :], v_tok[bass.ds(at, 2 * P), 0:P].rearrange("(t s) c -> s t c", t=2)).then_inc(row_here[b], 16)
                sp.dma_start(mk[:, b, :], masks[bass.ds(i, 1)].rearrange("o q k -> (o q) k")).then_inc(row_here[b], 16)

            blocks(sp, body)

        @block.gpsimd
        def _(pool):
            nc.gpsimd.memset(kk[:, :, :, :, :], 0.0).then_inc(zero, 1)
            yv = yatt.rearrange("(g h d) s -> d g h s", g=KV, h=G)

            def body(i, ii, b):
                pool.wait_ge(y_done, 2 * (i + 1) + 1)
                for g in range(KV):
                    pool.dma_start(yv[:, g, :, bass.ds(i * P, P)], y[:, b, g, :, :]).then_inc(y_stored[b], 16)
                pool.wait_ge(y_stored[b], 32 * (ii + 1))
                pool.sem_inc(y_free[b], 1)

            blocks(pool, body)

        @block.tensor
        def _(pe):
            def body(i, ii, b):
                pe.wait_ge(row_here[b], 80 * (ii + 1))
                for g in range(KV):
                    u = 2 * i + g
                    pe.wait_ge(m_done, u + 1)
                    for t in range(2):
                        last = nc.tensor.matmul(ps_s[:, g, 2 * t:2 * t + 2, :], q[:, b, 2 * g + t, :], kk[:, b, g, :, :],
                                                start=True, stop=True)
                    last.then_inc(s_done, 1)
                for g in range(KV):
                    u = 2 * i + g
                    pe.wait_ge(n_done, u + 1)
                    pe.wait_ge(c_done, u + 1)
                    for k in range(2):
                        for h in range(G):
                            last = nc.tensor.transpose(ps_t[:, k, h, :], sc[:, g, h, k * P:(k + 1) * P], ident[:, :])
                    last.then_inc(t_done, 1)
                    pe.wait_ge(c_done, u + 2)
                    pe.wait_ge(y_done, u + 1)
                    for k in range(2):
                        last = nc.tensor.matmul(ps_o[:, :, :], vb[:, b, k, 64 * g:64 * g + 64], pt[:, g, k, :, :],
                                                start=(k == 0), stop=(k == 1))
                    last.then_inc(o_done, 1)

            blocks(pe, body)

        @block.scalar
        def _(act):
            act.sem_inc(c_done, 1)

            def body(i, ii, b):
                for g in range(KV):
                    u = 2 * i + g
                    act.wait_ge(m_done, u + 3)
                    for h in range(G):
                        nc.scalar.activation(sc[:, g, h, :], sc[:, g, h, :], ACT.Exp, bias=st[:, g, 1, h:h + 1],
                                             accum_out=st[:, g, 2, h:h + 1])
                    nc.scalar.activation(st[:, g, 4, :], st[:, g, 3, :], ACT.Exp)
                    act.drain().then_inc(p_done, 1)
                for g in range(KV):
                    u = 2 * i + g
                    act.wait_ge(t_done, u + 1)
                    nc.scalar.activation(pt[:, g, :, :, :], ps_t[:, :, :, :], ACT.Copy).then_inc(c_done, 1)

            blocks(act, body)

        @block.vector
        def _(dve):
            dve.sem_inc(m_done, 2)
            dve.sem_inc(y_done, 1)
            dve.sem_inc(used, 2)
            dve.wait_ge(sinks_here, 16)

            def body(i, ii, b):
                for g in range(KV):
                    u = 2 * i + g
                    dve.wait_ge(s_done, u + 1)
                    if g == 0:
                        dve.wait_ge(row_here[b], 80 * (ii + 1))
                    nc.vector.scalar_tensor_tensor(out=sc[:, g, :, :], in0=ps_s[:, g, :, :], scalar=HEAD ** -0.5,
                                                   in1=mk[:, b:b + 1, :].broadcast_to([P, G, 2 * P]), op0=ALU.mult, op1=ALU.add)
                    dve.drain()
                    nc.vector.tensor_reduce(st[:, g, 0, :], sc[:, g, :, :], AX.X, ALU.max)
                    dve.drain()
                    nc.vector.tensor_tensor(st[:, g, 0, :], st[:, g, 0, :], sk[:, G * g:G * g + G], ALU.max)
                    dve.drain()
                    nc.vector.tensor_scalar(st[:, g, 1, :], st[:, g, 0, :], -1.0, None, ALU.mult)
                    nc.vector.tensor_tensor(st[:, g, 3, :], sk[:, G * g:G * g + G], st[:, g, 0, :], ALU.subtract)
                    dve.drain().then_inc(m_done, 1)
                for g in range(KV):
                    u = 2 * i + g
                    dve.wait_ge(p_done, u + 1)
                    nc.vector.tensor_tensor(st[:, g, 5, :], st[:, g, 2, :], st[:, g, 4, :], ALU.add)
                    dve.drain()
                    nc.vector.reciprocal(st[:, g, 5, :], st[:, g, 5, :])
                    dve.drain()
                    for h in range(G):
                        nc.vector.tensor_scalar(sc[:, g, h, :], sc[:, g, h, :], st[:, g, 5, h:h + 1], None, ALU.mult)
                    dve.drain().then_inc(n_done, 1)
                dve.wait_ge(y_free[b], ii + 1)
                for g in range(KV):
                    u = 2 * i + g
                    dve.wait_ge(o_done, u + 1)
                    nc.vector.tensor_copy(y[:, b, g, :, :], ps_o[:, :, :]).then_inc(y_done, 1)
                dve.sem_inc(used, 1)

            for b in range(2):
                dve.sem_inc(y_free[b], 1)
            blocks(dve, body)


LEVELS = (64, 32, 16, 8, 4, 2, 1)
NL = len(LEVELS)
GLA_H, GLA_DV = 4, 128


def decay_stage(core, h, inverse, w_low, w_alpha, b_low, b_alpha, la):
    nc = core.nc
    n, w = pieces(COLS)
    low_done, low_here, z_done, z_here, soft = (core.sem(f"decay_{s}") for s in ("low_mm", "low", "z_mm", "z", "soft"))
    with ExitStack() as mem:
        low = mem.enter_context(nc.sbuf_tensor("decay_low", [16, COLS], F32))
        z = mem.enter_context(nc.sbuf_tensor("decay_z", [P, 2, COLS], F32))
        e = mem.enter_context(nc.sbuf_tensor("decay_e", [P, 2, COLS], F32))
        ps = mem.enter_context(nc.psum_tensor("decay_ps", [P, 2, n, 512], F32))
        cut = lambda a: a.rearrange("p (c w) -> p c w", c=n)
        block = mem.enter_context(core.block())

        @block.tensor
        def _(pe):
            for c in range(n):
                for k in range(KT):
                    for i, part in enumerate(h):
                        last = nc.tensor.matmul(ps[0:16, 0, c, 0:w], w_low[:, k, :], part[:, k, c * w:(c + 1) * w].bitcast(F32),
                                                start=(k == 0 and i == 0), stop=(k == KT - 1 and i == 1))
            last.then_inc(low_done, 1)
            pe.wait_ge(low_here, 1)
            for m in range(2):
                for c in range(n):
                    last = nc.tensor.matmul(ps[:, m, c, 0:w], w_alpha[:, m * P:(m + 1) * P], low[:, c * w:(c + 1) * w],
                                            start=True, stop=True)
                last.then_inc(z_done, 1)

        @block.vector
        def _(dve):
            nc.vector.memset(la[:, :, 0:LEAD - P], 0.0)
            dve.wait_ge(low_done, 1)
            nc.vector.tensor_tensor(cut(low[:, :]), ps[0:16, 0, :, 0:w], cut(inverse[0:16, :]), ALU.mult)
            dve.drain()
            nc.vector.tensor_scalar(low[:, :], low[:, :], b_low, None, ALU.add).then_inc(low_here, 1)
            for m in range(2):
                dve.wait_ge(z_done, m + 1)
                nc.vector.tensor_scalar(cut(z[:, m, :]), ps[:, m, :, 0:w], b_alpha[:, m:m + 1], None, ALU.add)
            dve.drain().then_inc(z_here, 1)
            dve.wait_ge(soft, 1)
            nc.vector.tensor_scalar(z[:, :, :], z[:, :, :], 0.0, None, ALU.min)
            dve.drain()
            nc.vector.tensor_tensor(z[:, :, :], z[:, :, :], e[:, :, :], ALU.subtract)
            dve.drain()
            nc.vector.tensor_scalar(la[:, :, LEAD - P:], z[:, :, 0:LTOK], 1.0 / 16, None, ALU.mult)

        @block.scalar
        def _(act):
            act.wait_ge(z_here, 1)
            nc.scalar.activation(e[:, :, :], z[:, :, :], ACT.Abs)
            act.drain()
            nc.scalar.activation(e[:, :, :], e[:, :, :], ACT.Exp, scale=-1.0)
            act.drain()
            nc.scalar.activation(e[:, :, :], e[:, :, :], ACT.Ln, bias=1.0).then_inc(soft, 1)


def gla_stage(core, z2, v_tok, la, y, pad, level_masks, ident):
    nc = core.nc
    d_done, e_done, k_done, a_done, m_done, t_done, c_done, o_done, y_done, u_done, s_done, q_here, seen = (
        core.sem(f"gla_{s}") for s in ("diffs", "exps", "scaled", "scores", "masked", "turned", "copied", "outs", "ys",
                                       "update", "state", "here", "seen"))
    v_here = [core.sem(f"gla_v{b}") for b in range(2)]
    with ExitStack() as mem:
        sb = lambda n, s: mem.enter_context(nc.sbuf_tensor(f"gla_{n}", s, F32))
        q, k = sb("q", [P, 2, BLOCKS * P]), sb("k", [P, 2, BLOCKS * P])
        one = sb("one", [P, P])
        e = sb("e", [P, NL + 2, 2, P])
        qz = sb("qz", [P, NL + 2, 2, 2, P])
        ke = sb("ke", [P, NL + 1, 2, P])
        kd = sb("kd", [P, 2, P])
        kt = sb("kt", [P, 2, P])
        bs = sb("bs", [P, 2, P])
        v = sb("v", [P, 2, GLA_H * GLA_DV])
        a_t = sb("a_t", [P, GLA_H, P])
        mk = sb("mk", [P, NL + 1, P])
        s = sb("s", [P, GLA_H, GLA_DV])
        ps_a = mem.enter_context(nc.psum_tensor("gla_ps_a", [P, 2, GLA_H, P], F32))
        ps_t = mem.enter_context(nc.psum_tensor("gla_ps_t", [P, 512], F32))
        ps_o = mem.enter_context(nc.psum_tensor("gla_ps_o", [P, GLA_H, P], F32))
        ps_u = mem.enter_context(nc.psum_tensor("gla_ps_u", [P, 2, 2 * P], F32))
        block = mem.enter_context(core.block())

        def chunks(eng, body):
            body(0, 0, 1)
            with eng.Fori(0, BLOCKS // 2) as ii:
                body(2 * ii + 1, 1, ii + 1)
                body(2 * ii + 2, 0, ii + 2)

        @block.sync
        def _(sp):
            cols = slice(P, P + BLOCKS * P)
            sp.dma_start(q[:, :, :], z2[5:7, :, cols].rearrange("t c s -> c t s")).then_inc(q_here, 16)
            sp.dma_start(k[:, :, :], z2[7:9, :, cols].rearrange("t c s -> c t s")).then_inc(q_here, 16)
            sp.dma_start(mk[:, :, :], level_masks).then_inc(q_here, 16)

            def load(c, b):
                sp.dma_start(v[:, b, :], v_tok[bass.ds(c * P + P, P), P:]).then_inc(v_here[b], 16)

            load(0, 0)
            load(1, 1)
            with sp.Fori(0, (BLOCKS - 3) // 2) as ii:
                for b in range(2):
                    sp.wait_ge(s_done, 2 * ii + b + 1)
                    load(2 * ii + b + 2, b)
            sp.wait_ge(s_done, BLOCKS - 2)
            load(BLOCKS - 1, 0)

        @block.tensor
        def _(pe):
            def body(c, b, turn):
                pe.wait_ge(k_done, c + 1)
                for t in range(2):
                    last = nc.tensor.transpose(ps_t[:, t * P:(t + 1) * P], kd[:, t, :], ident[:, :])
                last.then_inc(t_done, 1)
                for l in range(NL + 1):
                    if l >= 2:
                        pe.wait_ge(m_done, c * (NL + 1) + l - 1)
                    for t in range(2):
                        last = nc.tensor.matmul(ps_a[:, l % 2, 2 * t:2 * t + 2, :], ke[:, l, t, :],
                                                qz[:, l if l < NL else NL + 1, t, :, :], start=True, stop=True)
                    last.then_inc(a_done, 1)
                pe.wait_ge(v_here[b], 16 * turn)
                pe.wait_ge(m_done, (c + 1) * (NL + 1))
                if not isinstance(c, int):
                    pe.wait_ge(s_done, c)
                    pe.wait_ge(y_done, c)
                for h in range(GLA_H):
                    nc.tensor.matmul(ps_o[:, h, :], v[:, b, h * GLA_DV:(h + 1) * GLA_DV], a_t[:, h, :], start=True, stop=False)
                    last = nc.tensor.matmul(ps_o[:, h, :], s[:, h, :], qz[:, NL, h // 2, h % 2, :], start=False, stop=True)
                last.then_inc(o_done, 1)
                pe.wait_ge(c_done, c + 1)
                for t in range(2):
                    last = nc.tensor.matmul(ps_u[:, t, :], kt[:, t, :], v[:, b, 2 * t * P:2 * (t + 1) * P], start=True, stop=True)
                last.then_inc(u_done, 1)

            chunks(pe, body)

        @block.scalar
        def _(act):
            def body(c, b, turn):
                act.wait_ge(d_done, c + 1)
                nc.scalar.activation(e[:, :, :, :], e[:, :, :, :], ACT.Exp).then_inc(e_done, 1)
                act.wait_ge(t_done, c + 1)
                nc.scalar.activation(kt[:, :, :], ps_t[:, 0:2 * P].rearrange("p (t s) -> p t s", t=2), ACT.Copy).then_inc(c_done, 1)
                act.wait_ge(o_done, c + 1)
                if isinstance(c, int):
                    nc.scalar.activation(y[:, :, 0:META], ps_o[:, :, P - META:P], ACT.Copy, scale=0.125).then_inc(y_done, 1)
                else:
                    nc.scalar.activation(y[:, :, bass.ds(c * P + (META - P), P)], ps_o[:, :, :], ACT.Copy,
                                         scale=0.125).then_inc(y_done, 1)

            chunks(act, body)

        @block.vector
        def _(dve):
            nc.vector.memset(pad, 0.0)
            for tile, value in ((one[:, :], 1.0), (qz[:, :, :, :, :], 0.0), (a_t[:, :, :], 0.0), (s[:, :, :], 0.0)):
                nc.vector.memset(tile, value)
            dve.drain()
            dve.wait_ge(q_here, 48)
            halves = [slice(0, 64), slice(64, 128)]
            TT = nc.vector.tensor_tensor

            def body(c, b, turn):
                cols = bass.ds(c * P, P)
                for t in range(2):
                    nc.vector.tensor_tensor_scan(bs[:, t, :], one[:, :], la[:, t, cols], 0.0, ALU.mult, ALU.add)
                dve.drain()
                for l, half in enumerate(LEVELS):
                    cut = lambda a: a.rearrange("p t (n r) -> p t n r", r=2 * half)
                    mid = cut(bs[:, :, :])[:, :, :, half - 1:half].broadcast_to([P, 2, P // (2 * half), half])
                    src, dst = cut(bs[:, :, :]), cut(e[:, l, :, :])
                    TT(dst[:, :, :, 0:half], mid, src[:, :, :, 0:half], ALU.subtract)
                    TT(dst[:, :, :, half:], src[:, :, :, half:], mid, ALU.subtract)
                nc.vector.tensor_copy(e[:, NL, :, :], bs[:, :, :])
                TT(e[:, NL + 1, :, :], bs[:, :, P - 1:P].broadcast_to([P, 2, P]), bs[:, :, :], ALU.subtract)
                dve.drain().then_inc(d_done, 1)
                dve.wait_ge(e_done, c + 1)
                TT(kd[:, :, :], k[:, :, cols], e[:, NL + 1, :, :], ALU.mult)
                TT(ke[:, 0:NL, :, :], k[:, :, cols].unsqueeze(1).broadcast_to([P, NL, 2, P]), e[:, 0:NL, :, :], ALU.mult)
                nc.vector.tensor_copy(ke[:, NL, :, :], k[:, :, cols])
                for a, r in enumerate(halves):
                    TT(qz[r, 0:NL + 1, :, a, :], q[r, :, cols].unsqueeze(1).broadcast_to([64, NL + 1, 2, P]),
                       e[r, 0:NL + 1, :, :], ALU.mult)
                    nc.vector.tensor_copy(qz[r, NL + 1, :, a, :], q[r, :, cols])
                dve.drain().then_inc(k_done, 1)
                for l in range(NL + 1):
                    dve.wait_ge(a_done, c * (NL + 1) + l + 1)
                    dve.sem_inc(seen, 1)
                    nc.vector.copy_predicated(a_t[:, :, :], mk[:, l:l + 1, :].bitcast(mybir.dt.int32).broadcast_to([P, GLA_H, P]),
                                              ps_a[:, l % 2, :, :])
                    dve.drain().then_inc(m_done, 1)
                dve.wait_ge(u_done, c + 1)
                for h in range(GLA_H):
                    t, a = h // 2, h % 2
                    r = halves[a]
                    nc.vector.scalar_tensor_tensor(out=s[r, h, :], in0=s[r, h, :], scalar=e[r, NL, t, P - 1:P],
                                                   in1=ps_u[r, t, a * P:(a + 1) * P], op0=ALU.mult, op1=ALU.add)
                dve.drain().then_inc(s_done, 1)

            chunks(dve, body)


FF = 2816
FT = FF // P
FF_PARTS = ((0, 8), (8, 7), (15, 7))


def block_two(core, A, x_t, mats, vec, dram, stop):
    nc = core.nc
    ident = mats["ident"]
    z2, v_tok, qk, yatt = dram("z2", (34, P, WIDE)), dram("v_tok2", (LEAD + LTOK, 640)), dram("qk", (5, P, WIDE)), dram("yatt", (512, BLOCKS * P))
    zero_stage(core, x_t, A["meta"], z2, 14)
    zrow = lambda u: (lambda j: z2[bass.ds(2 * j + u, 1), :, LEAD:].rearrange("o p s -> p (o s)"))
    with nc.sbuf_tensor("y2", [P, KT, COLS], F32) as y_all:
        y = y_all[:, :, :]
        with nc.sbuf_tensor("b2_la", [P, 2, BLOCKS * P], F32) as la:
            with ExitStack() as inner:
                h = split_buffers(core, inner, "h2")
                rms = inner.enter_context(nc.sbuf_tensor("rms2_all", [P, COLS], F32))
                rms_split_stage(core, "rms2", x_t, h, rms, vec["mix_norm"], 1e-6, 0, COLS)
                gemm_stage(core, "in2", [(A["w_in2"], of(h), lambda j: 2 * j), (A["w_in2"], of(h), lambda j: 2 * j + 1)],
                           17, COLS, None, normed_out(nc, rms, vec["b_in"]), rms=rms, out=[zrow(0), zrow(1)])
                if stop == "z2": return z2[:, :, LEAD:]
                wl = inner.enter_context(nc.sbuf_tensor("b2_wl", [P, KT, 16], F32))
                wa = inner.enter_context(nc.sbuf_tensor("b2_wa", [16, 2 * P], F32))
                bl = inner.enter_context(nc.sbuf_tensor("b2_bl", [16, 1], F32))
                with nc.allow_non_contiguous_dma(reason="16 biases"):
                    load_stage(core, "w2", [(wl[:, :, :], A["w_low"]), (wa[:, :], A["w_alpha"]), (bl[:, :], A["b_low"])])
                decay_stage(core, h, rms, wl, wa, bl[:, 0:1], vec["b_alpha"], la)
            turn_stage(core, "turn2", lambda j: z2[9:14, :, bass.ds(P * j, P)].rearrange("t c s -> c t s"),
                       lambda j: v_tok[bass.ds(P * j, P), :], 5, (LEAD + LTOK) // P, ident)
            gla_stage(core, z2, v_tok, la, y[:, 4:8, :], y[:, :, LTOK:COLS], A["level_masks"], ident)
        norm_stage(core, "gla_norm", y[:, 4:8, :], [[k] for k in range(4)], mats["mean128"], 1e-6, False,
                   vec["gla_norm"], None, ACT.Identity)
        if stop == "gla": return y[:, 4:8, 0:LTOK]
        gate_stage(core, "gate2", lambda i: z2[14 + i, :, LEAD:], y[:, 4:8, :], 4, ACT.Silu)
        rope_stage(core, "rope2", z2[:, :, LEAD:], qk, A["rope_tables"], mats["rope"], 5, LEAD, COLS)
        swa_stage(core, qk, v_tok, A["swa_masks"], A["sinks"], yatt, ident)
        load_stage(core, "yatt", [(y[:, 0:4, 0:LTOK], yatt[:, P - META:].rearrange("(t c) s -> c t s", c=P))])
        if stop == "yatt": return y[:, 0:4, 0:LTOK]
        mixing(core, A, y, z2, x_t)
    if stop == "h2": return x_t[:, :, 0:LTOK]
    with ExitStack() as mem:
        h = split_buffers(core, mem, "h2f")
        rms = mem.enter_context(nc.sbuf_tensor("rms2b_all", [P, COLS], F32))
        rms_split_stage(core, "rms2b", x_t, h, rms, vec["ffn_norm"], 1e-6, 0, COLS)
        for part, (first, tiles) in enumerate(FF_PARTS):
            with ExitStack() as inner:
                g = split_buffers(core, inner, f"ff2_{part}", tiles)
                conv_ff_stage(core, f"up2_{part}", A["w_up2"], h, g, vec["ff_conv"], vec["ff_conv_b"], first, tiles, rms)
                w = A[f"w_down2_{part}"]
                gemm_stage(core, f"down2_{part}", [(w, of(g), lambda j: 2 * j), (w, of(g), lambda j: 2 * j + 1)],
                           4, COLS, None, add_part(nc, x_t, 0, COLS))
    rms_stage(core, "rms2f", x_t, vec["final_norm2"], 1e-6, META, SEQ)


def mixing(core, A, y, z2, x_t):
    nc = core.nc
    with ExitStack() as mem:
        ys = split_buffers(core, mem, "y2s")
        split_stage(core, "split2", y, ys)

        def open_gates(act, u, j, ps, t):
            nc.scalar.activation(t[f"gate{u}"][:, :], t[f"gate{u}"][:, :], ACT.Sigmoid)

        def join(dve, u, j, ps, t):
            g = t["view"](t[f"gate{u}"][:, :])
            row = t["view"](y[:, bass.ds(j, 1), :].rearrange("p o s -> p (o s)"))
            if u == 0:
                nc.vector.tensor_tensor(row, ps, g, ALU.mult)
            else:
                nc.vector.tensor_tensor(g, ps, g, ALU.mult)
                dve.drain()
                nc.vector.tensor_tensor(row, row, g, ALU.add)

        grow = lambda first: (lambda j: z2[bass.ds(j + first, 1), :, LEAD:].rearrange("o p s -> p (o s)"))
        gemm_stage(core, "proj", [(A["w_att"], of(ys), lambda j: j), (A["w_gla"], of(ys, 4), lambda j: j)],
                   8, COLS, open_gates, join, extras=[(0, grow(18), "gate0"), (1, grow(26), "gate1")])
    with ExitStack() as mem:
        ms = split_buffers(core, mem, "mix_s")
        split_stage(core, "split_mix", y, ms)
        gemm_stage(core, "out2", [(A["w_out2"], of(ms), lambda j: 2 * j), (A["w_out2"], of(ms), lambda j: 2 * j + 1)],
                   4, COLS, None, add_part(nc, x_t, 0, COLS))


def split_row(dve, nc, row, pair, j):
    at = lambda x: x[:, bass.ds(j, 1), :].rearrange("p o s -> p (o s)")
    nc.vector.tensor_copy(at(pair[0]), row)
    dve.drain()
    nc.vector.tensor_tensor(at(pair[1]), row, at(pair[0]).bitcast(F32), ALU.subtract)


def conv_ff_stage(core, name, w_up, h, g, cw, cb, first, tiles, rms):
    nc = core.nc

    def act_ff(act, u, j, ps, t):
        nc.scalar.activation(t["conv"][:, :], t["conv"][:, :], ACT.Gelu_apprx_tanh)

    def dve_ff(dve, u, j, ps, t):
        inverse = t["view"](rms[:, :])
        conv = t["view"](t["conv"][:, :])
        if u == 0:
            nc.vector.memset(t["a"][:, 0:2], 0.0)
            nc.vector.tensor_tensor(t["view"](t["a"][:, 2:2 + COLS]), ps, inverse, ALU.mult)
            dve.drain()
            nc.vector.tensor_scalar(t["conv"][:, :], t["a"][:, 2:2 + COLS], cw[:, bass.ds(j + (2 * FT + first), 1)],
                                    cb[:, bass.ds(j + first, 1)], ALU.mult, ALU.add)
            for i in (1, 0):
                dve.drain()
                nc.vector.scalar_tensor_tensor(out=t["conv"][:, :], in0=t["a"][:, i:i + COLS], scalar=cw[:, bass.ds(j + (i * FT + first), 1)],
                                               in1=t["conv"][:, :], op0=ALU.mult, op1=ALU.add)
        else:
            nc.vector.tensor_tensor(conv, ps, conv, ALU.mult)
            dve.drain()
            nc.vector.tensor_tensor(conv, conv, inverse, ALU.mult)
            dve.drain()
            split_row(dve, nc, t["conv"][:, :], g, j)

    gemm_stage(core, name, [(w_up, of(h), lambda j: j + first), (w_up, of(h), lambda j: j + (FT + first))],
               tiles, COLS, act_ff, dve_ff, temps=[("a", COLS + 2), ("conv", COLS)], chained=True, rms=rms if first == 0 else None)


RET_H, RET_D, RET_C = 4, 128, 128


def retention_stage(core, qk, v_tok, y, decay, from_start, to_end, chunk_decay, ident):
    nc = core.nc
    s_done, a_done, t_done, c_done, q_done, o_done, y_done, u_done, r_done, tabs = (
        core.sem(f"ret_{s}") for s in ("scores", "decayed", "turned", "copied", "scaled", "outs", "ys", "update", "state", "tables"))
    here = [core.sem(f"ret_here{b}") for b in range(2)]
    with ExitStack() as mem:
        sb = lambda n, s: mem.enter_context(nc.sbuf_tensor(f"ret_{n}", s, F32))
        x = sb("qk", [P, 2, 2 * RET_H, P])
        v = sb("v", [P, 2, RET_H * P])
        dk = sb("decay", [P, RET_H, P])
        fs = sb("from_start", [P, RET_H, P])
        te = sb("to_end", [P, RET_H])
        a_t = sb("a_t", [P, RET_H, P])
        qs = sb("qs", [P, RET_H, P])
        kt = sb("kt", [P, RET_H, P])
        r = sb("r", [P, RET_H, P])
        ps = [mem.enter_context(nc.psum_tensor(f"ret_ps{i}", [P, RET_H, P], F32)) for i in range(4)]
        ps_s, ps_t, ps_o, ps_u = ps
        block = mem.enter_context(core.block())
        chunks = SEQ // RET_C

        def loop(eng, body):
            with eng.Fori(0, chunks // 2) as ii:
                for b in range(2):
                    body(2 * ii + b, ii, b)

        @block.sync
        def _(sp):
            for dst, src in ((dk[:, :, :], decay), (fs[:, :, :], from_start), (te[:, :], to_end)):
                sp.dma_start(dst, src).then_inc(tabs, 16)

            def body(c, ii, b):
                sp.wait_ge(r_done, c + 1)
                sp.dma_start(x[:, b, :, :], qk[:, :, bass.ds(c * P, P)].rearrange("t c s -> c t s")).then_inc(here[b], 16)
                sp.dma_start(v[:, b, :], v_tok[bass.ds(c * P, P), :]).then_inc(here[b], 16)

            loop(sp, body)

        @block.tensor
        def _(pe):
            def body(c, ii, b):
                pe.wait_ge(here[b], 32 * (ii + 1))
                for h in range(RET_H):
                    last = nc.tensor.matmul(ps_s[:, h, :], x[:, b, RET_H + h, :], x[:, b, h, :], start=True, stop=True)
                last.then_inc(s_done, 1)
                for h in range(RET_H):
                    last = nc.tensor.transpose(ps_t[:, h, :], x[:, b, RET_H + h, :], ident[:, :])
                last.then_inc(t_done, 1)
                pe.wait_ge(a_done, c + 1)
                pe.wait_ge(q_done, c + 1)
                pe.wait_ge(r_done, c + 2)
                pe.wait_ge(y_done, c + 1)
                for h in range(RET_H):
                    nc.tensor.matmul(ps_o[:, h, :], v[:, b, h * P:(h + 1) * P], a_t[:, h, :], start=True, stop=False)
                    last = nc.tensor.matmul(ps_o[:, h, :], r[:, h, :], qs[:, h, :], start=False, stop=True)
                last.then_inc(o_done, 1)
                pe.wait_ge(c_done, c + 1)
                for h in range(RET_H):
                    last = nc.tensor.matmul(ps_u[:, h, :], kt[:, h, :], v[:, b, h * P:(h + 1) * P], start=True, stop=True)
                last.then_inc(u_done, 1)

            loop(pe, body)

        @block.scalar
        def _(act):
            act.sem_inc(y_done, 1)
            act.wait_ge(tabs, 48)

            def body(c, ii, b):
                act.wait_ge(t_done, c + 1)
                for h in range(RET_H):
                    nc.scalar.activation(kt[:, h, :], ps_t[:, h, :], ACT.Copy, scale=te[:, h:h + 1])
                act.drain().then_inc(c_done, 1)
                act.wait_ge(o_done, c + 1)
                nc.scalar.activation(y[:, :, bass.ds(c * P, P)], ps_o[:, :, :], ACT.Copy).then_inc(y_done, 1)

            loop(act, body)

        @block.vector
        def _(dve):
            nc.vector.memset(r[:, :, :], 0.0)
            dve.drain().then_inc(r_done, 2)
            dve.wait_ge(tabs, 48)

            def body(c, ii, b):
                dve.wait_ge(s_done, c + 1)
                nc.vector.tensor_tensor(a_t[:, :, :], ps_s[:, :, :], dk[:, :, :], ALU.mult).then_inc(a_done, 1)
                nc.vector.tensor_tensor(qs[:, :, :], x[:, b, 0:RET_H, :], fs[:, :, :], ALU.mult).then_inc(q_done, 1)
                dve.wait_ge(u_done, c + 1)
                for h in range(RET_H):
                    nc.vector.scalar_tensor_tensor(out=r[:, h, :], in0=r[:, h, :], scalar=chunk_decay[h], in1=ps_u[:, h, :],
                                                   op0=ALU.mult, op1=ALU.add)
                dve.drain().then_inc(r_done, 1)

            loop(dve, body)


RW_C = 64
RW_CH = SEQ // RW_C
PAIRS = 4
KINDS = 5
RW_LEVELS = (2, 4, 8, 16, 32)


def rwkv_prep_stage(core, z, mats, vec, w2a2, g2, rw, late):
    nc = core.nc
    rw_x, rw_e = rw
    here, lora, mm, u_here, lw_done, e_done, kk_done, sq_done, n_mm, n_here, root, bt, b_mm, out_done, x_free, g_copied, zeroed = (
        core.sem(f"prep_{s}") for s in ("here", "lora", "lora_mm", "sigmoids", "sums", "exps", "kk", "squares", "norm_mm", "norm",
                                        "root", "bonus", "bonus_mm", "out", "x_free", "g_copied", "zeroed"))
    stored = core.sem("prep_stored")
    with ExitStack() as mem:
        sb = lambda n, s: mem.enter_context(nc.sbuf_tensor(f"prep_{n}", s, F32))
        raw = sb("raw", [P, 3, SEQ + 1])
        lo = sb("lora", [P, 2, SEQ + 1])
        ls = sb("lora_s", [P, 2, SEQ])
        w = sb("w", [P, 512])
        g = sb("g2", [P, 512])
        reset = sb("reset", [P, SEQ])
        t = {k: sb(k, [P, SEQ]) for k in ("r", "k", "v", "tmp", "lw", "a", "g", "w_in", "w_ex", "kk", "sq", "rn", "bv")}
        out = sb("out", [P, KINDS, SEQ])
        ew = sb("ew", [P, RW_CH, PAIRS])
        ps = mem.enter_context(nc.psum_tensor("prep_ps", [P, 4, 2, 512], F32))
        cut = lambda x: x.rearrange("p (c w) -> p c w", c=2)
        block = mem.enter_context(core.block())
        TT, TS, STT = nc.vector.tensor_tensor, nc.vector.tensor_scalar, nc.vector.scalar_tensor_tensor

        @block.sync
        def _(sp):
            sp.dma_start(w[:, :], w2a2).then_inc(here, 16)
            sp.dma_start(g[:, :], g2).then_inc(here, 16)
            sp.dma_start(lo[:, :, 1:], z[28:30].rearrange("t c s -> c t s")).then_inc(here, 16)
            for m in range(4):
                if m:
                    sp.wait_ge(x_free, m)
                for i in range(3):
                    sp.dma_start(raw[:, i, 1:], z[16 + 4 * i + m]).then_inc(here, 16)
                sp.wait_ge(out_done, m + 1)
                for k in range(KINDS):
                    sp.dma_start(rw_x[:, :, k, m, :].rearrange("n c s -> c n s"),
                                 out[:, k, :].rearrange("c (n s) -> c n s", s=RW_C)).then_inc(stored, 16)
                sp.dma_start(late[m], t["g"][:, :]).then_inc(stored, 16)
                sp.dma_start(late[4 + m], t["bv"][:, :]).then_inc(stored, 16)
            sp.dma_start(rw_e, ew[:, :, :]).then_inc(stored, 16)
            sp.wait_ge(stored, 16 * (4 * (KINDS + 2) + 1))

        @block.tensor
        def _(pe):
            for m in range(4):
                cols = slice(m * P, (m + 1) * P)
                if m == 0:
                    pe.wait_ge(lora, 2)
                else:
                    pe.wait_ge(u_here, m)
                for c in range(2):
                    tok = slice(c * 512, (c + 1) * 512)
                    nc.tensor.matmul(ps[:, 0, c, :], w[0:64, cols], ls[0:64, 0, tok], start=True, stop=True)
                    nc.tensor.matmul(ps[:, 1, c, :], w[64:128, cols], ls[64:128, 0, tok], start=True, stop=True)
                    last = nc.tensor.matmul(ps[:, 2, c, :], g[:, cols], ls[:, 1, tok], start=True, stop=True)
                last.then_inc(mm, 1)
                pe.wait_ge(sq_done, m + 1)
                for c in range(2):
                    last = nc.tensor.matmul(ps[:, 3, c, :], mats["mean64"], t["sq"][:, c * 512:(c + 1) * 512], start=True, stop=True)
                last.then_inc(n_mm, 1)
                pe.wait_ge(bt, m + 1)
                for c in range(2):
                    last = nc.tensor.matmul(ps[:, 3, c, :], mats["mean64"], t["tmp"][:, c * 512:(c + 1) * 512], start=True, stop=True)
                last.then_inc(b_mm, 1)

        @block.scalar
        def _(act):
            act.wait_ge(lora, 1)
            nc.scalar.activation(ls[0:64, 0, :], ls[0:64, 0, :], ACT.Tanh)
            nc.scalar.activation(ls[:, 1, :], ls[:, 1, :], ACT.Sigmoid)
            act.drain().then_inc(lora, 1)
            for m in range(4):
                act.wait_ge(mm, m + 1)
                if m:
                    act.wait_ge(g_copied, m)
                nc.scalar.activation(cut(t["lw"][:, :]), ps[:, 0, :, :], ACT.Sigmoid, bias=vec["rw_w0"][:, m:m + 1])
                nc.scalar.activation(cut(t["a"][:, :]), ps[:, 1, :, :], ACT.Sigmoid, bias=vec["rw_a0"][:, m:m + 1])
                nc.scalar.activation(cut(t["g"][:, :]), ps[:, 2, :, :], ACT.Copy)
                act.drain().then_inc(u_here, 1)
                act.wait_ge(lw_done, m + 1)
                nc.scalar.activation(t["rn"][:, :], t["w_in"][:, :], ACT.Exp, scale=-1.0)
                nc.scalar.activation(t["w_ex"][:, :], t["w_ex"][:, :], ACT.Exp)
                act.drain()
                nc.scalar.activation(t["w_in"][:, :], t["w_in"][:, :], ACT.Exp)
                act.drain().then_inc(e_done, 1)
                act.wait_ge(kk_done, m + 1)
                nc.scalar.activation(t["sq"][:, :], t["kk"][:, :], ACT.Square).then_inc(sq_done, 1)
                act.wait_ge(n_here, m + 1)
                nc.scalar.activation(t["sq"][:, :], t["sq"][:, :], ACT.Sqrt).then_inc(root, 1)

        @block.vector
        def _(dve):
            nc.vector.memset(raw[:, :, 0:1], 0.0)
            nc.vector.memset(lo[:, :, 0:1], 0.0)
            nc.vector.memset(reset[:, :], 1.0)
            dve.drain()
            nc.vector.memset(reset[:, :].rearrange("p (n s) -> p n s", s=RW_C)[:, :, 0:1], 0.0)
            dve.wait_ge(here, 96)

            def shift(dst, src, mu, tmp):
                TT(tmp, src[:, 0:SEQ], src[:, 1:], ALU.subtract)
                dve.drain()
                STT(out=dst, in0=tmp, scalar=mu, in1=src[:, 1:], op0=ALU.mult, op1=ALU.add)
                dve.drain()

            for i in range(2):
                shift(ls[:, i, :], lo[:, i, :], vec["rw_mu"][:, 12 + i:13 + i], t["tmp"][:, :])
            dve.drain().then_inc(lora, 1)
            for m in range(4):
                col = slice(m, m + 1)
                dve.wait_ge(here, 48 * (m + 2))
                if m:
                    dve.wait_ge(stored, 16 * (KINDS + 2) * m)
                    dve.sem_inc(g_copied, 1)
                for i, name in enumerate("rkv"):
                    shift(t[name][:, :], raw[:, i, :], vec["rw_mu"][:, 4 * i + m:4 * i + m + 1], t["tmp"][:, :])
                dve.sem_inc(x_free, 1)
                TS(t["kk"][:, :], t["k"][:, :], vec["rw_kk"][:, col], None, ALU.mult)
                dve.drain().then_inc(kk_done, 1)
                dve.wait_ge(u_here, m + 1)
                TS(t["lw"][:, :], t["lw"][:, :], -float(np.exp(-0.5)), None, ALU.mult)
                dve.drain()
                nc.vector.tensor_tensor_scan(t["w_in"][:, :], reset[:, :], t["lw"][:, :], 0.0, ALU.mult, ALU.add)
                dve.drain()
                TT(t["w_ex"][:, :], t["w_in"][:, :], t["lw"][:, :], ALU.subtract)
                dve.drain().then_inc(lw_done, 1)
                dve.wait_ge(n_mm, m + 1)
                TS(cut(t["sq"][:, :]), ps[:, 3, :, :], 64.0, 1e-24, ALU.mult, ALU.max)
                TS(t["tmp"][:, :], t["a"][:, :], -1.0, vec["rw_ka"][:, col], ALU.add, ALU.mult)
                dve.drain().then_inc(n_here, 1)
                STT(out=t["k"][:, :], in0=t["tmp"][:, :], scalar=1.0, in1=t["k"][:, :], op0=ALU.add, op1=ALU.mult)
                dve.drain()
                STT(out=t["tmp"][:, :], in0=t["r"][:, :], scalar=vec["rw_rk"][:, col], in1=t["k"][:, :], op0=ALU.mult, op1=ALU.mult)
                dve.drain().then_inc(bt, 1)
                dve.wait_ge(e_done, m + 1)
                dve.wait_ge(root, m + 1)
                nc.vector.reciprocal(t["sq"][:, :], t["sq"][:, :])
                TT(out[:, 1, :], t["r"][:, :], t["w_in"][:, :], ALU.mult)
                TT(out[:, 3, :], t["k"][:, :], t["rn"][:, :], ALU.mult)
                nc.vector.tensor_copy(out[:, 4, :], t["v"][:, :])
                nc.vector.tensor_copy(ew[:, :, m], t["w_in"][:, :].rearrange("p (n s) -> p n s", s=RW_C)[:, :, RW_C - 1])
                dve.drain()
                TT(t["kk"][:, :], t["kk"][:, :], t["sq"][:, :], ALU.mult)
                dve.drain()
                TT(out[:, 0, :], t["kk"][:, :], t["w_ex"][:, :], ALU.mult)
                TT(out[:, 2, :], t["kk"][:, :], t["a"][:, :], ALU.mult)
                dve.drain()
                TT(out[:, 2, :], out[:, 2, :], t["rn"][:, :], ALU.mult)
                dve.wait_ge(b_mm, m + 1)
                STT(out=cut(t["bv"][:, :]), in0=ps[:, 3, :, :], scalar=64.0, in1=cut(t["v"][:, :]), op0=ALU.mult, op1=ALU.mult)
                dve.drain().then_inc(out_done, 1)


def rwkv_stage(core, rw, y, mask4, neg1, level_masks, ident):
    nc = core.nc
    rw_x, rw_e = rw
    NV = len(RW_LEVELS)
    sc_done, tr_done, lt_done, tok_done, off_done, off_used, x_mm, x_copied, t_mm, t_done = (
        core.sem(f"rw_{s}") for s in ("scores", "turned", "masked", "copied", "offs", "offs_used", "lt_mm", "lt_copied", "tlt_mm", "inverse"))
    cx, cxn, cu, cuc, cy, y_out, s_done, tabs, zero = (
        core.sem(f"rw_{s}") for s in ("chain_x", "chain_x_sb", "chain_u", "chain_u_sb", "chain_y", "y_out", "state", "tables", "zero"))
    here = [core.sem(f"rw_here{g}") for g in range(2)]
    with ExitStack() as mem:
        sb = lambda n, s: mem.enter_context(nc.sbuf_tensor(f"rw_{n}", s, F32))
        z = sb("z", [P, 2, KINDS, PAIRS, 2, RW_C])
        tok = sb("tok", [P, 2, PAIRS, 3, P])
        lt = sb("lt", [P, 2, PAIRS, 4, P])
        ti = sb("t", [P, 2, PAIRS, P])
        tt = sb("tt", [P, 2, PAIRS, P])
        off = sb("off", [P, 2, 2, PAIRS, P])
        xl = sb("xl", [P, 2, PAIRS, P])
        xn, us, s = sb("xn", [P, PAIRS, P]), sb("us", [P, PAIRS, P]), sb("s", [P, PAIRS, P])
        ew = sb("ew", [P, RW_CH, PAIRS])
        m4, n1, lm = sb("m4", [P, 4, P]), sb("n1", [P, 2, P]), sb("lm", [P, NV, P])
        bank = mem.enter_context(nc.psum_tensor("rw_ps", [P, 8, PAIRS, P], F32))
        block = mem.enter_context(core.block())
        pad = lambda g, kind, p: z[:, g, kind, p, :, :].rearrange("c a s -> c (a s)")

        def steps(eng, body):
            with eng.Fori(0, RW_CH // 2) as i:
                body(i)

        @block.sync
        def _(sp):
            for dst, src in ((ew[:, :, :], rw_e), (m4[:, :, :], mask4), (n1[:, :, :], neg1), (lm[:, :, :], level_masks[:, 1:6, :])):
                sp.dma_start(dst, src).then_inc(tabs, 16)
            sp.wait_ge(zero, 1)

            def body(i):
                for g in range(2):
                    sp.wait_ge(s_done, 2 * i + g + 1)
                    for a in range(2):
                        r = slice(64 * a, 64 * a + 64)
                        sp.dma_start(z[r, g, :, :, a, :].rearrange("c k p s -> c (k p) s"),
                                     rw_x[bass.ds(2 * i + g, 1), r].rearrange("o c k p s -> (o c) (k p) s")).then_inc(here[g], 16)

            steps(sp, body)

        @block.gpsimd
        def _(pool):
            nc.gpsimd.memset(z[:, :, :, :, :, :], 0.0).then_inc(zero, 1)
            pool.wait_ge(tabs, 64)

            def body(i):
                for l in range(NV):
                    for g in range(2):
                        if l == 0:
                            pool.wait_ge(lt_done, 2 * i + g + 1)
                        pool.wait_ge(off_used, 2 * NV * i + 2 * l + g + 1)
                        nc.gpsimd.tensor_tensor(off[:, g, l % 2, :, :], lt[:, g, :, 0, :],
                                                lm[:, NV - 1 - l:NV - l, :].broadcast_to([P, PAIRS, P]), ALU.mult).then_inc(off_done, 1)

            steps(pool, body)

        @block.tensor
        def _(pe):
            pe.sem_inc(off_used, 4)
            mm = nc.tensor.matmul

            def chain(i, g):
                c = 2 * i + g
                pe.wait_ge(s_done, c + 2)
                for p in range(PAIRS):
                    mm(bank[:, 6, p, :], lt[:, g, p, 2, :], tok[:, g, p, 2, :], start=True, stop=False)
                    last = mm(bank[:, 6, p, :], pad(g, 0, p), s[:, p, :], start=False, stop=True)
                last.then_inc(cx, 1)
                pe.wait_ge(cxn, c + 1)
                for p in range(PAIRS):
                    last = mm(bank[:, 7, p, :], tt[:, g, p, :], xn[:, p, :], start=True, stop=True)
                last.then_inc(cu, 1)
                pe.wait_ge(cuc, c + 1)
                for p in range(PAIRS):
                    mm(bank[:, 2 + g, p, :], tok[:, g, p, 0, :], us[:, p, :], start=True, stop=False)
                    mm(bank[:, 2 + g, p, :], tok[:, g, p, 1, :], tok[:, g, p, 2, :], start=False, stop=True)
                for p in range(PAIRS):
                    mm(bank[:, g, p, :], s[:, p, :], pad(g, 1, p), start=True, stop=False)
                    mm(bank[:, g, p, :], us[:, p, :], lt[:, g, p, 1, :], start=False, stop=False)
                    last = mm(bank[:, g, p, :], tok[:, g, p, 2, :], lt[:, g, p, 3, :], start=False, stop=True)
                last.then_inc(cy, 1)

            def body(i):
                pe.wait_ge(y_out, 2 * i + 1)
                pe.wait_ge(s_done, 2 * i + 2)
                for g in range(2):
                    pe.wait_ge(here[g], 32 * (i + 1))
                    if g:
                        pe.wait_ge(lt_done, 2 * i + 1)
                    for p in range(PAIRS):
                        for n, kind in enumerate((2, 3)):
                            mm(bank[:, p, 2 * n:2 * n + 2, :], pad(g, kind, p),
                               z[:, g, 0:2, p, :, :].rearrange("c k a s -> c k (a s)"), start=True, stop=True)
                        last = mm(bank[:, 4, p, :], pad(g, 0, p), pad(g, 2, p), start=True, stop=True)
                    last.then_inc(sc_done, 1)
                    if g:
                        pe.wait_ge(tok_done, 2 * i + 1)
                    for p in range(PAIRS):
                        for n in range(3):
                            last = nc.tensor.transpose(bank[:, 5 + n, p, :], pad(g, 2 + n, p), ident[:, :])
                    last.then_inc(tr_done, 1)
                pe.wait_ge(lt_done, 2 * i + 2)
                pe.wait_ge(tok_done, 2 * i + 2)
                for l in range(NV):
                    k = 2 * NV * i + 2 * l
                    for g in range(2):
                        pe.wait_ge(off_done, k + g + 1)
                        if l:
                            pe.wait_ge(t_done, k + g - 1)
                        for p in range(PAIRS):
                            last = mm(bank[:, g, p, :], off[:, g, l % 2, p, :], ti[:, g, p, :], start=True, stop=True)
                        last.then_inc(x_mm, 1)
                    for g in range(2):
                        pe.wait_ge(x_copied, k + g + 1)
                        for p in range(PAIRS):
                            mm(bank[:, 2 + g, p, :], tt[:, g, p, :], xl[:, g, p, :], start=True, stop=True)
                            last = mm(bank[:, 4 + g, p, :], xl[:, g, p, :], tt[:, g, p, :], start=True, stop=True)
                        last.then_inc(t_mm, 1)
                for g in range(2):
                    pe.wait_ge(t_done, 2 * NV * (i + 1) - 1 + g)
                    chain(i, g)

            steps(pe, body)

        @block.scalar
        def _(act):
            act.sem_inc(y_out, 1)

            def body(i):
                for g in range(2):
                    act.wait_ge(tr_done, 2 * i + g + 1)
                    nc.scalar.activation(tok[:, g, :, :, :], bank[:, 5:8, :, :].rearrange("c n p s -> c p n s"),
                                         ACT.Copy).then_inc(tok_done, 1)
                for l in range(NV):
                    for g in range(2):
                        act.wait_ge(x_mm, 2 * NV * i + 2 * l + g + 1)
                        nc.scalar.activation(xl[:, g, :, :], bank[:, g, :, :], ACT.Copy)
                        act.drain().then_inc(x_copied, 1)
                for g in range(2):
                    c = 2 * i + g
                    act.wait_ge(cx, c + 1)
                    nc.scalar.activation(xn[:, :, :], bank[:, 6, :, :], ACT.Copy, scale=-1.0).then_inc(cxn, 1)
                    act.wait_ge(cu, c + 1)
                    nc.scalar.activation(us[:, :, :], bank[:, 7, :, :], ACT.Copy).then_inc(cuc, 1)
                    act.wait_ge(cy, c + 1)
                    for a in range(2):
                        r = slice(64 * a, 64 * a + 64)
                        nc.scalar.activation(y[r, :, bass.ds(c * RW_C, RW_C)], bank[r, g, :, RW_C * a:RW_C * (a + 1)], ACT.Copy)
                act.drain().then_inc(y_out, 2)

            steps(act, body)

        @block.vector
        def _(dve):
            nc.vector.memset(s[:, :, :], 0.0)
            dve.drain().then_inc(s_done, 2)
            dve.wait_ge(tabs, 64)
            TT = nc.vector.tensor_tensor
            all_p = lambda x: x.unsqueeze(1).broadcast_to([P, PAIRS, P])

            def body(i):
                for g in range(2):
                    dve.wait_ge(sc_done, 2 * i + g + 1)
                    TT(lt[:, g, :, :, :], bank[:, 0:4, :, :], m4[:, :, :].unsqueeze(1).broadcast_to([P, PAIRS, 4, P]), ALU.mult)
                    TT(ti[:, g, :, :], bank[:, 4, :, :], all_p(n1[:, 0, :]), ALU.mult)
                    dve.drain()
                    TT(tt[:, g, :, :], lt[:, g, :, 0, :], all_p(n1[:, 1, :]), ALU.mult)
                    TT(ti[:, g, :, :], ti[:, g, :, :], all_p(ident[:, :]), ALU.add)
                    dve.drain()
                    TT(tt[:, g, :, :], tt[:, g, :, :], all_p(ident[:, :]), ALU.add)
                    dve.drain().then_inc(lt_done, 1)
                for l in range(NV):
                    for g in range(2):
                        dve.wait_ge(t_mm, 2 * NV * i + 2 * l + g + 1)
                        dve.sem_inc(off_used, 1)
                        TT(ti[:, g, :, :], ti[:, g, :, :], bank[:, 2 + g, :, :], ALU.subtract)
                        TT(tt[:, g, :, :], tt[:, g, :, :], bank[:, 4 + g, :, :], ALU.subtract)
                        dve.drain().then_inc(t_done, 1)
                for g in range(2):
                    c = 2 * i + g
                    dve.wait_ge(cy, c + 1)
                    TT(s[:, :, :], s[:, :, :], bank[:, 2 + g, :, :], ALU.add)
                    dve.drain()
                    for p in range(PAIRS):
                        nc.vector.tensor_scalar(s[:, p, :], s[:, p, :], ew[:, bass.ds(c, 1), p], None, ALU.mult)
                    dve.drain().then_inc(s_done, 1)

            steps(dve, body)


def finish_stage(core, late, y):
    nc = core.nc
    here, used = [core.sem(f"fin_here{b}") for b in range(2)], core.sem("fin_used")
    with ExitStack() as mem:
        x = mem.enter_context(nc.sbuf_tensor("fin_x", [P, 2, 2, SEQ], F32))
        block = mem.enter_context(core.block())

        @block.sync
        def _(sp):
            for m in range(4):
                if m >= 2:
                    sp.wait_ge(used, m - 1)
                for i in range(2):
                    sp.dma_start(x[:, m % 2, i, :], late[4 * i + m]).then_inc(here[m % 2], 16)

        @block.vector
        def _(dve):
            for m in range(4):
                dve.wait_ge(here[m % 2], 32 * (m // 2 + 1))
                nc.vector.tensor_tensor(y[:, m, :], y[:, m, :], x[:, m % 2, 1, :], ALU.add)
                dve.drain()
                nc.vector.tensor_tensor(y[:, m, :], y[:, m, :], x[:, m % 2, 0, :], ALU.mult)
                dve.drain().then_inc(used, 1)


def block_three(core, A, x_t, mats, vec, dram, stop):
    nc = core.nc
    ident = mats["ident"]
    z3, v_tok, qk = dram("z3", (30, P, SEQ)), dram("v_tok3", (SEQ, 512)), dram("qk3", (8, P, SEQ))
    rw = dram("rw_x", (RW_CH, P, KINDS, PAIRS, RW_C)), dram("rw_e", (P, RW_CH, PAIRS))
    late = dram("rw_late", (8, P, SEQ))
    T = slice(META, META + SEQ)
    row = lambda d, u: (lambda j: d[bass.ds(2 * j + u, 1)].rearrange("o p s -> p (o s)"))
    with ExitStack() as mem:
        h = split_buffers(core, mem, "h3")
        rms = mem.enter_context(nc.sbuf_tensor("rms3_all", [P, SEQ], F32))
        rms_split_stage(core, "rms3", x_t, h, rms, vec["norm_mix"], 1e-6, META, SEQ)
        gemm_stage(core, "in3", [(A["w_in3"], of(h, 0, META), lambda j: 2 * j), (A["w_in3"], of(h, 0, META), lambda j: 2 * j + 1)],
                   15, SEQ, None, normed_out(nc, rms), rms=rms, out=[row(z3, 0), row(z3, 1)])
    with ExitStack() as mem:
        y = mem.enter_context(nc.sbuf_tensor("y3", [P, KT, SEQ], F32))[:, :, :]
        ret, rwy = y[:, 0:4, :], y[:, 4:8, :]
        rope_stage(core, "rope3", z3, qk, A["ret_tables"], mats["rot2"], 8, 0, SEQ)
        turn_stage(core, "turn3", lambda j: z3[8:12, :, bass.ds(P * j, P)].rearrange("t c s -> c t s"),
                   lambda j: v_tok[bass.ds(P * j, P), :], 4, SEQ // P, ident)
        retention_stage(core, qk, v_tok, ret, A["ret_decay"], A["ret_start"], A["ret_end"], chunk_decays(), ident)
        norm_stage(core, "ret_norm", ret, [[k] for k in range(4)], mats["mean128"], 1e-5, True, vec["ret_norm"], None, ACT.Identity)
        gate_stage(core, "gate3", lambda i: z3[12 + i], ret, 4, ACT.Silu)
        if stop == "yret": return ret
        rwkv_prep_stage(core, z3, mats, vec, A["rw_w2a2"], A["rw_g2"], rw, late)
        rwkv_stage(core, rw, rwy, A["rw_mask4"], A["rw_neg1"], A["level_masks"], ident)
        norm_stage(core, "rw_norm", rwy, [[k] for k in range(4)], mats["mean64"], 64e-5, True, vec["rw_ln_w"], vec["rw_ln_b"], ACT.Identity)
        finish_stage(core, late, rwy)
        if stop == "yrw": return rwy
        ys = split_buffers(core, mem, "y3s", KT, SEQ)
        split_stage(core, "split3", y, ys)
        gemm_stage(core, "out3", [(A["w_o3"], of(ys), lambda j: 2 * j), (A["w_o3"], of(ys), lambda j: 2 * j + 1)],
                   4, SEQ, None, add_part(nc, x_t, META, SEQ))
    if stop == "x3a": return x_t[:, :, T]
    with ExitStack() as mem:
        h = split_buffers(core, mem, "h3f", KT, COLS)
        rms = mem.enter_context(nc.sbuf_tensor("rms3b_all", [P, SEQ], F32))
        rms_split_stage(core, "rms3b", x_t, h, rms, vec["norm_ffn"], 1e-6, META, SEQ)
        for part, (first, tiles) in enumerate(FF_PARTS):
            with ExitStack() as inner:
                g = split_buffers(core, inner, f"ff3_{part}", tiles, SEQ)
                gated_ff_stage(core, f"up3_{part}", A["w_gate3"], A["w_up3"], h, g, first, tiles, rms)
                w = A[f"w_down3_{part}"]
                gemm_stage(core, f"down3_{part}", [(w, of(g), lambda j: 2 * j), (w, of(g), lambda j: 2 * j + 1)],
                           4, SEQ, None, add_part(nc, x_t, META, SEQ))
    with ExitStack() as mem:
        h = split_buffers(core, mem, "h3p", KT, COLS)
        rms = mem.enter_context(nc.sbuf_tensor("rms3c_all", [P, SEQ], F32))
        rms_split_stage(core, "rms3c", x_t, h, rms, vec["norm_ple"], 1e-6, META, SEQ)
        p_t = mem.enter_context(nc.sbuf_tensor("b3_p", [P, 2, SEQ], F32))
        ps_ = split_buffers(core, mem, "p3s", 2, SEQ)
        load_stage(core, "p", [(p_t[:, :, :], A["p3"].rearrange("(k p) s -> p k s", p=P))])
        split_stage(core, "split_p", p_t[:, :, :], ps_)

        def act_ple(act, u, j, ps, t):
            nc.scalar.activation(t["gate"][:, :], t["gate"][:, :], ACT.Sigmoid)

        def dve_ple(dve, u, j, ps, t):
            gate = t["view"](t["gate"][:, :])
            if u == 0:
                nc.vector.tensor_tensor(gate, ps, t["view"](rms[:, :]), ALU.mult)
            else:
                x_row = x_t[:, bass.ds(j, 1), T].rearrange("p o s -> p (o s)")
                nc.vector.tensor_tensor(gate, ps, gate, ALU.mult)
                dve.drain()
                nc.vector.tensor_tensor(x_row, x_row, t["gate"][:, :], ALU.add)

        gemm_stage(core, "ple", [(A["w_ple_gate"], of(h, 0, META), lambda j: j), (A["w_ple_up"], of(ps_), lambda j: j)],
                   8, SEQ, act_ple, dve_ple, temps=[("gate", SEQ)], chained=True, rms=rms)
    rms_stage(core, "rms3f", x_t, vec["final_norm3"], 1e-6, META, SEQ)


def gated_ff_stage(core, name, w_gate, w_up, h, g, first, tiles, rms):
    nc = core.nc

    def act_ff(act, u, j, ps, t):
        nc.scalar.activation(t["gate"][:, :], t["gate"][:, :], ACT.Silu)

    def dve_ff(dve, u, j, ps, t):
        inverse, gate = t["view"](rms[:, :]), t["view"](t["gate"][:, :])
        if u == 0:
            nc.vector.tensor_tensor(gate, ps, inverse, ALU.mult)
        else:
            nc.vector.tensor_tensor(gate, ps, gate, ALU.mult)
            dve.drain()
            nc.vector.tensor_tensor(gate, gate, inverse, ALU.mult)
            dve.drain()
            split_row(dve, nc, t["gate"][:, :], g, j)

    gemm_stage(core, name, [(w_gate, of(h, 0, META), lambda j: j + first), (w_up, of(h, 0, META), lambda j: j + first)],
               tiles, SEQ, act_ff, dve_ff, temps=[("gate", SEQ)], chained=True, rms=rms if first == 0 else None)


def log_gammas():
    return np.log(np.float32(1.0) - np.float32(2.0) ** (-5.0 - np.arange(RET_H, dtype=np.float32))).astype(np.float64)


def chunk_decays():
    return [float(np.exp(g * RET_C)) for g in log_gammas()]


def retention_tables():
    ang = (np.float32(1.0) / (np.float32(10000.0) ** np.linspace(0.0, 1.0, RET_D // 2, dtype=np.float32))).astype(np.float32)
    phase = np.arange(SEQ, dtype=np.float32)[None] * np.repeat(ang, 2)[:, None]
    tables = np.stack([np.cos(phase), np.sin(phase)], axis=1).astype(np.float32)
    g = log_gammas()
    j, i = np.arange(P)[:, None, None], np.arange(P)[None, None]
    scale = RET_D ** -0.5
    decay = np.where(i >= j, np.exp(g[None, :, None] * np.maximum(i - j, 0)), 0.0) * scale
    start = np.broadcast_to(np.exp(g[None, :, None] * (i + 1.0)), (P, RET_H, P))
    end = np.exp(g[None] * (P - 1 - np.arange(P)[:, None])) * scale
    return tables, decay.astype(np.float32), np.ascontiguousarray(start.astype(np.float32)), end.astype(np.float32)


def rwkv_masks():
    s, t = np.arange(P)[:, None], np.arange(P)[None]
    strict, incl = (s < t).astype(np.float32), (s <= t).astype(np.float32)
    one = ((s // 2 == t // 2) & (s < t)).astype(np.float32)
    return np.ascontiguousarray(np.stack([strict, incl, strict, incl], axis=1)), np.ascontiguousarray(np.stack([-one.T, -one], axis=1))


def start_stage(core, loads):
    nc = core.nc
    here = core.sem("start_here")
    with core.block() as block:
        @block.sync
        def _(sp):
            for dst, src in loads:
                sp.dma_start(dst, src).then_inc(here, 16)
            sp.wait_ge(here, 16 * len(loads))

        @block.vector
        def _(dve):
            for value, tile in core.eps.items():
                nc.vector.memset(tile, value)


def normed_out(nc, inverse, bias=None):
    def part(dve, u, j, ps, t):
        o = t["view"](t["out"][:, u, :])
        nc.vector.tensor_tensor(o, ps, t["view"](inverse[:, :]), ALU.mult)
        if bias is not None:
            dve.drain()
            nc.vector.tensor_scalar(o, o, bias[:, bass.ds(2 * j + u, 1)], None, ALU.add)
    return part


def add_part(nc, x_t, c0, total):
    def part(dve, u, j, ps, t):
        row = t["view"](x_t[:, bass.ds(2 * j + u, 1), c0:c0 + total].rearrange("p o s -> p (o s)"))
        nc.vector.tensor_tensor(row, ps, row, ALU.add)
    return part


def split_buffers(core, mem, name, tiles=KT, cols=COLS):
    return [mem.enter_context(core.nc.sbuf_tensor(f"{name}_{part}", [P, tiles, cols], F32R)) for part in ("high", "low")]


def of(pair, first=0, at=0):
    return lambda k, c, w: [x[:, first + k, at + c:at + c + w] for x in pair]


def block_one(core, A, x_t, mats, vec, dram, stop):
    nc = core.nc
    T = slice(META, META + SEQ)
    x_main = x_t[:, :, T]
    z1, v_tok, ya_tok, ya = dram("z1", (24, P, SEQ)), dram("v_tok", (SEQ, 256)), dram("ya_tok", (SEQ, 256)), dram("ya", (2, P, SEQ))
    ident = mats["ident"]
    load_stage(core, "x", [(x_main, A["x"].rearrange("(k p) s -> p k s", p=P))])
    with ExitStack() as mem:
        h = split_buffers(core, mem, "h1")
        rms = mem.enter_context(nc.sbuf_tensor("rms1_all", [P, SEQ], F32))
        rms_split_stage(core, "rms1", x_t, h, rms, vec["norm_g"], 1e-6, META, SEQ)
        gemm_stage(core, "in1", [(A["w_in"], of(h, 0, META), lambda j: 2 * j), (A["w_in"], of(h, 0, META), lambda j: 2 * j + 1)],
                   12, SEQ, None, normed_out(nc, rms), rms=rms,
                   out=[lambda j: z1[bass.ds(2 * j, 1)].rearrange("o p s -> p (o s)"),
                        lambda j: z1[bass.ds(2 * j + 1, 1)].rearrange("o p s -> p (o s)")])
    if stop == "z1": return z1
    turn_stage(core, "turn_v", lambda j: z1[4:6, :, bass.ds(P * j, P)].rearrange("t c s -> c t s"),
               lambda j: v_tok[bass.ds(P * j, P), :], 2, SEQ // P, ident)
    na_stage(core, z1, v_tok, A["na_bias"], ya_tok, ident)
    turn_stage(core, "turn_y", lambda j: ya_tok[bass.ds(P * j, P), :].rearrange("s (t c) -> s t c", t=2),
               lambda j: ya[:, :, bass.ds(P * j, P)].rearrange("t c s -> c t s"), 2, SEQ // P, ident)
    if stop == "ya": return ya
    with ExitStack() as outer:
        y = outer.enter_context(nc.sbuf_tensor("y1", [P, KT, SEQ], F32))[:, :, :]
        with ExitStack() as mem:
            sb = lambda n, s: mem.enter_context(nc.sbuf_tensor(f"b1_{n}", s, F32))
            v, u = sb("v", [P, 2, SEQ]), sb("u", [P, 2, SEQ])
            taps, pw, pool_w, ws, bs = sb("taps", [P, 2, CONV_W]), sb("pw", [P, 2, 2 * P]), sb("pool_w", [P, 2, 64]), sb("ws", [P, 4, P]), sb("bs", [P, 2, P])
            load_stage(core, "w1", [(taps[:, :, :], A["conv_w"]), (pw[:, :, :], A["conv_pw"]), (pool_w[:, :, :], A["pool_w"]),
                                    (ws[:, :, :], A["sgu_w"]), (bs[:, :, :], A["sgu_b"]),
                                    (y[:, 0:2, :], ya.rearrange("t c s -> c t s"))])
            conv_stage(core, z1, v, taps, vec["dw_b"])
            norm_stage(core, "ln_b", v, [[0, 1]], mats["mean256"], 1e-5, True, vec["conv_g"], vec["conv_b"], ACT.Silu)
            full = slice(0, P)
            product_stage(core, "pw", y[:, 2:4, :],
                          [[(pw[:, k, m * P:(m + 1) * P], full, full, k, k == 0, k == 1) for k in range(2)] for m in range(2)], v)
            pool_stage(core, z1, v, A["inv_count"])
            halves = [slice(0, 64), slice(64, 128)]
            product_stage(core, "pool_w", y[:, 4:6, :],
                          [[(pool_w[r, k, :], r, r, k, True, True) for r in halves] for k in range(2)], v, vec["pool_scale"])
            load_stage(core, "sgu", [(u[:, :, :], z1[12:14].rearrange("t c s -> c t s")),
                                     (v[:, :, :], z1[14:16].rearrange("t c s -> c t s"))], ACT.Gelu_apprx_tanh)
            norm_stage(core, "ln_d", v, [[0, 1]], mats["mean256"], 1e-5, True, vec["sgu_g"], vec["sgu_bb"], ACT.Identity)
            mix_stage(core, v, u, y[:, 6:8, :], ws, bs, ident)
        gate_stage(core, "gate1", lambda i: z1[16 + i], y, 8, ACT.Silu)
        ys = split_buffers(core, outer, "y1s", KT, SEQ)
        split_stage(core, "split1", y, ys)
        gemm_stage(core, "out1", [(A["w_out"], of(ys), lambda j: 2 * j), (A["w_out"], of(ys), lambda j: 2 * j + 1)],
                   4, SEQ, None, add_part(nc, x_t, META, SEQ))
    rms_stage(core, "rms1f", x_t, vec["final_g"], 1e-6, META, SEQ)


VECS = {}


def program(nc, A, out, stop=None):
    with ExitStack() as ctx:
        core = Core(nc)
        sb = lambda n, s: ctx.enter_context(nc.sbuf_tensor(n, s, F32))
        dram = lambda n, s: nc.dram_tensor(f"scratch_{n}", s, F32, kind="Internal").ap()
        x_t = sb("x_t", [P, KT, COLS])
        mat = sb("mats", [P, len(MATS), P])
        vecs = sb("vecs", [P, A["vecs"].shape[1]])
        core.eps = {e: sb(f"eps{i}", [P, 1])[:, :] for i, e in enumerate(EPSILONS)}
        mats = {name: mat[:, i, :] for i, name in enumerate(MATS)}
        vec, at = {}, 0
        for name, _, count in VEC_LIST:
            vec[name] = vecs[:, at:at + count]
            at += count
        start_stage(core, [(mat[:, :, :], A["mats"]), (vecs[:, :], A["vecs"])])
        res = block_one(core, A, x_t, mats, vec, dram, stop)
        if res is None and stop != "b1":
            res = block_two(core, A, x_t, mats, vec, dram, stop)
        if res is None and stop not in ("b1", "b2"):
            res = block_three(core, A, x_t, mats, vec, dram, stop)
        done = core.sem("out_done")
        with core.block() as block:
            @block.sync
            def _(sp):
                if res is not None:
                    sp.dma_start(out, res).then_inc(done, 16)
                else:
                    sp.dma_start(out.rearrange("(k p) s -> p k s", p=P), x_t[:, :, META:META + SEQ]).then_inc(done, 16)
                sp.wait_ge(done, 16)


EPSILONS = (1e-6, 1e-5, 64e-5)
MATS = ("ident", "mean256", "mean128", "mean64", "rope", "rot2", "causal")
VEC_LIST = [("norm_g", "norm_g", 8), ("dw_b", "conv_dw_b", 2), ("conv_g", "conv_ln_g", 2), ("conv_b", "conv_ln_b", 2),
            ("pool_scale", "pool_scale", 2), ("sgu_g", "sgu_ln_g", 2), ("sgu_bb", "sgu_ln_b", 2), ("final_g", "final_g", 8),
            ("mix_norm", "mix_norm_2", 8), ("b_in", "b_in_2", 34), ("b_alpha", "b_alpha_2", 2), ("gla_norm", "gla_head_norm_2", 4),
            ("ffn_norm", "ffn_norm_2", 8), ("ff_conv", "conv_w_2", 66), ("ff_conv_b", "conv_b_2", 22), ("final_norm2", "final_norm_2", 8),
            ("norm_mix", "norm_mix_w_3", 8), ("ret_norm", "ret_norm_w_3", 4), ("rw_mu", "rw_mu_3", 14), ("rw_w0", "rw_w0_3", 4),
            ("rw_a0", "rw_a0_3", 4), ("rw_kk", "rw_k_k_3", 4), ("rw_ka", "rw_k_a_3", 4), ("rw_rk", "rw_r_k_3", 4),
            ("rw_ln_w", "rw_ln_w_3", 4), ("rw_ln_b", "rw_ln_b_3", 4), ("norm_ffn", "norm_ffn_w_3", 8), ("norm_ple", "norm_ple_w_3", 8),
            ("final_norm3", "final_norm_w_3", 8)]


def tiles(w):
    k, n = w.shape
    return np.ascontiguousarray(w.reshape(k // P, P, n // P, P).transpose(2, 1, 0, 3).reshape(n // P, P, k))


def columns(v):
    return v.reshape(-1, P).T


def constants():
    i = np.arange(P)
    eye = np.eye(P, dtype=np.float32)
    rope = np.zeros((P, P), np.float32)
    for d in range(P):
        o = d % 64
        if o < 32:
            rope[d + 32, d] = -1
        else:
            rope[d - 32, d] = 1
    rot2 = np.zeros((P, P), np.float32)
    rot2[i[1::2], i[0::2]] = -1
    rot2[i[0::2], i[1::2]] = 1
    m = {"ident": eye, "mean256": np.full((P, P), 1 / 256, np.float32), "mean128": np.full((P, P), 1 / 128, np.float32),
         "mean64": ((i[:, None] // 64 == i[None] // 64) / 64).astype(np.float32), "rope": rope, "rot2": rot2,
         "causal": (i[:, None] <= i[None]).astype(np.float32)}
    return np.ascontiguousarray(np.stack([m[k] for k in MATS], axis=1))


def window_counts():
    t = np.arange(SEQ)
    out = np.zeros((P, 2, SEQ), np.float32)
    for g, w in enumerate((2, 4, 8, 16)):
        n = np.clip(t - w // 2 + w, 0, SEQ) - np.clip(t - w // 2, 0, SEQ)
        out[64 * (g % 2):64 * (g % 2) + 64, g // 2] = 1.0 / n.astype(np.float32)
    return out


def layout(i):
    c = np.ascontiguousarray
    A = {"x": c(i["x"][0].T), "w_in": tiles(i["w_in"][0]), "w_out": tiles(i["w_out"][0])}
    q, k = np.arange(GRID_W)[:, None], np.arange(GRID_W)[None]
    start = np.clip(q - NA_COLS // 2, 0, GRID_W - NA_COLS)
    ok = (k >= start) & (k < start + NA_COLS)
    rel = np.clip(k - q, 1 - NA_COLS, NA_COLS - 1) + NA_COLS - 1
    bias = i["na_rpb"][0][:, :, rel]
    bias = np.where(ok[None, None], bias, np.float32(NEG)).transpose(0, 2, 1, 3)
    A["na_bias"] = c(bias.reshape(4, 2, GRID_W, 15 * GRID_W).transpose(1, 2, 0, 3).reshape(P, 4, 15 * GRID_W))
    A["conv_w"] = c(i["conv_dw_w"][0].reshape(CONV_W, 2, P).transpose(2, 1, 0))
    A["conv_pw"] = c(i["conv_pw"][0].reshape(2, P, 256).transpose(1, 0, 2))
    A["pool_w"] = c(i["pool_w"][0].reshape(2, 2, 64, 64).transpose(1, 2, 0, 3).reshape(P, 2, 64))
    A["inv_count"] = window_counts()
    A["sgu_w"] = c(i["sgu_w"][0].transpose(2, 0, 1))
    A["sgu_b"] = c(np.repeat(i["sgu_b"][0].reshape(2, 2, P).transpose(1, 0, 2), 64, axis=0))
    A["mats"] = constants()
    i = dict(i)
    cols = order_two()
    A["meta"] = c(i["meta_tokens_2"].T.reshape(KT, P, META).transpose(1, 0, 2))
    A["w_in2"] = tiles(c(i["w_in_2"][0][:, cols]))
    low = slice(2304, 2320)
    A["w_low"] = c(i["w_in_2"][0][:, low].reshape(KT, P, 16).transpose(1, 0, 2))
    A["b_low"] = c(i["b_in_2"][0][low].reshape(16, 1))
    A["w_alpha"] = c(i["w_alpha_2"][0])
    i["b_in_2"] = i["b_in_2"][0][cols]
    i["gla_head_norm_2"] = np.tile(i["gla_head_norm_2"].reshape(-1), 4)
    A["level_masks"], A["swa_masks"], A["rope_tables"] = level_masks(), swa_masks(), rope_tables()
    A["sinks"] = c(i["attn_sinks_2"][0])
    A["w_att"], A["w_gla"], A["w_out2"] = (tiles(i[n][0]) for n in ("w_proj_attn_2", "w_proj_gla_2", "w_out_2"))
    A["w_up2"] = tiles(i["w_up_2"][0])
    for part, (first, count) in enumerate(FF_PARTS):
        rows = slice(first * P, (first + count) * P)
        A[f"w_down2_{part}"], A[f"w_down3_{part}"] = tiles(i["w_down_2"][0][rows]), tiles(i["w_down_3"][0][rows])
    A["ret_tables"], A["ret_decay"], A["ret_start"], A["ret_end"] = retention_tables()
    A["rw_mask4"], A["rw_neg1"] = rwkv_masks()
    A["p3"] = c(i["p_3"][0, 0].T)
    A["rw_w2a2"] = c(np.concatenate([i["rw_w2_3"][0], i["rw_a2_3"][0]], axis=0))
    A["rw_g2"] = c(i["rw_g2_3"][0])
    for name, src in (("w_in3", "w_in_3"), ("w_o3", "w_o_3"), ("w_gate3", "w_gate_3"), ("w_up3", "w_up_3"), 
                      ("w_ple_gate", "w_ple_gate_3"), ("w_ple_up", "w_ple_up_3")):
        A[name] = tiles(i[src][0])
    A["vecs"] = c(np.concatenate([columns(np.asarray(i[src]).reshape(-1)) for _, src, _ in VEC_LIST], axis=1))
    return A


def order_two():
    r = lambda a, n: list(range(a, a + n))
    return r(0, 512) + r(512, 128) + r(768, 256) + r(1024, 256) + r(640, 128) + r(1280, 512) + r(1792, 512) + r(2320, 2048)


def level_masks():
    i, j = np.arange(P)[None], np.arange(P)[:, None]
    m = [(i // (2 * s) == j // (2 * s)) & (j % (2 * s) < s) & (i % (2 * s) >= s) for s in LEVELS] + [i == j]
    return np.ascontiguousarray(np.stack(m, axis=1).astype(np.float32))


def swa_masks():
    q, k = np.arange(P)[:, None], np.arange(2 * P)[None]
    rel = q + P - k
    out = []
    for i in range(BLOCKS):
        pos = i * P + k - LEAD
        out.append(np.where((rel >= 0) & (rel < P) & (pos >= 0), 0.0, NEG))
    return np.stack(out).astype(np.float32)


def rope_tables():
    half = HEAD // 2
    inv = (np.float32(10000.0) ** (-np.arange(half, dtype=np.float32) / np.float32(half))).astype(np.float32)
    ang = np.arange(COLS, dtype=np.float32)[None] * inv[np.arange(P) % half][:, None]
    return np.ascontiguousarray(np.stack([np.cos(ang), np.sin(ang)], axis=1).astype(np.float32))


def kernel(**inputs):
    import concourse.bacc as bacc
    from concourse.bass_utils import run_bass_kernel_spmd

    arrays = layout({k: np.asarray(v) for k, v in inputs.items()})
    nc = bacc.Bacc("TRN2", target_bir_lowering=False, num_devices=1)
    A = {n: nc.dram_tensor(f"in_{n}", a.shape, F32, kind="ExternalInput").ap() for n, a in arrays.items()}
    out = nc.dram_tensor("out", (D, SEQ), F32, kind="ExternalOutput").ap()
    program(nc, A, out)
    r = run_bass_kernel_spmd(nc, [{f"in_{n}": a for n, a in arrays.items()}], core_ids=[0])
    return np.ascontiguousarray(r.results[0]["out"].T).reshape(1, SEQ, D)
```

```python
from contextlib import ExitStack, contextmanager

import numpy as np

import concourse.bass as bass
from concourse import mybir

F32 = mybir.dt.float32
F32R = mybir.dt.float32r
ALU = mybir.AluOpType
ACT = mybir.ActivationFunctionType
AX = mybir.AxisListType

P = 128
D = 1024
SEQ = 1024
META = 16
KT = D // P
LTOK = META + SEQ
COLS = LTOK + 4
NEG = -1.0e30


class Core:

    def __init__(self, nc):
        self.nc, self.now, self.before, self.eps = nc, [], [], {}

    def sem(self, name):
        self.now.append(self.nc.alloc_semaphore(name=name))
        return self.now[-1]

    @contextmanager
    def block(self):
        if self.before:
            self.nc.clear_and_free_semaphores(self.before)
        with self.nc.Block() as block:
            yield block
        self.before, self.now = self.now, []


def pieces(total):
    n = -(-total // 512)
    assert total % n == 0
    return n, total // n


def rms_stage(core, name, x_t, gain, eps, c0, total):
    nc = core.nc
    n, w = pieces(total)
    ready, squared, summed, root, summing = (core.sem(f"{name}_{s}") for s in ("ones", "squared", "summed", "root", "summing"))
    with ExitStack() as mem:
        sq = mem.enter_context(nc.sbuf_tensor(f"{name}_sq", [P, 2, total], F32))
        total_sq = mem.enter_context(nc.sbuf_tensor(f"{name}_total", [P, total], F32))
        rstd = mem.enter_context(nc.sbuf_tensor(f"{name}_rstd", [P, total], F32))
        ones = mem.enter_context(nc.sbuf_tensor(f"{name}_ones", [P, P], F32))
        ss = mem.enter_context(nc.psum_tensor(f"{name}_ss", [P, n, 512], F32))
        block = mem.enter_context(core.block())
        cols = slice(c0, c0 + total)

        @block.scalar
        def _(act):
            for k in range(KT):
                if k >= 2:
                    act.wait_ge(summing, k - 1)
                nc.scalar.activation(sq[:, k % 2, :], x_t[:, k, cols], ACT.Square).then_inc(squared, 1)
            act.wait_ge(summed, 1)
            nc.scalar.activation(rstd[:, :].rearrange("p (c w) -> p c w", c=n), ss[:, :, 0:w], ACT.Sqrt,
                                 scale=1.0 / D, bias=core.eps[eps]).then_inc(root, 1)

        @block.tensor
        def _(pe):
            pe.wait_ge(ready, 1)
            pe.wait_ge(summing, KT)
            for c in range(n):
                last = nc.tensor.matmul(ss[:, c, 0:w], ones[:, :], total_sq[:, c * w:(c + 1) * w], start=True, stop=True)
            last.then_inc(summed, 1)

        @block.vector
        def _(dve):
            nc.vector.memset(ones[:, :], 1.0).then_inc(ready, 1)
            add_squares(dve, nc, total_sq, sq, squared, summing)
            dve.wait_ge(root, 1)
            nc.vector.reciprocal(rstd[:, :], rstd[:, :])
            dve.drain()
            for k in range(KT):
                nc.vector.scalar_tensor_tensor(out=x_t[:, k, cols], in0=x_t[:, k, cols], scalar=gain[:, k:k + 1], in1=rstd[:, :],
                                               op0=ALU.mult, op1=ALU.mult)


def add_squares(dve, nc, total_sq, sq, squared, summing, between=lambda k: None):
    for k in range(KT):
        dve.wait_ge(squared, k + 1)
        if k == 0:
            nc.vector.tensor_copy(total_sq[:, :], sq[:, 0, :])
        else:
            nc.vector.tensor_tensor(total_sq[:, :], total_sq[:, :], sq[:, k % 2, :], ALU.add)
        dve.drain().then_inc(summing, 1)
        between(k)


def rms_split_stage(core, name, x_t, out, rms, gain, eps, c0, total):
    nc = core.nc
    n, w = pieces(total)
    ready, squared, summed, rounded, summing = (core.sem(f"{name}_{s}") for s in ("ones", "squared", "summed", "rounded", "summing"))
    with ExitStack() as mem:
        sq = mem.enter_context(nc.sbuf_tensor(f"{name}_sq", [P, 2, total], F32))
        total_sq = mem.enter_context(nc.sbuf_tensor(f"{name}_total", [P, total], F32))
        ones = mem.enter_context(nc.sbuf_tensor(f"{name}_ones", [P, P], F32))
        ss = mem.enter_context(nc.psum_tensor(f"{name}_ss", [P, n, 512], F32))
        block = mem.enter_context(core.block())
        cols = slice(c0, c0 + total)

        @block.scalar
        def _(act):
            for k in range(KT):
                if k >= 2:
                    act.wait_ge(summing, k - 1)
                nc.scalar.activation(sq[:, k % 2, :], x_t[:, k, cols], ACT.Square).then_inc(squared, 1)
                nc.scalar.activation(out[0][:, k, cols], x_t[:, k, cols], ACT.Copy, scale=gain[:, k:k + 1]).then_inc(rounded, 1)
            act.wait_ge(summed, 1)
            nc.scalar.activation(rms[:, :].rearrange("p (c w) -> p c w", c=n), ss[:, :, 0:w], ACT.Sqrt,
                                 scale=1.0 / D, bias=core.eps[eps])

        @block.tensor
        def _(pe):
            pe.wait_ge(ready, 1)
            pe.wait_ge(summing, KT)
            for c in range(n):
                last = nc.tensor.matmul(ss[:, c, 0:w], ones[:, :], total_sq[:, c * w:(c + 1) * w], start=True, stop=True)
            last.then_inc(summed, 1)

        @block.vector
        def _(dve):
            nc.vector.memset(ones[:, :], 1.0).then_inc(ready, 1)

            def low(k):
                dve.wait_ge(rounded, k + 1)
                nc.vector.scalar_tensor_tensor(out=out[1][:, k, cols], in0=x_t[:, k, cols], scalar=gain[:, k:k + 1],
                                               in1=out[0][:, k, cols].bitcast(F32), op0=ALU.mult, op1=ALU.subtract)

            add_squares(dve, nc, total_sq, sq, squared, summing, low)


def split_stage(core, name, src, out):
    nc = core.nc
    high, low = core.sem(f"{name}_high"), core.sem(f"{name}_low")
    with core.block() as block:
        @block.scalar
        def _(act):
            for k in range(src.shape[1]):
                nc.scalar.activation(out[0][:, k, :], src[:, k, :], ACT.Copy).then_inc(high, 1)

        @block.vector
        def _(dve):
            for k in range(src.shape[1]):
                dve.wait_ge(high, k + 1)
                nc.vector.tensor_tensor(out[1][:, k, :], src[:, k, :], out[0][:, k, :].bitcast(F32), ALU.subtract).then_inc(low, 1)


def gemm_stage(core, name, units, steps, total, act_part, dve_part, out=None, extras=(), temps=(), chained=False, rms=None):
    nc = core.nc
    n, w = pieces(total)
    kts = [wt.shape[2] // P for wt, _, _ in units]
    mm_done, act_done, unit_done, w_high, w_split = (
        core.sem(f"{name}_{s}") for s in ("mm_done", "act_done", "unit_done", "w_high", "w_split"))
    w_here, x_here, stored = ([core.sem(f"{name}_{s}{u}") for u in range(2)] for s in ("w_here", "x_here", "stored"))
    AHEAD = 2
    with ExitStack() as mem:
        wb = [mem.enter_context(nc.sbuf_tensor(f"{name}_w{u}", [P, kts[u], P], F32)) for u in range(2)]
        wh = [mem.enter_context(nc.sbuf_tensor(f"{name}_wh{u}", [P, kts[u], P], F32R)) for u in range(2)]
        wl = [mem.enter_context(nc.sbuf_tensor(f"{name}_wl{u}", [P, kts[u], P], F32R)) for u in range(2)]
        ps = mem.enter_context(nc.psum_tensor(f"{name}_ps", [P, 2, n, 512], F32))
        t = {k: mem.enter_context(nc.sbuf_tensor(f"{name}_{k}", [P, size], F32)) for k, size in temps}
        for u, _, k in extras:
            t[k] = mem.enter_context(nc.sbuf_tensor(f"{name}_{k}", [P, total], F32))
        if out:
            t["out"] = mem.enter_context(nc.sbuf_tensor(f"{name}_out", [P, 2, total], F32))
        view = lambda a: a.rearrange("p (c w) -> p c w", c=n)
        t["view"] = view
        nx = [sum(1 for e in extras if e[0] == u) for u in range(2)]
        has_out = [bool(out and out[u]) for u in range(2)]
        block = mem.enter_context(core.block())

        @block.sync
        def _(sp):
            def load(j, u):
                wt, _, at = units[u]
                sp.dma_start(wb[u][:, :, :], wt[bass.ds(at(j), 1)].rearrange("o p (k c) -> p (o k) c", c=P)
                             ).then_inc(w_here[u], 16)

            def load_extras(j, u):
                for ux, rows, k in extras:
                    if ux == u:
                        sp.dma_start(t[k][:, :], rows(j)).then_inc(x_here[u], 16)

            def step(j, more):
                for u in range(2):
                    if more:
                        sp.wait_ge(w_split, 2 * j + u + 1)
                        load(j + 1, u)
                    if has_out[u] or (nx[u] and more):
                        sp.wait_ge(unit_done, 2 * j + u + 1 + AHEAD)
                    if has_out[u]:
                        sp.dma_start(out[u](j), t["out"][:, u, :]).then_inc(stored[u], 16)
                    if more:
                        load_extras(j + 1, u)

            for u in range(2):
                load(0, u)
                load_extras(0, u)
            if steps > 1:
                with sp.Fori(0, steps - 1) as j:
                    step(j, True)
            step(steps - 1, False)
            for u in range(2):
                if has_out[u]:
                    sp.wait_ge(stored[u], 16 * (steps + 1))

        @block.tensor
        def _(pe):
            pe.sem_inc(mm_done, AHEAD)
            with pe.Fori(0, steps) as j:
                for u in range(2):
                    pe.wait_ge(w_split, 2 * j + u + 1)
                    pe.wait_ge(unit_done, 2 * j + u + 1)
                    for c in range(n):
                        for k in range(kts[u]):
                            x_high, x_low = units[u][1](k, c * w, w)
                            for i, (a, x) in enumerate(((wh, x_high), (wh, x_low), (wl, x_high))):
                                last = nc.tensor.matmul(ps[:, u, c, 0:w], a[u][:, k, :], x, start=(k == 0 and i == 0),
                                                        stop=(k == kts[u] - 1 and i == 2))
                    last.then_inc(mm_done, 1)

        def lagged(eng, split, part, before=None):
            split(0, 0)
            if before:
                before()

            def step(j, more):
                split(j, 1)
                part(j, 0)
                if more:
                    split(j + 1, 0)
                part(j, 1)

            if steps > 1:
                with eng.Fori(0, steps - 1) as j:
                    step(j, True)
            step(steps - 1, False)

        @block.scalar
        def _(act):
            def split(j, u):
                act.wait_ge(w_here[u], 16 * (j + 1))
                act.wait_ge(mm_done, 2 * j + u + 1)
                nc.scalar.activation(wh[u][:, :, :], wb[u][:, :, :], ACT.Copy).then_inc(w_high, 1)

            def part(j, u):
                if act_part is None or (chained and u == 0):
                    return
                act.wait_ge(mm_done, 2 * j + u + 1 + AHEAD)
                act.wait_ge(unit_done, 2 * j + u + 1 + (1 if chained else 0))
                if nx[u]:
                    act.wait_ge(x_here[u], 16 * nx[u] * (j + 1))
                act_part(act, u, j, ps[:, u, :, 0:w], t)
                act.drain().then_inc(act_done, 1)

            lagged(act, split, part)

        @block.vector
        def _(dve):
            dve.sem_inc(unit_done, AHEAD)
            for u in range(2):
                if has_out[u]:
                    dve.sem_inc(stored[u], 16)

            def split(j, u):
                dve.wait_ge(w_high, 2 * j + u + 1)
                nc.vector.tensor_tensor(wl[u][:, :, :], wb[u][:, :, :], wh[u][:, :, :].bitcast(F32), ALU.subtract).then_inc(w_split, 1)

            def part(j, u):
                if chained and u:
                    dve.wait_ge(act_done, j + 1)
                elif act_part and not chained:
                    dve.wait_ge(act_done, 2 * j + u + 1)
                else:
                    dve.wait_ge(mm_done, 2 * j + u + 1 + AHEAD)
                if nx[u]:
                    dve.wait_ge(x_here[u], 16 * nx[u] * (j + 1))
                if has_out[u]:
                    dve.wait_ge(stored[u], 16 * (j + 1))
                dve_part(dve, u, j, ps[:, u, :, 0:w], t)
                dve.drain().then_inc(unit_done, 1)

            def invert():
                nc.vector.reciprocal(rms[:, :], rms[:, :])
                dve.drain()

            lagged(dve, split, part, invert if rms is not None else None)


def turn_stage(core, name, load, store, blocks, steps, ident):
    nc = core.nc
    loaded, stored = ([core.sem(f"{name}_{s}{b}") for b in range(2)] for s in ("loaded", "stored"))
    turned, copied = core.sem(f"{name}_turned"), core.sem(f"{name}_copied")
    AHEAD = 2
    assert steps % 2 == 0 and blocks <= 8
    with ExitStack() as mem:
        src = mem.enter_context(nc.sbuf_tensor(f"{name}_src", [P, 2, blocks, P], F32))
        dst = mem.enter_context(nc.sbuf_tensor(f"{name}_dst", [P, 2, blocks * P], F32))
        ps = mem.enter_context(nc.psum_tensor(f"{name}_ps", [P, 2, -(-blocks // 4) * 4 * P], F32))
        block = mem.enter_context(core.block())

        @block.sync
        def _(sp):
            with sp.Fori(0, steps // 2) as jj:
                for b in range(2):
                    j = 2 * jj + b
                    sp.wait_ge(copied, j + 1)
                    sp.dma_start(src[:, b, :, :], load(j)).then_inc(loaded[b], 16)

        @block.tensor
        def _(pe):
            with pe.Fori(0, steps // 2) as jj:
                for b in range(2):
                    j = 2 * jj + b
                    pe.wait_ge(loaded[b], 16 * (jj + 1))
                    pe.wait_ge(copied, j + 1)
                    for c in range(blocks):
                        last = nc.tensor.transpose(ps[:, b, c * P:(c + 1) * P], src[:, b, c, :], ident[:, :])
                    last.then_inc(turned, 1)

        @block.vector
        def _(dve):
            dve.sem_inc(copied, AHEAD)
            for b in range(2):
                dve.sem_inc(stored[b], 16)
            with dve.Fori(0, steps // 2) as jj:
                for b in range(2):
                    j = 2 * jj + b
                    dve.wait_ge(turned, j + 1)
                    dve.wait_ge(stored[b], 16 * (jj + 1))
                    nc.vector.tensor_copy(dst[:, b, :], ps[:, b, 0:blocks * P]).then_inc(copied, 1)

        @block.scalar
        def _(act):
            with act.Fori(0, steps // 2) as jj:
                for b in range(2):
                    j = 2 * jj + b
                    act.wait_ge(copied, j + 1 + AHEAD)
                    act.dma_start(store(j), dst[:, b, :]).then_inc(stored[b], 16)
            for b in range(2):
                act.wait_ge(stored[b], 16 * (steps // 2 + 1))


NA_HEADS, GRID_W, NA_ROWS, NA_COLS = 8, 64, 8, 16
GRID_H = SEQ // GRID_W
NA_DH = 32
BAND = NA_ROWS * GRID_W


def na_stage(core, z, v_tok, bias, ya_tok, ident):
    nc = core.nc
    DR = 2 * NA_ROWS - 1
    PAIRS = NA_HEADS // 2
    ROWS = 4
    UNITS = ROWS * PAIRS
    TURN_LAG, OUT_LAG = 2, 3
    s_done, p_done, t_done, c_done, o_done, y_done, m_done, row_scored, q_done, qk_here, v_here, bias_here = (
        core.sem(f"na_{s}") for s in ("scores", "probs", "turned", "copied", "outs", "ys", "softmaxed", "row_scored",
                                      "queries", "qk_here", "v_here", "bias"))
    y_stored = [core.sem(f"na_stored{b}") for b in range(2)]
    ranges = [(0, 1, lambda r: 0, lambda r: (NA_ROWS - 1 - r) * GRID_W),
              (1, 3, lambda r: r - NA_ROWS // 2, lambda r: (NA_ROWS // 2 - 1) * GRID_W),
              (3, 4, lambda r: GRID_H - NA_ROWS, lambda r: (GRID_H - 1 - r) * GRID_W)]
    with ExitStack() as mem:
        sb = lambda n, s: mem.enter_context(nc.sbuf_tensor(f"na_{n}", s, F32))
        q = sb("q", [P, 2, SEQ])
        kb = sb("k", [P, 2, SEQ])
        v = [sb(f"v{a}", [P, SEQ // P - a, 2 * P]) for a in range(2)]
        qz = sb("qz", [P, 2, PAIRS, P])
        bt = sb("bias_t", [P, PAIRS, DR * GRID_W])
        sc = sb("sc", [P, PAIRS, BAND])
        pr = sb("pr", [P, PAIRS, BAND])
        pt = sb("pt", [P, PAIRS, 4, P])
        st = sb("st", [P, 3, 2, PAIRS])
        y = sb("y", [P, 2, PAIRS, NA_DH])
        ps_s = mem.enter_context(nc.psum_tensor("na_ps_s", [P, PAIRS, BAND], F32))
        ps_t = mem.enter_context(nc.psum_tensor("na_ps_t", [P, 2, 4, P], F32))
        ps_o = mem.enter_context(nc.psum_tensor("na_ps_o", [P, 2, 512], F32))
        block = mem.enter_context(core.block())

        def bodies(eng, body):
            for lo, hi, start, first in ranges:
                if hi - lo == 1:
                    body(lo, start, first)
                else:
                    with eng.Fori(lo, hi) as g:
                        body(g, start, first)

        def pipeline(stages):
            for s in range(UNITS + OUT_LAG):
                for lag, stage in stages:
                    if 0 <= s - lag < UNITS:
                        stage((s - lag) // PAIRS, (s - lag) % PAIRS)

        @block.sync
        def _(sp):
            sp.dma_start(q[:, :, :], z[0:2].rearrange("t c s -> c t s")).then_inc(qk_here, 16)
            sp.dma_start(kb[:, :, :], z[2:4].rearrange("t c s -> c t s")).then_inc(qk_here, 16)
            for a in range(2):
                sp.dma_start(v[a][:, :, :], v_tok[GRID_W * a:SEQ - GRID_W * a].rearrange("(t p) c -> p t c", p=P)
                             ).then_inc(v_here, 16)
            yr = ya_tok.rearrange("(r w) (p a d) -> a r w p d", w=GRID_W, a=2, d=NA_DH)

            def body(g, start, first):
                for i in range(ROWS):
                    r = ROWS * g + i
                    sp.wait_ge(y_done, PAIRS * ROWS * g + PAIRS * (i + 1) + 2)
                    for a in range(2):
                        sp.dma_start(yr[a, bass.ds(r, 1)].rearrange("o w p d -> (o w) p d"),
                                     y[64 * a:64 * a + 64, i % 2, :, :]).then_inc(y_stored[i % 2], 16)

            bodies(sp, body)
            for b in range(2):
                sp.wait_ge(y_stored[b], 32 * (GRID_H // 2 + 1))

        @block.tensor
        def _(pe):
            pe.wait_ge(qk_here, 32)

            def body(g, start, first):
                def scores(i, p):
                    if p == 0:
                        pe.wait_ge(q_done, ROWS * g + i + 1)
                    pe.wait_ge(m_done, UNITS * g + PAIRS * i + p + 1)
                    nc.tensor.matmul(ps_s[:, p, :], qz[:, i % 2, p, :],
                                     kb[:, p // 2, bass.ds(start(ROWS * g + i) * GRID_W, BAND)], start=True, stop=True).then_inc(s_done, 1)

                def turn(i, p):
                    u = UNITS * g + PAIRS * i + p
                    pe.wait_ge(p_done, u + 1)
                    pe.wait_ge(c_done, u + 1)
                    for c in range(4):
                        last = nc.tensor.transpose(ps_t[:, p % 2, c, :], pr[:, p, c * P:(c + 1) * P], ident[:, :])
                    last.then_inc(t_done, 1)

                def outs(i, p):
                    u = UNITS * g + PAIRS * i + p
                    if lo_start(g, i) is None:
                        odd, tile = i % 2, lambda c: bass.ds(2 * g + (i // 2 + c - 2), 1)
                    else:
                        odd, tile = 0, lambda c: slice(lo_start(g, i) + c, lo_start(g, i) + c + 1)
                    pe.wait_ge(c_done, u + 3)
                    pe.wait_ge(y_done, u + 1)
                    for c in range(4):
                        last = nc.tensor.matmul(ps_o[:, p % 2, 0:64], pt[:, p, c, :],
                                                v[odd][:, tile(c), 64 * p:64 * p + 64].rearrange("k o d -> k (o d)"),
                                                start=(c == 0), stop=(c == 3))
                    last.then_inc(o_done, 1)

                def lo_start(g, i):
                    return start(0) // 2 if isinstance(g, int) else None

                if isinstance(g, int) and g == 0:
                    pe.wait_ge(v_here, 32)
                pipeline(((0, scores), (TURN_LAG, turn), (OUT_LAG, outs)))

            bodies(pe, body)

        @block.scalar
        def _(act):
            act.dma_start(bt[:, :, :], bias).then_inc(bias_here, 16)
            act.sem_inc(c_done, 2)

            def body(g, start, first):
                def probs(i, p):
                    act.wait_ge(m_done, UNITS * g + PAIRS * i + p + PAIRS + 1)
                    nc.scalar.activation(pr[:, p, :], sc[:, p, :], ACT.Exp, bias=st[:, 0, i % 2, p:p + 1],
                                         accum_out=st[:, 1, i % 2, p:p + 1]).then_inc(p_done, 1)

                def copy(i, p):
                    act.wait_ge(t_done, UNITS * g + PAIRS * i + p + 1)
                    nc.scalar.activation(pt[:, p, :, :], ps_t[:, p % 2, :, :], ACT.Copy).then_inc(c_done, 1)

                pipeline(((0, probs), (TURN_LAG, copy)))

            bodies(act, body)

        @block.vector
        def _(dve):
            dve.sem_inc(m_done, PAIRS)
            dve.sem_inc(y_done, 2)
            dve.sem_inc(row_scored, 2)
            for b in range(2):
                dve.sem_inc(y_stored[b], 32)
            dve.wait_ge(bias_here, 16)

            def body(g, start, first):
                def softmax(i, p):
                    dve.wait_ge(s_done, UNITS * g + PAIRS * i + p + 1)
                    at = first(ROWS * g + i)
                    nc.vector.scalar_tensor_tensor(out=sc[:, p, :], in0=ps_s[:, p, :], scalar=NA_DH ** -0.5,
                                                   in1=bt[:, p, at:at + BAND], op0=ALU.mult, op1=ALU.add)
                    dve.drain()
                    nc.vector.tensor_reduce(st[:, 0, i % 2, p:p + 1], sc[:, p, :], AX.X, ALU.max, negate=True)
                    dve.drain().then_inc(m_done, 1)
                    if p == PAIRS - 1:
                        dve.sem_inc(row_scored, 1)

                def norm(i, p):
                    dve.wait_ge(o_done, UNITS * g + PAIRS * i + p + 1)
                    if p == 0:
                        dve.wait_ge(y_stored[i % 2], ROWS * 16 * g + 32 * (i // 2 + 1))
                    nc.vector.reciprocal(st[:, 2, i % 2, p:p + 1], st[:, 1, i % 2, p:p + 1])
                    dve.drain()
                    for a in range(2):
                        rows_a = slice(64 * a, 64 * a + 64)
                        nc.vector.tensor_scalar(y[rows_a, i % 2, p, :], ps_o[rows_a, p % 2, NA_DH * a:NA_DH * (a + 1)],
                                                st[rows_a, 2, i % 2, p:p + 1], None, ALU.mult)
                    dve.drain().then_inc(y_done, 1)

                pipeline(((0, softmax), (OUT_LAG, norm)))

            bodies(dve, body)

        @block.gpsimd
        def _(pool):
            nc.gpsimd.memset(qz[:, :, :, :], 0.0)
            pool.drain()
            pool.wait_ge(qk_here, 32)

            def body(g, start, first):
                for i in range(ROWS):
                    r = ROWS * g + i
                    pool.wait_ge(row_scored, r + 1)
                    for h in range(PAIRS):
                        at = NA_DH * h
                        nc.gpsimd.tensor_copy(qz[at:at + NA_DH, i % 2, h // 2::2, 64 * (h % 2):64 * (h % 2) + 64],
                                              q[at:at + NA_DH, :, bass.ds(r * GRID_W, GRID_W)])
                    pool.drain().then_inc(q_done, 1)

            bodies(pool, body)




def norm_stage(core, name, v, groups, stat, eps, mean, scale, bias, func):
    nc = core.nc
    total = v.shape[2]
    n, w = pieces(total)
    m_done, sub, squared, v_done, root, normed, ended = (
        core.sem(f"{name}_{s}") for s in ("mean", "centred", "squared", "var", "root", "normed", "ended"))
    with ExitStack() as mem:
        sq = mem.enter_context(nc.sbuf_tensor(f"{name}_sq", [P, len(groups[0]), total], F32))
        rstd = mem.enter_context(nc.sbuf_tensor(f"{name}_rstd", [P, total], F32))
        ps = mem.enter_context(nc.psum_tensor(f"{name}_ps", [P, 2, n, 512], F32))
        cut = lambda a: a.rearrange("p (c w) -> p c w", c=n)
        block = mem.enter_context(core.block())

        @block.tensor
        def _(pe):
            for g, tiles in enumerate(groups):
                if mean:
                    if g:
                        pe.wait_ge(sub, g)
                    for c in range(n):
                        for i, k in enumerate(tiles):
                            last = nc.tensor.matmul(ps[:, 0, c, 0:w], stat, v[:, k, c * w:(c + 1) * w],
                                                    start=(i == 0), stop=(i == len(tiles) - 1))
                    last.then_inc(m_done, 1)
                pe.wait_ge(squared, g + 1)
                for c in range(n):
                    for i, k in enumerate(tiles):
                        last = nc.tensor.matmul(ps[:, 1, c, 0:w], stat, sq[:, i, c * w:(c + 1) * w],
                                                start=(i == 0), stop=(i == len(tiles) - 1))
                last.then_inc(v_done, 1)

        @block.vector
        def _(dve):
            for g, tiles in enumerate(groups):
                if mean:
                    dve.wait_ge(m_done, g + 1)
                    for k in tiles:
                        nc.vector.tensor_tensor(cut(v[:, k, :]), cut(v[:, k, :]), ps[:, 0, :, 0:w], ALU.subtract)
                    dve.drain().then_inc(sub, 1)
                dve.wait_ge(root, g + 1)
                nc.vector.reciprocal(rstd[:, :], rstd[:, :])
                dve.drain()
                for k in tiles:
                    nc.vector.tensor_tensor(v[:, k, :], v[:, k, :], rstd[:, :], ALU.mult)
                dve.drain().then_inc(normed, 1)

        @block.scalar
        def _(act):
            for g, tiles in enumerate(groups):
                if mean:
                    act.wait_ge(sub, g + 1)
                for i, k in enumerate(tiles):
                    nc.scalar.activation(sq[:, i, :], v[:, k, :], ACT.Square)
                act.drain().then_inc(squared, 1)
                act.wait_ge(v_done, g + 1)
                nc.scalar.activation(cut(rstd[:, :]), ps[:, 1, :, 0:w], ACT.Sqrt, bias=core.eps[eps]).then_inc(root, 1)
                act.wait_ge(normed, g + 1)
                for k in tiles:
                    nc.scalar.activation(v[:, k, :], v[:, k, :], func, scale=scale[:, k:k + 1],
                                         bias=bias[:, k:k + 1] if bias is not None else 0.0)
                act.drain().then_inc(ended, 1)


def packed_norm_stage(core, name, v, packs, stat, eps, scale, bias=None):
    nc = core.nc
    total = v.shape[2]
    tiles = v.shape[1]
    n, w = pieces(total)
    ROT = 4
    units = [(k, slice(c * w, (c + 1) * w)) for k in range(tiles) for c in range(n)]
    here, m_done, sub, squared, v_done, root, inverted, spread, applied = (
        core.sem(f"{name}_{s}") for s in ("packs", "mean", "centred", "squared", "var", "root", "inverted", "spread", "applied"))
    with ExitStack() as mem:
        pk = mem.enter_context(nc.sbuf_tensor(f"{name}_pk", [P, 2 * tiles, P], F32))
        sq = mem.enter_context(nc.sbuf_tensor(f"{name}_sq", [P, tiles, total], F32))
        rstd = mem.enter_context(nc.sbuf_tensor(f"{name}_rstd", [P, total], F32))
        ps_v = mem.enter_context(nc.psum_tensor(f"{name}_ps_v", [P, n, 512], F32))
        ps_r = mem.enter_context(nc.psum_tensor(f"{name}_ps_r", [P, ROT, 512], F32))
        block = mem.enter_context(core.block())

        @block.sync
        def _(sp):
            sp.dma_start(pk[:, :, :], packs).then_inc(here, 16)

        @block.tensor
        def _(pe):
            if stat is not None:
                for q, (k, cols) in enumerate(units):
                    if q >= ROT:
                        pe.wait_ge(sub, q - ROT + 1)
                    nc.tensor.matmul(ps_r[:, q % ROT, 0:w], stat, v[:, k, cols], start=True, stop=True).then_inc(m_done, 1)
            pe.wait_ge(here, 16)
            for k in range(tiles):
                pe.wait_ge(squared, k + 1)
                for c in range(n):
                    last = nc.tensor.matmul(ps_v[:, c, 0:w], pk[:, k, :], sq[:, k, c * w:(c + 1) * w],
                                            start=(k == 0), stop=(k == tiles - 1))
            last.then_inc(v_done, 1)
            pe.wait_ge(inverted, 1)
            for q, (k, cols) in enumerate(units):
                if q >= ROT:
                    pe.wait_ge(applied, q - ROT + 1)
                nc.tensor.matmul(ps_r[:, q % ROT, 0:w], pk[:, tiles + k, :], rstd[:, cols], start=True, stop=True).then_inc(spread, 1)

        @block.scalar
        def _(act):
            for k in range(tiles):
                if stat is not None:
                    act.wait_ge(sub, n * (k + 1))
                nc.scalar.activation(sq[:, k, :], v[:, k, :], ACT.Square).then_inc(squared, 1)
            act.wait_ge(v_done, 1)
            nc.scalar.activation(rstd[:, :].rearrange("p (c w) -> p c w", c=n), ps_v[:, :, 0:w], ACT.Sqrt, bias=core.eps[eps]).then_inc(root, 1)
            if bias is not None:
                for k in range(tiles):
                    act.wait_ge(applied, n * (k + 1))
                    nc.scalar.activation(v[:, k, :], v[:, k, :], ACT.Identity, bias=bias[:, k:k + 1])

        @block.vector
        def _(dve):
            if stat is not None:
                for q, (k, cols) in enumerate(units):
                    dve.wait_ge(m_done, q + 1)
                    nc.vector.tensor_tensor(v[:, k, cols], v[:, k, cols], ps_r[:, q % ROT, 0:w], ALU.subtract).then_inc(sub, 1)
            dve.wait_ge(root, 1)
            nc.vector.reciprocal(rstd[:, :], rstd[:, :])
            dve.drain().then_inc(inverted, 1)
            for q, (k, cols) in enumerate(units):
                dve.wait_ge(spread, q + 1)
                nc.vector.scalar_tensor_tensor(out=v[:, k, cols], in0=v[:, k, cols], scalar=scale[:, k:k + 1],
                                               in1=ps_r[:, q % ROT, 0:w], op0=ALU.mult, op1=ALU.mult).then_inc(applied, 1)


CONV_W = 31


def conv_stage(core, z, v, taps, dw_b):
    nc = core.nc
    half = CONV_W // 2
    here, sig = core.sem("conv_here"), core.sem("conv_sigmoid")
    with ExitStack() as mem:
        a = mem.enter_context(nc.sbuf_tensor("conv_a", [P, 2, SEQ + 2 * half], F32))
        b = mem.enter_context(nc.sbuf_tensor("conv_b", [P, 2, SEQ], F32))
        odd = mem.enter_context(nc.sbuf_tensor("conv_odd", [P, 2, SEQ], F32))
        zero = core.sem("conv_zero")
        block = mem.enter_context(core.block())

        @block.sync
        def _(sp):
            sp.dma_start(a[:, :, half:half + SEQ], z[6:8].rearrange("t c s -> c t s")).then_inc(here, 16)
            sp.dma_start(b[:, :, :], z[8:10].rearrange("t c s -> c t s")).then_inc(here, 16)

        @block.scalar
        def _(act):
            act.wait_ge(here, 32)
            nc.scalar.activation(b[:, :, :], b[:, :, :], ACT.Sigmoid).then_inc(sig, 1)

        @block.vector
        def _(dve):
            nc.vector.memset(a[:, :, 0:half], 0.0)
            nc.vector.memset(a[:, :, half + SEQ:], 0.0)
            dve.wait_ge(sig, 1)
            nc.vector.tensor_tensor(a[:, :, half:half + SEQ], a[:, :, half:half + SEQ], b[:, :, :], ALU.mult)
            dve.drain()
            sums = lambda q, k: v[:, k, :] if q == 0 else odd[:, k, :]
            for k in range(2):
                nc.vector.tensor_scalar(sums(0, k), a[:, k, 0:SEQ], taps[:, k, 0:1], dw_b[:, k:k + 1], ALU.mult, ALU.add)
                nc.vector.tensor_scalar(sums(1, k), a[:, k, 1:1 + SEQ], taps[:, k, 1:2], None, ALU.mult)
            dve.drain()

            def add_tap(i, q, k):
                nc.vector.scalar_tensor_tensor(out=sums(q, k), in0=a[:, k, bass.ds(i, SEQ)], scalar=taps[:, k, bass.ds(i, 1)],
                                               in1=sums(q, k), op0=ALU.mult, op1=ALU.add)

            with dve.Fori(1, CONV_W // 2) as i:
                for q in range(2):
                    for k in range(2):
                        add_tap(2 * i + q, q, k)
                dve.drain()
            for k in range(2):
                add_tap(CONV_W - 1, 0, k)
            dve.drain()
            nc.vector.tensor_tensor(v[:, :, :], v[:, :, :], odd[:, :, :], ALU.add)


def product_stage(core, name, out, mats, v, scale=None):
    nc = core.nc
    n, w = pieces(v.shape[2])
    done = core.sem(f"{name}_done")
    with ExitStack() as mem:
        ps = mem.enter_context(nc.psum_tensor(f"{name}_ps", [P, len(mats), n, 512], F32))
        block = mem.enter_context(core.block())

        @block.tensor
        def _(pe):
            for m, parts in enumerate(mats):
                for c in range(n):
                    for lhs, rows, orows, k, first, end in parts:
                        last = nc.tensor.matmul(ps[orows, m, c, 0:w], lhs, v[rows, k, c * w:(c + 1) * w],
                                                start=first, stop=end)
                last.then_inc(done, 1)

        @block.vector
        def _(dve):
            for m in range(len(mats)):
                dve.wait_ge(done, m + 1)
                o = out[:, m, :].rearrange("p (c w) -> p c w", c=n)
                if scale is None:
                    nc.vector.tensor_copy(o, ps[:, m, :, 0:w])
                else:
                    nc.vector.tensor_scalar(o, ps[:, m, :, 0:w], scale[:, m:m + 1], None, ALU.mult)


def pool_stage(core, z, v, inv_count):
    nc = core.nc
    E = 8
    here = core.sem("pool_here")
    with ExitStack() as mem:
        x = mem.enter_context(nc.sbuf_tensor("pool_x", [P, 2, SEQ + 2 * E], F32))
        s = [mem.enter_context(nc.sbuf_tensor(f"pool_s{i}", [P, 2, SEQ + 2 * E], F32)) for i in range(3)]
        inv = mem.enter_context(nc.sbuf_tensor("pool_inv", [P, 2, SEQ], F32))
        block = mem.enter_context(core.block())

        @block.sync
        def _(sp):
            sp.dma_start(x[:, :, E:E + SEQ], z[10:12].rearrange("t c s -> c t s")).then_inc(here, 16)
            sp.dma_start(inv[:, :, :], inv_count).then_inc(here, 16)

        @block.vector
        def _(dve):
            nc.vector.memset(x[:, :, 0:E], 0.0)
            nc.vector.memset(x[:, :, E + SEQ:], 0.0)
            dve.drain()
            dve.wait_ge(here, 32)
            end = SEQ + 2 * E
            top, low = slice(64, 128), slice(0, 64)
            add = lambda out, a, b: nc.vector.tensor_tensor(out, a, b, ALU.add)
            s2, s4, s8 = s
            add(s2[:, :, 1:end], x[:, :, 0:end - 1], x[:, :, 1:end])
            dve.drain()
            add(s4[:, :, 2:end - 1], s2[:, :, 1:end - 2], s2[:, :, 3:end])
            dve.drain()
            add(s8[:, 1, 4:end - 3], s4[:, 1, 2:end - 5], s4[:, 1, 6:end - 1])
            dve.drain()
            tok = slice(E, E + SEQ)
            mul = lambda out, a, b: nc.vector.tensor_tensor(out, a, b, ALU.mult)
            mul(v[low, 0, :], s2[low, 0, tok], inv[low, 0, :])
            mul(v[top, 0, :], s4[top, 0, tok], inv[top, 0, :])
            mul(v[low, 1, :], s8[low, 1, tok], inv[low, 1, :])
            add(v[top, 1, :], s8[top, 1, E - 4:E - 4 + SEQ], s8[top, 1, E + 4:E + 4 + SEQ])
            dve.drain()
            mul(v[top, 1, :], v[top, 1, :], inv[top, 1, :])
            dve.drain()
            nc.vector.tensor_tensor(v[:, :, :], v[:, :, :], x[:, :, tok], ALU.subtract)


def load_stage(core, name, loads, func=None):
    nc = core.nc
    here = [core.sem(f"{name}_here{i}") for i in range(len(loads))]
    with ExitStack() as mem:
        block = mem.enter_context(core.block())

        @block.sync
        def _(sp):
            for (dst, src), h in zip(loads, here):
                sp.dma_start(dst, src).then_inc(h, 16)
            if func is None:
                for h in here:
                    sp.wait_ge(h, 16)

        @block.scalar
        def _(act):
            if func is not None:
                for (dst, _), h in zip(loads, here):
                    act.wait_ge(h, 16)
                    nc.scalar.activation(dst, dst, func)


SGU_HEADS, SGU_CHUNK = 4, 128


def mix_stage(core, v, u, y, ws, bs, ident):
    nc = core.nc
    chunks = SEQ // SGU_CHUNK
    turned, copied, mixed, added = (core.sem(f"mix_{s}") for s in ("turned", "copied", "mixed", "added"))
    with ExitStack() as mem:
        vt = mem.enter_context(nc.sbuf_tensor("mix_vt", [P, 2, 2 * P], F32))
        m = mem.enter_context(nc.sbuf_tensor("mix_m", [P, 2, P], F32))
        ps_t = mem.enter_context(nc.psum_tensor("mix_ps_t", [P, 2, 512], F32))
        ps_m = mem.enter_context(nc.psum_tensor("mix_ps_m", [P, 2, 512], F32))
        block = mem.enter_context(core.block())

        @block.tensor
        def _(pe):
            for i in range(chunks):
                b, tok = i % 2, slice(i * P, (i + 1) * P)
                if i >= 2:
                    pe.wait_ge(copied, i - 1)
                for k in range(2):
                    last = nc.tensor.transpose(ps_t[:, b, k * P:(k + 1) * P], v[:, k, tok], ident[:, :])
                last.then_inc(turned, 1)
                pe.wait_ge(copied, i + 1)
                if i >= 2:
                    pe.wait_ge(added, i - 1)
                for h in range(SGU_HEADS):
                    a, k = 64 * (h % 2), h // 2
                    last = nc.tensor.matmul(ps_m[a:a + 64, b, k * P:(k + 1) * P], vt[:, b, 64 * h:64 * h + 64],
                                            ws[:, h, :], start=True, stop=True)
                last.then_inc(mixed, 1)

        @block.scalar
        def _(act):
            for i in range(chunks):
                act.wait_ge(turned, i + 1)
                nc.scalar.activation(vt[:, i % 2, :], ps_t[:, i % 2, 0:2 * P], ACT.Copy).then_inc(copied, 1)

        @block.vector
        def _(dve):
            for i in range(chunks):
                tok = slice(i * P, (i + 1) * P)
                dve.wait_ge(mixed, i + 1)
                nc.vector.tensor_tensor(m[:, :, :], ps_m[:, i % 2, 0:2 * P].rearrange("p (k s) -> p k s", k=2),
                                        bs[:, :, :], ALU.add)
                dve.drain().then_inc(added, 1)
                nc.vector.tensor_tensor(y[:, :, tok], u[:, :, tok], m[:, :, :], ALU.mult)
                dve.drain()


def gate_stage(core, name, z, y, tiles, func, out=None):
    nc = core.nc
    BUFS = 4
    here = [core.sem(f"{name}_here{b}") for b in range(BUFS)]
    opened, used, high = (core.sem(f"{name}_{s}") for s in ("opened", "used", "high"))
    total = y.shape[2]
    with ExitStack() as mem:
        g = mem.enter_context(nc.sbuf_tensor(f"{name}_g", [P, BUFS, total], F32))
        block = mem.enter_context(core.block())

        @block.sync
        def _(sp):
            for i in range(tiles):
                if i >= BUFS:
                    sp.wait_ge(used, i - BUFS + 1)
                sp.dma_start(g[:, i % BUFS, :], z(i)).then_inc(here[i % BUFS], 16)

        @block.scalar
        def _(act):
            for i in range(tiles + 1):
                if i < tiles:
                    act.wait_ge(here[i % BUFS], 16 * (i // BUFS + 1))
                    nc.scalar.activation(g[:, i % BUFS, :], g[:, i % BUFS, :], func).then_inc(opened, 1)
                if out is not None and i:
                    act.wait_ge(used, i)
                    nc.scalar.activation(out[0][:, i - 1, :], y[:, i - 1, :], ACT.Copy).then_inc(high, 1)

        @block.vector
        def _(dve):
            for i in range(tiles + 1):
                if i < tiles:
                    dve.wait_ge(opened, i + 1)
                    nc.vector.tensor_tensor(y[:, i, :], y[:, i, :], g[:, i % BUFS, :], ALU.mult).then_inc(used, 1)
                if out is not None and i:
                    dve.wait_ge(high, i)
                    nc.vector.tensor_tensor(out[1][:, i - 1, :], y[:, i - 1, :], out[0][:, i - 1, :].bitcast(F32), ALU.subtract)


LEAD = 240
WIDE = LEAD + COLS
AHEADS, HEAD, KV = 8, 64, 2
BLOCKS = 9


def zero_stage(core, x_t, meta, z2, width):
    nc = core.nc
    here, zeroed = core.sem("zero_here"), core.sem("zeroed")
    with nc.sbuf_tensor("zero_row", [P, 1, LEAD], F32) as zero, core.block() as block:
        @block.sync
        def _(sp):
            with nc.allow_non_contiguous_dma(reason="16 columns of each row"):
                sp.dma_start(x_t[:, :, 0:META], meta).then_inc(here, 16)
            sp.wait_ge(zeroed, 1)
            sp.dma_start(z2[0:width, :, 0:LEAD].rearrange("t c s -> c t s"), zero[:, :, :].broadcast_to([P, width, LEAD])
                         ).then_inc(here, 16)
            sp.wait_ge(here, 32)

        @block.vector
        def _(dve):
            nc.vector.memset(x_t[:, :, LTOK:COLS], 0.0)
            nc.vector.memset(zero[:, :, :], 0.0).then_inc(zeroed, 1)


def rope_stage(core, name, z, qk, tables, perm, count, lead, total):
    nc = core.nc
    n, w = pieces(total)
    here = [core.sem(f"{name}_here{b}") for b in range(2)]
    tab, rotated, ended, stored = (core.sem(f"{name}_{s}") for s in ("tables", "rotated", "ended", "stored"))
    with ExitStack() as mem:
        cs = mem.enter_context(nc.sbuf_tensor(f"{name}_cs", [P, 2, total], F32))
        x = mem.enter_context(nc.sbuf_tensor(f"{name}_x", [P, 2, total], F32))
        o = mem.enter_context(nc.sbuf_tensor(f"{name}_o", [P, count, lead + total], F32))
        r = mem.enter_context(nc.sbuf_tensor(f"{name}_r", [P, total], F32))
        ps = mem.enter_context(nc.psum_tensor(f"{name}_ps", [P, 2, n, 512], F32))
        block = mem.enter_context(core.block())

        @block.sync
        def _(sp):
            sp.dma_start(cs[:, :, :], tables).then_inc(tab, 16)
            for i in range(2):
                sp.dma_start(x[:, i, :], z[i]).then_inc(here[i], 16)
            for i in range(count):
                sp.wait_ge(ended, i + 1)
                if i + 2 < count:
                    sp.dma_start(x[:, i % 2, :], z[i + 2]).then_inc(here[i % 2], 16)
                sp.dma_start(qk[i], o[:, i, :]).then_inc(stored, 16)
            sp.wait_ge(stored, 16 * count)

        @block.tensor
        def _(pe):
            for i in range(count):
                pe.wait_ge(here[i % 2], 16 * (i // 2 + 1))
                if i >= 2:
                    pe.wait_ge(ended, i - 1)
                for c in range(n):
                    last = nc.tensor.matmul(ps[:, i % 2, c, 0:w], perm, x[:, i % 2, c * w:(c + 1) * w], start=True, stop=True)
                last.then_inc(rotated, 1)

        @block.vector
        def _(dve):
            if lead:
                nc.vector.memset(o[:, :, 0:lead], 0.0)
            dve.wait_ge(tab, 16)
            cut = lambda a: a.rearrange("p (c w) -> p c w", c=n)
            for i in range(count):
                dve.wait_ge(rotated, i + 1)
                nc.vector.tensor_tensor(cut(r[:, :]), ps[:, i % 2, :, 0:w], cut(cs[:, 1, :]), ALU.mult)
                nc.vector.tensor_tensor(o[:, i, lead:], x[:, i % 2, :], cs[:, 0, :], ALU.mult)
                dve.drain()
                nc.vector.tensor_tensor(o[:, i, lead:], o[:, i, lead:], r[:, :], ALU.add)
                dve.drain().then_inc(ended, 1)


def swa_stage(core, qk, v_tok, masks, sinks, yatt, ident):
    nc = core.nc
    G = AHEADS // KV
    s_done, m_done, p_done, n_done, t_done, c_done, o_done, y_done, used, zero, sinks_here = (
        core.sem(f"swa_{s}") for s in ("scores", "maxed", "probs", "normed", "turned", "copied", "outs", "ys", "used", "zero", "sinks"))
    row_here, v_here, y_stored, y_free = ([core.sem(f"swa_{s}{b}") for b in range(2)] for s in ("row", "v", "stored", "free"))
    scored = core.sem("swa_scored")
    with ExitStack() as mem:
        sb = lambda n, s: mem.enter_context(nc.sbuf_tensor(f"swa_{n}", s, F32))
        q = sb("q", [P, 2, 4, P])
        kk = sb("kk", [P, 2, KV, 2, 2 * P])
        vb = sb("v", [P, 2, 2, P])
        mk = sb("mask", [P, 2, 2 * P])
        sk = sb("sinks", [P, AHEADS])
        sc = sb("sc", [P, 2, KV, G, 2 * P])
        st = sb("st", [P, 2, KV, 6, G])
        pt = sb("pt", [P, 2, 2, G, P])
        y = sb("y", [64, 2, KV, G, P])
        ps_s = mem.enter_context(nc.psum_tensor("swa_ps_s", [P, 2, G, 2 * P], F32))
        ps_t = mem.enter_context(nc.psum_tensor("swa_ps_t", [P, 2, G, P], F32))
        ps_o = mem.enter_context(nc.psum_tensor("swa_ps_o", [64, G, P], F32))
        block = mem.enter_context(core.block())

        def blocks(eng, body):
            with eng.Fori(0, BLOCKS // 2) as ii:
                for b in range(2):
                    body(2 * ii + b, ii, b)
            body(BLOCKS - 1, BLOCKS // 2, 0)

        @block.sync
        def _(sp):
            sp.dma_start(sk[:, :], sinks.partition_broadcast(P)).then_inc(sinks_here, 16)
            sp.wait_ge(zero, 1)

            def body(i, ii, b):
                sp.wait_ge(scored, i + 1)
                at = i * P
                sp.dma_start(q[:, b, :, :], qk[0:4, :, bass.ds(at + P, P)].rearrange("t c s -> c t s")).then_inc(row_here[b], 16)
                for a in range(2):
                    sp.dma_start(kk[64 * a:64 * a + 64, b, :, a, :],
                                 qk[4].rearrange("(g c) s -> c g s", g=KV)[:, :, bass.ds(at, 2 * P)]).then_inc(row_here[b], 16)
                sp.dma_start(mk[:, b, :], masks[bass.ds(i, 1)].rearrange("o q k -> (o q) k")).then_inc(row_here[b], 16)
                sp.wait_ge(used, i + 1)
                sp.dma_start(vb[:, b, :, :], v_tok[bass.ds(at, 2 * P), 0:P].rearrange("(t s) c -> s t c", t=2)).then_inc(v_here[b], 16)

            blocks(sp, body)

        @block.gpsimd
        def _(pool):
            nc.gpsimd.memset(kk[:, :, :, :, :], 0.0).then_inc(zero, 1)
            yv = yatt.rearrange("(g h d) s -> d g h s", g=KV, h=G)

            def body(i, ii, b):
                pool.wait_ge(y_done, 2 * (i + 1) + 1)
                for g in range(KV):
                    pool.dma_start(yv[:, g, :, bass.ds(i * P, P)], y[:, b, g, :, :]).then_inc(y_stored[b], 16)
                pool.wait_ge(y_stored[b], 32 * (ii + 1))
                pool.sem_inc(y_free[b], 1)

            blocks(pool, body)

        @block.tensor
        def _(pe):
            def scores(i, ii, b):
                pe.wait_ge(row_here[b], 64 * (ii + 1))
                for g in range(KV):
                    u = 2 * i + g
                    pe.wait_ge(m_done, u + 1)
                    for t in range(2):
                        last = nc.tensor.matmul(ps_s[:, g, 2 * t:2 * t + 2, :], q[:, b, 2 * g + t, :], kk[:, b, g, :, :],
                                                start=True, stop=True)
                    last.then_inc(s_done, 1)

            def outs(i, ii, b):
                pe.wait_ge(v_here[b], 16 * (ii + 1))
                for g in range(KV):
                    u = 2 * i + g
                    pe.wait_ge(n_done, u + 1)
                    pe.wait_ge(c_done, u + 1)
                    for k in range(2):
                        for h in range(G):
                            last = nc.tensor.transpose(ps_t[:, k, h, :], sc[:, b, g, h, k * P:(k + 1) * P], ident[:, :])
                    last.then_inc(t_done, 1)
                    pe.wait_ge(c_done, u + 2)
                    pe.wait_ge(y_done, u + 1)
                    for k in range(2):
                        last = nc.tensor.matmul(ps_o[:, :, :], vb[:, b, k, 64 * g:64 * g + 64], pt[:, g, k, :, :],
                                                start=(k == 0), stop=(k == 1))
                    last.then_inc(o_done, 1)

            scores(0, 0, 0)

            def body(i, ii, b):
                if not isinstance(i, int):
                    scores(i + 1, ii + b, 1 - b)
                outs(i, ii, b)

            blocks(pe, body)

        @block.scalar
        def _(act):
            act.sem_inc(c_done, 1)

            def probs(i, ii, b, g):
                u = 2 * i + g
                act.wait_ge(m_done, u + 3)
                for h in range(G):
                    nc.scalar.activation(sc[:, b, g, h, :], sc[:, b, g, h, :], ACT.Exp, bias=st[:, b, g, 1, h:h + 1],
                                         accum_out=st[:, b, g, 2, h:h + 1])
                nc.scalar.activation(st[:, b, g, 4, :], st[:, b, g, 3, :], ACT.Exp)
                act.drain().then_inc(p_done, 1)

            def copy(i, ii, b, g):
                u = 2 * i + g
                act.wait_ge(t_done, u + 1)
                nc.scalar.activation(pt[:, g, :, :, :], ps_t[:, :, :, :], ACT.Copy).then_inc(c_done, 1)

            for g in range(KV):
                probs(0, 0, 0, g)

            def body(i, ii, b):
                for g in range(KV):
                    copy(i, ii, b, g)
                    if not isinstance(i, int):
                        probs(i + 1, ii + b, 1 - b, g)

            blocks(act, body)

        @block.vector
        def _(dve):
            dve.sem_inc(m_done, 2)
            dve.sem_inc(y_done, 1)
            dve.sem_inc(used, 2)
            dve.sem_inc(scored, 2)
            dve.wait_ge(sinks_here, 16)

            def maxima(i, ii, b):
                for g in range(KV):
                    u = 2 * i + g
                    dve.wait_ge(s_done, u + 1)
                    if g == 0:
                        dve.wait_ge(row_here[b], 64 * (ii + 1))
                    nc.vector.scalar_tensor_tensor(out=sc[:, b, g, :, :], in0=ps_s[:, g, :, :], scalar=HEAD ** -0.5,
                                                   in1=mk[:, b:b + 1, :].broadcast_to([P, G, 2 * P]), op0=ALU.mult, op1=ALU.add)
                    dve.drain()
                    nc.vector.tensor_reduce(st[:, b, g, 0, :], sc[:, b, g, :, :], AX.X, ALU.max)
                    dve.drain()
                    nc.vector.tensor_tensor(st[:, b, g, 0, :], st[:, b, g, 0, :], sk[:, G * g:G * g + G], ALU.max)
                    dve.drain()
                    nc.vector.tensor_scalar(st[:, b, g, 1, :], st[:, b, g, 0, :], -1.0, None, ALU.mult)
                    nc.vector.tensor_tensor(st[:, b, g, 3, :], sk[:, G * g:G * g + G], st[:, b, g, 0, :], ALU.subtract)
                    dve.drain().then_inc(m_done, 1)
                dve.sem_inc(scored, 1)

            def norm(i, ii, b, g):
                u = 2 * i + g
                dve.wait_ge(p_done, u + 1)
                nc.vector.tensor_tensor(st[:, b, g, 5, :], st[:, b, g, 2, :], st[:, b, g, 4, :], ALU.add)
                dve.drain()
                nc.vector.reciprocal(st[:, b, g, 5, :], st[:, b, g, 5, :])
                dve.drain()
                for h in range(G):
                    nc.vector.tensor_scalar(sc[:, b, g, h, :], sc[:, b, g, h, :], st[:, b, g, 5, h:h + 1], None, ALU.mult)
                dve.drain().then_inc(n_done, 1)

            def result(i, ii, b, g):
                if g == 0:
                    dve.wait_ge(y_free[b], ii + 1)
                u = 2 * i + g
                dve.wait_ge(o_done, u + 1)
                nc.vector.tensor_copy(y[:, b, g, :, :], ps_o[:, :, :]).then_inc(y_done, 1)
                if g == KV - 1:
                    dve.sem_inc(used, 1)

            for b in range(2):
                dve.sem_inc(y_free[b], 1)
            maxima(0, 0, 0)
            for g in range(KV):
                norm(0, 0, 0, g)

            def body(i, ii, b):
                if not isinstance(i, int):
                    maxima(i + 1, ii + b, 1 - b)
                for g in range(KV):
                    result(i, ii, b, g)
                    if not isinstance(i, int):
                        norm(i + 1, ii + b, 1 - b, g)

            blocks(dve, body)


LEVELS = (64, 32, 16, 8, 4, 2, 1)
NL = len(LEVELS)
GLA_H, GLA_DV = 4, 128


def decay_stage(core, h, inverse, w_low, w_alpha, b_low, b_alpha, la):
    nc = core.nc
    n, w = pieces(COLS)
    w_high, w_split, low_done, low_here, z_done, z_here, soft = (
        core.sem(f"decay_{s}") for s in ("w_high", "w_split", "low_mm", "low", "z_mm", "z", "soft"))
    with ExitStack() as mem:
        low = mem.enter_context(nc.sbuf_tensor("decay_low", [16, COLS], F32))
        wh, wl = (mem.enter_context(nc.sbuf_tensor(f"decay_w_{s}", [P, KT, 16], F32R)) for s in ("high", "low"))
        z = mem.enter_context(nc.sbuf_tensor("decay_z", [P, 2, COLS], F32))
        e = mem.enter_context(nc.sbuf_tensor("decay_e", [P, 2, COLS], F32))
        ps = mem.enter_context(nc.psum_tensor("decay_ps", [P, 2, n, 512], F32))
        cut = lambda a: a.rearrange("p (c w) -> p c w", c=n)
        block = mem.enter_context(core.block())

        @block.tensor
        def _(pe):
            pe.wait_ge(w_split, 1)
            for c in range(n):
                for k in range(KT):
                    for i, (a, x) in enumerate(((wh, h[0]), (wh, h[1]), (wl, h[0]))):
                        last = nc.tensor.matmul(ps[0:16, 0, c, 0:w], a[:, k, :], x[:, k, c * w:(c + 1) * w],
                                                start=(k == 0 and i == 0), stop=(k == KT - 1 and i == 2))
            last.then_inc(low_done, 1)
            pe.wait_ge(low_here, 1)
            for m in range(2):
                for c in range(n):
                    last = nc.tensor.matmul(ps[:, m, c, 0:w], w_alpha[:, m * P:(m + 1) * P], low[:, c * w:(c + 1) * w],
                                            start=True, stop=True)
                last.then_inc(z_done, 1)

        @block.vector
        def _(dve):
            nc.vector.memset(la[:, :, 0:LEAD - P], 0.0)
            dve.wait_ge(w_high, 1)
            nc.vector.tensor_tensor(wl[:, :, :], w_low[:, :, :], wh[:, :, :].bitcast(F32), ALU.subtract).then_inc(w_split, 1)
            dve.wait_ge(low_done, 1)
            nc.vector.tensor_tensor(cut(low[:, :]), ps[0:16, 0, :, 0:w], cut(inverse[0:16, :]), ALU.mult)
            dve.drain()
            nc.vector.tensor_scalar(low[:, :], low[:, :], b_low, None, ALU.add).then_inc(low_here, 1)
            for m in range(2):
                dve.wait_ge(z_done, m + 1)
                nc.vector.tensor_scalar(cut(z[:, m, :]), ps[:, m, :, 0:w], b_alpha[:, m:m + 1], None, ALU.add)
            dve.drain().then_inc(z_here, 1)
            dve.wait_ge(soft, 1)
            nc.vector.tensor_scalar(z[:, :, :], z[:, :, :], 0.0, None, ALU.min)
            dve.drain()
            nc.vector.tensor_tensor(z[:, :, :], z[:, :, :], e[:, :, :], ALU.subtract)
            dve.drain()
            nc.vector.tensor_scalar(la[:, :, LEAD - P:], z[:, :, 0:LTOK], 1.0 / 16, None, ALU.mult)

        @block.scalar
        def _(act):
            nc.scalar.activation(wh[:, :, :], w_low[:, :, :], ACT.Copy).then_inc(w_high, 1)
            act.wait_ge(z_here, 1)
            nc.scalar.activation(e[:, :, :], z[:, :, :], ACT.Abs)
            act.drain()
            nc.scalar.activation(e[:, :, :], e[:, :, :], ACT.Exp, scale=-1.0)
            act.drain()
            nc.scalar.activation(e[:, :, :], e[:, :, :], ACT.Ln, bias=1.0).then_inc(soft, 1)


def gla_stage(core, z2, v_tok, la, y, pad, level_masks, ident):
    nc = core.nc
    d_done, e_done, k_done, a_done, m_done, t_done, c_done, o_done, y_done, u_done, s_done, q_here, seen, plain_done = (
        core.sem(f"gla_{s}") for s in ("diffs", "exps", "scaled", "scores", "masked", "turned", "copied", "outs", "ys",
                                       "update", "state", "here", "seen", "plain"))
    v_here = [core.sem(f"gla_v{b}") for b in range(2)]
    with ExitStack() as mem:
        sb = lambda n, s: mem.enter_context(nc.sbuf_tensor(f"gla_{n}", s, F32))
        q, k = sb("q", [P, 2, BLOCKS * P]), sb("k", [P, 2, BLOCKS * P])
        one = sb("one", [P, P])
        e = sb("e", [P, 2, NL + 2, 2, P])
        qz = sb("qz", [P, 2, NL + 2, 2, 2, P])
        ke = sb("ke", [P, 2, NL + 1, 2, P])
        kd = sb("kd", [P, 2, 2, P])
        kt = sb("kt", [P, 2, P])
        bs = sb("bs", [P, 2, P])
        v = sb("v", [P, 2, GLA_H * GLA_DV])
        a_t = sb("a_t", [P, GLA_H, P])
        mk = sb("mk", [P, NL + 1, P])
        s = sb("s", [P, GLA_H, GLA_DV])
        ps_a = mem.enter_context(nc.psum_tensor("gla_ps_a", [P, 2, GLA_H, P], F32))
        ps_t = mem.enter_context(nc.psum_tensor("gla_ps_t", [P, 512], F32))
        ps_o = mem.enter_context(nc.psum_tensor("gla_ps_o", [P, GLA_H, P], F32))
        ps_u = mem.enter_context(nc.psum_tensor("gla_ps_u", [P, 2, 2 * P], F32))
        block = mem.enter_context(core.block())

        def chunks(eng, body):
            body(0, 0, 1, True, False)
            with eng.Fori(0, BLOCKS // 2 - 1) as ii:
                body(2 * ii + 1, 1, ii + 1, False, False)
                body(2 * ii + 2, 0, ii + 2, False, False)
            body(BLOCKS - 2, 1, BLOCKS // 2, False, False)
            body(BLOCKS - 1, 0, BLOCKS // 2 + 1, False, True)

        @block.sync
        def _(sp):
            cols = slice(P, P + BLOCKS * P)
            sp.dma_start(q[:, :, :], z2[5:7, :, cols].rearrange("t c s -> c t s")).then_inc(q_here, 16)
            sp.dma_start(k[:, :, :], z2[7:9, :, cols].rearrange("t c s -> c t s")).then_inc(q_here, 16)
            sp.dma_start(mk[:, :, :], level_masks).then_inc(q_here, 16)

            def load(c, b):
                sp.dma_start(v[:, b, :], v_tok[bass.ds(c * P + P, P), P:]).then_inc(v_here[b], 16)

            load(0, 0)
            load(1, 1)
            with sp.Fori(0, (BLOCKS - 3) // 2) as ii:
                for b in range(2):
                    sp.wait_ge(s_done, 2 * ii + b + 1)
                    load(2 * ii + b + 2, b)
            sp.wait_ge(s_done, BLOCKS - 2)
            load(BLOCKS - 1, 0)

        @block.tensor
        def _(pe):
            def body(c, b, turn, first, last_chunk):
                pe.wait_ge(k_done, c + 1)
                pe.wait_ge(plain_done, c + 1)
                for t in range(2):
                    last = nc.tensor.transpose(ps_t[:, t * P:(t + 1) * P], kd[:, b, t, :], ident[:, :])
                last.then_inc(t_done, 1)
                for l in range(NL + 1):
                    if l >= 2:
                        pe.wait_ge(m_done, c * (NL + 1) + l - 1)
                    for t in range(2):
                        last = nc.tensor.matmul(ps_a[:, l % 2, 2 * t:2 * t + 2, :], ke[:, b, l, t, :],
                                                qz[:, b, l if l < NL else NL + 1, t, :, :], start=True, stop=True)
                    last.then_inc(a_done, 1)
                pe.wait_ge(v_here[b], 16 * turn)
                pe.wait_ge(m_done, (c + 1) * (NL + 1))
                if not first:
                    pe.wait_ge(s_done, c)
                    pe.wait_ge(y_done, c)
                for h in range(GLA_H):
                    nc.tensor.matmul(ps_o[:, h, :], v[:, b, h * GLA_DV:(h + 1) * GLA_DV], a_t[:, h, :], start=True, stop=False)
                    last = nc.tensor.matmul(ps_o[:, h, :], s[:, h, :], qz[:, b, NL, h // 2, h % 2, :], start=False, stop=True)
                last.then_inc(o_done, 1)
                pe.wait_ge(c_done, c + 1)
                for t in range(2):
                    last = nc.tensor.matmul(ps_u[:, t, :], kt[:, t, :], v[:, b, 2 * t * P:2 * (t + 1) * P], start=True, stop=True)
                last.then_inc(u_done, 1)

            chunks(pe, body)

        @block.scalar
        def _(act):
            def exps(c, b):
                act.wait_ge(d_done, c + 1)
                nc.scalar.activation(e[:, b, 0:NL, :, :], e[:, b, 0:NL, :, :], ACT.Exp)
                nc.scalar.activation(e[:, b, NL, :, :], bs[:, :, :], ACT.Exp)
                for t in range(2):
                    nc.scalar.activation(e[:, b, NL + 1, t, :], bs[:, t, :], ACT.Exp, scale=-1.0, bias=bs[:, t, P - 1:P])
                act.drain().then_inc(e_done, 1)
                cols = bass.ds(c * P, P)
                nc.scalar.activation(ke[:, b, NL, :, :], k[:, :, cols], ACT.Copy)
                for a in range(2):
                    r = slice(64 * a, 64 * a + 64)
                    nc.scalar.activation(qz[r, b, NL + 1, :, a, :], q[r, :, cols], ACT.Copy)
                act.drain().then_inc(plain_done, 1)

            act.wait_ge(q_here, 48)
            exps(0, 0)

            def body(c, b, turn, first, last_chunk):
                if not last_chunk:
                    exps(c + 1, 1 - b)
                act.wait_ge(t_done, c + 1)
                nc.scalar.activation(kt[:, :, :], ps_t[:, 0:2 * P].rearrange("p (t s) -> p t s", t=2), ACT.Copy).then_inc(c_done, 1)
                act.wait_ge(o_done, c + 1)
                if first:
                    nc.scalar.activation(y[:, :, 0:META], ps_o[:, :, P - META:P], ACT.Copy, scale=0.125).then_inc(y_done, 1)
                else:
                    nc.scalar.activation(y[:, :, bass.ds(c * P + (META - P), P)], ps_o[:, :, :], ACT.Copy,
                                         scale=0.125).then_inc(y_done, 1)

            chunks(act, body)

        @block.vector
        def _(dve):
            nc.vector.memset(pad, 0.0)
            for tile, value in ((one[:, :], 1.0), (qz[:, :, :, :, :, :], 0.0), (a_t[:, :, :], 0.0), (s[:, :, :], 0.0)):
                nc.vector.memset(tile, value)
            dve.drain()
            dve.wait_ge(q_here, 48)
            halves = [slice(0, 64), slice(64, 128)]
            TT = nc.vector.tensor_tensor

            def exponents(c, b):
                cols = bass.ds(c * P, P)
                for t in range(2):
                    nc.vector.tensor_tensor_scan(bs[:, t, :], one[:, :], la[:, t, cols], 0.0, ALU.mult, ALU.add)
                dve.drain()
                for l, half in enumerate(LEVELS):
                    cut = lambda a: a.rearrange("p t (n r) -> p t n r", r=2 * half)
                    mid = cut(bs[:, :, :])[:, :, :, half - 1:half].broadcast_to([P, 2, P // (2 * half), half])
                    src, dst = cut(bs[:, :, :]), cut(e[:, b, l, :, :])
                    TT(dst[:, :, :, 0:half], mid, src[:, :, :, 0:half], ALU.subtract)
                    TT(dst[:, :, :, half:], src[:, :, :, half:], mid, ALU.subtract)
                dve.drain().then_inc(d_done, 1)

            def scale(c, b):
                cols = bass.ds(c * P, P)
                dve.wait_ge(e_done, c + 1)
                TT(kd[:, b, :, :], k[:, :, cols], e[:, b, NL + 1, :, :], ALU.mult)
                TT(ke[:, b, 0:NL, :, :], k[:, :, cols].unsqueeze(1).broadcast_to([P, NL, 2, P]), e[:, b, 0:NL, :, :], ALU.mult)
                for a, r in enumerate(halves):
                    TT(qz[r, b, 0:NL + 1, :, a, :], q[r, :, cols].unsqueeze(1).broadcast_to([64, NL + 1, 2, P]),
                       e[r, b, 0:NL + 1, :, :], ALU.mult)
                dve.drain().then_inc(k_done, 1)

            exponents(0, 0)
            scale(0, 0)

            def body(c, b, turn, first, last_chunk):
                if not last_chunk:
                    exponents(c + 1, 1 - b)
                for l in range(NL + 1):
                    dve.wait_ge(a_done, c * (NL + 1) + l + 1)
                    dve.sem_inc(seen, 1)
                    nc.vector.copy_predicated(a_t[:, :, :], mk[:, l:l + 1, :].bitcast(mybir.dt.int32).broadcast_to([P, GLA_H, P]),
                                              ps_a[:, l % 2, :, :])
                    dve.drain().then_inc(m_done, 1)
                if not last_chunk:
                    scale(c + 1, 1 - b)
                dve.wait_ge(u_done, c + 1)
                for h in range(GLA_H):
                    t, a = h // 2, h % 2
                    r = halves[a]
                    nc.vector.scalar_tensor_tensor(out=s[r, h, :], in0=s[r, h, :], scalar=e[r, b, NL, t, P - 1:P],
                                                   in1=ps_u[r, t, a * P:(a + 1) * P], op0=ALU.mult, op1=ALU.add)
                dve.drain().then_inc(s_done, 1)

            chunks(dve, body)


FF = 2816
FT = FF // P
FF_PARTS = ((0, 8), (8, 7), (15, 7))


def block_two(core, A, x_t, mats, vec, dram, stop):
    nc = core.nc
    ident = mats["ident"]
    z2, v_tok, qk, yatt = dram("z2", (34, P, WIDE)), dram("v_tok2", (LEAD + LTOK, 640)), dram("qk", (5, P, WIDE)), dram("yatt", (512, BLOCKS * P))
    zero_stage(core, x_t, A["meta"], z2, 14)
    zrow = lambda u: (lambda j: z2[bass.ds(2 * j + u, 1), :, LEAD:].rearrange("o p s -> p (o s)"))
    with nc.sbuf_tensor("y2", [P, KT, COLS], F32) as y_all:
        y = y_all[:, :, :]
        with nc.sbuf_tensor("b2_la", [P, 2, BLOCKS * P], F32) as la:
            with ExitStack() as inner:
                h = split_buffers(core, inner, "h2")
                rms = inner.enter_context(nc.sbuf_tensor("rms2_all", [P, COLS], F32))
                rms_split_stage(core, "rms2", x_t, h, rms, vec["mix_norm"], 1e-6, 0, COLS)
                gemm_stage(core, "in2", [(A["w_in2"], of(h), lambda j: 2 * j), (A["w_in2"], of(h), lambda j: 2 * j + 1)],
                           17, COLS, None, normed_out(nc, rms, vec["b_in"]), rms=rms, out=[zrow(0), zrow(1)])
                if stop == "z2": return z2[:, :, LEAD:]
                wl = inner.enter_context(nc.sbuf_tensor("b2_wl", [P, KT, 16], F32))
                wa = inner.enter_context(nc.sbuf_tensor("b2_wa", [16, 2 * P], F32))
                bl = inner.enter_context(nc.sbuf_tensor("b2_bl", [16, 1], F32))
                with nc.allow_non_contiguous_dma(reason="16 biases"):
                    load_stage(core, "w2", [(wl[:, :, :], A["w_low"]), (wa[:, :], A["w_alpha"]), (bl[:, :], A["b_low"])])
                decay_stage(core, h, rms, wl, wa, bl[:, 0:1], vec["b_alpha"], la)
            turn_stage(core, "turn2", lambda j: z2[9:14, :, bass.ds(P * j, P)].rearrange("t c s -> c t s"),
                       lambda j: v_tok[bass.ds(P * j, P), :], 5, (LEAD + LTOK) // P, ident)
            gla_stage(core, z2, v_tok, la, y[:, 4:8, :], y[:, :, LTOK:COLS], A["level_masks"], ident)
        packed_norm_stage(core, "gla_norm", y[:, 4:8, :], A["packs128"], None, 1e-6, vec["gla_norm"])
        if stop == "gla": return y[:, 4:8, 0:LTOK]
        gate_stage(core, "gate2", lambda i: z2[14 + i, :, LEAD:], y[:, 4:8, :], 4, ACT.Silu)
        rope_stage(core, "rope2", z2[:, :, LEAD:], qk, A["rope_tables"], mats["rope"], 5, LEAD, COLS)
        swa_stage(core, qk, v_tok, A["swa_masks"], A["sinks"], yatt, ident)
        load_stage(core, "yatt", [(y[:, 0:4, 0:LTOK], yatt[:, P - META:].rearrange("(t c) s -> c t s", c=P))])
        if stop == "yatt": return y[:, 0:4, 0:LTOK]
        mixing(core, A, y, z2, x_t)
    if stop == "h2": return x_t[:, :, 0:LTOK]
    with ExitStack() as mem:
        h = split_buffers(core, mem, "h2f")
        rms = mem.enter_context(nc.sbuf_tensor("rms2b_all", [P, COLS], F32))
        rms_split_stage(core, "rms2b", x_t, h, rms, vec["ffn_norm"], 1e-6, 0, COLS)
        for part, (first, tiles) in enumerate(FF_PARTS):
            with ExitStack() as inner:
                g = split_buffers(core, inner, f"ff2_{part}", tiles)
                conv_ff_stage(core, f"up2_{part}", A["w_up2"], h, g, vec["ff_conv"], vec["ff_conv_b"], first, tiles, rms)
                w = A[f"w_down2_{part}"]
                gemm_stage(core, f"down2_{part}", [(w, of(g), lambda j: 2 * j), (w, of(g), lambda j: 2 * j + 1)],
                           4, COLS, None, add_part(nc, x_t, 0, COLS))
    rms_stage(core, "rms2f", x_t, vec["final_norm2"], 1e-6, META, SEQ)


def mixing(core, A, y, z2, x_t):
    nc = core.nc
    with ExitStack() as mem:
        ys = split_buffers(core, mem, "y2s")
        split_stage(core, "split2", y, ys)

        def open_gates(act, u, j, ps, t):
            nc.scalar.activation(t[f"gate{u}"][:, :], t[f"gate{u}"][:, :], ACT.Sigmoid)

        def join(dve, u, j, ps, t):
            g = t["view"](t[f"gate{u}"][:, :])
            row = t["view"](y[:, bass.ds(j, 1), :].rearrange("p o s -> p (o s)"))
            if u == 0:
                nc.vector.tensor_tensor(row, ps, g, ALU.mult)
            else:
                nc.vector.tensor_tensor(g, ps, g, ALU.mult)
                dve.drain()
                nc.vector.tensor_tensor(row, row, g, ALU.add)

        grow = lambda first: (lambda j: z2[bass.ds(j + first, 1), :, LEAD:].rearrange("o p s -> p (o s)"))
        gemm_stage(core, "proj", [(A["w_att"], of(ys), lambda j: j), (A["w_gla"], of(ys, 4), lambda j: j)],
                   8, COLS, open_gates, join, extras=[(0, grow(18), "gate0"), (1, grow(26), "gate1")])
    with ExitStack() as mem:
        ms = split_buffers(core, mem, "mix_s")
        split_stage(core, "split_mix", y, ms)
        gemm_stage(core, "out2", [(A["w_out2"], of(ms), lambda j: 2 * j), (A["w_out2"], of(ms), lambda j: 2 * j + 1)],
                   4, COLS, None, add_part(nc, x_t, 0, COLS))


def split_row(dve, nc, row, pair, j):
    at = lambda x: x[:, bass.ds(j, 1), :].rearrange("p o s -> p (o s)")
    nc.vector.tensor_copy(at(pair[0]), row)
    dve.drain()
    nc.vector.tensor_tensor(at(pair[1]), row, at(pair[0]).bitcast(F32), ALU.subtract)


def conv_ff_stage(core, name, w_up, h, g, cw, cb, first, tiles, rms):
    nc = core.nc

    def act_ff(act, u, j, ps, t):
        nc.scalar.activation(t["conv"][:, :], t["conv"][:, :], ACT.Gelu_apprx_tanh)

    def dve_ff(dve, u, j, ps, t):
        inverse = t["view"](rms[:, :])
        conv = t["view"](t["conv"][:, :])
        if u == 0:
            nc.vector.memset(t["a"][:, 0:2], 0.0)
            nc.vector.tensor_tensor(t["view"](t["a"][:, 2:2 + COLS]), ps, inverse, ALU.mult)
            dve.drain()
            nc.vector.tensor_scalar(t["conv"][:, :], t["a"][:, 2:2 + COLS], cw[:, bass.ds(j + (2 * FT + first), 1)],
                                    cb[:, bass.ds(j + first, 1)], ALU.mult, ALU.add)
            for i in (1, 0):
                dve.drain()
                nc.vector.scalar_tensor_tensor(out=t["conv"][:, :], in0=t["a"][:, i:i + COLS], scalar=cw[:, bass.ds(j + (i * FT + first), 1)],
                                               in1=t["conv"][:, :], op0=ALU.mult, op1=ALU.add)
        else:
            nc.vector.tensor_tensor(conv, ps, conv, ALU.mult)
            dve.drain()
            nc.vector.tensor_tensor(conv, conv, inverse, ALU.mult)
            dve.drain()
            split_row(dve, nc, t["conv"][:, :], g, j)

    gemm_stage(core, name, [(w_up, of(h), lambda j: j + first), (w_up, of(h), lambda j: j + (FT + first))],
               tiles, COLS, act_ff, dve_ff, temps=[("a", COLS + 2), ("conv", COLS)], chained=True, rms=rms if first == 0 else None)


RET_H, RET_D, RET_C = 4, 128, 128


def retention_stage(core, qk, v_tok, y, decay, from_start, to_end, chunk_decay, ident):
    nc = core.nc
    s_done, a_done, t_done, c_done, q_done, o_done, y_done, u_done, r_done, tabs = (
        core.sem(f"ret_{s}") for s in ("scores", "decayed", "turned", "copied", "scaled", "outs", "ys", "update", "state", "tables"))
    here = [core.sem(f"ret_here{b}") for b in range(2)]
    with ExitStack() as mem:
        sb = lambda n, s: mem.enter_context(nc.sbuf_tensor(f"ret_{n}", s, F32))
        x = sb("qk", [P, 2, 2 * RET_H, P])
        v = sb("v", [P, 2, RET_H * P])
        dk = sb("decay", [P, RET_H, P])
        fs = sb("from_start", [P, RET_H, P])
        te = sb("to_end", [P, RET_H])
        a_t = sb("a_t", [P, RET_H, P])
        qs = sb("qs", [P, RET_H, P])
        kt = sb("kt", [P, RET_H, P])
        r = sb("r", [P, RET_H, P])
        ps = [mem.enter_context(nc.psum_tensor(f"ret_ps{i}", [P, RET_H, P], F32)) for i in range(4)]
        ps_s, ps_t, ps_o, ps_u = ps
        block = mem.enter_context(core.block())
        chunks = SEQ // RET_C

        def loop(eng, body):
            with eng.Fori(0, chunks // 2) as ii:
                for b in range(2):
                    body(2 * ii + b, ii, b)

        @block.sync
        def _(sp):
            for dst, src in ((dk[:, :, :], decay), (fs[:, :, :], from_start), (te[:, :], to_end)):
                sp.dma_start(dst, src).then_inc(tabs, 16)

            def body(c, ii, b):
                sp.wait_ge(r_done, c + 1)
                sp.dma_start(x[:, b, :, :], qk[:, :, bass.ds(c * P, P)].rearrange("t c s -> c t s")).then_inc(here[b], 16)
                sp.dma_start(v[:, b, :], v_tok[bass.ds(c * P, P), :]).then_inc(here[b], 16)

            loop(sp, body)

        @block.tensor
        def _(pe):
            def body(c, ii, b):
                pe.wait_ge(here[b], 32 * (ii + 1))
                for h in range(RET_H):
                    last = nc.tensor.matmul(ps_s[:, h, :], x[:, b, RET_H + h, :], x[:, b, h, :], start=True, stop=True)
                last.then_inc(s_done, 1)
                for h in range(RET_H):
                    last = nc.tensor.transpose(ps_t[:, h, :], x[:, b, RET_H + h, :], ident[:, :])
                last.then_inc(t_done, 1)
                pe.wait_ge(a_done, c + 1)
                pe.wait_ge(q_done, c + 1)
                pe.wait_ge(r_done, c + 2)
                pe.wait_ge(y_done, c + 1)
                for h in range(RET_H):
                    nc.tensor.matmul(ps_o[:, h, :], v[:, b, h * P:(h + 1) * P], a_t[:, h, :], start=True, stop=False)
                    last = nc.tensor.matmul(ps_o[:, h, :], r[:, h, :], qs[:, h, :], start=False, stop=True)
                last.then_inc(o_done, 1)
                pe.wait_ge(c_done, c + 1)
                for h in range(RET_H):
                    last = nc.tensor.matmul(ps_u[:, h, :], kt[:, h, :], v[:, b, h * P:(h + 1) * P], start=True, stop=True)
                last.then_inc(u_done, 1)

            loop(pe, body)

        @block.scalar
        def _(act):
            act.sem_inc(y_done, 1)
            act.wait_ge(tabs, 48)

            def body(c, ii, b):
                act.wait_ge(t_done, c + 1)
                for h in range(RET_H):
                    nc.scalar.activation(kt[:, h, :], ps_t[:, h, :], ACT.Copy, scale=te[:, h:h + 1])
                act.drain().then_inc(c_done, 1)
                act.wait_ge(o_done, c + 1)
                nc.scalar.activation(y[:, :, bass.ds(c * P, P)], ps_o[:, :, :], ACT.Copy).then_inc(y_done, 1)

            loop(act, body)

        @block.vector
        def _(dve):
            nc.vector.memset(r[:, :, :], 0.0)
            dve.drain().then_inc(r_done, 2)
            dve.wait_ge(tabs, 48)

            def body(c, ii, b):
                dve.wait_ge(s_done, c + 1)
                nc.vector.tensor_tensor(a_t[:, :, :], ps_s[:, :, :], dk[:, :, :], ALU.mult).then_inc(a_done, 1)
                nc.vector.tensor_tensor(qs[:, :, :], x[:, b, 0:RET_H, :], fs[:, :, :], ALU.mult).then_inc(q_done, 1)
                dve.wait_ge(u_done, c + 1)
                for h in range(RET_H):
                    nc.vector.scalar_tensor_tensor(out=r[:, h, :], in0=r[:, h, :], scalar=chunk_decay[h], in1=ps_u[:, h, :],
                                                   op0=ALU.mult, op1=ALU.add)
                dve.drain().then_inc(r_done, 1)

            loop(dve, body)


RW_C = 64
RW_CH = SEQ // RW_C
PAIRS = 4
KINDS = 5
RW_LEVELS = (2, 4, 8, 16, 32)


def rwkv_prep_stage(core, z, mats, vec, w2a2, g2, rw, late):
    nc = core.nc
    rw_x, rw_e = rw
    here, lora, mm, u_here, lw_done, e_done, kk_done, sq_done, n_mm, n_here, root, bt, b_mm, out_done, x_free, g_copied, zeroed = (
        core.sem(f"prep_{s}") for s in ("here", "lora", "lora_mm", "sigmoids", "sums", "exps", "kk", "squares", "norm_mm", "norm",
                                        "root", "bonus", "bonus_mm", "out", "x_free", "g_copied", "zeroed"))
    out_stored = [core.sem(f"prep_stored{b}") for b in range(2)]
    g_stored, bv_stored, ew_stored = (core.sem(f"prep_{s}") for s in ("g_stored", "bv_stored", "ew_stored"))
    with ExitStack() as mem:
        sb = lambda n, s: mem.enter_context(nc.sbuf_tensor(f"prep_{n}", s, F32))
        raw = sb("raw", [P, 3, SEQ + 1])
        lo = sb("lora", [P, 2, SEQ + 1])
        ls = sb("lora_s", [P, 2, SEQ])
        w = sb("w", [P, 512])
        g = sb("g2", [P, 512])
        reset = sb("reset", [P, SEQ])
        t = {k: sb(k, [P, SEQ]) for k in ("r", "k", "v", "tmp", "lw", "a", "g", "w_in", "w_ex", "kk", "sq", "rn", "bv")}
        outs = sb("out", [P, 2, KINDS, SEQ])
        ew = sb("ew", [P, RW_CH, PAIRS])
        ps = mem.enter_context(nc.psum_tensor("prep_ps", [P, 4, 2, 512], F32))
        cut = lambda x: x.rearrange("p (c w) -> p c w", c=2)
        block = mem.enter_context(core.block())
        TT, TS, STT = nc.vector.tensor_tensor, nc.vector.tensor_scalar, nc.vector.scalar_tensor_tensor

        @block.sync
        def _(sp):
            sp.dma_start(w[:, :], w2a2).then_inc(here, 16)
            sp.dma_start(g[:, :], g2).then_inc(here, 16)
            sp.dma_start(lo[:, :, 1:], z[28:30].rearrange("t c s -> c t s")).then_inc(here, 16)

            def load(m):
                for i in range(3):
                    sp.dma_start(raw[:, i, 1:], z[16 + 4 * i + m]).then_inc(here, 16)

            load(0)
            for m in range(4):
                if m < 3:
                    sp.wait_ge(x_free, m + 1)
                    load(m + 1)
                sp.wait_ge(u_here, m + 1)
                sp.dma_start(late[m], t["g"][:, :]).then_inc(g_stored, 16)
                sp.wait_ge(out_done, m + 1)
                sp.dma_start(rw_x[:, :, m, :], outs[:, m % 2, :, :]).then_inc(out_stored[m % 2], 16)
                sp.dma_start(late[4 + m], t["bv"][:, :]).then_inc(bv_stored, 16)
            sp.dma_start(rw_e, ew[:, :, :]).then_inc(ew_stored, 16)
            for b in range(2):
                sp.wait_ge(out_stored[b], 32)
            sp.wait_ge(g_stored, 64)
            sp.wait_ge(bv_stored, 64)
            sp.wait_ge(ew_stored, 16)

        @block.tensor
        def _(pe):
            for m in range(4):
                cols = slice(m * P, (m + 1) * P)
                if m == 0:
                    pe.wait_ge(lora, 2)
                else:
                    pe.wait_ge(u_here, m)
                for c in range(2):
                    tok = slice(c * 512, (c + 1) * 512)
                    nc.tensor.matmul(ps[:, 0, c, :], w[0:64, cols], ls[0:64, 0, tok], start=True, stop=True)
                    nc.tensor.matmul(ps[:, 1, c, :], w[64:128, cols], ls[64:128, 0, tok], start=True, stop=True)
                    last = nc.tensor.matmul(ps[:, 2, c, :], g[:, cols], ls[:, 1, tok], start=True, stop=True)
                last.then_inc(mm, 1)
                pe.wait_ge(sq_done, m + 1)
                for c in range(2):
                    last = nc.tensor.matmul(ps[:, 3, c, :], mats["mean64"], t["sq"][:, c * 512:(c + 1) * 512], start=True, stop=True)
                last.then_inc(n_mm, 1)
                pe.wait_ge(bt, m + 1)
                for c in range(2):
                    last = nc.tensor.matmul(ps[:, 3, c, :], mats["mean64"], t["tmp"][:, c * 512:(c + 1) * 512], start=True, stop=True)
                last.then_inc(b_mm, 1)

        @block.scalar
        def _(act):
            act.wait_ge(lora, 1)
            nc.scalar.activation(ls[0:64, 0, :], ls[0:64, 0, :], ACT.Tanh)
            nc.scalar.activation(ls[:, 1, :], ls[:, 1, :], ACT.Sigmoid)
            act.drain().then_inc(lora, 1)
            for m in range(4):
                act.wait_ge(mm, m + 1)
                if m:
                    act.wait_ge(g_copied, m)
                    act.wait_ge(g_stored, 16 * m)
                nc.scalar.activation(cut(t["lw"][:, :]), ps[:, 0, :, :], ACT.Sigmoid, bias=vec["rw_w0"][:, m:m + 1])
                nc.scalar.activation(cut(t["a"][:, :]), ps[:, 1, :, :], ACT.Sigmoid, bias=vec["rw_a0"][:, m:m + 1])
                nc.scalar.activation(cut(t["g"][:, :]), ps[:, 2, :, :], ACT.Copy)
                act.drain().then_inc(u_here, 1)
                act.wait_ge(lw_done, m + 1)
                nc.scalar.activation(t["rn"][:, :], t["w_in"][:, :], ACT.Exp, scale=-1.0)
                nc.scalar.activation(t["w_ex"][:, :], t["w_ex"][:, :], ACT.Exp)
                act.drain()
                nc.scalar.activation(t["w_in"][:, :], t["w_in"][:, :], ACT.Exp)
                act.drain().then_inc(e_done, 1)
                act.wait_ge(kk_done, m + 1)
                nc.scalar.activation(t["sq"][:, :], t["kk"][:, :], ACT.Square).then_inc(sq_done, 1)
                act.wait_ge(n_here, m + 1)
                nc.scalar.activation(t["sq"][:, :], t["sq"][:, :], ACT.Sqrt).then_inc(root, 1)

        @block.vector
        def _(dve):
            nc.vector.memset(raw[:, :, 0:1], 0.0)
            nc.vector.memset(lo[:, :, 0:1], 0.0)
            nc.vector.memset(reset[:, :], 1.0)
            dve.drain()
            nc.vector.memset(reset[:, :].rearrange("p (n s) -> p n s", s=RW_C)[:, :, 0:1], 0.0)
            dve.wait_ge(here, 96)

            def shift(dst, src, mu, tmp):
                TT(tmp, src[:, 0:SEQ], src[:, 1:], ALU.subtract)
                dve.drain()
                STT(out=dst, in0=tmp, scalar=mu, in1=src[:, 1:], op0=ALU.mult, op1=ALU.add)
                dve.drain()

            for i in range(2):
                shift(ls[:, i, :], lo[:, i, :], vec["rw_mu"][:, 12 + i:13 + i], t["tmp"][:, :])
            dve.drain().then_inc(lora, 1)
            for m in range(4):
                col = slice(m, m + 1)
                out = outs[:, m % 2, :, :]
                dve.wait_ge(here, 48 * (m + 2))
                if m:
                    dve.sem_inc(g_copied, 1)
                for i, name in enumerate("rkv"):
                    shift(t[name][:, :], raw[:, i, :], vec["rw_mu"][:, 4 * i + m:4 * i + m + 1], t["tmp"][:, :])
                dve.sem_inc(x_free, 1)
                TS(t["kk"][:, :], t["k"][:, :], vec["rw_kk"][:, col], None, ALU.mult)
                dve.drain().then_inc(kk_done, 1)
                dve.wait_ge(u_here, m + 1)
                TS(t["lw"][:, :], t["lw"][:, :], -float(np.exp(-0.5)), None, ALU.mult)
                dve.drain()
                nc.vector.tensor_tensor_scan(t["w_in"][:, :], reset[:, :], t["lw"][:, :], 0.0, ALU.mult, ALU.add)
                dve.drain()
                TT(t["w_ex"][:, :], t["w_in"][:, :], t["lw"][:, :], ALU.subtract)
                dve.drain().then_inc(lw_done, 1)
                dve.wait_ge(n_mm, m + 1)
                TS(cut(t["sq"][:, :]), ps[:, 3, :, :], 64.0, 1e-24, ALU.mult, ALU.max)
                TS(t["tmp"][:, :], t["a"][:, :], -1.0, vec["rw_ka"][:, col], ALU.add, ALU.mult)
                dve.drain().then_inc(n_here, 1)
                STT(out=t["k"][:, :], in0=t["tmp"][:, :], scalar=1.0, in1=t["k"][:, :], op0=ALU.add, op1=ALU.mult)
                dve.drain()
                STT(out=t["tmp"][:, :], in0=t["r"][:, :], scalar=vec["rw_rk"][:, col], in1=t["k"][:, :], op0=ALU.mult, op1=ALU.mult)
                dve.drain().then_inc(bt, 1)
                dve.wait_ge(e_done, m + 1)
                dve.wait_ge(root, m + 1)
                nc.vector.reciprocal(t["sq"][:, :], t["sq"][:, :])
                if m >= 2:
                    dve.wait_ge(out_stored[m % 2], 16)
                TT(out[:, 0, :], t["r"][:, :], t["w_in"][:, :], ALU.mult)
                TT(out[:, 3, :], t["k"][:, :], t["rn"][:, :], ALU.mult)
                nc.vector.tensor_copy(out[:, 4, :], t["v"][:, :])
                nc.vector.tensor_copy(ew[:, :, m], t["w_in"][:, :].rearrange("p (n s) -> p n s", s=RW_C)[:, :, RW_C - 1])
                dve.drain()
                TT(t["kk"][:, :], t["kk"][:, :], t["sq"][:, :], ALU.mult)
                dve.drain()
                TT(out[:, 1, :], t["kk"][:, :], t["w_ex"][:, :], ALU.mult)
                TT(out[:, 2, :], t["kk"][:, :], t["a"][:, :], ALU.mult)
                dve.drain()
                TT(out[:, 2, :], out[:, 2, :], t["rn"][:, :], ALU.mult)
                dve.wait_ge(b_mm, m + 1)
                if m:
                    dve.wait_ge(bv_stored, 16 * m)
                STT(out=cut(t["bv"][:, :]), in0=ps[:, 3, :, :], scalar=64.0, in1=cut(t["v"][:, :]), op0=ALU.mult, op1=ALU.mult)
                dve.drain().then_inc(out_done, 1)


def rwkv_stage(core, rw, y, masks, level_masks, ident):
    nc = core.nc
    rw_x, rw_e = rw
    NV = len(RW_LEVELS)
    STEPS = RW_CH // 2
    sc_done, tr_done, lt_done, tok_done, off_done, off_used, x_mm, xp_copied, t_mm, t_done = (
        core.sem(f"rw_{s}") for s in ("scores", "turned", "masked", "tok_copied", "offs", "offs_used", "lt_mm",
                                      "lt_padded", "tlt_mm", "inverse"))
    cx, cxn, cu, cuc, cs, cy, y_out, s_done, tabs, zero, padded = (
        core.sem(f"rw_{s}") for s in ("chain_x", "chain_x_sb", "chain_u", "chain_u_sb", "chain_s", "chain_y", "y_out", "state", "tables", "zero", "padded"))
    here = [[core.sem(f"rw_here{b}{g}") for g in range(2)] for b in range(2)]
    with ExitStack() as mem:
        sb = lambda n, s: mem.enter_context(nc.sbuf_tensor(f"rw_{n}", s, F32))
        zp = sb("zp", [P, 2, 2, KINDS - 1, PAIRS, 2, RW_C])
        zc = sb("zc", [P, 2, 2, 3, PAIRS, RW_C])
        tokp = sb("tokp", [P, 2, 2, 3, PAIRS, 2, RW_C])
        vc = sb("vc", [P, 2, 2, PAIRS, RW_C])
        ltc = sb("ltc", [P, 2, 2, PAIRS, 2, RW_C])
        ltp = sb("ltp", [P, 2, 2, PAIRS, 2, 2, RW_C])
        ttp = sb("ttp", [P, 2, 2, PAIRS, 2, RW_C])
        tp, xp = sb("tp", [P, 2, PAIRS, 2, RW_C]), sb("xp", [P, 2, PAIRS, 2, RW_C])
        off = sb("off", [P, 2, 2, PAIRS, P])
        xn, uc, up = sb("xn", [P, PAIRS, RW_C]), sb("uc", [P, PAIRS, RW_C]), sb("up", [P, PAIRS, 2, RW_C])
        s, s_p = sb("s", [P, PAIRS, RW_C]), sb("s_p", [P, PAIRS, 2, RW_C])
        ew = sb("ew", [P, RW_CH, PAIRS])
        mk, lm = sb("mk", [P, 5, RW_C]), sb("lm", [P, NV, P])
        bank = [mem.enter_context(nc.psum_tensor(f"rw_ps{i}", [P, PAIRS, P], F32)) for i in range(8)]
        ps_sc = lambda p: bank[p // 2][:, 2 * (p % 2):2 * (p % 2) + 2, :]
        two = lambda x: x[:, :, :].rearrange("c a b -> c (a b)").rearrange("c (n p s) -> c n p s", n=2, p=PAIRS)
        ps_l, ps_bk, ps_c, ps_u, ps_y = two(bank[2]), two(bank[3]), two(bank[6]), two(bank[4])[:, 0], two(bank[7])[:, 0]
        ps_x, ps_t, ps_tt = (bank[3], bank[4]), (bank[0], bank[2]), (bank[1], bank[5])
        block = mem.enter_context(core.block())
        flat = lambda a: a.rearrange("c a s -> c (a s)")
        halves = [(a, slice(64 * a, 64 * a + 64)) for a in range(2)]

        def steps(eng, body):
            with eng.Fori(0, STEPS // 2 - 1) as ii:
                for b in range(2):
                    body(2 * ii + b, b, ii, True)
            for b in range(2):
                body(STEPS - 2 + b, b, STEPS // 2 - 1, b == 0)

        @block.sync
        def _(sp):
            for dst, src in ((ew[:, :, :], rw_e), (mk[:, :, :], masks), (lm[:, :, :], level_masks[:, 1:6, :])):
                sp.dma_start(dst, src).then_inc(tabs, 16)
            sp.wait_ge(zero, 1)

            def body(i, b, ii, more):
                for g in range(2):
                    sp.wait_ge(y_out, 2 * i + g + 1)
                    x = rw_x[:, :, :, bass.ds((2 * i + g) * RW_C, RW_C)]
                    sp.dma_start(zc[:, b, g, :, :, :], x[:, 0:3]).then_inc(here[b][g], 16)
                    for a, r in halves:
                        sp.dma_start(zp[r, b, g, :, :, a, :].rearrange("c k p s -> c (k p) s"),
                                     x[r, 1:].rearrange("c k p s -> c (k p) s")).then_inc(here[b][g], 16)

            steps(sp, body)

        @block.gpsimd
        def _(pool):
            nc.gpsimd.memset(zp[:, :, :, :, :, :, :], 0.0)
            pool.drain().then_inc(zero, 1)
            pool.wait_ge(tabs, 48)

            def body(i, b, ii, more):
                for l in range(NV):
                    for g in range(2):
                        if l == 0:
                            pool.wait_ge(lt_done, 2 * i + g + 2)
                        pool.wait_ge(off_used, 2 * NV * i + 2 * l + g + 1)
                        nc.gpsimd.tensor_tensor(off[:, g, l % 2, :, :], ltp[:, b, g, :, 0, :, :].rearrange("c p a s -> c p (a s)"),
                                                lm[:, NV - 1 - l:NV - l, :].broadcast_to([P, PAIRS, P]), ALU.mult).then_inc(off_done, 1)

            steps(pool, body)

        @block.tensor
        def _(pe):
            pe.sem_inc(off_used, 4)
            mm = nc.tensor.matmul

            def scores(i, b, ii, g, levels_done=None):
                pe.wait_ge(here[b][g], 48 * (ii + 1))
                pe.wait_ge(lt_done, 2 * i + g + 1)
                if levels_done is not None:
                    pe.wait_ge(t_done, levels_done)
                for p in range(PAIRS):
                    for n in range(2):
                        mm(ps_sc(p)[:, n, :], flat(zp[:, b, g, 1 + n, p, :, :]), zc[:, b, g, 0:2, p, :], start=True, stop=True)
                    mm(ps_l[:, 0, p, :], flat(zp[:, b, g, 0, p, :, :]), zc[:, b, g, 2, p, :], start=True, stop=True)
                    last = mm(ps_l[:, 1, p, :], flat(zp[:, b, g, 3, p, :, :]), mk[:, 4, :], start=True, stop=True)
                last.then_inc(sc_done, 1)

            def turns(i, b, g):
                pe.wait_ge(tok_done, 2 * i + g + 1)
                for p in range(PAIRS):
                    for n in range(2):
                        last = mm(ps_bk[:, n, p, :], flat(zp[:, b, g, 1 + n, p, :, :]), mk[:, 4, :], start=True, stop=True)
                last.then_inc(tr_done, 1)

            def chain(i, b, g, fill):
                c = 2 * i + g
                pe.wait_ge(s_done, c + 2)
                for p in range(PAIRS):
                    mm(ps_c[:, 0, p, :], flat(ltp[:, b, g, p, 1, :, :]), vc[:, b, g, p, :], start=True, stop=False)
                    last = mm(ps_c[:, 0, p, :], flat(zp[:, b, g, 0, p, :, :]), s[:, p, :], start=False, stop=True)
                last.then_inc(cx, 1)
                fill(0)
                pe.wait_ge(cxn, c + 1)
                for p in range(PAIRS):
                    last = mm(ps_c[:, 1, p, :], flat(ttp[:, b, g, p, :, :]), xn[:, p, :], start=True, stop=True)
                last.then_inc(cu, 1)
                fill(1)
                pe.wait_ge(cuc, c + 1)
                for p in range(PAIRS):
                    mm(ps_u[:, p, :], flat(tokp[:, b, g, 0, p, :, :]), uc[:, p, :], start=True, stop=False)
                    last = mm(ps_u[:, p, :], flat(tokp[:, b, g, 1, p, :, :]), vc[:, b, g, p, :], start=False, stop=True)
                last.then_inc(cs, 1)
                pe.wait_ge(y_out, c + 4)
                for p in range(PAIRS):
                    mm(ps_y[:, p, :], flat(s_p[:, p, :, :]), zc[:, b, g, 0, p, :], start=True, stop=False)
                    mm(ps_y[:, p, :], flat(up[:, p, :, :]), ltc[:, b, g, p, 0, :], start=False, stop=False)
                    last = mm(ps_y[:, p, :], flat(tokp[:, b, g, 2, p, :, :]), ltc[:, b, g, p, 1, :], start=False, stop=True)
                last.then_inc(cy, 1)

            def levels(i, b):
                for l in range(NV):
                    k = 2 * NV * i + 2 * l
                    for g in range(2):
                        pe.wait_ge(off_done, k + g + 1)
                        if l:
                            pe.wait_ge(t_done, k + g - 1)
                        for p in range(PAIRS):
                            last = mm(ps_x[g][:, p, :], off[:, g, l % 2, p, :], flat(tp[:, g, p, :, :]), start=True, stop=True)
                        last.then_inc(x_mm, 1)
                    for g in range(2):
                        pe.wait_ge(xp_copied, k + g + 1)
                        for p in range(PAIRS):
                            last = mm(ps_tt[g][:, p, :], flat(xp[:, g, p, :, :]), flat(ttp[:, b, g, p, :, :]), start=True, stop=True)
                        if l < NV - 1:
                            for p in range(PAIRS):
                                last = mm(ps_t[g][:, p, :], flat(ttp[:, b, g, p, :, :]), flat(xp[:, g, p, :, :]), start=True, stop=True)
                        last.then_inc(t_mm, 1)

            def body(i, b, ii, more):
                pe.wait_ge(s_done, 2 * i + 2)
                pe.wait_ge(lt_done, 2 * i + 3)
                pe.wait_ge(tok_done, 2 * i + 3)
                levels(i, b)
                after = ii + b
                for g in range(2):
                    pe.wait_ge(t_done, 2 * NV * (i + 1) - 1 + g)

                    def fill(n):
                        if more and n == 0:
                            scores(i + 1, 1 - b, after, g, 2 * NV * (i + 1))
                        if more and n == 1:
                            turns(i + 1, 1 - b, g)

                    chain(i, b, g, fill)

            pe.wait_ge(tabs, 48)
            for g in range(2):
                scores(0, 0, 0, g)
                turns(0, 0, g)
            steps(pe, body)

        @block.scalar
        def _(act):
            act.sem_inc(y_out, 4)
            act.sem_inc(tok_done, 1)

            def turned(i, b, g):
                act.wait_ge(lt_done, 2 * i + g + 2)
                act.wait_ge(tr_done, 2 * i + g + 1)
                for a, r in halves:
                    nc.scalar.activation(tokp[r, b, g, 0:2, :, a, :], ps_bk[r, :, :, :], ACT.Copy)
                    nc.scalar.activation(tokp[r, b, g, 2, :, a, :], vc[r, b, g, :, :], ACT.Copy)
                act.drain().then_inc(tok_done, 1)

            def body(i, b, ii, more):
                for l in range(NV):
                    for g in range(2):
                        act.wait_ge(x_mm, 2 * NV * i + 2 * l + g + 1)
                        nc.scalar.activation(xp[:, g, :, :, :].rearrange("c p a s -> c p (a s)"), ps_x[g][:, :, :], ACT.Copy).then_inc(xp_copied, 1)
                for g in range(2):
                    c = 2 * i + g
                    act.wait_ge(cx, c + 1)
                    nc.scalar.activation(xn[:, :, :], ps_c[:, 0, :, :], ACT.Copy, scale=-1.0).then_inc(cxn, 1)
                    act.wait_ge(s_done, c + 2)
                    for a, r in halves:
                        nc.scalar.activation(s_p[r, :, a, :], s[r, :, :], ACT.Copy)
                    act.wait_ge(cu, c + 1)
                    nc.scalar.activation(uc[:, :, :], ps_c[:, 1, :, :], ACT.Copy)
                    for a, r in halves:
                        nc.scalar.activation(up[r, :, a, :], ps_c[r, 1, :, :], ACT.Copy)
                    act.drain().then_inc(cuc, 1)
                    if more:
                        turned(i + 1, 1 - b, g)
                    act.wait_ge(cy, c + 1)
                    nc.scalar.activation(y[:, :, bass.ds(c * RW_C, RW_C)], ps_y, ACT.Copy).then_inc(y_out, 1)

            act.wait_ge(padded, 1)
            for g in range(2):
                turned(0, 0, g)
            steps(act, body)

        @block.vector
        def _(dve):
            for pad in (tokp[:, :, :, :, :, :, :], up[:, :, :, :], s_p[:, :, :, :]):
                nc.vector.memset(pad, 0.0)
            dve.drain().then_inc(padded, 1)
            for pad in (ltp[:, :, :, :, :, :, :], tp[:, :, :, :, :], ttp[:, :, :, :, :, :]):
                nc.vector.memset(pad, 0.0)
            nc.vector.memset(s[:, :, :], 0.0)
            dve.drain().then_inc(s_done, 2)
            dve.sem_inc(lt_done, 1)
            dve.wait_ge(tabs, 48)
            TT = nc.vector.tensor_tensor

            def masked(i, b, g):
                dve.wait_ge(sc_done, 2 * i + g + 1)
                for a, r in halves:
                    for h in range(2):
                        ps = bank[h][r, :, :].rearrange("c (q n) (k s) -> c q n k s", n=2, k=2)
                        TT(ltp[r, b, g, 2 * h:2 * h + 2, :, a, :], ps[:, :, :, 1, :], mk[r, 1:2, :].unsqueeze(1).broadcast_to([64, 2, 2, RW_C]), ALU.mult)
                        TT(ttp[r, b, g, 2 * h:2 * h + 2, a, :], ps[:, :, 0, 1, :], mk[r, 3:4, :].broadcast_to([64, 2, RW_C]), ALU.mult)
                    TT(tp[r, g, :, a, :], ps_l[r, 0, :, :], mk[r, 2:3, :].broadcast_to([64, PAIRS, RW_C]), ALU.mult)
                nc.vector.tensor_copy(vc[:, b, g, :, :], ps_l[:, 1, :, :])
                for h in range(2):
                    ps = bank[h][:, :, :].rearrange("c (q n) (k s) -> c q n k s", n=2, k=2)
                    TT(ltc[:, b, g, 2 * h:2 * h + 2, :, :], ps[:, :, :, 0, :], mk[:, 0:1, :].unsqueeze(1).broadcast_to([P, 2, 2, RW_C]), ALU.mult)
                dve.drain()
                for t in (tp[:, g, :, :, :], ttp[:, b, g, :, :, :]):
                    t = t.rearrange("c p a s -> c p (a s)")
                    TT(t, t, ident[:, :].unsqueeze(1).broadcast_to([P, PAIRS, P]), ALU.add)
                dve.drain().then_inc(lt_done, 1)

            def body(i, b, ii, more):
                for l in range(NV):
                    k = 2 * NV * i + 2 * l
                    for g in range(2):
                        dve.wait_ge(t_mm, k + g + 1)
                        dve.sem_inc(off_used, 1)
                        t = ttp[:, b, g, :, :, :].rearrange("c p a s -> c p (a s)")
                        TT(t, t, ps_tt[g][:, :, :], ALU.subtract)
                        if l < NV - 1:
                            t = tp[:, g, :, :, :].rearrange("c p a s -> c p (a s)")
                            TT(t, t, ps_t[g][:, :, :], ALU.subtract)
                        dve.drain().then_inc(t_done, 1)
                for g in range(2):
                    c = 2 * i + g
                    if more:
                        masked(i + 1, 1 - b, g)
                    dve.wait_ge(cs, c + 1)
                    dve.wait_ge(cuc, c + 1)
                    TT(s[:, :, :], s[:, :, :], ps_u, ALU.add)
                    dve.drain()
                    TT(s[:, :, :], s[:, :, :], ew[:, bass.ds(c, 1), :].rearrange("c o p -> c (o p)").unsqueeze(2).broadcast_to([P, PAIRS, RW_C]), ALU.mult)
                    dve.drain().then_inc(s_done, 1)

            for g in range(2):
                masked(0, 0, g)
            steps(dve, body)


def finish_stage(core, late, y):
    nc = core.nc
    here, used = [core.sem(f"fin_here{b}") for b in range(2)], core.sem("fin_used")
    with ExitStack() as mem:
        x = mem.enter_context(nc.sbuf_tensor("fin_x", [P, 2, 2, SEQ], F32))
        block = mem.enter_context(core.block())

        @block.sync
        def _(sp):
            for m in range(4):
                if m >= 2:
                    sp.wait_ge(used, m - 1)
                for i in range(2):
                    sp.dma_start(x[:, m % 2, i, :], late[4 * i + m]).then_inc(here[m % 2], 16)

        @block.vector
        def _(dve):
            for m in range(4):
                dve.wait_ge(here[m % 2], 32 * (m // 2 + 1))
                nc.vector.tensor_tensor(y[:, m, :], y[:, m, :], x[:, m % 2, 1, :], ALU.add)
                dve.drain()
                nc.vector.tensor_tensor(y[:, m, :], y[:, m, :], x[:, m % 2, 0, :], ALU.mult)
                dve.drain().then_inc(used, 1)


def block_three(core, A, x_t, mats, vec, dram, stop):
    nc = core.nc
    ident = mats["ident"]
    z3, v_tok, qk = dram("z3", (30, P, SEQ)), dram("v_tok3", (SEQ, 512)), dram("qk3", (8, P, SEQ))
    rw = dram("rw_x", (P, KINDS, PAIRS, SEQ)), dram("rw_e", (P, RW_CH, PAIRS))
    late = dram("rw_late", (8, P, SEQ))
    T = slice(META, META + SEQ)
    row = lambda d, u: (lambda j: d[bass.ds(2 * j + u, 1)].rearrange("o p s -> p (o s)"))
    with ExitStack() as mem:
        h = split_buffers(core, mem, "h3")
        rms = mem.enter_context(nc.sbuf_tensor("rms3_all", [P, SEQ], F32))
        rms_split_stage(core, "rms3", x_t, h, rms, vec["norm_mix"], 1e-6, META, SEQ)
        gemm_stage(core, "in3", [(A["w_in3"], of(h, 0, META), lambda j: 2 * j), (A["w_in3"], of(h, 0, META), lambda j: 2 * j + 1)],
                   15, SEQ, None, normed_out(nc, rms), rms=rms, out=[row(z3, 0), row(z3, 1)])
    with ExitStack() as mem:
        y = mem.enter_context(nc.sbuf_tensor("y3", [P, KT, SEQ], F32))[:, :, :]
        ret, rwy = y[:, 0:4, :], y[:, 4:8, :]
        rope_stage(core, "rope3", z3, qk, A["ret_tables"], mats["rot2"], 8, 0, SEQ)
        turn_stage(core, "turn3", lambda j: z3[8:12, :, bass.ds(P * j, P)].rearrange("t c s -> c t s"),
                   lambda j: v_tok[bass.ds(P * j, P), :], 4, SEQ // P, ident)
        retention_stage(core, qk, v_tok, ret, A["ret_decay"], A["ret_start"], A["ret_end"], chunk_decays(), ident)
        packed_norm_stage(core, "ret_norm", ret, A["packs128"], mats["mean128"], 1e-5, vec["ret_norm"])
        gate_stage(core, "gate3", lambda i: z3[12 + i], ret, 4, ACT.Silu)
        if stop == "yret": return ret
        rwkv_prep_stage(core, z3, mats, vec, A["rw_w2a2"], A["rw_g2"], rw, late)
        rwkv_stage(core, rw, rwy, A["rw_masks"], A["level_masks"], ident)
        packed_norm_stage(core, "rw_norm", rwy, A["packs64"], mats["mean64"], 64e-5, vec["rw_ln_w"], vec["rw_ln_b"])
        finish_stage(core, late, rwy)
        if stop == "yrw": return rwy
        ys = split_buffers(core, mem, "y3s", KT, SEQ)
        split_stage(core, "split3", y, ys)
        gemm_stage(core, "out3", [(A["w_o3"], of(ys), lambda j: 2 * j), (A["w_o3"], of(ys), lambda j: 2 * j + 1)],
                   4, SEQ, None, add_part(nc, x_t, META, SEQ))
    if stop == "x3a": return x_t[:, :, T]
    with ExitStack() as mem:
        h = split_buffers(core, mem, "h3f", KT, COLS)
        rms = mem.enter_context(nc.sbuf_tensor("rms3b_all", [P, SEQ], F32))
        rms_split_stage(core, "rms3b", x_t, h, rms, vec["norm_ffn"], 1e-6, META, SEQ)
        for part, (first, tiles) in enumerate(FF_PARTS):
            with ExitStack() as inner:
                g = split_buffers(core, inner, f"ff3_{part}", tiles, SEQ)
                gated_ff_stage(core, f"up3_{part}", A["w_gate3"], A["w_up3"], h, g, first, tiles, rms)
                w = A[f"w_down3_{part}"]
                gemm_stage(core, f"down3_{part}", [(w, of(g), lambda j: 2 * j), (w, of(g), lambda j: 2 * j + 1)],
                           4, SEQ, None, add_part(nc, x_t, META, SEQ))
    with ExitStack() as mem:
        h = split_buffers(core, mem, "h3p", KT, COLS)
        rms = mem.enter_context(nc.sbuf_tensor("rms3c_all", [P, SEQ], F32))
        rms_split_stage(core, "rms3c", x_t, h, rms, vec["norm_ple"], 1e-6, META, SEQ)
        p_t = mem.enter_context(nc.sbuf_tensor("b3_p", [P, 2, SEQ], F32))
        ps_ = split_buffers(core, mem, "p3s", 2, SEQ)
        load_stage(core, "p", [(p_t[:, :, :], A["p3"].rearrange("(k p) s -> p k s", p=P))])
        split_stage(core, "split_p", p_t[:, :, :], ps_)

        def act_ple(act, u, j, ps, t):
            nc.scalar.activation(t["gate"][:, :], t["gate"][:, :], ACT.Sigmoid)

        def dve_ple(dve, u, j, ps, t):
            gate = t["view"](t["gate"][:, :])
            if u == 0:
                nc.vector.tensor_tensor(gate, ps, t["view"](rms[:, :]), ALU.mult)
            else:
                x_row = x_t[:, bass.ds(j, 1), T].rearrange("p o s -> p (o s)")
                nc.vector.tensor_tensor(gate, ps, gate, ALU.mult)
                dve.drain()
                nc.vector.tensor_tensor(x_row, x_row, t["gate"][:, :], ALU.add)

        gemm_stage(core, "ple", [(A["w_ple_gate"], of(h, 0, META), lambda j: j), (A["w_ple_up"], of(ps_), lambda j: j)],
                   8, SEQ, act_ple, dve_ple, temps=[("gate", SEQ)], chained=True, rms=rms)
    rms_stage(core, "rms3f", x_t, vec["final_norm3"], 1e-6, META, SEQ)


def gated_ff_stage(core, name, w_gate, w_up, h, g, first, tiles, rms):
    nc = core.nc

    def act_ff(act, u, j, ps, t):
        nc.scalar.activation(t["gate"][:, :], t["gate"][:, :], ACT.Silu)

    def dve_ff(dve, u, j, ps, t):
        inverse, gate = t["view"](rms[:, :]), t["view"](t["gate"][:, :])
        if u == 0:
            nc.vector.tensor_tensor(gate, ps, inverse, ALU.mult)
        else:
            nc.vector.tensor_tensor(gate, ps, gate, ALU.mult)
            dve.drain()
            nc.vector.tensor_tensor(gate, gate, inverse, ALU.mult)
            dve.drain()
            split_row(dve, nc, t["gate"][:, :], g, j)

    gemm_stage(core, name, [(w_gate, of(h, 0, META), lambda j: j + first), (w_up, of(h, 0, META), lambda j: j + first)],
               tiles, SEQ, act_ff, dve_ff, temps=[("gate", SEQ)], chained=True, rms=rms if first == 0 else None)


def log_gammas():
    return np.log(np.float32(1.0) - np.float32(2.0) ** (-5.0 - np.arange(RET_H, dtype=np.float32))).astype(np.float64)


def chunk_decays():
    return [float(np.exp(g * RET_C)) for g in log_gammas()]


def retention_tables():
    ang = (np.float32(1.0) / (np.float32(10000.0) ** np.linspace(0.0, 1.0, RET_D // 2, dtype=np.float32))).astype(np.float32)
    phase = np.arange(SEQ, dtype=np.float32)[None] * np.repeat(ang, 2)[:, None]
    tables = np.stack([np.cos(phase), np.sin(phase)], axis=1).astype(np.float32)
    g = log_gammas()
    j, i = np.arange(P)[:, None, None], np.arange(P)[None, None]
    scale = RET_D ** -0.5
    decay = np.where(i >= j, np.exp(g[None, :, None] * np.maximum(i - j, 0)), 0.0) * scale
    start = np.broadcast_to(np.exp(g[None, :, None] * (i + 1.0)), (P, RET_H, P))
    end = np.exp(g[None] * (P - 1 - np.arange(P)[:, None])) * scale
    return tables, decay.astype(np.float32), np.ascontiguousarray(start.astype(np.float32)), end.astype(np.float32)


def rwkv_masks():
    s, t = np.arange(P)[:, None] % RW_C, np.arange(RW_C)[None]
    strict, incl = (s < t).astype(np.float32), (s <= t).astype(np.float32)
    one, up = ((s // 2 == t // 2) & (s > t)).astype(np.float32), ((s // 2 == t // 2) & (s < t)).astype(np.float32)
    return np.ascontiguousarray(np.stack([incl, strict, -one, -up, (s == t).astype(np.float32)], axis=1))


def start_stage(core, loads):
    nc = core.nc
    here = core.sem("start_here")
    with core.block() as block:
        @block.sync
        def _(sp):
            for dst, src in loads:
                sp.dma_start(dst, src).then_inc(here, 16)
            sp.wait_ge(here, 16 * len(loads))

        @block.vector
        def _(dve):
            for value, tile in core.eps.items():
                nc.vector.memset(tile, value)


def normed_out(nc, inverse, bias=None):
    def part(dve, u, j, ps, t):
        o = t["view"](t["out"][:, u, :])
        nc.vector.tensor_tensor(o, ps, t["view"](inverse[:, :]), ALU.mult)
        if bias is not None:
            dve.drain()
            nc.vector.tensor_scalar(o, o, bias[:, bass.ds(2 * j + u, 1)], None, ALU.add)
    return part


def add_part(nc, x_t, c0, total):
    def part(dve, u, j, ps, t):
        row = t["view"](x_t[:, bass.ds(2 * j + u, 1), c0:c0 + total].rearrange("p o s -> p (o s)"))
        nc.vector.tensor_tensor(row, ps, row, ALU.add)
    return part


def split_buffers(core, mem, name, tiles=KT, cols=COLS):
    return [mem.enter_context(core.nc.sbuf_tensor(f"{name}_{part}", [P, tiles, cols], F32R)) for part in ("high", "low")]


def of(pair, first=0, at=0):
    return lambda k, c, w: [x[:, first + k, at + c:at + c + w] for x in pair]


def block_one(core, A, x_t, mats, vec, dram, stop):
    nc = core.nc
    T = slice(META, META + SEQ)
    x_main = x_t[:, :, T]
    z1, v_tok, ya_tok, ya = dram("z1", (24, P, SEQ)), dram("v_tok", (SEQ, 256)), dram("ya_tok", (SEQ, 256)), dram("ya", (2, P, SEQ))
    ident = mats["ident"]
    load_stage(core, "x", [(x_main, A["x"].rearrange("(k p) s -> p k s", p=P))])
    with ExitStack() as mem:
        h = split_buffers(core, mem, "h1")
        rms = mem.enter_context(nc.sbuf_tensor("rms1_all", [P, SEQ], F32))
        rms_split_stage(core, "rms1", x_t, h, rms, vec["norm_g"], 1e-6, META, SEQ)
        gemm_stage(core, "in1", [(A["w_in"], of(h, 0, META), lambda j: 2 * j), (A["w_in"], of(h, 0, META), lambda j: 2 * j + 1)],
                   12, SEQ, None, normed_out(nc, rms), rms=rms,
                   out=[lambda j: z1[bass.ds(2 * j, 1)].rearrange("o p s -> p (o s)"),
                        lambda j: z1[bass.ds(2 * j + 1, 1)].rearrange("o p s -> p (o s)")])
    if stop == "z1": return z1
    turn_stage(core, "turn_v", lambda j: z1[4:6, :, bass.ds(P * j, P)].rearrange("t c s -> c t s"),
               lambda j: v_tok[bass.ds(P * j, P), :], 2, SEQ // P, ident)
    na_stage(core, z1, v_tok, A["na_bias"], ya_tok, ident)
    turn_stage(core, "turn_y", lambda j: ya_tok[bass.ds(P * j, P), :].rearrange("s (t c) -> s t c", t=2),
               lambda j: ya[:, :, bass.ds(P * j, P)].rearrange("t c s -> c t s"), 2, SEQ // P, ident)
    if stop == "ya": return ya
    with ExitStack() as outer:
        y = outer.enter_context(nc.sbuf_tensor("y1", [P, KT, SEQ], F32))[:, :, :]
        with ExitStack() as mem:
            sb = lambda n, s: mem.enter_context(nc.sbuf_tensor(f"b1_{n}", s, F32))
            v, u = sb("v", [P, 2, SEQ]), sb("u", [P, 2, SEQ])
            taps, pw, pool_w, ws, bs = sb("taps", [P, 2, CONV_W]), sb("pw", [P, 2, 2 * P]), sb("pool_w", [P, 2, 64]), sb("ws", [P, 4, P]), sb("bs", [P, 2, P])
            load_stage(core, "w1", [(taps[:, :, :], A["conv_w"]), (pw[:, :, :], A["conv_pw"]), (pool_w[:, :, :], A["pool_w"]),
                                    (ws[:, :, :], A["sgu_w"]), (bs[:, :, :], A["sgu_b"]),
                                    (y[:, 0:2, :], ya.rearrange("t c s -> c t s"))])
            conv_stage(core, z1, v, taps, vec["dw_b"])
            norm_stage(core, "ln_b", v, [[0, 1]], mats["mean256"], 1e-5, True, vec["conv_g"], vec["conv_b"], ACT.Silu)
            full = slice(0, P)
            product_stage(core, "pw", y[:, 2:4, :],
                          [[(pw[:, k, m * P:(m + 1) * P], full, full, k, k == 0, k == 1) for k in range(2)] for m in range(2)], v)
            pool_stage(core, z1, v, A["inv_count"])
            halves = [slice(0, 64), slice(64, 128)]
            product_stage(core, "pool_w", y[:, 4:6, :],
                          [[(pool_w[r, k, :], r, r, k, True, True) for r in halves] for k in range(2)], v, vec["pool_scale"])
            load_stage(core, "sgu", [(u[:, :, :], z1[12:14].rearrange("t c s -> c t s")),
                                     (v[:, :, :], z1[14:16].rearrange("t c s -> c t s"))], ACT.Gelu_apprx_tanh)
            norm_stage(core, "ln_d", v, [[0, 1]], mats["mean256"], 1e-5, True, vec["sgu_g"], vec["sgu_bb"], ACT.Identity)
            mix_stage(core, v, u, y[:, 6:8, :], ws, bs, ident)
        ys = split_buffers(core, outer, "y1s", KT, SEQ)
        gate_stage(core, "gate1", lambda i: z1[16 + i], y, 8, ACT.Silu, ys)
        gemm_stage(core, "out1", [(A["w_out"], of(ys), lambda j: 2 * j), (A["w_out"], of(ys), lambda j: 2 * j + 1)],
                   4, SEQ, None, add_part(nc, x_t, META, SEQ))
    rms_stage(core, "rms1f", x_t, vec["final_g"], 1e-6, META, SEQ)


def program(nc, A, out, stop=None):
    with ExitStack() as ctx:
        core = Core(nc)
        sb = lambda n, s: ctx.enter_context(nc.sbuf_tensor(n, s, F32))
        dram = lambda n, s: nc.dram_tensor(f"scratch_{n}", s, F32, kind="Internal").ap()
        x_t = sb("x_t", [P, KT, COLS])
        mat = sb("mats", [P, len(MATS), P])
        vecs = sb("vecs", [P, A["vecs"].shape[1]])
        core.eps = {e: sb(f"eps{i}", [P, 1])[:, :] for i, e in enumerate(EPSILONS)}
        mats = {name: mat[:, i, :] for i, name in enumerate(MATS)}
        vec, at = {}, 0
        for name, _, count in VEC_LIST:
            vec[name] = vecs[:, at:at + count]
            at += count
        start_stage(core, [(mat[:, :, :], A["mats"]), (vecs[:, :], A["vecs"])])
        res = block_one(core, A, x_t, mats, vec, dram, stop)
        if res is None and stop != "b1":
            res = block_two(core, A, x_t, mats, vec, dram, stop)
        if res is None and stop not in ("b1", "b2"):
            res = block_three(core, A, x_t, mats, vec, dram, stop)
        done = core.sem("out_done")
        with core.block() as block:
            @block.sync
            def _(sp):
                if res is not None:
                    sp.dma_start(out, res).then_inc(done, 16)
                else:
                    sp.dma_start(out.rearrange("(k p) s -> p k s", p=P), x_t[:, :, META:META + SEQ]).then_inc(done, 16)
                sp.wait_ge(done, 16)


EPSILONS = (1e-6, 1e-5, 64e-5)
MATS = ("ident", "mean256", "mean128", "mean64", "rope", "rot2", "causal")
VEC_LIST = [("norm_g", "norm_g", 8), ("dw_b", "conv_dw_b", 2), ("conv_g", "conv_ln_g", 2), ("conv_b", "conv_ln_b", 2),
            ("pool_scale", "pool_scale", 2), ("sgu_g", "sgu_ln_g", 2), ("sgu_bb", "sgu_ln_b", 2), ("final_g", "final_g", 8),
            ("mix_norm", "mix_norm_2", 8), ("b_in", "b_in_2", 34), ("b_alpha", "b_alpha_2", 2), ("gla_norm", "gla_head_norm_2", 4),
            ("ffn_norm", "ffn_norm_2", 8), ("ff_conv", "conv_w_2", 66), ("ff_conv_b", "conv_b_2", 22), ("final_norm2", "final_norm_2", 8),
            ("norm_mix", "norm_mix_w_3", 8), ("ret_norm", "ret_norm_w_3", 4), ("rw_mu", "rw_mu_3", 14), ("rw_w0", "rw_w0_3", 4),
            ("rw_a0", "rw_a0_3", 4), ("rw_kk", "rw_k_k_3", 4), ("rw_ka", "rw_k_a_3", 4), ("rw_rk", "rw_r_k_3", 4),
            ("rw_ln_w", "rw_ln_w_3", 4), ("rw_ln_b", "rw_ln_b_3", 4), ("norm_ffn", "norm_ffn_w_3", 8), ("norm_ple", "norm_ple_w_3", 8),
            ("final_norm3", "final_norm_w_3", 8)]


def tiles(w):
    k, n = w.shape
    return np.ascontiguousarray(w.reshape(k // P, P, n // P, P).transpose(2, 1, 0, 3).reshape(n // P, P, k))


def columns(v):
    return v.reshape(-1, P).T


def constants():
    i = np.arange(P)
    eye = np.eye(P, dtype=np.float32)
    rope = np.zeros((P, P), np.float32)
    for d in range(P):
        o = d % 64
        if o < 32:
            rope[d + 32, d] = -1
        else:
            rope[d - 32, d] = 1
    rot2 = np.zeros((P, P), np.float32)
    rot2[i[1::2], i[0::2]] = -1
    rot2[i[0::2], i[1::2]] = 1
    m = {"ident": eye, "mean256": np.full((P, P), 1 / 256, np.float32), "mean128": np.full((P, P), 1 / 128, np.float32),
         "mean64": ((i[:, None] // 64 == i[None] // 64) / 64).astype(np.float32), "rope": rope, "rot2": rot2,
         "causal": (i[:, None] <= i[None]).astype(np.float32)}
    return np.ascontiguousarray(np.stack([m[k] for k in MATS], axis=1))


def norm_packs(size):
    out = np.zeros((P, 8, P), np.float32)
    c = np.arange(P)
    for k in range(4):
        out[c, k, 32 * k + c // size] = 1 / size
        out[32 * k + c // size, 4 + k, c] = 1
    return out


def window_counts():
    t = np.arange(SEQ)
    out = np.zeros((P, 2, SEQ), np.float32)
    for g, w in enumerate((2, 4, 8, 16)):
        n = np.clip(t - w // 2 + w, 0, SEQ) - np.clip(t - w // 2, 0, SEQ)
        out[64 * (g % 2):64 * (g % 2) + 64, g // 2] = 1.0 / n.astype(np.float32)
    return out


def layout(i):
    c = np.ascontiguousarray
    A = {"x": c(i["x"][0].T), "w_in": tiles(i["w_in"][0]), "w_out": tiles(i["w_out"][0])}
    q, k = np.arange(GRID_W)[:, None], np.arange(GRID_W)[None]
    start = np.clip(q - NA_COLS // 2, 0, GRID_W - NA_COLS)
    ok = (k >= start) & (k < start + NA_COLS)
    rel = np.clip(k - q, 1 - NA_COLS, NA_COLS - 1) + NA_COLS - 1
    bias = i["na_rpb"][0][:, :, rel]
    bias = np.where(ok[None, None], bias, np.float32(NEG)).transpose(0, 2, 1, 3)
    A["na_bias"] = c(bias.reshape(4, 2, GRID_W, 15 * GRID_W).transpose(1, 2, 0, 3).reshape(P, 4, 15 * GRID_W))
    A["conv_w"] = c(i["conv_dw_w"][0].reshape(CONV_W, 2, P).transpose(2, 1, 0))
    A["conv_pw"] = c(i["conv_pw"][0].reshape(2, P, 256).transpose(1, 0, 2))
    A["pool_w"] = c(i["pool_w"][0].reshape(2, 2, 64, 64).transpose(1, 2, 0, 3).reshape(P, 2, 64))
    A["inv_count"] = window_counts()
    A["sgu_w"] = c(i["sgu_w"][0].transpose(2, 0, 1))
    A["sgu_b"] = c(np.repeat(i["sgu_b"][0].reshape(2, 2, P).transpose(1, 0, 2), 64, axis=0))
    A["mats"] = constants()
    A["packs128"], A["packs64"] = norm_packs(128), norm_packs(64)
    i = dict(i)
    cols = order_two()
    A["meta"] = c(i["meta_tokens_2"].T.reshape(KT, P, META).transpose(1, 0, 2))
    A["w_in2"] = tiles(c(i["w_in_2"][0][:, cols]))
    low = slice(2304, 2320)
    A["w_low"] = c(i["w_in_2"][0][:, low].reshape(KT, P, 16).transpose(1, 0, 2))
    A["b_low"] = c(i["b_in_2"][0][low].reshape(16, 1))
    A["w_alpha"] = c(i["w_alpha_2"][0])
    i["b_in_2"] = i["b_in_2"][0][cols]
    i["gla_head_norm_2"] = np.tile(i["gla_head_norm_2"].reshape(-1), 4)
    A["level_masks"], A["swa_masks"], A["rope_tables"] = level_masks(), swa_masks(), rope_tables()
    A["sinks"] = c(i["attn_sinks_2"][0])
    A["w_att"], A["w_gla"], A["w_out2"] = (tiles(i[n][0]) for n in ("w_proj_attn_2", "w_proj_gla_2", "w_out_2"))
    A["w_up2"] = tiles(i["w_up_2"][0])
    for part, (first, count) in enumerate(FF_PARTS):
        rows = slice(first * P, (first + count) * P)
        A[f"w_down2_{part}"], A[f"w_down3_{part}"] = tiles(i["w_down_2"][0][rows]), tiles(i["w_down_3"][0][rows])
    A["ret_tables"], A["ret_decay"], A["ret_start"], A["ret_end"] = retention_tables()
    A["rw_masks"] = rwkv_masks()
    A["p3"] = c(i["p_3"][0, 0].T)
    A["rw_w2a2"] = c(np.concatenate([i["rw_w2_3"][0], i["rw_a2_3"][0]], axis=0))
    A["rw_g2"] = c(i["rw_g2_3"][0])
    for name, src in (("w_in3", "w_in_3"), ("w_o3", "w_o_3"), ("w_gate3", "w_gate_3"), ("w_up3", "w_up_3"), 
                      ("w_ple_gate", "w_ple_gate_3"), ("w_ple_up", "w_ple_up_3")):
        A[name] = tiles(i[src][0])
    A["vecs"] = c(np.concatenate([columns(np.asarray(i[src]).reshape(-1)) for _, src, _ in VEC_LIST], axis=1))
    return A


def order_two():
    r = lambda a, n: list(range(a, a + n))
    return r(0, 512) + r(512, 128) + r(768, 256) + r(1024, 256) + r(640, 128) + r(1280, 512) + r(1792, 512) + r(2320, 2048)


def level_masks():
    i, j = np.arange(P)[None], np.arange(P)[:, None]
    m = [(i // (2 * s) == j // (2 * s)) & (j % (2 * s) < s) & (i % (2 * s) >= s) for s in LEVELS] + [i == j]
    return np.ascontiguousarray(np.stack(m, axis=1).astype(np.float32))


def swa_masks():
    q, k = np.arange(P)[:, None], np.arange(2 * P)[None]
    rel = q + P - k
    out = []
    for i in range(BLOCKS):
        pos = i * P + k - LEAD
        out.append(np.where((rel >= 0) & (rel < P) & (pos >= 0), 0.0, NEG))
    return np.stack(out).astype(np.float32)


def rope_tables():
    half = HEAD // 2
    inv = (np.float32(10000.0) ** (-np.arange(half, dtype=np.float32) / np.float32(half))).astype(np.float32)
    ang = np.arange(COLS, dtype=np.float32)[None] * inv[np.arange(P) % half][:, None]
    return np.ascontiguousarray(np.stack([np.cos(ang), np.sin(ang)], axis=1).astype(np.float32))


def kernel(**inputs):
    import concourse.bacc as bacc
    from concourse.bass_utils import run_bass_kernel_spmd

    arrays = layout({k: np.asarray(v) for k, v in inputs.items()})
    nc = bacc.Bacc("TRN2", target_bir_lowering=False, num_devices=1)
    A = {n: nc.dram_tensor(f"in_{n}", a.shape, F32, kind="ExternalInput").ap() for n, a in arrays.items()}
    out = nc.dram_tensor("out", (D, SEQ), F32, kind="ExternalOutput").ap()
    program(nc, A, out)
    r = run_bass_kernel_spmd(nc, [{f"in_{n}": a for n, a in arrays.items()}], core_ids=[0])
    return np.ascontiguousarray(r.results[0]["out"].T).reshape(1, SEQ, D)
```
